# Optimizing a Trainium2 kernel written in Bass

```python
import math
import jax
import jax.numpy as jnp
from jax import lax
import numpy as np

D_MODEL = 1024
BATCH = 1
SEQ = 1024
DEPTH = 1
DEC_BATCH = 8
DEC_SEQ = 1
PAST_LEN = 8192
PAGE_SIZE = 128

HEAD_DIM = 64
D_MIX = D_MODEL
SSD_HEADS = 8
SSD_D = SSD_HEADS * HEAD_DIM
SSD_GROUPS = 2
SSD_HEADS_PER_GROUP = SSD_HEADS // SSD_GROUPS
SSD_STATE = 128
SSD_CONV = 4
SSD_CONV_CH = SSD_D + 2 * SSD_GROUPS * SSD_STATE
SSD_CHUNK = 128
NSA_HEADS = 8
NSA_KV_HEADS = 2
NSA_GQA = NSA_HEADS // NSA_KV_HEADS
NSA_D = NSA_HEADS * HEAD_DIM
KV_D = NSA_KV_HEADS * HEAD_DIM
CMP_BLOCK = 64
CMP_HIDDEN = 128
SEL_BLOCK = 64
TOP_N = 16
WINDOW = 512
Q_BLOCK = 128
ROT_DIM = HEAD_DIM // 4
ROPE_THETA = 500000.0
N_EXPERTS = 64
TOP_K = 6
N_EXPERT_GROUPS = 8
TOPK_GROUPS = 4
D_EXPERT = 256
D_SHARED = 256
ROUTED_SCALE = 2.5
MOE_BLOCK = 128
DEEPNORM_ALPHA = (2.0 * DEPTH) ** 0.25
DEEPNORM_BETA = (8.0 * DEPTH) ** -0.25
LN_EPS = 1e-5
RMS_EPS = 1e-5
NEG = -1e30
FORCED_SCORE = 1e4
IN_SIZES = (SSD_D, SSD_CONV_CH, SSD_HEADS, NSA_D, KV_D, KV_D, KV_D, KV_D, KV_D, KV_D, 3 * NSA_HEADS)
D_IN = sum(IN_SIZES)

kernel_name = 'hymba_ssd_nsa_moe_deepnorm_step'

def layer_norm(x, g, b):
    xf = x.astype(jnp.float32)
    mu = jnp.mean(xf, -1, keepdims=True)
    var = jnp.mean(jnp.square(xf - mu), -1, keepdims=True)
    return ((xf - mu) * lax.rsqrt(var + LN_EPS) * g + b).astype(x.dtype)

def in_proj_split(h, w):
    u = jnp.einsum('btd,df->btf', h, w)
    return jnp.split(u, np.cumsum(IN_SIZES)[:-1].tolist(), axis=-1)

def to_heads(a, n):
    return a.reshape(a.shape[0], a.shape[1], n, HEAD_DIM)

def group_heads(q):
    return q.reshape(q.shape[0], q.shape[1], NSA_KV_HEADS, NSA_GQA, HEAD_DIM)

def partial_rope(x, pos):
    half = ROT_DIM // 2
    inv = ROPE_THETA ** (-jnp.arange(half, dtype=jnp.float32) / half)
    ang = pos.astype(jnp.float32)[:, None] * inv
    cos = jnp.cos(ang)[:, None, :]
    sin = jnp.sin(ang)[:, None, :]
    xr = x[..., :ROT_DIM].astype(jnp.float32)
    x1, x2 = xr[..., :half], xr[..., half:]
    rot = jnp.concatenate([x1 * cos - x2 * sin, x2 * cos + x1 * sin], -1).astype(x.dtype)
    return jnp.concatenate([rot, x[..., ROT_DIM:]], -1)

def masked_softmax(s, mask):
    p = jax.nn.softmax(jnp.where(mask, s, NEG), axis=-1)
    return jnp.where(mask, p, 0.0)

def attend_shared(q, k, v, mask):
    s = jnp.einsum('bthgd,bkhd->bthgk', q, k, preferred_element_type=jnp.float32) * HEAD_DIM ** -0.5
    p = masked_softmax(s, mask)
    return jnp.einsum('bthgk,bkhd->bthgd', p.astype(v.dtype), v), p

def attend_gathered(q, k, v, mask):
    s = jnp.einsum('...hgd,...hkd->...hgk', q, k, preferred_element_type=jnp.float32) * HEAD_DIM ** -0.5
    p = masked_softmax(s, mask[..., None, :])
    return jnp.einsum('...hgk,...hkd->...hgd', p.astype(v.dtype), v)

def compress_blocks(raw, pe, w1, b1, w2, b2):
    bn, length = raw.shape[0], raw.shape[1]
    nc = length // CMP_BLOCK
    blk = raw[:, :nc * CMP_BLOCK].reshape(bn, nc, CMP_BLOCK, NSA_KV_HEADS, HEAD_DIM) + pe[:, None, :]
    hid = jax.nn.silu(jnp.einsum('bclhd,ldf->bchf', blk, w1) + b1)
    return jnp.einsum('bchf,fd->bchd', hid, w2) + b2

def compress_kv(raw_k, raw_v, cmp_pe, cmp_w1, cmp_b1, cmp_w2, cmp_b2):
    kc = compress_blocks(raw_k, cmp_pe[0], cmp_w1[0], cmp_b1[0], cmp_w2[0], cmp_b2[0])
    vc = compress_blocks(raw_v, cmp_pe[1], cmp_w1[1], cmp_b1[1], cmp_w2[1], cmp_b2[1])
    return kc, vc

def compressed_branch(q_c, raw_k, raw_v, pos, cmp_args):
    kc, vc = compress_kv(raw_k, raw_v, *cmp_args)
    nc = kc.shape[1]
    vis = (jnp.arange(nc)[None, :] + 1) * CMP_BLOCK - 1 <= pos[:, None]
    return attend_shared(q_c, kc, vc, vis[None, :, None, None, :])

def select_blocks(p_cmp, pos, length):
    imp = jnp.sum(p_cmp, axis=3)
    nc = imp.shape[-1]
    n_cand = max(-(-length // SEL_BLOCK), TOP_N)
    imp = jnp.pad(imp, ((0, 0), (0, 0), (0, 0), (0, n_cand - nc)))
    j = jnp.arange(n_cand)[None, :]
    cur = (pos // SEL_BLOCK)[:, None]
    future = (j > cur)[:, None, :]
    forced = ((j == 0) | (j == cur) | (j == cur - 1))[:, None, :]
    score = jnp.where(future, NEG, jnp.where(forced, FORCED_SCORE, imp))
    top_s, idx = lax.top_k(score, TOP_N)
    return idx, top_s > 0.5 * NEG

def block_rows(idx):
    rows = idx[..., None] * SEL_BLOCK + jnp.arange(SEL_BLOCK)
    return rows.reshape(idx.shape[:-1] + (TOP_N * SEL_BLOCK,))

def combine_branches(gate_logits, o_cmp, o_slc, o_win):
    bn, t = gate_logits.shape[0], gate_logits.shape[1]
    g = jax.nn.sigmoid(gate_logits.astype(jnp.float32)).reshape(bn, t, NSA_KV_HEADS, NSA_GQA, 3).astype(o_cmp.dtype)
    o = g[..., 0:1] * o_cmp + g[..., 1:2] * o_slc + g[..., 2:3] * o_win
    return o.reshape(bn, t, NSA_D)

def nsa_prompt(q, k_cmp, v_cmp, k_sel, v_sel, k_win, v_win, gate_logits, cmp_args):
    bn, t = q.shape[0], q.shape[1]
    pos = jnp.arange(t)
    q_c = group_heads(q)
    q_r = group_heads(partial_rope(q, pos))
    k_sel = partial_rope(k_sel, pos)
    k_win = partial_rope(k_win, pos)
    o_cmp, p_cmp = compressed_branch(q_c, k_cmp, v_cmp, pos, cmp_args)
    idx, valid = select_blocks(p_cmp, pos, t)
    nqb = t // Q_BLOCK
    hk = jnp.arange(NSA_KV_HEADS)[None, :, None]

    def sel_item(item):
        b, qb, q_i, idx_i, val_i = item
        qpos = qb * Q_BLOCK + jnp.arange(Q_BLOCK)
        rows = jnp.minimum(block_rows(idx_i), t - 1)
        mask = jnp.repeat(val_i, SEL_BLOCK, axis=-1) & (rows <= qpos[:, None, None])
        return attend_gathered(q_i, k_sel[b, rows, hk], v_sel[b, rows, hk], mask)

    items = (jnp.repeat(jnp.arange(bn), nqb), jnp.tile(jnp.arange(nqb), bn),
             q_r.reshape(bn * nqb, Q_BLOCK, NSA_KV_HEADS, NSA_GQA, HEAD_DIM),
             idx.reshape(bn * nqb, Q_BLOCK, NSA_KV_HEADS, TOP_N),
             valid.reshape(bn * nqb, Q_BLOCK, NSA_KV_HEADS, TOP_N))
    o_slc = lax.map(sel_item, items).reshape(bn, t, NSA_KV_HEADS, NSA_GQA, HEAD_DIM)
    nkw = WINDOW + Q_BLOCK
    kw_pad = jnp.pad(k_win, ((0, 0), (WINDOW, 0), (0, 0), (0, 0)))
    vw_pad = jnp.pad(v_win, ((0, 0), (WINDOW, 0), (0, 0), (0, 0)))

    def win_block(i):
        s0 = i * Q_BLOCK
        qpos = s0 + jnp.arange(Q_BLOCK)
        kpos = s0 - WINDOW + jnp.arange(nkw)
        mask = (kpos[None] <= qpos[:, None]) & (kpos[None] >= qpos[:, None] - WINDOW) & (kpos[None] >= 0)
        o, _ = attend_shared(lax.dynamic_slice_in_dim(q_r, s0, Q_BLOCK, 1),
                             lax.dynamic_slice_in_dim(kw_pad, s0, nkw, 1),
                             lax.dynamic_slice_in_dim(vw_pad, s0, nkw, 1),
                             mask[None, :, None, None, :])
        return o

    o_win = jnp.moveaxis(lax.map(win_block, jnp.arange(nqb)), 0, 1).reshape(bn, t, NSA_KV_HEADS, NSA_GQA, HEAD_DIM)
    out = combine_branches(gate_logits, o_cmp, o_slc, o_win)
    n_keep = min(WINDOW, t)
    return (out, jnp.stack([k_cmp, v_cmp], 2), jnp.stack([k_sel, v_sel], 2),
            jnp.stack([k_win, v_win], 2)[:, t - n_keep:])

def fetch_rows(rows, pool, new, page_table, kind):
    bi = jnp.arange(rows.shape[0])[:, None, None, None]
    hk = jnp.arange(NSA_KV_HEADS)[None, None, :, None]
    past = jnp.minimum(rows, PAST_LEN - 1)
    phys = page_table[bi, past // PAGE_SIZE]
    from_pool = pool[phys, past % PAGE_SIZE, kind, hk]
    from_new = new[bi, jnp.clip(rows - PAST_LEN, 0, new.shape[1] - 1), kind, hk]
    return jnp.where((rows < PAST_LEN)[..., None], from_pool, from_new)

def nsa_sample(q, k_cmp, v_cmp, k_sel, v_sel, k_win, v_win, gate_logits,
               pool_cmp, pool_sel, page_table, buf_win, cmp_args):
    bn, t = q.shape[0], q.shape[1]
    length = PAST_LEN + t
    pos = PAST_LEN + jnp.arange(t)
    q_c = group_heads(q)
    q_r = group_heads(partial_rope(q, pos))
    new_cmp = jnp.stack([k_cmp, v_cmp], 2)
    new_sel = jnp.stack([partial_rope(k_sel, pos), v_sel], 2)
    new_win = jnp.stack([partial_rope(k_win, pos), v_win], 2)
    past_cmp = pool_cmp[page_table].reshape(bn, -1, 2, NSA_KV_HEADS, HEAD_DIM)
    full_cmp = jnp.concatenate([past_cmp, new_cmp], 1)
    o_cmp, p_cmp = compressed_branch(q_c, full_cmp[:, :, 0], full_cmp[:, :, 1], pos, cmp_args)
    idx, valid = select_blocks(p_cmp, pos, length)
    rows = jnp.minimum(block_rows(idx), length - 1)
    k_g = fetch_rows(rows, pool_sel, new_sel, page_table, 0)
    v_g = fetch_rows(rows, pool_sel, new_sel, page_table, 1)
    mask = jnp.repeat(valid, SEL_BLOCK, axis=-1) & (rows <= pos[None, :, None, None])
    o_slc = attend_gathered(q_r, k_g, v_g, mask)
    w = buf_win.shape[1]
    kv_w = jnp.concatenate([buf_win, new_win], 1)
    kpos = PAST_LEN - w + jnp.arange(w + t)
    mask_w = (kpos[None] <= pos[:, None]) & (kpos[None] >= pos[:, None] - WINDOW)
    o_win, _ = attend_shared(q_r, kv_w[:, :, 0], kv_w[:, :, 1], mask_w[None, :, None, None, :])
    out = combine_branches(gate_logits, o_cmp, o_slc, o_win)
    n_keep = min(WINDOW, length)
    return out, new_cmp, new_sel, kv_w[:, w + t - n_keep:]

def segsum(a):
    t = a.shape[-1]
    rep = jnp.broadcast_to(a[..., None], a.shape + (t,))
    cs = jnp.cumsum(jnp.where(jnp.tril(jnp.ones((t, t), bool), -1), rep, 0.0), axis=-2)
    return jnp.where(jnp.tril(jnp.ones((t, t), bool)), cs, -jnp.inf)

def ssd_chunked(x, a, bm, cm, h0, chunk):
    b, t, h, p = x.shape
    c = t // chunk
    x = x.reshape(b, c, chunk, h, p)
    bm = bm.reshape(b, c, chunk, h, -1)
    cm = cm.reshape(b, c, chunk, h, -1)
    a = a.reshape(b, c, chunk, h).transpose(0, 3, 1, 2)
    a_cum = jnp.cumsum(a, -1)

    def to_bclh(m):
        return m.transpose(0, 2, 3, 1)[..., None]

    cb = jnp.einsum('bclhn,bcshn->bhcls', cm, bm) * jnp.exp(segsum(a))
    y_diag = jnp.einsum('bhcls,bcshp->bclhp', cb, x)
    states = jnp.einsum('bclhn,bclhp->bchpn', bm, x * to_bclh(jnp.exp(a_cum[..., -1:] - a_cum)))
    states = jnp.concatenate([h0[:, None], states], 1)
    decay_chunk = jnp.exp(segsum(jnp.pad(a_cum[..., -1], ((0, 0), (0, 0), (1, 0)))))
    states = jnp.einsum('bhzc,bchpn->bzhpn', decay_chunk, states)
    y_off = jnp.einsum('bclhn,bchpn->bclhp', cm, states[:, :-1]) * to_bclh(jnp.exp(a_cum))
    return (y_diag + y_off).reshape(b, t, h, p), states[:, -1]

def ssd_mixer(z, xbc, dt_raw, conv_in, h0, conv_w, conv_b, dt_bias, a_log, d_skip, norm_w):
    bn, t = z.shape[0], z.shape[1]
    ext = jnp.concatenate([conv_in.astype(xbc.dtype), xbc], 1)
    xc = lax.conv_general_dilated(ext, conv_w[:, None, :].astype(xbc.dtype), (1,), 'VALID',
                                  dimension_numbers=('NWC', 'WIO', 'NWC'),
                                  feature_group_count=SSD_CONV_CH)
    xc = jax.nn.silu(xc + conv_b)
    new_conv = ext[:, ext.shape[1] - (SSD_CONV - 1):]
    xs, bm, cm = jnp.split(xc.astype(jnp.float32), [SSD_D, SSD_D + SSD_GROUPS * SSD_STATE], axis=-1)
    x = xs.reshape(bn, t, SSD_HEADS, HEAD_DIM)
    bm = jnp.repeat(bm.reshape(bn, t, SSD_GROUPS, SSD_STATE), SSD_HEADS_PER_GROUP, axis=2)
    cm = jnp.repeat(cm.reshape(bn, t, SSD_GROUPS, SSD_STATE), SSD_HEADS_PER_GROUP, axis=2)
    dt = jax.nn.softplus(dt_raw.astype(jnp.float32) + dt_bias)
    a = -jnp.exp(a_log.astype(jnp.float32))
    chunk = SSD_CHUNK if t % SSD_CHUNK == 0 else t
    y, h_new = ssd_chunked(x * dt[..., None], dt * a, bm, cm, h0.astype(jnp.float32), chunk)
    y = (y + d_skip[:, None] * x).reshape(bn, t, SSD_D) * jax.nn.silu(z.astype(jnp.float32))
    yg = y.reshape(bn, t, SSD_GROUPS, -1)
    yg = yg * lax.rsqrt(jnp.mean(jnp.square(yg), -1, keepdims=True) + RMS_EPS)
    y = yg.reshape(bn, t, SSD_D) * norm_w
    return y.astype(z.dtype), h_new.astype(z.dtype), new_conv

def swiglu(x, wg, wu, wd):
    return jnp.dot(jax.nn.silu(jnp.dot(x, wg)) * jnp.dot(x, wu), wd)

def moe_ffn(h, router_w, router_bias, w_gate, w_up, w_down, sh_gate, sh_up, sh_down):
    n, d = h.shape
    scores = jax.nn.sigmoid(jnp.dot(h, router_w, preferred_element_type=jnp.float32))
    biased = scores + router_bias.astype(jnp.float32)
    grp_score = jnp.sum(lax.top_k(biased.reshape(n, N_EXPERT_GROUPS, -1), 2)[0], -1)
    _, grp_idx = lax.top_k(grp_score, TOPK_GROUPS)
    grp_keep = jnp.any(grp_idx[:, :, None] == jnp.arange(N_EXPERT_GROUPS), axis=1)
    keep = jnp.repeat(grp_keep, N_EXPERTS // N_EXPERT_GROUPS, axis=1)
    _, idx = lax.top_k(jnp.where(keep, biased, NEG), TOP_K)
    w = jnp.take_along_axis(scores, idx, axis=1)
    w = w / jnp.sum(w, -1, keepdims=True) * ROUTED_SCALE
    nk = n * TOP_K
    flat_e = idx.reshape(nk)
    order = jnp.argsort(flat_e)
    e_sorted = flat_e[order]
    tok_sorted = (order // TOP_K).astype(jnp.int32)
    w_sorted = w.reshape(nk)[order]
    counts = jnp.bincount(flat_e, length=N_EXPERTS)
    padded = (counts + MOE_BLOCK - 1) // MOE_BLOCK * MOE_BLOCK
    pad_end = jnp.cumsum(padded)
    pad_start = pad_end - padded
    start = jnp.cumsum(counts) - counts
    dest = pad_start[e_sorted] + jnp.arange(nk) - start[e_sorted]
    n_blocks = -(-(nk + N_EXPERTS * (MOE_BLOCK - 1)) // MOE_BLOCK)
    cap = n_blocks * MOE_BLOCK
    slot_tok = jnp.full((cap,), n, jnp.int32).at[dest].set(tok_sorted).reshape(n_blocks, MOE_BLOCK)
    slot_w = jnp.zeros((cap,), jnp.float32).at[dest].set(w_sorted).reshape(n_blocks, MOE_BLOCK)
    block_e = jnp.minimum(jnp.searchsorted(pad_end, jnp.arange(n_blocks) * MOE_BLOCK, side='right'), N_EXPERTS - 1)
    h_pad = jnp.concatenate([h, jnp.zeros((1, d), h.dtype)], 0)

    def expert_block(i, acc):
        tok = slot_tok[i]
        e = block_e[i]
        y = swiglu(h_pad[tok], w_gate[e], w_up[e], w_down[e])
        return acc.at[tok].add(y.astype(jnp.float32) * slot_w[i][:, None])

    acc = lax.fori_loop(0, n_blocks, expert_block, jnp.zeros((n + 1, d), jnp.float32))
    return (acc[:n] + swiglu(h, sh_gate, sh_up, sh_down).astype(jnp.float32)).astype(h.dtype)

def setup_inputs(seed: int = 0) -> dict:
    keys = list(jax.random.split(jax.random.key(seed), 40))
    f32 = jnp.float32

    def nrm(shape, scale=1.0):
        return jax.random.normal(keys.pop(), shape, f32) * scale

    n_pages = PAST_LEN // PAGE_SIZE
    n_pool = (DEC_BATCH * n_pages * 5 + 3) // 4
    win_rows = min(WINDOW, PAST_LEN)
    x_prompt = nrm((BATCH, SEQ, D_MODEL))
    x_sample = nrm((DEC_BATCH, DEC_SEQ, D_MODEL))
    cache_kv_cmp = nrm((DEPTH, n_pool, PAGE_SIZE, 2, NSA_KV_HEADS, HEAD_DIM))
    cache_kv_sel = nrm((DEPTH, n_pool, PAGE_SIZE, 2, NSA_KV_HEADS, HEAD_DIM))
    page_table = jax.random.permutation(keys.pop(), n_pool)[:DEC_BATCH * n_pages].reshape(DEC_BATCH, n_pages).astype(jnp.int32)
    cache_kv_win = nrm((DEPTH, DEC_BATCH, win_rows, 2, NSA_KV_HEADS, HEAD_DIM))
    state_ssm = nrm((DEPTH, DEC_BATCH, SSD_HEADS, HEAD_DIM, SSD_STATE), 0.5)
    state_conv = nrm((DEPTH, DEC_BATCH, SSD_CONV - 1, SSD_CONV_CH))
    dt0 = jnp.exp(jax.random.uniform(keys.pop(), (DEPTH, SSD_HEADS), f32, math.log(1e-3), math.log(1e-1)))
    a0 = jax.random.uniform(keys.pop(), (DEPTH, SSD_HEADS), f32, 1.0, 16.0)
    return {
        'x_prompt': x_prompt,
        'x_sample': x_sample,
        'cache_kv_cmp': cache_kv_cmp,
        'cache_kv_sel': cache_kv_sel,
        'page_table': page_table,
        'cache_kv_win': cache_kv_win,
        'state_ssm': state_ssm,
        'state_conv': state_conv,
        'emb_ln_g': 1.0 + nrm((D_MODEL,), 0.02),
        'emb_ln_b': nrm((D_MODEL,), 0.01),
        'w_in': nrm((DEPTH, D_MODEL, D_IN), D_MODEL ** -0.5),
        'conv_w': nrm((DEPTH, SSD_CONV, SSD_CONV_CH), SSD_CONV ** -0.5),
        'conv_b': nrm((DEPTH, SSD_CONV_CH), 0.01),
        'dt_bias': dt0 + jnp.log(-jnp.expm1(-dt0)),
        'a_log': jnp.log(a0),
        'd_skip': 1.0 + nrm((DEPTH, SSD_HEADS), 0.1),
        'ssd_norm_w': 1.0 + nrm((DEPTH, SSD_D), 0.02),
        'cmp_pe': nrm((DEPTH, 2, CMP_BLOCK, HEAD_DIM), 0.1),
        'cmp_w1': nrm((DEPTH, 2, CMP_BLOCK, HEAD_DIM, CMP_HIDDEN), (CMP_BLOCK * HEAD_DIM) ** -0.5),
        'cmp_b1': nrm((DEPTH, 2, CMP_HIDDEN), 0.01),
        'cmp_w2': nrm((DEPTH, 2, CMP_HIDDEN, HEAD_DIM), CMP_HIDDEN ** -0.5),
        'cmp_b2': nrm((DEPTH, 2, HEAD_DIM), 0.01),
        'w_out': nrm((DEPTH, D_MIX, D_MODEL), DEEPNORM_BETA * D_MIX ** -0.5),
        'ln1_g': 1.0 + nrm((DEPTH, D_MODEL), 0.02),
        'ln1_b': nrm((DEPTH, D_MODEL), 0.01),
        'router_w': nrm((DEPTH, D_MODEL, N_EXPERTS), D_MODEL ** -0.5),
        'router_bias': nrm((DEPTH, N_EXPERTS), 0.01),
        'exp_w_gate': nrm((DEPTH, N_EXPERTS, D_MODEL, D_EXPERT), D_MODEL ** -0.5),
        'exp_w_up': nrm((DEPTH, N_EXPERTS, D_MODEL, D_EXPERT), D_MODEL ** -0.5),
        'exp_w_down': nrm((DEPTH, N_EXPERTS, D_EXPERT, D_MODEL), DEEPNORM_BETA * D_EXPERT ** -0.5),
        'sh_w_gate': nrm((DEPTH, D_MODEL, D_SHARED), D_MODEL ** -0.5),
        'sh_w_up': nrm((DEPTH, D_MODEL, D_SHARED), D_MODEL ** -0.5),
        'sh_w_down': nrm((DEPTH, D_SHARED, D_MODEL), DEEPNORM_BETA * D_SHARED ** -0.5),
        'ln2_g': 1.0 + nrm((DEPTH, D_MODEL), 0.02),
        'ln2_b': nrm((DEPTH, D_MODEL), 0.01),
    }

def reference(x_prompt, x_sample, cache_kv_cmp, cache_kv_sel, page_table, cache_kv_win, state_ssm, state_conv,
              emb_ln_g, emb_ln_b, w_in, conv_w, conv_b, dt_bias, a_log, d_skip, ssd_norm_w,
              cmp_pe, cmp_w1, cmp_b1, cmp_w2, cmp_b2, w_out, ln1_g, ln1_b,
              router_w, router_bias, exp_w_gate, exp_w_up, exp_w_down,
              sh_w_gate, sh_w_up, sh_w_down, ln2_g, ln2_b):
    hp = layer_norm(x_prompt, emb_ln_g, emb_ln_b)
    hs = layer_norm(x_sample, emb_ln_g, emb_ln_b)
    bp, tp = hp.shape[0], hp.shape[1]
    bs, ts = hs.shape[0], hs.shape[1]
    n_prompt = bp * tp
    kvc_p, kvs_p, kvw_p, ssm_p, conv_p = [], [], [], [], []
    kvc_s, kvs_s, kvw_s, ssm_s, conv_s = [], [], [], [], []
    for l in range(DEPTH):
        cmp_args = (cmp_pe[l], cmp_w1[l], cmp_b1[l], cmp_w2[l], cmp_b2[l])
        ssd_args = (conv_w[l], conv_b[l], dt_bias[l], a_log[l], d_skip[l], ssd_norm_w[l])
        z, xbc, dt, q, kc, vc, ks, vs, kw, vw, g = in_proj_split(hp, w_in[l])
        y_ssd, h_new, c_new = ssd_mixer(z, xbc, dt, jnp.zeros((bp, SSD_CONV - 1, SSD_CONV_CH), xbc.dtype),
                                        jnp.zeros((bp, SSD_HEADS, HEAD_DIM, SSD_STATE), jnp.float32), *ssd_args)
        y_nsa, n_cmp, n_sel, n_win = nsa_prompt(to_heads(q, NSA_HEADS), to_heads(kc, NSA_KV_HEADS), to_heads(vc, NSA_KV_HEADS),
                                                to_heads(ks, NSA_KV_HEADS), to_heads(vs, NSA_KV_HEADS),
                                                to_heads(kw, NSA_KV_HEADS), to_heads(vw, NSA_KV_HEADS), g, cmp_args)
        mix = jnp.einsum('btf,fd->btd', jnp.concatenate([y_ssd, y_nsa], -1), w_out[l])
        hp = layer_norm(DEEPNORM_ALPHA * hp + mix, ln1_g[l], ln1_b[l])
        kvc_p.append(n_cmp)
        kvs_p.append(n_sel)
        kvw_p.append(n_win)
        ssm_p.append(h_new)
        conv_p.append(c_new)
        z, xbc, dt, q, kc, vc, ks, vs, kw, vw, g = in_proj_split(hs, w_in[l])
        y_ssd, h_new, c_new = ssd_mixer(z, xbc, dt, state_conv[l], state_ssm[l], *ssd_args)
        y_nsa, n_cmp, n_sel, n_win = nsa_sample(to_heads(q, NSA_HEADS), to_heads(kc, NSA_KV_HEADS), to_heads(vc, NSA_KV_HEADS),
                                                to_heads(ks, NSA_KV_HEADS), to_heads(vs, NSA_KV_HEADS),
                                                to_heads(kw, NSA_KV_HEADS), to_heads(vw, NSA_KV_HEADS), g,
                                                cache_kv_cmp[l], cache_kv_sel[l], page_table, cache_kv_win[l], cmp_args)
        mix = jnp.einsum('btf,fd->btd', jnp.concatenate([y_ssd, y_nsa], -1), w_out[l])
        hs = layer_norm(DEEPNORM_ALPHA * hs + mix, ln1_g[l], ln1_b[l])
        kvc_s.append(n_cmp)
        kvs_s.append(n_sel)
        kvw_s.append(n_win)
        ssm_s.append(h_new)
        conv_s.append(c_new)
        tok = jnp.concatenate([hp.reshape(n_prompt, D_MODEL), hs.reshape(bs * ts, D_MODEL)], 0)
        f = moe_ffn(tok, router_w[l], router_bias[l], exp_w_gate[l], exp_w_up[l], exp_w_down[l],
                    sh_w_gate[l], sh_w_up[l], sh_w_down[l])
        hp = layer_norm(DEEPNORM_ALPHA * hp + f[:n_prompt].reshape(hp.shape), ln2_g[l], ln2_b[l])
        hs = layer_norm(DEEPNORM_ALPHA * hs + f[n_prompt:].reshape(hs.shape), ln2_g[l], ln2_b[l])
    return (hp, hs, jnp.stack(kvc_p), jnp.stack(kvs_p), jnp.stack(kvw_p), jnp.stack(ssm_p), jnp.stack(conv_p),
            jnp.stack(kvc_s), jnp.stack(kvs_s), jnp.stack(kvw_s), jnp.stack(ssm_s), jnp.stack(conv_s))


_drawn_inputs = setup_inputs


def setup_inputs(seed=0):
    import zlib

    import numpy as np

    out = dict(_drawn_inputs(seed))
    spreads = {}
    factors = {'cache_kv_sel': 6.192,
     'conv_b': 2.732,
     'cmp_b1': 5.869,
     'cmp_b2': 3.53,
     'ln2_g': 2.681,
     'ln2_b': 5.406}
    for name, (base, spread) in spreads.items():
        noise = np.random.default_rng([zlib.crc32(name.encode()), seed]).standard_normal(out[name].shape)
        drawn = base * np.exp(spread * noise) if base else spread * noise
        out[name] = jnp.asarray(drawn.astype(out[name].dtype))
    for name, factor in factors.items():
        out[name] = (out[name] * factor).astype(out[name].dtype)
    return out
```

```python
from contextlib import ExitStack

import numpy as np
import concourse.bass as bass
from concourse import mybir

F32 = mybir.dt.float32
I32 = mybir.dt.int32
U32 = mybir.dt.uint32
ALU = mybir.AluOpType
ACT = mybir.ActivationFunctionType
AX = mybir.AxisListType

P = 128
D = 1024
DC = D // P
SEQ = 1024
NT = SEQ // P
NS = 8
NTOK = SEQ + NS
PAST = 8192
PAGE = 128
NPAGE = PAST // PAGE
HD = 64
NH = 8
GQA = 4
RH = 8
KV = 256
NEG = -1e30
ALPHA = 2.0 ** 0.25
EPS = 1e-5
SCALE = HD ** -0.5
C_Q, C_KV, C_WG, C_Z, C_X = 0, 512, 1024, 1312, 1824
D_IN = 2848
WG = 288


class Names:
    pass


def bcast(ap, shape):
    return ap.to_broadcast(shape)


def persistent(nc, ctx):
    k = Names()
    k.sems = []

    def sb(name, shape, dt=F32):
        t = ctx.enter_context(nc.sbuf_tensor(name, shape, dt))
        return t

    k.ident = sb("ident", [P, P])
    k.mask_le = sb("mask_le", [P, P])
    k.ones = sb("ones", [P, P])
    k.gd = sb("gd", [P, NT + 1, 32])
    return k


def project(nc, k, d):
    with ExitStack() as ctx:
        def sb(name, shape, dt=F32):
            return ctx.enter_context(nc.sbuf_tensor(name, shape, dt))

        def ps(name, shape):
            return ctx.enter_context(nc.psum_tensor(name, shape, F32))

        def sem(name):
            k.sems.append(ctx.enter_context(nc.semaphore(name)))
            return k.sems[-1]

        w = sb("w_in_sb", [P, DC, D_IN])
        gain, bias = sb("emb_g", [P, D]), sb("emb_b", [P, D])
        rope_c, rope_s = sb("rope_c", [P, NT + 1, 2 * RH]), sb("rope_s", [P, NT + 1, 2 * RH])
        xin, xn = sb("xin", [P, D]), sb("xn", [P, D])
        hT = sb("hT", [P, DC, P])
        st = sb("st", [P, 1792])
        zst = sb("zst", [P, 512])
        stats, mv, rstd = sb("stats", [P, 2, 6]), sb("mv", [P, 2]), sb("rstd", [P, 2])
        mhalf, eps = sb("mhalf", [P, 1]), sb("eps", [P, 1])
        rt = sb("rt", [P, 8, 2 * RH])
        rt2 = sb("rt2", [P, 8, 2 * RH])
        pT = ps("pT", [P, 2, 512])
        pQ, pKV, pW, pZ = (ps(n, [P, 512]) for n in ("pQ", "pKV", "pW", "pZ"))
        pX = ps("pX", [P, 2, 512])

        w_in_loaded = [sem(f"w_in_loaded{i}") for i in range(2)]
        consts, x_loaded, x_taken = sem("consts"), sem("x_loaded"), sem("x_taken")
        stats_ready, rstd_ready, xn_ready, xn_stored = sem("stats_ready"), sem("rstd_ready"), sem("xn_ready"), sem("xn_stored")
        hT_in_psum, hT_ready = sem("hT_in_psum"), sem("hT_ready")
        kv_done, q_done, wg_done, xbc_done, z_done = sem("kv_done"), sem("q_done"), sem("wg_done"), sem("xbc_done"), sem("z_done")
        kv_out, wg_out, qr_out, q_out, xbc_out, z_out = (sem(n) for n in ("kv_out", "wg_out", "qr_out", "q_out", "xbc_out", "z_out"))
        roped, rows_stored, z_stored, heads_in_psum, heads_out = (sem(n) for n in ("roped", "rows_stored", "z_stored", "heads_in_psum", "heads_out"))

        block = ctx.enter_context(nc.Block())

        @block.sync
        def _(sp):
            sp.dma_start(k.ident[:], d["ident"]).then_inc(consts, 16)
            sp.dma_start(gain[:], bcast(d["emb_ln_g"], [P, D])).then_inc(consts, 16)
            sp.dma_start(bias[:], bcast(d["emb_ln_b"], [P, D])).then_inc(consts, 16)
            sp.dma_start(xin[:], d["x"][0:P]).then_inc(x_loaded, 16)
            w_dram = d["w_in"].rearrange("(c p) n -> p c n", p=P)
            sp.dma_start(w[:, :, 0:C_WG], w_dram[:, :, 0:C_WG]).then_inc(w_in_loaded[0], 16)
            sp.dma_start(w[:, :, C_WG:D_IN], w_dram[:, :, C_WG:D_IN]).then_inc(w_in_loaded[1], 16)
            sp.dma_start(rope_c[:], d["rope_c"]).then_inc(consts, 16)
            sp.dma_start(rope_s[:], d["rope_s"]).then_inc(consts, 16)
            sp.dma_start(k.mask_le[:], d["mask_le"]).then_inc(consts, 16)
            sp.dma_start(k.ones[:], d["ones"]).then_inc(consts, 16)

            def store_x(t, R):
                sp.wait_ge(xn_ready, t + 1)
                sp.dma_start(d["xres"][bass.ds(t * P, R)], xn[0:R, :]).then_inc(xn_stored, 16)

            def store_rows(t, R, cmp_rows, sel_rows):
                sp.wait_ge(roped, t + 1)
                sp.dma_start(cmp_rows, st[0:R, 1024:1280]).then_inc(rows_stored, 16)
                sp.dma_start(sel_rows, st[0:R, 1280:1536]).then_inc(rows_stored, 16)
                sp.dma_start(d["kv_win_all"][bass.ds(t * P, R)], st[0:R, 1536:1792]).then_inc(rows_stored, 16)
                sp.wait_ge(z_out, t + 2)
                sp.dma_start(d["z_silu"][bass.ds(t * P, R)], zst[0:R, :]).then_inc(z_stored, 16)

            with sp.Fori(0, NT - 1) as t:
                sp.wait_ge(x_taken, t + 1)
                sp.dma_start(xin[:], d["x"][bass.ds(t * P + P, P)]).then_inc(x_loaded, 16)
                store_x(t, P)
                store_rows(t, P, d["kv_cmp_prompt"][bass.ds(t * P, P)], d["kv_sel_prompt"][bass.ds(t * P, P)])
            sp.wait_ge(x_taken, NT)
            sp.dma_start(xin[0:NS, :], d["x"][SEQ:NTOK]).then_inc(x_loaded, 16)
            store_x(NT - 1, P)
            store_x(NT, NS)
            store_rows(NT - 1, P, d["kv_cmp_prompt"][SEQ - P:SEQ], d["kv_sel_prompt"][SEQ - P:SEQ])
            store_rows(NT, NS, d["kv_cmp_sample"], d["kv_sel_sample"])
            sp.wait_ge(rows_stored, 48 * (NT + 2))
            sp.wait_ge(z_stored, 16 * (NT + 2))
            sp.wait_ge(xn_stored, 16 * (NT + 1) + 16)

        @block.vector
        def _(v):
            v.memset(k.gd[:], 0.0)
            v.memset(k.xbcT[:, :, 0:3], 0.0)
            v.sem_inc(xn_stored, 16)
            v.sem_inc(rows_stored, 48)
            v.wait_ge(consts, 16 * 7)

            def layer_norm(t, R):
                v.wait_ge(x_loaded, t * 16 + 16)
                for i in range(2):
                    nc.vector.bn_stats(stats[0:R, i, :], xin[0:R, i * 512:(i + 1) * 512])
                v.drain()
                nc.vector.bn_aggr(mv[0:R, :], stats[0:R]).then_inc(stats_ready, 1)
                v.wait_ge(rstd_ready, t + 1)
                v.wait_ge(xn_stored, t * 16 + 16)
                v.wait_ge(hT_in_psum, t + 1)
                nc.vector.tensor_scalar(xn[0:R, :], xin[0:R, :], mv[0:R, 0:1], rstd[0:R, 1:2],
                                        ALU.subtract, ALU.mult).then_inc(x_taken, 1)
                v.drain()
                nc.vector.tensor_tensor(xn[0:R, :], xn[0:R, :], gain[0:R, :], ALU.mult)
                v.drain()
                nc.vector.tensor_tensor(xn[0:R, :], xn[0:R, :], bias[0:R, :], ALU.add).then_inc(xn_ready, 1)

            def rotate(dst, src, t, R, n):
                c = rope_c[0:R, bass.ds(t, 1), :].to_broadcast([R, n, 2 * RH])
                s = rope_s[0:R, bass.ds(t, 1), :].to_broadcast([R, n, 2 * RH])
                nc.vector.tensor_tensor(rt[0:R, 0:n, :], src[:, :, 0:2 * RH], c, ALU.mult)
                nc.vector.tensor_tensor(rt2[0:R, 0:n, 0:RH], src[:, :, RH:2 * RH], s[:, :, 0:RH], ALU.mult)
                nc.vector.tensor_tensor(rt2[0:R, 0:n, RH:2 * RH], src[:, :, 0:RH], s[:, :, RH:2 * RH], ALU.mult)
                v.drain()
                nc.vector.tensor_tensor(dst[:, :, 0:2 * RH], rt[0:R, 0:n, :], rt2[0:R, 0:n, :], ALU.add)

            def evacuate(t, R):
                v.wait_ge(kv_done, t + 1)
                v.wait_ge(rows_stored, t * 48 + 48)
                v.wait_ge(heads_in_psum, t + 1)
                nc.vector.tensor_copy(st[0:R, 1024:1536], pKV[0:R, :]).then_inc(kv_out, 1)
                v.wait_ge(q_done, t + 1)
                nc.vector.tensor_copy(st[0:R, 512:1024], pQ[0:R, :]).then_inc(qr_out, 1)
                v.wait_ge(wg_done, t + 1)
                nc.vector.tensor_copy(st[0:R, 1536:1792], pW[0:R, 0:256])
                nc.vector.tensor_copy(k.gd[0:R, bass.ds(t, 1), :].rearrange("p a b -> p (a b)"),
                                      pW[0:R, 256:288]).then_inc(wg_out, 1)
                v.drain()
                q8 = st[0:R, 512:1024].rearrange("p (h e) -> p h e", e=HD)
                rotate(q8, q8, t, R, NH)
                for base in (1280, 1536):
                    v.drain()
                    k2 = st[0:R, base:base + 128].rearrange("p (h e) -> p h e", e=HD)
                    rotate(k2, k2, t, R, 2)
                v.drain().then_inc(roped, 1)

            layer_norm(0, P)
            with v.Fori(0, NT - 1) as t:
                layer_norm(t + 1, P)
                evacuate(t, P)
            layer_norm(NT, NS)
            evacuate(NT - 1, P)
            evacuate(NT, NS)

        @block.gpsimd
        def _(g):
            g.memset(eps[:], EPS)
            g.memset(mhalf[:], -0.5)
            g.drain()

            def inv_std(t, R):
                g.wait_ge(stats_ready, t + 1)
                nc.gpsimd.tensor_tensor(rstd[0:R, 0:1], mv[0:R, 1:2], eps[0:R, :], ALU.add)
                g.drain()
                nc.gpsimd.tensor_tensor(rstd[0:R, 1:2], rstd[0:R, 0:1], mhalf[0:R, :], ALU.pow).then_inc(rstd_ready, 1)

            inv_std(0, P)
            with g.Fori(0, NT - 1) as t:
                inv_std(t + 1, P)
            inv_std(NT, NS)

        @block.tensor
        def _(pe):
            pe.sem_inc(hT_in_psum, 1)
            pe.sem_inc(heads_in_psum, 1)
            pe.wait_ge(consts, 16 * 7)

            def tile(t, R):
                pe.wait_ge(xn_ready, t + 1)
                pe.wait_ge(heads_out, t + 1)
                for c in range(DC):
                    last = nc.tensor.transpose(pT[:, c // 4, (c % 4) * P:(c % 4) * P + R],
                                               xn[0:R, c * P:(c + 1) * P], k.ident[0:R, 0:R])
                last.then_inc(hT_in_psum, 1)
                pe.wait_ge(hT_ready, t + 1)

                def rows(out, c0, n):
                    for c in range(DC):
                        mm = nc.tensor.matmul(out[0:R, 0:n], hT[:, c, 0:R], w[:, c, c0:c0 + n],
                                              start=(c == 0), stop=(c == DC - 1))
                    return mm

                pe.wait_ge(w_in_loaded[0], 16)
                rows(pKV, C_KV, 512).then_inc(kv_done, 1)
                pe.wait_ge(qr_out, t + 1)
                pe.wait_ge(q_out, t + 1)
                rows(pQ, C_Q, 512).then_inc(q_done, 1)
                pe.wait_ge(w_in_loaded[1], 16)
                pe.wait_ge(wg_out, t + 1)
                rows(pW, C_WG, WG).then_inc(wg_done, 1)
                pe.wait_ge(xbc_out, t + 1)
                for ch in range(DC):
                    for c in range(DC):
                        mm = nc.tensor.matmul(pX[:, ch // 4, (ch % 4) * P:(ch % 4) * P + R],
                                              w[:, c, C_X + ch * P:C_X + (ch + 1) * P], hT[:, c, 0:R],
                                              start=(c == 0), stop=(c == DC - 1))
                mm.then_inc(xbc_done, 1)
                pe.wait_ge(z_out, t + 1)
                rows(pZ, C_Z, 512).then_inc(z_done, 1)
                pe.wait_ge(q_out, t + 2)
                pe.wait_ge(roped, t + 1)
                pe.wait_ge(kv_out, t + 1)
                for c in range(4):
                    nc.tensor.transpose(pT[:, 0, c * P:c * P + R], st[0:R, c * P:(c + 1) * P], k.ident[0:R, 0:R])
                for c in range(4):
                    nc.tensor.transpose(pT[:, 1, c * P:c * P + R], st[0:R, 512 + c * P:512 + (c + 1) * P],
                                        k.ident[0:R, 0:R])
                nc.tensor.transpose(pKV[:, 0:R], st[0:R, 1280:1408], k.ident[0:R, 0:R])
                nc.tensor.transpose(pKV[:, P:P + R], st[0:R, 1536:1664],
                                    k.ident[0:R, 0:R]).then_inc(heads_in_psum, 1)

            with pe.Fori(0, NT) as t:
                tile(t, P)
            tile(NT, NS)

        @block.scalar
        def _(act):
            for free in (heads_out, qr_out, q_out, wg_out, xbc_out, z_out):
                act.sem_inc(free, 1)
            act.sem_inc(z_stored, 16)

            def tile(t, R, xbc_dst):
                act.wait_ge(hT_in_psum, t + 2)
                for i in range(2):
                    last = nc.scalar.copy(hT[:, i * 4:i * 4 + 4, 0:R],
                                          pT[:, i, :].rearrange("p (c r) -> p c r", r=P)[:, :, 0:R])
                last.then_inc(hT_ready, 1)
                act.wait_ge(qr_out, t + 2)
                nc.scalar.copy(st[0:R, 0:512], pQ[0:R, :]).then_inc(q_out, 1)
                act.wait_ge(xbc_done, t + 1)
                nc.scalar.copy(xbc_dst, pX[:, :, :].rearrange("p b (c r) -> p (b c) r", r=P)[:, :, 0:R]
                               ).then_inc(xbc_out, 1)
                act.wait_ge(z_done, t + 1)
                act.wait_ge(z_stored, t * 16 + 16)
                nc.scalar.activation(zst[0:R, :], pZ[0:R, :], ACT.Silu).then_inc(z_out, 1)
                act.wait_ge(heads_in_psum, t + 2)
                at = bass.ds(t * P, R)
                nc.scalar.copy(k.qT[:, :, at], pT[:, 0, :].rearrange("p (c r) -> p c r", r=P)[:, :, 0:R])
                nc.scalar.copy(k.qrT[:, :, at], pT[:, 1, :].rearrange("p (c r) -> p c r", r=P)[:, :, 0:R])
                nc.scalar.copy(k.kselT[:, at], pKV[:, 0:R])
                nc.scalar.copy(k.kwinT[:, at], pKV[:, P:P + R]).then_inc(heads_out, 1)

            with act.Fori(0, NT) as t:
                tile(t, P, k.xbcT[:, :, bass.ds(t * P + 3, P)])
            tile(NT, NS, k.xbcS[:, :, :])


def alloc_kept(nc, ctx, k):
    def sb(name, shape, dt=F32):
        return ctx.enter_context(nc.sbuf_tensor(name, shape, dt))
    k.qT, k.qrT = sb("qT", [P, 4, NTOK]), sb("qrT", [P, 4, NTOK])
    k.kselT, k.kwinT = sb("kselT", [P, NTOK]), sb("kwinT", [P, NTOK])
    k.kcT_p, k.vc_p = sb("kcT_p", [P, 2 * NT]), sb("vc_p", [2 * NT, 2, HD])
    k.kcT_s, k.vc_s = sb("kcT_s", [P, NS, P]), sb("vc_s", [P, NS, 2, HD])


def alloc_xbc(nc, ctx, k):
    def sb(name, shape, dt=F32):
        return ctx.enter_context(nc.sbuf_tensor(name, shape, dt))
    k.xbcT, k.xbcS = sb("xbcT", [P, DC, 3 + SEQ]), sb("xbcS", [P, DC, NS])


def ssd(nc, k, d):
    with ExitStack() as ctx:
        def sb(name, shape, dt=F32):
            return ctx.enter_context(nc.sbuf_tensor(name, shape, dt))

        def ps(name, shape):
            return ctx.enter_context(nc.psum_tensor(name, shape, F32))

        def sem(name):
            k.sems.append(ctx.enter_context(nc.semaphore(name)))
            return k.sems[-1]

        NG = 512
        G = 24
        cw, cb = sb("conv_w_sb", [P, DC, 4]), sb("conv_b_sb", [P, DC])
        dtb, alog = sb("dt_bias_sb", [P, 8]), sb("a_log_sb", [P, 8])
        dskip, normw = sb("d_skip_sb", [P, 8]), sb("norm_w_sb", [P, NG])
        mneg, expand = sb("mneg", [P, P]), sb("expand_h", [8, NG])
        sconv = sb("state_conv_sb", [P, DC, 3, NS])
        h0 = sb("state_ssm_sb", [P, NS, 4, P])
        cv = sb("cv", [P, DC, SEQ])
        cvs, cvt = sb("cvs", [P, DC, NS]), sb("cvt", [P, DC, NS])
        sp1, sp2, sp3, sp4 = (sb(f"softplus{i}", [P, NT + 1, 8]) for i in range(4))
        dt = sb("dt", [P, NT + 1, 8])
        dtA = sb("dtA", [P, NT + 1, 8])
        pr = sb("pr", [P, NT, 6, 8])
        prs, cs = sb("prs", [P, 6, 8]), sb("cs", [P, DC, P])
        Dm, xdt, xdd, Dx = sb("Dm", [P, 8, P]), sb("xdt", [P, NG]), sb("xdd", [P, NG]), sb("Dx", [P, NG])
        Bt, H = sb("Bt", [P, 256]), sb("H", [P, NG])
        y, y2, zt, sq = sb("y", [P, NG]), sb("y2", [P, NG]), sb("zt", [P, NG]), sb("sq", [P, NG])
        ms, mhalf = sb("ms", [P, 4]), sb("mhalf_ssd", [P, 2])
        dT, dE = sb("dT", [8, 17]), sb("dE", [P, 4, 17])
        bc, bcm = sb("bc", [8, NG]), sb("bcm", [8, NG])
        hx, ys = sb("hx", [P, 4, P]), sb("ys", [P, 4, NS])
        xdtS = sb("xdtS", [P, 4, NS])
        Hout, cvo = sb("Hout", [P, 4, P]), sb("cvo", [8, D])
        cvp = sb("cvp", [8, D])

        pX, pB, pS, pY1, pY2 = (ps(n, [P, 512]) for n in ("ssd_pX", "ssd_pB", "ssd_pS", "ssd_pY1", "ssd_pY2"))
        pR = ps("ssd_pR", [P, 2, 512])

        consts, z_loaded, silu_done = sem("ssd_consts"), sem("z_loaded"), sem("silu_done")
        conv_done, sp_v, sp_a, pr_ready, sums_done = sem("conv_done"), sem("sp_v"), sem("sp_a"), sem("pr_ready"), sem("sums_done")
        staged, in_psum, d_ready, exp_ready, m_ready = sem("staged"), sem("chunk_in_psum"), sem("d_ready"), sem("exp_ready"), sem("m_ready")
        yoff_done, ydiag_done, state_done, h_ready, xd_ready = (sem(n) for n in ("yoff_done", "ydiag_done", "state_done", "h_ready", "xd_ready"))
        ms_ready, rms_ready, y_ready, y_stored, chunk_done = (sem(n) for n in ("ms_ready", "rms_ready", "y_ready", "y_stored", "chunk_done"))
        side_ps, side_sb, side_st, bc_ready, bc_ps, hn_ready = (sem(n) for n in ("side_ps", "side_sb", "side_st", "bc_ready", "bc_ps", "hn_ready"))
        prep, y_used = sem("ssd_prep"), sem("y_used")
        block = ctx.enter_context(nc.Block())
        NCONST = 10

        @block.sync
        def _(sp):
            for dst, src in ((cw, d["conv_w"]), (cb, d["conv_b"]), (mneg, d["mask_neg"]), (expand, d["expand_h"]),
                             (sconv, d["state_conv"])):
                sp.dma_start(dst[:], src).then_inc(consts, 16)
            for dst, src in ((dtb, d["dt_bias"]), (alog, d["a_log"]), (dskip, d["d_skip"])):
                sp.dma_start(dst[:], bcast(src, [P, 8])).then_inc(consts, 16)
            sp.dma_start(normw[:], bcast(d["ssd_norm_w"], [P, NG])).then_inc(consts, 16)
            sp.dma_start(dT[:, 16:17], d["d_skip"].rearrange("a h -> h a")).then_inc(consts, 16)
            sp.dma_start(d["kv_win_prompt"], d["kv_win_all"][SEQ - 512:SEQ]).then_inc(side_st, 16)
            sp.dma_start(d["conv_sample"][:, 0:2, :], d["state_conv_rows"][:, 1:3, :]).then_inc(side_st, 16)
            sp.dma_start(zt[:], d["z_silu"][0:P]).then_inc(z_loaded, 16)
            for b in range(NS):
                sp.dma_start(h0[:, b], d["state_ssm"][b].rearrange("(c q) n -> q c n", q=P)).then_inc(prep, 16)
            with sp.Fori(0, NT - 1) as c:
                sp.wait_ge(y_ready, c + 1)
                sp.dma_start(zt[:], d["z_silu"][bass.ds(c * P + P, P)]).then_inc(z_loaded, 16)
                sp.dma_start(d["mix"][bass.ds(c * P, P), 0:NG], y2[:]).then_inc(y_stored, 16)
            sp.wait_ge(y_ready, NT)
            sp.dma_start(zt[0:NS], d["z_silu"][SEQ:NTOK]).then_inc(z_loaded, 16)
            sp.dma_start(d["mix"][SEQ - P:SEQ, 0:NG], y2[:]).then_inc(y_stored, 16)
            sp.wait_ge(side_sb, 1)
            sp.dma_start(d["conv_sample"][:, 2, :], cvo[:]).then_inc(side_st, 16)
            sp.dma_start(d["conv_prompt"], cvp[0:3]).then_inc(side_st, 16)
            sp.wait_ge(side_sb, 2)
            sp.dma_start(d["ssm_prompt"].rearrange("(c q) n -> q c n", q=P), Hout[:]).then_inc(side_st, 16)
            with sp.Fori(0, NS) as b:
                sp.wait_ge(hn_ready, b + 1)
                sp.dma_start(d["ssm_sample"][bass.ds(b, 1)].rearrange("b (c q) n -> q (b c) n", q=P),
                             h0[:, bass.ds(b, 1)].rearrange("q b c n -> q (b c) n")).then_inc(side_st, 16)
            sp.wait_ge(y_ready, NT + 1)
            sp.dma_start(d["mix"][SEQ:NTOK, 0:NG], y2[0:NS]).then_inc(y_stored, 16)
            sp.wait_ge(y_stored, 16 * (NT + 2))
            sp.wait_ge(side_st, 16 * (5 + NS))

        @block.gpsimd
        def _(g):
            g.memset(mhalf[:], -0.5)
            g.drain()

            def inv_rms(n, R):
                g.wait_ge(ms_ready, n + 1)
                nc.gpsimd.tensor_tensor(ms[0:R, 2:4], ms[0:R, 0:2], mhalf[0:R, :], ALU.pow).then_inc(rms_ready, 1)

            g.wait_ge(silu_done, DC)
            g.wait_ge(pr_ready, 1)
            with g.Fori(0, NT) as c:
                g.wait_ge(chunk_done, c + 1)
                g.nop()
                nc.gpsimd.tensor_copy(prs[:], pr[:, bass.ds(c, 1)].rearrange("p a k h -> p (a k) h"))
                nc.gpsimd.tensor_copy(cs[:], cv[:, :, bass.ds(c * P, P)])
                g.drain().then_inc(staged, 1)
                inv_rms(c, P)
            inv_rms(NT, NS)

        @block.vector
        def _(v):
            v.memset(H[:], 0.0)
            v.sem_inc(chunk_done, 1)
            v.sem_inc(h_ready, 1)
            v.sem_inc(y_stored, 16)
            v.wait_ge(consts, 16 * NCONST)
            for ch in range(DC):
                nc.vector.tensor_scalar(cv[:, ch], k.xbcT[:, ch, 0:SEQ], cw[:, ch, 0:1], None, ALU.mult)
                for tap in range(1, 4):
                    v.drain()
                    nc.vector.scalar_tensor_tensor(out=cv[:, ch], in0=k.xbcT[:, ch, tap:tap + SEQ],
                                                   scalar=cw[:, ch, tap:tap + 1], in1=cv[:, ch],
                                                   op0=ALU.mult, op1=ALU.add)
                v.drain().then_inc(conv_done, 1)

            def tap_w(tap):
                return bcast(cw[:, :, tap:tap + 1], [P, DC, NS])
            nc.vector.tensor_tensor(cvs[:], k.xbcS[:], tap_w(3), ALU.mult)
            for tap in range(3):
                nc.vector.tensor_tensor(cvt[:], sconv[:, :, tap, :], tap_w(tap), ALU.mult)
                v.drain()
                nc.vector.tensor_tensor(cvs[:], cvs[:], cvt[:], ALU.add)
                v.drain()
            nc.vector.tensor_tensor(cvs[:], cvs[:], bcast(cb[:].rearrange("p (c a) -> p c a", a=1), [P, DC, NS]), ALU.add)
            v.drain().then_inc(conv_done, 1)

            raw = k.gd[:, :, G:G + 8]
            b9 = bcast(dtb[:].rearrange("p (a h) -> p a h", a=1), [P, NT + 1, 8])
            nc.vector.tensor_tensor(sp1[:], raw, b9, ALU.add)
            v.drain()
            nc.vector.tensor_scalar(sp2[:], sp1[:], -1.0, None, ALU.mult)
            v.drain()
            nc.vector.tensor_tensor(sp2[:], sp2[:], sp1[:], ALU.min)
            nc.vector.tensor_scalar(dt[:], sp1[:], 0.0, None, ALU.max)
            v.drain().then_inc(sp_v, 1)
            v.wait_ge(sp_a, 1)
            nc.vector.tensor_scalar(sp1[:], sp2[:], 1.0, None, ALU.add)
            v.drain()
            nc.vector.tensor_scalar(sp1[:], sp1[:], 1.0, None, ALU.subtract)
            v.drain()
            nc.vector.tensor_scalar(sp4[:], sp1[:], 0.0, None, ALU.is_equal)
            nc.vector.tensor_scalar(sp1[:], sp1[:], 1e-30, None, ALU.max)
            v.drain()
            nc.vector.reciprocal(sp1[:], sp1[:])
            v.drain()
            nc.vector.tensor_tensor(sp3[:], sp3[:], sp1[:], ALU.mult)
            v.drain()
            nc.vector.tensor_tensor(sp3[:], sp3[:], sp4[:], ALU.add)
            v.drain()
            nc.vector.tensor_tensor(sp3[:], sp3[:], sp2[:], ALU.mult)
            v.drain()
            nc.vector.tensor_tensor(dt[:], dt[:], sp3[:], ALU.add)
            nc.vector.tensor_scalar(alog[:], alog[:], -1.0, None, ALU.mult)
            v.drain()
            nc.vector.tensor_tensor(dtA[:], dt[:], bcast(alog[:].rearrange("p (a h) -> p a h", a=1), [P, NT + 1, 8]), ALU.mult)
            nc.vector.tensor_scalar(k.gd[:, :, 0:G], k.gd[:, :, 0:G], 1.0, None, ALU.add)
            v.drain().then_inc(sp_v, 1)
            nc.vector.reciprocal(k.gd[:, :, 0:G], k.gd[:, :, 0:G])
            v.wait_ge(sums_done, 1)
            acum = pB[:, 0:64].rearrange("p (c h) -> p c h", h=8)
            nc.vector.tensor_copy(pr[:, :, 0], dt[:, 0:NT])
            nc.vector.tensor_copy(pr[:, :, 1], dtA[:, 0:NT])
            nc.vector.tensor_copy(pr[:, :, 2], acum)
            v.drain()
            nc.vector.tensor_tensor(pr[:, :, 4], pB[:, 64:128].rearrange("p (c h) -> p c h", h=8), pr[:, :, 2], ALU.subtract)
            nc.vector.tensor_copy(pr[:, :, 5], pB[:, 64:128].rearrange("p (c h) -> p c h", h=8))
            v.drain().then_inc(sp_v, 1)
            v.wait_ge(sp_a, 2)
            nc.vector.tensor_tensor(pr[:, :, 4], pr[:, :, 4], pr[:, :, 0], ALU.mult)
            v.drain().then_inc(pr_ready, 1)

            def gate_norm(yin, R, n):
                v.wait_ge(z_loaded, n * 16 + 16)
                v.wait_ge(y_stored, n * 16 + 16)
                nc.vector.tensor_tensor(y2[0:R], yin, zt[0:R], ALU.mult)
                v.drain()
                for gr in range(2):
                    nc.vector.tensor_tensor_reduce(sq[0:R, gr * 256:gr * 256 + 256], y2[0:R, gr * 256:gr * 256 + 256],
                                                   y2[0:R, gr * 256:gr * 256 + 256], 1.0 / 256, EPS, ALU.mult, ALU.add,
                                                   ms[0:R, gr:gr + 1])
                v.drain().then_inc(ms_ready, 1)
                v.wait_ge(rms_ready, n + 1)
                for gr in range(2):
                    cols = slice(gr * 256, gr * 256 + 256)
                    nc.vector.scalar_tensor_tensor(out=y2[0:R, cols], in0=y2[0:R, cols], scalar=ms[0:R, 2 + gr:3 + gr],
                                                   in1=normw[0:R, cols], op0=ALU.mult, op1=ALU.mult)
                v.drain().then_inc(y_ready, 1)

            def heads(ap):
                return ap.rearrange("p (h e) -> p h e", e=HD)

            def per_head(kind):
                return bcast(prs[:, kind, :].rearrange("p (h a) -> p h a", a=1), [P, 8, HD])

            dsk = bcast(dskip[:].rearrange("p (h a) -> p h a", a=1), [P, 8, HD])
            with v.Fori(0, NT) as c:
                v.wait_ge(in_psum, c + 1)
                for h in range(8):
                    nc.vector.scalar_tensor_tensor(out=Dm[:, h], in0=pR[:, h // 4, (h % 4) * P:(h % 4 + 1) * P],
                                                   scalar=prs[:, 2, h:h + 1], in1=mneg[:], op0=ALU.subtract, op1=ALU.add)
                v.drain().then_inc(d_ready, 1)
                nc.vector.tensor_tensor(heads(xdt[:]), heads(pX[:]), per_head(0), ALU.mult)
                nc.vector.tensor_tensor(heads(xdd[:]), heads(pX[:]), per_head(4), ALU.mult)
                nc.vector.tensor_tensor(heads(Dx[:]), heads(pX[:]), dsk, ALU.mult)
                nc.vector.tensor_copy(Bt[:], pB[:, 0:256])
                v.drain().then_inc(xd_ready, 1)
                v.wait_ge(exp_ready, c + 1)
                for gr in range(2):
                    cbt = bcast(pB[:, 256 + gr * P:384 + gr * P].rearrange("p (a l) -> p a l", a=1), [P, 4, P])
                    nc.vector.tensor_tensor(Dm[:, gr * 4:gr * 4 + 4], Dm[:, gr * 4:gr * 4 + 4], cbt, ALU.mult)
                v.drain().then_inc(m_ready, 1)
                v.wait_ge(yoff_done, c + 1)
                nc.vector.tensor_tensor(heads(H[:]), heads(H[:]), per_head(5), ALU.mult)
                nc.vector.tensor_tensor(heads(y[:]), heads(pY2[:]), per_head(3), ALU.mult)
                v.drain()
                nc.vector.tensor_tensor(y[:], y[:], Dx[:], ALU.add)
                v.wait_ge(state_done, c + 1)
                nc.vector.tensor_tensor(H[:], H[:], pS[:], ALU.add)
                v.drain().then_inc(h_ready, 1)
                nc.vector.tensor_tensor(y[:], y[:], pY1[:], ALU.add)
                v.drain().then_inc(chunk_done, 1)
                gate_norm(y[:], P, c)

            v.wait_ge(side_ps, 1)
            nc.vector.tensor_copy(cvo[:, 0:512], pX[0:8, :])
            nc.vector.tensor_copy(cvo[:, 512:D], pY1[0:8, :])
            nc.vector.tensor_copy(cvp[0:3, 0:512], pY2[0:3, :])
            nc.vector.tensor_copy(cvp[0:3, 512:D], pS[0:3, :])
            v.drain().then_inc(side_sb, 1)
            v.wait_ge(side_ps, 2)
            nc.vector.tensor_copy(Hout[:], pX[:].rearrange("p (c n) -> p c n", n=P))
            v.drain().then_inc(side_sb, 1)
            v.wait_ge(side_ps, 3)
            nc.vector.tensor_copy(dT[:, 0:16], pY1[0:8, 0:16])
            nc.vector.tensor_copy(bc[:], pY2[0:8, :])
            v.drain().then_inc(side_sb, 1)
            v.wait_ge(side_ps, 4)
            nc.vector.tensor_copy(dE[:], pS[:, 0:68].rearrange("p (c n) -> p c n", n=17))
            v.drain()
            nc.vector.tensor_tensor(xdtS[:], cvs[:, 0:4], dE[:, :, 0:8], ALU.mult)
            v.wait_ge(prep, 16 * NS)
            v.drain()
            with v.Fori(0, NS) as b:
                v.wait_ge(bc_ps, b + 1)
                nc.vector.tensor_scalar(bcm[:], bc[:], k.ident[0:8, bass.ds(b, 1)], None, ALU.mult)
                v.drain().then_inc(bc_ready, 1)
                hb = h0[:, bass.ds(b, 1)].rearrange("q b c n -> q (b c) n")
                nc.vector.tensor_tensor(hb, hb, bcast(dE[:, :, bass.ds(b + 8, 1)], [P, 4, P]), ALU.mult)
                v.wait_ge(bc_ps, b + 2)
                for gr in range(2):
                    bb = bcast(pX[:, gr * P:gr * P + P].rearrange("p (a l) -> p a l", a=1), [P, 2, P])
                    nc.vector.tensor_tensor(hx[:, 2 * gr:2 * gr + 2], bb,
                                            bcast(xdtS[:, 2 * gr:2 * gr + 2, bass.ds(b, 1)], [P, 2, P]), ALU.mult)
                v.drain()
                nc.vector.tensor_tensor(hb, hb, hx[:], ALU.add)
                v.drain().then_inc(hn_ready, 1)
                for gr in range(2):
                    cc = bcast(pX[:, 256 + gr * P:384 + gr * P].rearrange("p (a l) -> p a l", a=1), [P, 2, P])
                    hg = h0[:, bass.ds(b, 1), 2 * gr:2 * gr + 2].rearrange("q b c n -> q (b c) n")
                    nc.vector.tensor_tensor(hx[:, 2 * gr:2 * gr + 2], hg, cc, ALU.mult)
                v.drain()
                nc.vector.tensor_reduce(ys[:, :, bass.ds(b, 1)], hx[:], AX.X, ALU.add)
                v.drain()
            nc.vector.tensor_tensor(xdtS[:], cvs[:, 0:4], bcast(dE[:, :, 16:17], [P, 4, NS]), ALU.mult)
            v.drain()
            nc.vector.tensor_tensor(ys[:], ys[:], xdtS[:], ALU.add)
            v.drain().then_inc(bc_ready, 1)
            v.wait_ge(side_ps, 5)
            gate_norm(pY1[0:NS, :], NS, NT)

        @block.scalar
        def _(act):
            for ch in range(DC):
                act.wait_ge(conv_done, ch + 1)
                nc.scalar.activation(cv[:, ch], cv[:, ch], ACT.Silu, bias=cb[:, ch:ch + 1]).then_inc(silu_done, 1)
            act.wait_ge(conv_done, DC + 1)
            nc.scalar.activation(cvs[:], cvs[:], ACT.Silu).then_inc(silu_done, 1)
            nc.scalar.activation(k.gd[:, :, 0:G], k.gd[:, :, 0:G], ACT.Exp, scale=-1.0)
            nc.scalar.activation(alog[:], alog[:], ACT.Exp)
            act.wait_ge(sp_v, 1)
            nc.scalar.activation(sp2[:], sp2[:], ACT.Exp)
            act.drain()
            nc.scalar.activation(sp3[:], sp2[:], ACT.Ln, bias=1.0)
            act.drain().then_inc(sp_a, 1)
            act.wait_ge(sp_v, 3)
            nc.scalar.activation(pr[:, :, 3], pr[:, :, 2], ACT.Exp)
            nc.scalar.activation(pr[:, :, 4:6], pr[:, :, 4:6], ACT.Exp)
            nc.scalar.activation(sp1[0:8, NT], dtA[0:8, NT], ACT.Exp)
            act.drain().then_inc(sp_a, 1)
            with act.Fori(0, NT) as c:
                act.wait_ge(d_ready, c + 1)
                nc.scalar.activation(Dm[:], Dm[:], ACT.Exp).then_inc(exp_ready, 1)

        @block.tensor
        def _(pe):
            pe.sem_inc(bc_ps, 1)
            pe.wait_ge(sp_v, 2)
            nc.tensor.matmul(pB[:, 0:64], k.mask_le[:], dtA[:, 0:NT].rearrange("p c h -> p (c h)"), start=True, stop=True)
            nc.tensor.matmul(pB[:, 64:128], k.ones[:], dtA[:, 0:NT].rearrange("p c h -> p (c h)"), start=True,
                             stop=True).then_inc(sums_done, 1)
            with pe.Fori(0, NT) as c:
                pe.wait_ge(staged, c + 1)
                for i in range(4):
                    nc.tensor.transpose(pX[:, i * P:(i + 1) * P], cs[:, i], k.ident[:])
                for i in range(2):
                    nc.tensor.transpose(pB[:, i * P:(i + 1) * P], cs[:, 4 + i], k.ident[:])
                for gr in range(2):
                    nc.tensor.matmul(pB[:, 256 + gr * P:384 + gr * P], cs[:, 4 + gr], cs[:, 6 + gr], start=True, stop=True)
                for h in range(8):
                    mm = nc.tensor.matmul(pR[:, h // 4, (h % 4) * P:(h % 4 + 1) * P],
                                          bcast(prs[:, 1, h:h + 1], [P, P]), k.mask_le[:], start=True, stop=True)
                mm.then_inc(in_psum, 1)
                pe.wait_ge(h_ready, c + 1)
                for gr in range(2):
                    mm = nc.tensor.matmul(pY2[:, gr * 256:gr * 256 + 256], cs[:, 6 + gr], H[:, gr * 256:gr * 256 + 256],
                                          start=True, stop=True)
                mm.then_inc(yoff_done, 1)
                pe.wait_ge(m_ready, c + 1)
                for h in range(8):
                    mm = nc.tensor.matmul(pY1[:, h * HD:(h + 1) * HD], Dm[:, h], xdt[:, h * HD:(h + 1) * HD],
                                          start=True, stop=True)
                mm.then_inc(ydiag_done, 1)
                pe.wait_ge(xd_ready, c + 1)
                for gr in range(2):
                    mm = nc.tensor.matmul(pS[:, gr * 256:gr * 256 + 256], Bt[:, gr * P:(gr + 1) * P],
                                          xdd[:, gr * 256:gr * 256 + 256], start=True, stop=True)
                mm.then_inc(state_done, 1)
            pe.wait_ge(chunk_done, NT + 1)
            for i in range(DC):
                nc.tensor.transpose((pX if i < 4 else pY1)[0:8, (i % 4) * P:(i % 4 + 1) * P], k.xbcS[:, i], k.ident[:])
            for i in range(DC):
                mm = nc.tensor.transpose((pY2 if i < 4 else pS)[0:3, (i % 4) * P:(i % 4 + 1) * P],
                                         k.xbcT[:, i, SEQ:SEQ + 3], k.ident[:])
            mm.then_inc(side_ps, 1)
            pe.wait_ge(side_sb, 1)
            for i in range(4):
                mm = nc.tensor.transpose(pX[:, i * P:(i + 1) * P], H[:, i * P:(i + 1) * P], k.ident[:])
            mm.then_inc(side_ps, 1)
            pe.wait_ge(side_sb, 2)
            pe.wait_ge(silu_done, DC + 1)
            pe.wait_ge(sp_a, 2)
            nc.tensor.transpose(pY1[0:8, 0:8], dt[0:8, NT], k.ident[0:8, 0:8])
            nc.tensor.transpose(pY1[0:8, 8:16], sp1[0:8, NT], k.ident[0:8, 0:8])
            for i in range(4):
                mm = nc.tensor.transpose(pY2[0:8, i * P:(i + 1) * P], cvs[:, 4 + i], k.ident[:])
            mm.then_inc(side_ps, 1)
            pe.wait_ge(side_sb, 3)
            for i in range(4):
                mm = nc.tensor.matmul(pS[:, i * 17:(i + 1) * 17], expand[:, i * P:(i + 1) * P], dT[:], start=True, stop=True)
            mm.then_inc(side_ps, 1)
            with pe.Fori(0, NS) as b:
                pe.wait_ge(bc_ready, b + 1)
                nc.tensor.matmul(pX[:], k.ones[0:8, :], bcm[:], start=True, stop=True).then_inc(bc_ps, 1)
            pe.wait_ge(bc_ready, NS + 1)
            for i in range(4):
                mm = nc.tensor.transpose(pY1[0:8, i * P:(i + 1) * P], ys[:, i], k.ident[:])
            mm.then_inc(side_ps, 1)


GP = 32
EC = HD // 2
PB = 8
PROMPT_DMAS = 16 * (2 * 2 * NT + 1)


def compress(nc, k, d):
    with ExitStack() as ctx:
        def sb(name, shape, dt=F32):
            return ctx.enter_context(nc.sbuf_tensor(name, shape, dt))

        def ps(name, shape):
            return ctx.enter_context(nc.psum_tensor(name, shape, F32))

        def sem(name):
            k.sems.append(ctx.enter_context(nc.semaphore(name)))
            return k.sems[-1]

        w1 = sb("cmp_w1_sb", [P, 2, EC, P])
        w2 = sb("cmp_w2_sb", [P, 2, HD])
        b1, b1p = sb("cmp_b1_sb", [P, 2]), sb("cmp_b1_pe", [P, 2])
        b2k, b2v = sb("cmp_b2k", [P, 1]), sb("cmp_b2v", [P, HD])
        pt = sb("page_row", [1, NS * NPAGE], I32)
        X = [sb(f"pages{u}", [P, GP * KV]) for u in range(2)]
        hid = [sb(f"hid{u}", [P, 2, 2, 2 * GP]) for u in range(2)]
        ph = [ps(f"ph{u}", [P, 512]) for u in range(2)]
        pk, pv = ps("cmp_pk", [P, 512]), ps("cmp_pv", [P, 512])

        consts, w1_loaded = sem("cmp_consts"), sem("w1_loaded")
        pages_loaded = [sem(f"pages_loaded{u}") for u in range(2)]
        pages_used = [sem(f"pages_used{u}") for u in range(2)]
        hid_ready = [sem(f"hid_ready{u}") for u in range(2)]
        pe_folded, kv_in_psum, kv_copied = sem("pe_folded"), sem("cmp_kv_in_psum"), sem("cmp_kv_copied")
        pt_loaded = sem("pt_loaded")
        block = ctx.enter_context(nc.Block())
        NPP = SEQ // PAGE
        cached = [X[u][:].rearrange("p (g c k b) -> p c k g b", c=EC, k=2, b=4) for u in range(2)]
        prompt = X[0][:].rearrange("p (g b k h c) -> p g b k h c", b=2, k=2, h=2, c=EC)

        @block.sync
        def _(sp):
            sp.dma_start(pt[:], d["page_table"]).then_inc(pt_loaded, 16)
            rows = d["kv_cmp_prompt"].rearrange("(g b l) (k h s c) -> s l g b k h c", b=2, l=64, k=2, h=2, s=2)
            for s in range(2):
                for g in range(NPP):
                    for b in range(2):
                        sp.dma_start(prompt[s * 64:s * 64 + 64, g, b], rows[s, :, g, b]).then_inc(pages_loaded[0], 16)
            sp.dma_start(X[0][:, NPP * KV:(NPP + 1) * KV], d["pe_page"]).then_inc(pages_loaded[0], 16)
            sp.dma_start(w1[:], d["cmp_w1"]).then_inc(w1_loaded, 16)
            sp.dma_start(w2[:], d["cmp_w2"].rearrange("k f e -> f k e")).then_inc(consts, 16)
            sp.dma_start(b1[:], d["cmp_b1"]).then_inc(consts, 16)
            sp.dma_start(b2k[:], d["cmp_b2k"]).then_inc(consts, 16)
            sp.dma_start(b2v[:], bcast(d["cmp_b2v"], [P, HD])).then_inc(consts, 16)
            sp.wait_ge(pt_loaded, 16)
            with sp.Fori(0, NS) as b:
                for u in (1, 0):
                    sp.wait_ge(pages_used[u], b + 1)
                    for i in range(GP // PB):
                        _, pages = nc.values_load_multi_w_load_instructions(
                            pt[0:1, bass.ds(b * NPAGE + (GP if u == 0 else 0) + i * PB, PB)], engines=[sp.engine],
                            min_val=0, max_val=d["cache_kv_cmp"].shape[0] // PAGE - 1,
                            skip_runtime_bounds_check_because="a page table names pages of the pool")
                        for n, page in enumerate(pages):
                            at = (i * PB + n) * KV
                            sp.dma_start(X[u][:, at:at + KV],
                                         d["cache_kv_cmp"][bass.ds(page * PAGE, PAGE)]).then_inc(pages_loaded[u], 16)

        def layer1(u, moving, n):
            for kv in range(2):
                for c in range(EC):
                    mm = nc.tensor.matmul(ph[u][:, kv * P:kv * P + n], w1[:, kv, c], moving(c, kv),
                                          start=(c == 0), stop=(c == EC - 1))
            mm.then_inc(pages_used[u], 1)

        @block.tensor
        def _(pe):
            pe.wait_ge(w1_loaded, 16)
            pe.wait_ge(pages_loaded[0], PROMPT_DMAS)
            layer1(0, lambda c, kv: prompt[:, 0:NPP + 1, :, kv, :, c], 4 * (NPP + 1))
            pe.wait_ge(consts, 64)
            pe.wait_ge(hid_ready[0], 1)
            for g in range(2):
                nc.tensor.matmul(pk[g * 64:g * 64 + 64, 0:2 * NPP], w2[:, 0], hid[0][:, 0, g, 0:2 * NPP],
                                 start=True, stop=True)
                mm = nc.tensor.matmul(pv[0:2 * NPP, g * 64:g * 64 + 64], hid[0][:, 1, g, 0:2 * NPP], w2[:, 1],
                                      start=True, stop=True)
            mm.then_inc(kv_in_psum, 1)
            with pe.Fori(0, NS) as b:
                for u in (1, 0):
                    pe.wait_ge(pages_loaded[u], b * 16 * GP + 16 * GP + (PROMPT_DMAS if u == 0 else 0))
                    pe.wait_ge(hid_ready[u], b + 1)
                    layer1(u, lambda c, kv: cached[u][:, c, kv], 4 * GP)
                pe.wait_ge(kv_copied, b + 1)
                for u in (1, 0):
                    pe.wait_ge(hid_ready[u], b + 2)
                    at = GP * 2 if u == 0 else 0
                    for g in range(2):
                        nc.tensor.matmul(pk[g * 64:g * 64 + 64, at:at + 2 * GP], w2[:, 0], hid[u][:, 0, g],
                                         start=True, stop=True)
                        mm = nc.tensor.matmul(pv[at:at + 2 * GP, g * 64:g * 64 + 64], hid[u][:, 1, g], w2[:, 1],
                                              start=True, stop=True)
                mm.then_inc(kv_in_psum, 1)

        @block.scalar
        def _(act):
            act.sem_inc(hid_ready[1], 1)
            act.sem_inc(pages_used[1], 1)

            def silu(u, npages):
                for kv in range(2):
                    src = ph[u][:, kv * P:kv * P + 4 * npages].rearrange("f (gb h) -> f h gb", h=2)
                    nc.scalar.activation(hid[u][:, kv, :, 0:2 * npages], src, ACT.Silu, bias=b1p[:, kv:kv + 1])
                act.drain().then_inc(hid_ready[u], 1)

            act.wait_ge(pe_folded, 1)
            silu(0, NPP)
            with act.Fori(0, NS) as b:
                for u in (1, 0):
                    act.wait_ge(pages_used[u], b + 2)
                    act.wait_ge(kv_in_psum, b + 1)
                    silu(u, GP)

        @block.vector
        def _(v):
            v.wait_ge(consts, 64)
            v.wait_ge(pages_used[0], 1)
            nc.vector.tensor_tensor(b1p[:], b1[:], ph[0][:, 4 * NPP:4 * NPP + P + 1:P], ALU.add)
            v.drain().then_inc(pe_folded, 1)
            v.wait_ge(kv_in_psum, 1)
            n = 2 * NPP
            nc.vector.tensor_scalar(k.kcT_p[:], pk[:, 0:n], b2k[:, 0:1], None, ALU.add)
            nc.vector.tensor_tensor(k.vc_p[:], pv[0:n, 0:P].rearrange("p (h e) -> p h e", h=2),
                                    bcast(b2v[0:n].rearrange("p (a e) -> p a e", a=1), [n, 2, HD]), ALU.add)
            v.drain().then_inc(kv_copied, 1)
            with v.Fori(0, NS) as b:
                v.wait_ge(kv_in_psum, b + 2)
                nc.vector.tensor_scalar(k.kcT_s[:, bass.ds(b, 1)].rearrange("p a n -> p (a n)"), pk[:, 0:P],
                                        b2k[:, 0:1], None, ALU.add)
                nc.vector.tensor_tensor(k.vc_s[:, bass.ds(b, 1)].rearrange("p a h e -> p (a h) e"),
                                        pv[:, 0:P].rearrange("p (h e) -> p h e", h=2),
                                        bcast(b2v[:].rearrange("p (a e) -> p a e", a=1), [P, 2, HD]), ALU.add)
                v.drain().then_inc(kv_copied, 1)


WIN_T = 512 // P


def attend(nc, k, d):
    with ExitStack() as ctx:
        def sb(name, shape, dt=F32):
            return ctx.enter_context(nc.sbuf_tensor(name, shape, dt))

        def ps(name, shape):
            return ctx.enter_context(nc.psum_tensor(name, shape, F32))

        def sem(name):
            k.sems.append(ctx.enter_context(nc.semaphore(name)))
            return k.sems[-1]

        V = [sb(f"v_rows{br}", [P, NT, P]) for br in range(2)]
        K = [k.kselT, k.kwinT]
        diag, oldest = sb("mask_diag", [P, P]), sb("mask_oldest", [P, P])
        visn, vis = sb("cmp_mask", [P, NT, 16]), sb("cmp_vis", [P, NT, 16])
        spread, slot = sb("spread16", [16, P]), sb("slot_mask", [P, 8])
        kbd, vbd = sb("kc_blockdiag", [P, 32]), sb("vc_blockdiag", [P, 512])
        qst = [sb(f"q_staged{g}", [P, P]) for g in range(2)]
        Pr = [sb(f"probs{u}", [P, SEQ]) for u in range(2)]
        PT = sb("probsT", [P, NT, P])
        y = sb("nsa_y", [P, 512])
        nm, L, r = sb("neg_max", [P, 4]), sb("row_sum", [P, 4]), sb("gate_over_sum", [P, 4])
        Pc, PcT, mc, lc = sb("cmp_probs", [P, P]), sb("cmp_probsT", [P, P]), sb("cmp_max", [P, 8]), sb("cmp_sum", [P, 8])
        pS = [ps(f"att_pS{u}", [P, 2, 512]) for u in range(2)]
        pT = ps("att_pT", [P, 2, 512])
        pO = [ps(f"att_pO{u}", [P, 512]) for u in range(2)]

        consts = sem("att_consts")
        c_scores, c_shift, c_exp, c_probs, c_turned, c_turned_sb, c_out, y_start = (
            sem(n) for n in ("c_scores", "c_shift", "c_exp", "c_probs", "c_turned", "c_turned_sb", "c_out", "y_start"))
        staged, s_done, max_ready, exp_done, t_done, pt_copied, pv_done, o_used = (
            sem(n) for n in ("q_is_staged", "s_done", "max_ready", "exp_done", "t_done", "pt_copied", "pv_done", "o_used"))
        y_stored, y_free = sem("nsa_y_stored"), sem("vbd_ready")
        zeros_ready, filled = sem("zeros_ready"), sem("slots_filled")
        zeros = sb("zero_rows", [P, D])
        block = ctx.enter_context(nc.Block())
        NC_ = 8

        def branch(j):
            return j // 2, j % 2

        def first_key(t, br):
            return 0 if br == 0 else max(0, t - WIN_T) * P

        def keys(t, br):
            return (t + 1) * P - first_key(t, br)

        @block.sync
        def _(sp):
            for dst, src in ((diag, "mask_diag"), (oldest, "mask_neg"), (visn, "cmp_mask"), (vis, "cmp_vis"),
                             (spread, "spread16"), (slot, "slot_mask")):
                sp.dma_start(dst[:], d[src]).then_inc(consts, 16)
            for v_sb, rows in zip(V, (d["kv_sel_prompt"], d["kv_win_all"][0:SEQ])):
                sp.dma_start(v_sb[:], rows.rearrange("(t p) c -> p t c", p=P)[:, :, P:KV]).then_inc(consts, 16)
            sp.wait_ge(zeros_ready, 1)
            sp.dma_start(d["y_slots"][MIN_BLK * P:NBLK * P].rearrange("(n p) c -> p n c", p=P),
                         bcast(zeros[:].rearrange("p (a c) -> p a c", a=1), [P, NBLK - MIN_BLK, D])).then_inc(filled, 16)
            for t in range(NT):
                sp.wait_ge(o_used, 16 * (t + 1) + 2)
                sp.dma_start(d["mix"][t * P:(t + 1) * P, 512:D], y[:]).then_inc(y_stored, 16)
            sp.wait_ge(y_stored, 16 * NT)
            sp.wait_ge(filled, 16)

        @block.gpsimd
        def _(g):
            g.memset(qst[0][:], 0.0)
            g.memset(qst[1][:], 0.0)
            g.memset(zeros[:], 0.0)
            g.drain().then_inc(zeros_ready, 1)
            for t in range(NT):
                with g.Fori(0, 4) as c:
                    g.wait_ge(s_done, c * 4 + (t * 16 + 4))
                    g.nop()
                    for gr in range(2):
                        rows = slice(gr * 64, gr * 64 + 64)
                        nc.gpsimd.tensor_copy(qst[gr][rows, :],
                                              k.qrT[rows, bass.ds(c, 1), t * P:(t + 1) * P].rearrange("p a n -> p (a n)"))
                    g.drain().then_inc(staged, 1)

        @block.tensor
        def _(pe):
            pe.sem_inc(s_done, 4)
            pe.sem_inc(pv_done, 1)
            pe.wait_ge(consts, 16 * NC_)
            nc.tensor.matmul(pT[:, 0, 0:P], spread[:], k.vc_p[:].rearrange("p h e -> p (h e)"), start=True,
                             stop=True).then_inc(c_turned, 1)

            def scores(t, c, j):
                br, gr = branch(j)
                k0, n = first_key(t, br), keys(t, br)
                for i in range(0, n, 512):
                    w = min(512, n - i)
                    mm = nc.tensor.matmul(pS[j % 2][:, i // 512, 0:w], qst[gr][:], K[br][:, k0 + i:k0 + i + w],
                                          start=True, stop=True)
                mm.then_inc(s_done, 1)

            def values(t, c, j):
                br, gr = branch(j)
                k0, n = first_key(t, br) // P, keys(t, br) // P
                unit = c * 4 + (t * 16 + j)
                pe.wait_ge(exp_done, unit + 1)
                for i in range(n):
                    mm = nc.tensor.transpose(pT[:, i // 4, (i % 4) * P:(i % 4 + 1) * P], Pr[j % 2][:, i * P:(i + 1) * P],
                                             k.ident[:])
                mm.then_inc(t_done, 1)
                pe.wait_ge(pt_copied, unit + 1)
                pe.wait_ge(o_used, unit + 1)
                for i in range(n):
                    mm = nc.tensor.matmul(pO[j % 2][:, 0:P], PT[:, i], V[br][:, k0 + i], start=(i == 0), stop=(i == n - 1))
                mm.then_inc(pv_done, 1)

            for t in range(NT):
                if t:
                    pe.wait_ge(o_used, 16 * t + 2)
                else:
                    pe.wait_ge(y_free, 1)
                for c in range(4):
                    mm = nc.tensor.matmul(pS[0][:, 0, c * 32:c * 32 + 32], k.qT[:, c, t * P:(t + 1) * P], kbd[:],
                                          start=True, stop=True)
                mm.then_inc(c_scores, 1)
                pe.wait_ge(c_probs, t + 1)
                nc.tensor.transpose(pT[:, 0, 0:P], Pc[:], k.ident[:]).then_inc(c_turned, 1)
                pe.wait_ge(c_turned_sb, t + 1)
                nc.tensor.matmul(pO[0][:], PcT[:], vbd[:], start=True, stop=True).then_inc(c_out, 1)
                pe.wait_ge(y_start, t + 1)
                with pe.Fori(0, 4) as c:
                    pe.wait_ge(staged, c + (t * 4 + 1))
                    scores(t, c, 0)
                    for j in range(1, 4):
                        scores(t, c, j)
                        values(t, c, j - 1)
                    values(t, c, 3)

        @block.vector
        def _(v):
            v.sem_inc(o_used, 2)
            v.memset(kbd[:], 0.0)
            v.drain()
            nc.vector.tensor_copy(kbd[0:64, 0:16], k.kcT_p[0:64])
            nc.vector.tensor_copy(kbd[64:P, 16:32], k.kcT_p[64:P])
            v.wait_ge(c_turned, 1)
            for c in range(4):
                nc.vector.tensor_tensor(vbd[:, c * P:(c + 1) * P].rearrange("p (h e) -> p h e", e=HD),
                                        pT[:, 0, 0:P].rearrange("p (h e) -> p h e", e=HD),
                                        bcast(slot[:, 2 * c:2 * c + 2].rearrange("p (h a) -> p h a", a=1), [P, 2, HD]), ALU.mult)
            v.drain().then_inc(y_free, 1)

            def softmax_max(t, c, j):
                br, gr = branch(j)
                n = keys(t, br)
                S = pS[j % 2][:].rearrange("p a b -> p (a b)")
                v.wait_ge(s_done, c * 4 + (t * 16 + j + 5))
                nc.vector.tensor_tensor(S[:, n - P:n], S[:, n - P:n], diag[:], ALU.add)
                if br == 1 and t >= WIN_T:
                    nc.vector.tensor_tensor(S[:, 0:P], S[:, 0:P], oldest[:], ALU.add)
                v.drain()
                nc.vector.tensor_reduce(nm[:, j:j + 1], S[:, 0:n], AX.X, ALU.max)
                v.drain()
                nc.vector.tensor_scalar(nm[:, j:j + 1], nm[:, j:j + 1], -SCALE, None, ALU.mult).then_inc(max_ready, 1)

            def add_out(t, c, j):
                br, gr = branch(j)
                unit = c * 4 + (t * 16 + j)
                v.wait_ge(pv_done, unit + 2)
                nc.vector.reciprocal(r[:, j:j + 1], L[:, j:j + 1])
                v.drain()
                nc.vector.tensor_tensor(r[:, j:j + 1], r[:, j:j + 1],
                                        k.gd[:, t, bass.ds(c * 2 + ((br + 1) * 8 + gr), 1)], ALU.mult)
                v.drain()
                ys = y[:, bass.ds(c * P + gr * HD, HD)]
                nc.vector.scalar_tensor_tensor(out=ys, in0=pO[j % 2][:, gr * HD:gr * HD + HD], scalar=r[:, j:j + 1], in1=ys,
                                               op0=ALU.mult, op1=ALU.add)
                v.drain().then_inc(o_used, 1)

            for t in range(NT):
                v.wait_ge(c_scores, t + 1)
                hs = Pc[:].rearrange("p (h j) -> p h j", j=16)
                nc.vector.tensor_tensor(hs, pS[0][:, 0, 0:P].rearrange("p (h j) -> p h j", j=16),
                                        bcast(visn[:, t:t + 1], [P, 8, 16]), ALU.add)
                v.drain()
                nc.vector.tensor_reduce(mc[:], hs, AX.X, ALU.max)
                v.drain()
                nc.vector.tensor_tensor(hs, hs, bcast(mc[:].rearrange("p (h a) -> p h a", a=1), [P, 8, 16]), ALU.subtract)
                v.drain().then_inc(c_shift, 1)
                v.wait_ge(c_exp, t + 1)
                nc.vector.tensor_reduce(lc[:], hs, AX.X, ALU.add)
                v.drain()
                nc.vector.tensor_tensor(hs, hs, bcast(vis[:, t:t + 1], [P, 8, 16]), ALU.mult)
                v.drain()
                nc.vector.reciprocal(lc[:], lc[:])
                v.drain()
                nc.vector.tensor_tensor(lc[:], lc[:], k.gd[:, t, 0:8], ALU.mult)
                v.drain()
                nc.vector.tensor_tensor(hs, hs, bcast(lc[:].rearrange("p (h a) -> p h a", a=1), [P, 8, 16]), ALU.mult)
                v.drain().then_inc(c_probs, 1)
                v.wait_ge(c_turned, t + 2)
                nc.vector.tensor_copy(PcT[:], pT[:, 0, 0:P])
                v.drain().then_inc(c_turned_sb, 1)
                v.wait_ge(c_out, t + 1)
                if t:
                    v.wait_ge(y_stored, 16 * t)
                nc.vector.tensor_copy(y[:], pO[0][:])
                v.drain().then_inc(y_start, 1)
                with v.Fori(0, 4) as c:
                    softmax_max(t, c, 0)
                    for j in range(1, 4):
                        softmax_max(t, c, j)
                        add_out(t, c, j - 1)
                    add_out(t, c, 3)

        @block.scalar
        def _(act):
            def exp(t, c, j):
                br, gr = branch(j)
                n = keys(t, br)
                act.wait_ge(max_ready, c * 4 + (t * 16 + j + 1))
                nc.scalar.activation(Pr[j % 2][:, 0:n], pS[j % 2][:].rearrange("p a b -> p (a b)")[:, 0:n], ACT.Exp,
                                     bias=nm[:, j:j + 1], scale=SCALE, accum_out=L[:, j:j + 1])
                act.drain().then_inc(exp_done, 1)

            def turn(t, c, j):
                br, gr = branch(j)
                unit = c * 4 + (t * 16 + j)
                n = keys(t, br) // P
                act.wait_ge(t_done, unit + 1)
                act.wait_ge(pv_done, unit + 1)
                nc.scalar.copy(PT[:].rearrange("p a b -> p (a b)")[:, 0:n * P],
                               pT[:].rearrange("p a b -> p (a b)")[:, 0:n * P]).then_inc(pt_copied, 1)

            for t in range(NT):
                act.wait_ge(c_shift, t + 1)
                nc.scalar.activation(Pc[:], Pc[:], ACT.Exp, scale=SCALE).then_inc(c_exp, 1)
                with act.Fori(0, 4) as c:
                    exp(t, c, 0)
                    for j in range(1, 4):
                        exp(t, c, j)
                        turn(t, c, j - 1)
                    turn(t, c, 3)


NJ = 16
QR = 32
UNITS = [(0, 0, 0), (0, 0, 1), (0, 1, 0), (0, 1, 1), (1, 0, 0), (1, 1, 0)]


def sample(nc, k, d):
    with ExitStack() as ctx:
        def sb(name, shape, dt=F32):
            return ctx.enter_context(nc.sbuf_tensor(name, shape, dt))

        def ps(name, shape):
            return ctx.enter_context(nc.psum_tensor(name, shape, F32))

        def sem(name):
            k.sems.append(ctx.enter_context(nc.semaphore(name)))
            return k.sems[-1]

        grp4, pick, e8, e8t = sb("grp4", [64, 16]), sb("pick_bg", [16, 2, P]), sb("e8", [8, P]), sb("e8t", [P, 8])
        jmask, iota, parity, wmask = sb("jmask", [P, NJ]), sb("iota128", [P, P]), sb("parity", [P, P]), sb("wmask", [P, 1])
        pti, ptf = sb("pt_int", [8, NPAGE], I32), sb("pt_f", [8, NPAGE])
        sA, sP, sPT = sb("cmpS", [P, 64]), sb("cmpP", [64, P]), sb("cmpPT", [P, 64])
        st1 = sb("cmp_stat", [64, 4])
        score, score2 = sb("score", [16, P]), sb("score2", [16, P])
        top, topi = sb("top", [16, 2, 8]), sb("topi", [16, 2, 8], U32)
        topf = sb("topf", [16, 16])
        pj, blk, T2, oh = sb("pj", [P, 2, NJ]), sb("blk", [P, 2]), sb("T2", [P, P]), sb("oh", [P, P])
        half, idxf, idx = sb("half", [P, 2]), sb("idxf", [P, 2, 2]), sb("idx", [P, 4], U32)
        oc, qtok, qb = sb("oc", [64, 8, 8]), sb("qtok", [8, 512]), sb("qb", [P, 512])
        W = QR + 1
        tile = [sb(f"kv_piece{u}", [P, W, 2, 2, HD]) for u in range(2)]
        prod = sb("prod", [P, 4 * W * HD])
        S = sb("piece_S", [P, 4, W])
        m, l = sb("piece_m", [P, 6, 4]), sb("piece_l", [P, 6, 4])
        O = sb("piece_O", [P, 6, 4, HD])
        mm_, mt, mtx = sb("both_m", [P, 2, 2, 4]), sb("m_by_sample", [16, 8]), sb("m_spread", [16, 8, NJ])
        Ms, w = sb("M", [P, 2, 2, 4]), sb("w", [P, 6, 4])
        lw, Ow = sb("lw", [P, 2, 2, 4]), sb("Ow", [P, 2, 2, 4, HD])
        g3, y, t8 = sb("g3", [8, 2, 2, 4]), sb("y8", [8, 4, 2, HD]), sb("t8", [8, 4, 2, HD])
        pA, pB, pC, pD = (ps(f"smp_p{c}", [P, 512]) for c in "ABCD")

        consts, dve, pe_, act_ = sem("smp_consts"), sem("smp_dve"), sem("smp_pe"), sem("smp_act")
        piece_loaded = [sem(f"piece_loaded{u}") for u in range(2)]
        gathered = [sem(f"gathered{u}") for u in range(2)]
        piece_used, idx_ready, shifted, expd, new_rows, stored, y_ready = (
            sem(n) for n in ("piece_used", "idx_ready", "shifted", "expd", "new_rows", "smp_stored", "y8_ready"))
        block = ctx.enter_context(nc.Block())
        NC_ = 10

        @block.sync
        def _(sp):
            for dst, name in ((grp4, "grp4"), (pick, "pick_bg"), (e8, "e8"), (e8t, "e8t"), (jmask, "jmask"), (iota, "iota"),
                              (parity, "parity"), (wmask, "wmask")):
                sp.dma_start(dst[:], d[name]).then_inc(consts, 16)
            sp.dma_start(pti[:], d["page_table"].rearrange("a (b p) -> (a b) p", p=NPAGE)).then_inc(consts, 16)
            sp.dma_start(d["kv_win_sample"][:, 0:511, :], d["cache_kv_win"][:, 1:512, :]).then_inc(stored, 16)
            sp.dma_start(d["kv_win_sample"][:, 511, :], d["kv_win_all"][SEQ:NTOK]).then_inc(stored, 16)
            sp.dma_start(tile[0][:, 0:QR].rearrange("p r a h e -> p (r a h e)"),
                         d["cache_kv_win"].rearrange("b (j r) c -> (b j) (r c)", r=QR)).then_inc(piece_loaded[0], 16)
            for b in range(NS):
                sp.dma_start(tile[0][b * NJ:(b + 1) * NJ, QR].rearrange("p a h e -> p (a h e)"),
                             bcast(d["kv_win_all"][SEQ + b:SEQ + b + 1], [NJ, KV])).then_inc(piece_loaded[0], 16)
            for n in range(4):
                u = (n + 1) % 2
                sp.wait_ge(gathered[u], 16 * (n // 2 + 1))
                for b in range(NS):
                    sp.dma_start(tile[u][b * NJ + NJ - 1:b * NJ + NJ, 0:QR].rearrange("p r a h e -> p r (a h e)"),
                                 bcast(d["kv_sel_sample"][b:b + 1].rearrange("a (c e) -> a c e", c=1), [1, QR, KV])
                                 ).then_inc(piece_loaded[u], 16)
            sp.wait_ge(y_ready, 1)
            sp.dma_start(d["mix"][SEQ:NTOK, 512:D], y[:].rearrange("p a b c -> p (a b c)")).then_inc(stored, 16)
            sp.wait_ge(stored, 48)

        @block.gpsimd
        def _(g):
            g.wait_ge(idx_ready, 1)
            for n in range(4):
                u = (n + 1) % 2
                if n:
                    g.wait_ge(piece_used, n)
                g.indirect_dma_start(tile[u][:, 0:QR].rearrange("p r a h e -> p (r a h e)"), None, d["cache_kv_sel"],
                                     bass.IndirectOffsetOnAxis(idx[:, n:n + 1], 0)).then_inc(gathered[u], 16)

        @block.tensor
        def _(pe):
            pe.wait_ge(consts, 16 * (NC_ - 1))
            for b in range(NS):
                for gr in range(2):
                    rows = slice(gr * 64, gr * 64 + 64)
                    nc.tensor.matmul((pA, pC)[gr][:, b * 4:b * 4 + 4], k.kcT_s[rows, b], k.qT[rows, :, SEQ + b],
                                     start=True, stop=True)
            for c in range(4):
                mm = nc.tensor.transpose(pB[0:8, c * P:(c + 1) * P], k.qrT[:, c, SEQ:NTOK], k.ident[:])
            mm.then_inc(pe_, 1)
            pe.wait_ge(dve, 1)
            nc.tensor.transpose(pC[0:64, 0:P], sA[:], k.ident[:]).then_inc(pe_, 1)
            nc.tensor.matmul(pD[:], e8[:], qtok[:], start=True, stop=True).then_inc(pe_, 1)
            nc.tensor.matmul(pA[:, 0:NPAGE], e8[:], ptf[:], start=True, stop=True).then_inc(pe_, 1)
            pe.wait_ge(dve, 2)
            nc.tensor.matmul(pC[0:16, P:2 * P], grp4[:], sP[:], start=True, stop=True)
            nc.tensor.transpose(pC[:, 2 * P:2 * P + 64], sP[:], k.ident[0:64, 0:64]).then_inc(pe_, 1)
            pe.wait_ge(dve, 3)
            for gr in range(2):
                mm = nc.tensor.matmul(pB[:, gr * NJ:(gr + 1) * NJ], pick[:, gr], topf[:], start=True, stop=True)
            mm.then_inc(pe_, 1)
            pe.wait_ge(dve, 4)
            for b in range(NS):
                for gr in range(2):
                    at = b * 8 + gr * 4
                    mm = nc.tensor.matmul(pA[0:64, at:at + 4], k.vc_s[:, b, gr], sPT[:, at:at + 4], start=True, stop=True)
            mm.then_inc(pe_, 1)
            pe.wait_ge(dve, 5)
            for h in range(8):
                mm = nc.tensor.transpose(pD[0:8, h * HD:(h + 1) * HD], oc[:, h], k.ident[0:64, 0:64])
            mm.then_inc(pe_, 1)
            pe.wait_ge(dve, 6)
            nc.tensor.transpose(pC[0:16, 0:P], mm_[:].rearrange("p a b c -> p (a b c)"), k.ident[:]).then_inc(pe_, 1)
            pe.wait_ge(dve, 7)
            nc.tensor.transpose(pC[:, P:P + 16], mtx[:].rearrange("p a b -> p (a b)"), k.ident[0:16, 0:16]).then_inc(pe_, 1)
            pe.wait_ge(dve, 8)
            nc.tensor.matmul(pC[0:8, 0:16], e8t[:], lw[:].rearrange("p a b c -> p (a b c)"), start=True, stop=True)
            for br, out in enumerate((pA, pB)):
                mm = nc.tensor.matmul(out[0:8, :], e8t[:], Ow[:, br].rearrange("p b c e -> p (b c e)"), start=True, stop=True)
            mm.then_inc(pe_, 1)

        @block.scalar
        def _(act):
            act.wait_ge(shifted, 1)
            nc.scalar.activation(sP[:], sP[:], ACT.Exp, scale=SCALE, accum_out=st1[:, 1:2])
            act.drain().then_inc(expd, 1)
            for n in range(6):
                act.wait_ge(shifted, n + 2)
                rows = QR + (1 if n < 2 else 0)
                nc.scalar.activation(S[:, :, 0:rows], S[:, :, 0:rows], ACT.Exp, scale=SCALE).then_inc(expd, 1)
            act.wait_ge(shifted, 8)
            nc.scalar.activation(w[:], w[:], ACT.Exp, scale=SCALE).then_inc(expd, 1)

        @block.vector
        def _(v):
            v.wait_ge(consts, 16 * (NC_ - 1))
            v.wait_ge(pe_, 1)
            for gr in range(2):
                nc.vector.tensor_copy(sA[:].rearrange("p (b g c) -> p b g c", b=8, g=2)[:, :, gr],
                                      (pA, pC)[gr][:, 0:32].rearrange("p (b c) -> p b c", c=4))
            nc.vector.tensor_copy(qtok[:], pB[0:8, :])
            nc.vector.tensor_copy(ptf[:], pti[:])
            v.drain().then_inc(dve, 1)
            v.wait_ge(pe_, 2)
            nc.vector.tensor_reduce(st1[:, 0:1], pC[0:64, 0:P], AX.X, ALU.max)
            v.drain()
            nc.vector.tensor_scalar(sP[:], pC[0:64, 0:P], st1[:, 0:1], None, ALU.subtract)
            v.drain().then_inc(shifted, 1)
            v.wait_ge(pe_, 3)
            nc.vector.tensor_copy(qb[:], pD[:])
            v.wait_ge(pe_, 4)
            T3 = T2[:].rearrange("p (a two) -> p a two", two=2)
            nc.vector.scalar_tensor_tensor(out=T3, in0=bcast(pA[:, 0:NPAGE].rearrange("p (a b) -> p a b", b=1), [P, NPAGE, 2]),
                                           scalar=2.0, in1=parity[:].rearrange("p (a two) -> p a two", two=2), op0=ALU.mult,
                                           op1=ALU.add)
            v.wait_ge(expd, 1)
            nc.vector.reciprocal(st1[:, 2:3], st1[:, 1:2])
            v.drain()
            nc.vector.tensor_scalar(sP[:], sP[:], st1[:, 2:3], None, ALU.mult)
            v.drain().then_inc(dve, 1)
            v.wait_ge(pe_, 5)
            nc.vector.tensor_copy(score[:], pC[0:16, P:2 * P])
            nc.vector.tensor_copy(sPT[:], pC[:, 2 * P:2 * P + 64])
            v.drain()
            v.memset(score[:, 0:P:P - 1], 1e4)
            v.drain()
            nc.vector.max(top[:, 0], score[:])
            v.drain()
            nc.vector.max_index(topi[:, 0], top[:, 0], score[:])
            nc.vector.match_replace(score2[:], top[:, 0], score[:], -1.0)
            v.drain()
            nc.vector.max(top[:, 1], score2[:])
            v.drain()
            nc.vector.max_index(topi[:, 1], top[:, 1], score2[:])
            v.drain()
            nc.vector.tensor_copy(topf[:], topi[:].rearrange("p a b -> p (a b)"))
            v.drain().then_inc(dve, 1)
            v.wait_ge(pe_, 6)
            nc.vector.tensor_tensor(pj[:], pB[:, 0:2 * NJ].rearrange("p (g j) -> p g j", g=2),
                                    bcast(jmask[:].rearrange("p (a j) -> p a j", a=1), [P, 2, NJ]), ALU.mult)
            v.drain()
            nc.vector.tensor_reduce(blk[:], pj[:], AX.X, ALU.add)
            for gr in range(2):
                v.drain()
                nc.vector.tensor_scalar(oh[:], iota[:], blk[:, gr:gr + 1], None, ALU.is_equal)
                v.drain()
                nc.vector.tensor_tensor(oh[:], oh[:], T2[:], ALU.mult)
                v.drain()
                nc.vector.tensor_reduce(half[:, gr:gr + 1], oh[:], AX.X, ALU.add)
            v.drain()
            for q in range(2):
                nc.vector.tensor_scalar(idxf[:, :, q], half[:], 2.0, float(q), ALU.mult, ALU.add)
            v.drain()
            nc.vector.tensor_copy(idx[:], idxf[:].rearrange("p g q -> p (g q)"))
            v.drain().then_inc(idx_ready, 1)
            v.drain().then_inc(dve, 1)
            v.wait_ge(pe_, 7)
            nc.vector.tensor_copy(oc[:].rearrange("p (c g) b -> p b g c", g=2),
                                  pA[0:64, 0:64].rearrange("p (b g c) -> p b g c", b=8, g=2))
            v.drain().then_inc(dve, 1)

            def piece(n, u, unit, rows):
                br, gr, _ = UNITS[unit]
                Kr = tile[u][:, 0:rows, 0, gr]
                Vr = tile[u][:, 0:rows, 1, gr]
                pk = prod[:, 0:4 * rows * HD].rearrange("p (c r e) -> p c r e", c=4, e=HD)
                for c in range(4):
                    nc.vector.tensor_tensor(pk[:, c], Kr, bcast(qb[:, (c * 2 + gr) * HD:(c * 2 + gr + 1) * HD].rearrange(
                        "p (a e) -> p a e", a=1), [P, rows, HD]), ALU.mult)
                v.drain()
                nc.vector.tensor_reduce(S[:, :, 0:rows], pk, AX.X, ALU.add)
                v.drain()
                if rows > QR:
                    nc.vector.tensor_scalar(S[:, :, QR], S[:, :, QR], wmask[:, 0:1], None, ALU.add)
                    v.drain()
                nc.vector.tensor_reduce(m[:, unit], S[:, :, 0:rows], AX.X, ALU.max)
                v.drain()
                nc.vector.tensor_tensor(S[:, :, 0:rows], S[:, :, 0:rows],
                                        bcast(m[:, unit].rearrange("p (c a) -> p c a", a=1), [P, 4, rows]), ALU.subtract)
                v.drain().then_inc(shifted, 1)
                v.wait_ge(expd, n + 2)
                nc.vector.tensor_reduce(l[:, unit], S[:, :, 0:rows], AX.X, ALU.add)
                pv = prod[:, 0:4 * rows * HD].rearrange("p (c e r) -> p c e r", c=4, e=HD)
                for c in range(4):
                    nc.vector.tensor_tensor(pv[:, c], Vr.rearrange("p r e -> p e r"),
                                            bcast(S[:, c:c + 1, 0:rows], [P, HD, rows]), ALU.mult)
                v.drain()
                nc.vector.tensor_reduce(O[:, unit], pv, AX.X, ALU.add)
                v.drain()

            v.wait_ge(piece_loaded[0], 16 * (1 + NS))
            piece(0, 0, 4, QR + 1)
            piece(1, 0, 5, QR + 1)
            v.drain().then_inc(piece_used, 1)
            for n in range(4):
                u = (n + 1) % 2
                v.wait_ge(piece_loaded[u], (16 * (1 + NS) if u == 0 else 0) + 16 * NS * (n // 2 + 1))
                v.wait_ge(gathered[u], 16 * (n // 2 + 1))
                piece(n + 2, u, n, QR)
                v.drain().then_inc(piece_used, 1)

            ms = m[:, 0:4].rearrange("p (g q) c -> p g q c", g=2)
            nc.vector.tensor_tensor(mm_[:, 0], ms[:, :, 0], ms[:, :, 1], ALU.max)
            nc.vector.tensor_copy(mm_[:, 1], m[:, 4:6])
            v.drain().then_inc(dve, 1)
            v.wait_ge(pe_, 9)
            nc.vector.tensor_reduce(mt[:], pC[0:16, 0:P].rearrange("p (b j) -> p b j", j=NJ), AX.X, ALU.max)
            v.drain()
            nc.vector.tensor_copy(mtx[:], bcast(mt[:].rearrange("p (b a) -> p b a", a=1), [16, 8, NJ]))
            v.drain().then_inc(dve, 1)
            v.wait_ge(pe_, 10)
            nc.vector.tensor_copy(Ms[:].rearrange("p a b c -> p (a b c)"), pC[:, P:P + 16])
            v.drain()
            for q in range(2):
                nc.vector.tensor_tensor(w[:, 0:4].rearrange("p (g q) c -> p g q c", g=2)[:, :, q], ms[:, :, q], Ms[:, 0], ALU.subtract)
            nc.vector.tensor_tensor(w[:, 4:6], m[:, 4:6], Ms[:, 1], ALU.subtract)
            v.drain().then_inc(shifted, 1)
            v.wait_ge(expd, 8)
            nc.vector.tensor_tensor(l[:], l[:], w[:], ALU.mult)
            nc.vector.tensor_tensor(O[:].rearrange("p u c e -> p (u c) e"), O[:].rearrange("p u c e -> p (u c) e"),
                                    bcast(w[:].rearrange("p u (c a) -> p (u c) a", a=1), [P, 24, HD]), ALU.mult)
            v.drain()
            l4 = l[:, 0:4].rearrange("p (g q) c -> p g q c", g=2)
            O4 = O[:, 0:4].rearrange("p (g q) c e -> p g q (c e)", g=2)
            nc.vector.tensor_tensor(lw[:, 0], l4[:, :, 0], l4[:, :, 1], ALU.add)
            nc.vector.tensor_copy(lw[:, 1], l[:, 4:6])
            nc.vector.tensor_tensor(Ow[:, 0].rearrange("p g c e -> p g (c e)"), O4[:, :, 0], O4[:, :, 1], ALU.add)
            nc.vector.tensor_copy(Ow[:, 1], O[:, 4:6])
            v.drain().then_inc(dve, 1)
            v.wait_ge(pe_, 11)
            nc.vector.reciprocal(g3[:].rearrange("p a b c -> p (a b c)"), pC[0:8, 0:16])
            v.drain()
            for br in range(2):
                nc.vector.tensor_tensor(g3[:, br], g3[:, br], k.gd[0:8, NT, 8 * (br + 1):8 * (br + 2)].rearrange(
                    "p (c g) -> p g c", g=2), ALU.mult)
            nc.vector.tensor_tensor(y[:], pD[0:8, :].rearrange("p (c g e) -> p c g e", g=2, e=HD),
                                    bcast(k.gd[0:8, NT, 0:8].rearrange("p (c g a) -> p c g a", g=2, a=1), [8, 4, 2, HD]), ALU.mult)
            for br, src in enumerate((pA, pB)):
                v.drain()
                for gr in range(2):
                    nc.vector.tensor_tensor(t8[:, :, gr], src[0:8, gr * 256:gr * 256 + 256].rearrange("p (c e) -> p c e", e=HD),
                                            bcast(g3[:, br, gr].rearrange("p (c a) -> p c a", a=1), [8, 4, HD]), ALU.mult)
                v.drain()
                nc.vector.tensor_tensor(y[:], y[:], t8[:], ALU.add)
            v.drain().then_inc(y_ready, 1)


NE, TOPK, NGRP, KGRP = 64, 6, 8, 4
NBLK = (NTOK * TOPK + NE * (P - 1)) // P + 1
MIN_BLK = NTOK * TOPK // P
FE = 256


def alloc_routing(nc, ctx, k):
    def sb(name, shape, dt=F32):
        return ctx.enter_context(nc.sbuf_tensor(name, shape, dt))
    k.dest = sb("dest_slot", [P, NT + 1, TOPK], I32)
    k.wsel = sb("choice_weight", [P, NT + 1, TOPK])
    k.toks = sb("slot_token", [P, NBLK], I32)
    k.plan = sb("block_plan", [1, P], I32)


def route(nc, k, d):
    with ExitStack() as ctx:
        def sb(name, shape, dt=F32):
            return ctx.enter_context(nc.sbuf_tensor(name, shape, dt))

        def ps(name, shape):
            return ctx.enter_context(nc.psum_tensor(name, shape, F32))

        def sem(name):
            k.sems.append(ctx.enter_context(nc.semaphore(name)))
            return k.sems[-1]

        wo, wr = sb("w_out_sb", [P, DC, D]), sb("router_sb", [P, DC, P])
        sgu, sd = sb("shared_gu", [P, DC, 2 * FE]), sb("shared_down", [P, 2, D])
        gain, bias, rbias = sb("ln1_g_sb", [P, D]), sb("ln1_b_sb", [P, D]), sb("router_bias_sb", [P, NE])
        mx, xr, xs = sb("mix_tile", [P, D]), sb("res_tile", [P, D]), sb("x1_tile", [P, D])
        acc = sb("acc_tile", [P, D])
        mT, xT = sb("mixT", [P, DC, P]), sb("x1T", [P, DC, P])
        hs, eg, hT = sb("sh_h", [P, FE]), sb("sh_e", [P, FE]), sb("sh_hT", [P, 2, P])
        stats, mv, rstd = sb("stats1", [P, 2, 6]), sb("mv1", [P, 2]), sb("rstd1", [P, 2])
        mhalf, eps = sb("mhalf1", [P, 1]), sb("eps1", [P, 1])
        sc_, bi = sb("scores", [P, NE]), sb("biased", [P, NE])
        g8, gs, gt, gi, gif = sb("grp_top", [P, 8, 8]), sb("grp_score", [P, 8]), sb("grp_sorted", [P, 8]), sb("grp_idx", [P, 8], U32), sb("grp_idx_f", [P, 8])
        gk, keep = sb("grp_oh", [P, 8, KGRP]), sb("grp_keep", [P, 8])
        et, ei, ef = sb("exp_top", [P, 8]), sb("exp_idx", [P, 8], U32), sb("exp_choice", [P, NT + 1, TOPK])
        io64, lt, thr = sb("iota64", [P, NE]), sb("mask_lt", [P, P]), sb("block_starts", [P, 16])
        oh, ohw = sb("choice_oh", [P, TOPK, NE]), sb("choice_prod", [P, TOPK, NE])
        ws = sb("w_sum", [P, 2])
        mask, pre, dst = sb("chosen", [P, NT + 1, NE]), sb("tokens_before", [P, NT + 1, NE]), sb("dest_all", [P, NT + 1, NE])
        cmp_, nbl, incl = sb("cnt_cmp", [P, NE, 16]), sb("n_blocks_e", [P, NE]), sb("blocks_incl", [P, NE])
        dstf = sb("dest_f", [P, NT + 1, TOPK])
        tokf, toki = sb("tok_f", [P, NT + 1]), sb("tok_i", [P, NT + 1], I32)
        ip, ble, be = sb("iota_p", [P, 1]), sb("blk_cmp", [P, NE]), sb("blk_expert", [P, 1])
        half_counts = sb("half_counts", [1, NE])
        zi, st_i, st_f = sb("zero_i", [NBLK, P], I32), sb("slot_rows", [NBLK, P], I32), sb("slot_rows_f", [NBLK, P])
        pT = ps("r_pT", [P, 2, 512])
        pO = ps("r_pO", [P, 2, 512])
        pR, pG, pH = ps("r_pR", [P, 512]), ps("r_pG", [P, 512]), ps("r_pH", [P, 512])

        consts, w_loaded, in_loaded, mix_in_psum, mixT_ready, proj_done, in_used = (
            sem(n) for n in ("r_consts", "w_out_loaded", "in_loaded", "mix_in_psum", "mixT_ready", "proj_done", "in_used"))
        stats_ready, rstd_ready, x1_ready, x1_stored, x1_in_psum, x1T_ready, router_done, gu_done = (
            sem(n) for n in ("r_stats", "r_rstd", "x1_ready", "x1_stored", "x1_in_psum", "x1T_ready", "router_done", "gu_done"))
        exp_ready, h_ready, h_in_psum, hT_ready, down_done, acc_ready, acc_stored, r_free = (
            sem(n) for n in ("r_exp", "sh_h_ready", "sh_h_in_psum", "sh_hT_ready", "sh_down_done", "acc_ready", "acc_stored", "router_read"))
        dv, pp, zero_stored, dest_ready, scattered, slots_loaded, po_free = (
            sem(n) for n in ("d_steps", "p_steps", "zero_stored", "dest_ready", "scattered", "slots_loaded", "po_free"))
        block = ctx.enter_context(nc.Block())

        @block.sync
        def _(sp):
            sp.dma_start(wo[:], d["w_out"].rearrange("(c p) n -> p c n", p=P)).then_inc(w_loaded, 16)

            def load(t, R):
                sp.wait_ge(in_used, t + 1)
                sp.dma_start(mx[0:R], d["mix"][bass.ds(t * P, R)]).then_inc(in_loaded, 16)
                sp.dma_start(xr[0:R], d["xres"][bass.ds(t * P, R)]).then_inc(in_loaded, 16)

            def store(t, R):
                sp.wait_ge(x1_ready, t + 1)
                sp.dma_start(d["x1"][bass.ds(t * P, R)], xs[0:R]).then_inc(x1_stored, 16)
                sp.wait_ge(acc_ready, t + 1)
                sp.dma_start(d["acc"][bass.ds(t * P, R)], acc[0:R]).then_inc(acc_stored, 16)

            load(0, P)
            for dst_, src in ((gain, bcast(d["ln1_g"], [P, D])), (bias, bcast(d["ln1_b"], [P, D])),
                              (rbias, bcast(d["router_bias"], [P, NE])), (wr, d["router_w"].rearrange("(c p) n -> p c n", p=P)),
                              (sgu[:, :, 0:FE], d["sh_gate"].rearrange("(c p) n -> p c n", p=P)),
                              (sgu[:, :, FE:2 * FE], d["sh_up"].rearrange("(c p) n -> p c n", p=P)),
                              (sd, d["sh_down"].rearrange("(c p) n -> p c n", p=P)), (io64, d["iota"][:, 0:NE]),
                              (lt, d["mask_lt"]), (thr, d["block_starts"]), (tokf, d["token_ids"]), (ip, d["iota_p"])):
                sp.dma_start(dst_[:] if not isinstance(dst_, bass.AP) else dst_, src).then_inc(consts, 16)
            with sp.Fori(0, NT - 1) as t:
                load(t + 1, P)
                store(t, P)
            load(NT, NS)
            store(NT - 1, P)
            store(NT, NS)
            sp.wait_ge(dv, 1)
            sp.dma_start(d["slot_tok"].rearrange("(n s) a -> n (s a)", s=P), zi[:]).then_inc(zero_stored, 16)
            sp.wait_ge(scattered, 16 * TOPK * (NT + 1))
            sp.wait_ge(zero_stored, 16)
            sp.dma_start(st_i[:], d["slot_tok"].rearrange("(n s) a -> n (s a)", s=P)).then_inc(slots_loaded, 16)
            sp.wait_ge(x1_stored, 16 * (NT + 2))
            sp.wait_ge(acc_stored, 16 * (NT + 2))

        @block.gpsimd
        def _(g):
            g.memset(eps[:], EPS)
            g.memset(mhalf[:], -0.5)
            g.drain()

            def inv_std(t, R):
                g.wait_ge(stats_ready, t + 1)
                nc.gpsimd.tensor_tensor(rstd[0:R, 0:1], mv[0:R, 1:2], eps[0:R, :], ALU.add)
                g.drain()
                nc.gpsimd.tensor_tensor(rstd[0:R, 1:2], rstd[0:R, 0:1], mhalf[0:R, :], ALU.pow).then_inc(rstd_ready, 1)

            with g.Fori(0, NT) as t:
                inv_std(t, P)
            inv_std(NT, NS)
            g.wait_ge(dest_ready, 1)
            g.wait_ge(zero_stored, 16)
            for t in range(NT + 1):
                R = P if t < NT else NS
                for c in range(TOPK):
                    g.indirect_dma_start(d["slot_tok"], bass.IndirectOffsetOnAxis(k.dest[0:R, t, c:c + 1], 0),
                                         toki[0:R, t:t + 1], None).then_inc(scattered, 16)

        @block.tensor
        def _(pe):
            pe.wait_ge(consts, 16 * 12)

            def tile(t, R):
                pe.wait_ge(in_loaded, t * 32 + 32)
                for c in range(DC):
                    mm = nc.tensor.transpose(pT[:, c // 4, (c % 4) * P:(c % 4) * P + R], mx[0:R, c * P:(c + 1) * P],
                                             k.ident[0:R, 0:R])
                mm.then_inc(mix_in_psum, 1)
                pe.wait_ge(mixT_ready, t + 1)
                pe.wait_ge(w_loaded, 16)
                pe.wait_ge(po_free, t + 1)
                for i in range(2):
                    for c in range(DC):
                        mm = nc.tensor.matmul(pO[0:R, i], mT[:, c, 0:R], wo[:, c, i * 512:(i + 1) * 512],
                                              start=(c == 0), stop=(c == DC - 1))
                mm.then_inc(proj_done, 1)
                pe.wait_ge(x1_ready, t + 1)
                for c in range(DC):
                    mm = nc.tensor.transpose(pT[:, c // 4, (c % 4) * P:(c % 4) * P + R], xs[0:R, c * P:(c + 1) * P],
                                             k.ident[0:R, 0:R])
                mm.then_inc(x1_in_psum, 1)
                pe.wait_ge(x1T_ready, t + 1)
                for c in range(DC):
                    mm = nc.tensor.matmul(pR[0:R, 0:P], xT[:, c, 0:R], wr[:, c], start=(c == 0), stop=(c == DC - 1))
                mm.then_inc(router_done, 1)
                for c in range(DC):
                    mm = nc.tensor.matmul(pG[0:R], xT[:, c, 0:R], sgu[:, c], start=(c == 0), stop=(c == DC - 1))
                mm.then_inc(gu_done, 1)
                pe.wait_ge(h_ready, t + 1)
                for i in range(2):
                    mm = nc.tensor.transpose(pH[:, i * P:i * P + R], hs[0:R, i * P:(i + 1) * P], k.ident[0:R, 0:R])
                mm.then_inc(h_in_psum, 1)
                pe.wait_ge(hT_ready, t + 1)
                for i in range(2):
                    for c in range(2):
                        mm = nc.tensor.matmul(pO[0:R, i], hT[:, c, 0:R], sd[:, c, i * 512:(i + 1) * 512],
                                              start=(c == 0), stop=(c == 1))
                mm.then_inc(down_done, 1)

            with pe.Fori(0, NT) as t:
                tile(t, P)
            tile(NT, NS)
            pe.wait_ge(dv, 1)
            m2 = mask[:].rearrange("p t e -> p (t e)")
            for i, (a, b) in enumerate(((0, 512), (512, (NT + 1) * NE))):
                nc.tensor.matmul(pT[:, i, 0:b - a], lt[:], m2[:, a:b], start=True, stop=True)
                mm = nc.tensor.matmul(pO[:, i, 0:b - a], k.ones[:], m2[:, a:b], start=True, stop=True)
            mm.then_inc(pp, 1)
            pe.wait_ge(dv, 2)
            nc.tensor.transpose(pR[0:1, 0:P], be[:], k.ident[:]).then_inc(pp, 1)
            pe.wait_ge(dv, 3)
            nc.tensor.transpose(pG[:, 0:NBLK], st_f[:], k.ident[0:NBLK, 0:NBLK]).then_inc(pp, 1)

        @block.scalar
        def _(act):
            def tile(t, R):
                act.wait_ge(mix_in_psum, t + 1)
                for i in range(2):
                    nc.scalar.copy(mT[:, i * 4:i * 4 + 4, 0:R], pT[:, i, :].rearrange("p (c r) -> p c r", r=P)[:, :, 0:R])
                act.drain().then_inc(mixT_ready, 1)
                act.wait_ge(x1_in_psum, t + 1)
                for i in range(2):
                    nc.scalar.copy(xT[:, i * 4:i * 4 + 4, 0:R], pT[:, i, :].rearrange("p (c r) -> p c r", r=P)[:, :, 0:R])
                act.drain().then_inc(x1T_ready, 1)
                act.wait_ge(router_done, t + 1)
                act.wait_ge(r_free, t + 1)
                nc.scalar.activation(sc_[0:R], pR[0:R, 0:NE], ACT.Exp, scale=-1.0)
                act.wait_ge(gu_done, t + 1)
                nc.scalar.activation(eg[0:R], pG[0:R, 0:FE], ACT.Exp, scale=-1.0)
                act.drain().then_inc(exp_ready, 1)
                act.wait_ge(h_in_psum, t + 1)
                nc.scalar.copy(hT[:, :, 0:R], pH[:, 0:2 * P].rearrange("p (c r) -> p c r", r=P)[:, :, 0:R]).then_inc(hT_ready, 1)

            with act.Fori(0, NT) as t:
                tile(t, P)
            tile(NT, NS)

        @block.vector
        def _(v):
            v.sem_inc(in_used, 1)
            v.sem_inc(po_free, 1)
            v.sem_inc(r_free, 1)
            v.sem_inc(x1_stored, 16)
            v.sem_inc(acc_stored, 16)
            v.memset(mask[:], 0.0)
            v.memset(ef[:], 0.0)
            v.memset(k.wsel[:], 0.0)
            v.memset(zi[:], 0)
            v.wait_ge(consts, 16 * 12)
            nc.vector.tensor_copy(toki[:], tokf[:])
            v.drain()

            def e3(ap, shape):
                return bcast(ap, shape)

            def tile(t, R):
                v.wait_ge(proj_done, t + 1)
                v.wait_ge(in_loaded, t * 32 + 32)
                v.wait_ge(x1_stored, t * 16 + 16)
                nc.vector.scalar_tensor_tensor(out=xs[0:R], in0=xr[0:R], scalar=ALPHA, in1=pO[0:R].rearrange("p a b -> p (a b)"),
                                               op0=ALU.mult, op1=ALU.add)
                v.drain().then_inc(in_used, 1)
                for i in range(2):
                    nc.vector.bn_stats(stats[0:R, i, :], xs[0:R, i * 512:(i + 1) * 512])
                v.drain()
                nc.vector.bn_aggr(mv[0:R, :], stats[0:R])
                v.drain().then_inc(stats_ready, 1)
                v.wait_ge(rstd_ready, t + 1)
                nc.vector.tensor_scalar(xs[0:R, :], xs[0:R, :], mv[0:R, 0:1], rstd[0:R, 1:2], ALU.subtract, ALU.mult)
                v.drain()
                nc.vector.tensor_tensor(xs[0:R, :], xs[0:R, :], gain[0:R, :], ALU.mult)
                v.drain()
                nc.vector.tensor_tensor(xs[0:R, :], xs[0:R, :], bias[0:R, :], ALU.add)
                v.drain().then_inc(x1_ready, 1)
                v.wait_ge(exp_ready, t + 1)
                nc.vector.tensor_scalar(eg[0:R], eg[0:R], 1.0, None, ALU.add)
                nc.vector.tensor_scalar(sc_[0:R], sc_[0:R], 1.0, None, ALU.add)
                v.drain()
                nc.vector.reciprocal(eg[0:R], eg[0:R])
                nc.vector.reciprocal(sc_[0:R], sc_[0:R])
                v.drain()
                nc.vector.tensor_tensor(hs[0:R], eg[0:R], pG[0:R, 0:FE], ALU.mult)
                v.drain()
                nc.vector.tensor_tensor(hs[0:R], hs[0:R], pG[0:R, FE:2 * FE], ALU.mult)
                v.drain().then_inc(h_ready, 1)
                nc.vector.tensor_tensor(bi[0:R], sc_[0:R], rbias[0:R], ALU.add)
                v.drain()
                for gr in range(NGRP):
                    nc.vector.max(g8[0:R, gr], bi[0:R, gr * 8:gr * 8 + 8])
                v.drain()
                nc.vector.tensor_tensor(gs[0:R], g8[0:R, :, 0], g8[0:R, :, 1], ALU.add)
                v.drain()
                nc.vector.max(gt[0:R], gs[0:R])
                v.drain()
                nc.vector.max_index(gi[0:R], gt[0:R], gs[0:R])
                v.drain()
                nc.vector.tensor_copy(gif[0:R], gi[0:R])
                v.drain()
                nc.vector.tensor_tensor(gk[0:R], e3(io64[0:R, 0:8].rearrange("p (g a) -> p g a", a=1), [R, 8, KGRP]),
                                        e3(gif[0:R, 0:KGRP].rearrange("p (a j) -> p a j", a=1), [R, 8, KGRP]), ALU.is_equal)
                v.drain()
                nc.vector.tensor_reduce(keep[0:R], gk[0:R], AX.X, ALU.add)
                v.drain()
                b3 = bi[0:R].rearrange("p (g e) -> p g e", e=8)
                k3 = e3(keep[0:R].rearrange("p (g a) -> p g a", a=1), [R, 8, 8])
                nc.vector.tensor_tensor(b3, b3, k3, ALU.mult)
                nc.vector.tensor_scalar(gs[0:R], keep[0:R], 1.0, 1e30, ALU.subtract, ALU.mult)
                v.drain()
                nc.vector.tensor_tensor(b3, b3, e3(gs[0:R].rearrange("p (g a) -> p g a", a=1), [R, 8, 8]), ALU.add)
                v.drain()
                nc.vector.max(et[0:R], bi[0:R])
                v.drain()
                nc.vector.max_index(ei[0:R], et[0:R], bi[0:R])
                v.drain()
                efs = ef[0:R, bass.ds(t, 1)].rearrange("p a c -> p (a c)")
                nc.vector.tensor_copy(efs, ei[0:R, 0:TOPK])
                v.drain()
                i3 = e3(io64[0:R].rearrange("p (a e) -> p a e", a=1), [R, TOPK, NE])
                nc.vector.tensor_tensor(oh[0:R], i3, e3(ef[0:R, bass.ds(t, 1)].rearrange("p a c -> p c a"), [R, TOPK, NE]),
                                        ALU.is_equal)
                v.drain()
                nc.vector.tensor_reduce(mask[0:R, bass.ds(t, 1)].rearrange("p a e -> p (a e)"),
                                        oh[0:R].rearrange("p c e -> p e c"), AX.X, ALU.add)
                nc.vector.tensor_tensor(ohw[0:R], oh[0:R], e3(sc_[0:R].rearrange("p (a e) -> p a e", a=1), [R, TOPK, NE]), ALU.mult)
                v.drain().then_inc(r_free, 1)
                wt = k.wsel[0:R, bass.ds(t, 1)].rearrange("p a c -> p (a c)")
                nc.vector.tensor_reduce(wt, ohw[0:R], AX.X, ALU.add)
                v.drain()
                nc.vector.tensor_reduce(ws[0:R, 0:1], wt, AX.X, ALU.add)
                v.drain()
                nc.vector.reciprocal(ws[0:R, 1:2], ws[0:R, 0:1])
                v.drain()
                nc.vector.tensor_scalar(wt, wt, ws[0:R, 1:2], 2.5, ALU.mult, ALU.mult)
                v.wait_ge(down_done, t + 1)
                v.wait_ge(acc_stored, t * 16 + 16)
                nc.vector.scalar_tensor_tensor(out=acc[0:R], in0=xs[0:R], scalar=ALPHA, in1=pO[0:R].rearrange("p a b -> p (a b)"),
                                               op0=ALU.mult, op1=ALU.add)
                v.drain().then_inc(acc_ready, 1)
                v.sem_inc(po_free, 1)

            with v.Fori(0, NT) as t:
                tile(t, P)
            tile(NT, NS)
            v.drain().then_inc(dv, 1)
            v.wait_ge(pp, 1)
            TE = (NT + 1) * NE
            d2 = dst[:].rearrange("p t e -> p (t e)")
            p2 = pre[:].rearrange("p t e -> p (t e)")
            nc.vector.tensor_copy(d2[:, 0:512], pT[:, 0])
            nc.vector.tensor_copy(d2[:, 512:TE], pT[:, 1, 0:TE - 512])
            v.memset(pre[:, 0], 0.0)
            v.drain()
            for t in range(NT):
                src = pO[:, 0, t * NE:(t + 1) * NE] if t < 8 else pO[:, 1, 0:NE]
                nc.vector.tensor_tensor(pre[:, t + 1], pre[:, t], src, ALU.add)
                v.drain()
            nc.vector.tensor_tensor(d2, d2, p2, ALU.add)
            nc.vector.tensor_tensor(ble[:], pre[:, NT], pO[:, 1, 0:NE], ALU.add)
            v.drain()
            nc.vector.tensor_tensor(cmp_[:], e3(ble[:].rearrange("p (e a) -> p e a", a=1), [P, NE, 16]),
                                    e3(thr[:].rearrange("p (a j) -> p a j", a=1), [P, NE, 16]), ALU.is_gt)
            v.drain()
            nc.vector.tensor_reduce(nbl[:], cmp_[:], AX.X, ALU.add)
            v.drain()
            nc.vector.tensor_tensor_scan(incl[:], k.ones[:, 0:NE], nbl[:], 0.0, ALU.mult, ALU.add)
            v.drain()
            nc.vector.tensor_tensor(nbl[:], incl[:], nbl[:], ALU.subtract)
            nc.vector.tensor_scalar(ble[:], incl[:], ip[:, 0:1], None, ALU.is_le)
            v.drain()
            nc.vector.tensor_reduce(be[:], ble[:], AX.X, ALU.add)
            nc.vector.tensor_scalar(nbl[:], nbl[:], float(P), None, ALU.mult)
            v.drain()
            nc.vector.tensor_scalar(be[:], be[:], float(NE - 1), None, ALU.min)
            v.drain().then_inc(dv, 1)
            nc.vector.tensor_tensor(dst[:], dst[:], e3(nbl[:].rearrange("p (a e) -> p a e", a=1), [P, NT + 1, NE]), ALU.add)
            v.drain()
            for t in range(NT + 1):
                nc.vector.tensor_tensor(oh[:], e3(io64[:].rearrange("p (a e) -> p a e", a=1), [P, TOPK, NE]),
                                        e3(ef[:, t].rearrange("p (c a) -> p c a", a=1), [P, TOPK, NE]), ALU.is_equal)
                v.drain()
                nc.vector.tensor_tensor(oh[:], oh[:], e3(dst[:, t].rearrange("p (a e) -> p a e", a=1), [P, TOPK, NE]), ALU.mult)
                v.drain()
                nc.vector.tensor_reduce(dstf[:, t], oh[:], AX.X, ALU.add)
                v.drain()
            nc.vector.tensor_copy(k.dest[:], dstf[:])
            v.drain().then_inc(dest_ready, 1)
            v.wait_ge(pp, 2)
            nc.vector.tensor_copy(k.plan[:, 0:NBLK], pR[0:1, 0:NBLK])
            nc.vector.tensor_copy(k.plan[:, P - 1:P], incl[0:1, NE - 1:NE])
            nc.vector.tensor_scalar(half_counts[:, 0:NBLK // 2], io64[0:1, 0:NBLK // 2], 2.0, incl[0:1, NE - 1:NE], ALU.mult, ALU.is_lt)
            v.drain()
            nc.vector.tensor_reduce(ws[0:1, 0:1], half_counts[:, 0:NBLK // 2], AX.X, ALU.add)
            v.drain()
            nc.vector.tensor_tensor(ws[0:1, 1:2], incl[0:1, NE - 1:NE], ws[0:1, 0:1], ALU.subtract)
            v.drain()
            nc.vector.tensor_copy(k.plan[:, P - 3:P - 1], ws[0:1, 0:2])
            v.wait_ge(slots_loaded, 16)
            nc.vector.tensor_copy(st_f[:], st_i[:])
            v.drain().then_inc(dv, 1)
            v.wait_ge(pp, 3)
            nc.vector.tensor_copy(k.toks[:], pG[:, 0:NBLK])


def experts(nc, k, d):
    with ExitStack() as ctx:
        def sb(name, shape, dt=F32):
            return ctx.enter_context(nc.sbuf_tensor(name, shape, dt))

        def ps(name, shape):
            return ctx.enter_context(nc.psum_tensor(name, shape, F32))

        def sem(name):
            k.sems.append(ctx.enter_context(nc.semaphore(name)))
            return k.sems[-1]

        def two(make, name, *a):
            return [make(f"{name}{u}", *a) for u in range(2)]

        wg, wu, wd = two(sb, "e_gate", [P, DC, FE]), two(sb, "e_up", [P, DC, FE]), two(sb, "e_down", [P, 2, D])
        idx, xg, xT = two(sb, "e_idx", [P, 1], I32), two(sb, "e_x", [P, D]), two(sb, "e_xT", [P, DC, P])
        sg, hT, ysb = two(sb, "e_silu", [P, 2 * P]), two(sb, "e_hT", [P, 2 * P]), two(sb, "e_y", [P, 2, 512])
        pT = ps("e_pT", [P, 2, 512])
        pG, pY = two(ps, "e_pG", [P, 512]), two(ps, "e_pY", [P, 2, 512])

        gu_loaded, down_loaded, gathered = two(sem, "gu_loaded"), two(sem, "down_loaded"), two(sem, "x_gathered")
        y_stored, slots_complete = two(sem, "y_stored_e"), sem("slots_complete")
        x_turned, xT_act, xT_dve, gu_done, silu_ready, h_ready, down_done, y_act, y_dve = (
            sem(n) for n in ("x_turned", "xT_act", "xT_dve", "e_gu_done", "e_silu_ready", "e_h_ready", "e_down_done", "y_act", "y_dve"))
        block = ctx.enter_context(nc.Block())

        def number_of_blocks(eng):
            return plan_entry(eng, P - 1, 1, NBLK)

        def plan_entry(eng, at, low, high):
            return eng.value_load(k.plan[0:1, at:at + 1], min_val=low, max_val=high)

        @block.sync
        def _(sp):
            nb = number_of_blocks(sp)

            def load(n, i, u):
                e = sp.value_load(k.plan[0:1, bass.ds(n, 1)], min_val=0, max_val=NE - 1)
                rows = bass.ds(e * P, P)
                sp.wait_ge(gu_done, n + 1)
                sp.dma_start(wg[u][:].rearrange("p c f -> p (c f)"), d["exp_gate"][rows]).then_inc(gu_loaded[u], 16)
                sp.dma_start(wu[u][:].rearrange("p c f -> p (c f)"), d["exp_up"][rows]).then_inc(gu_loaded[u], 16)
                sp.wait_ge(down_done, n + 1)
                sp.dma_start(wd[u][:].rearrange("p c f -> p (c f)"), d["exp_down"][rows]).then_inc(down_loaded[u], 16)

            def store(n, u):
                sp.wait_ge(y_act, n + 1)
                sp.nop()
                sp.wait_ge(y_dve, n + 1)
                sp.dma_start(d["y_slots"][bass.ds(n * P, P)], ysb[u][:].rearrange("p a b -> p (a b)")).then_inc(y_stored[u], 16)

            load(0, 0, 0)
            with sp.If(nb > 1):
                load(1, 0, 1)
            with sp.Fori(0, NBLK // 2) as i:
                for u in range(2):
                    n = i * 2 + u
                    with sp.If(nb > n):
                        store(n, u)
                        with sp.If(nb > n + 2):
                            load(n + 2, i + 1, u)
            even, odd = plan_entry(sp, P - 3, 1, NBLK), plan_entry(sp, P - 2, 0, NBLK)
            sp.wait_ge(y_stored[0], even * 16 + 16)
            sp.wait_ge(y_stored[1], odd * 16 + 16)
            sp.sem_inc(slots_complete, 1)

        @block.gpsimd
        def _(g):
            nb = number_of_blocks(g)
            with g.Fori(0, NBLK // 2) as i:
                for u in range(2):
                    n = i * 2 + u
                    with g.If(nb > n):
                        g.wait_ge(x_turned, n + 1)
                        g.nop()
                        nc.gpsimd.tensor_copy(idx[u][:], k.toks[:, bass.ds(n, 1)])
                        g.drain()
                        g.indirect_dma_start(xg[u][:], None, d["x1"], bass.IndirectOffsetOnAxis(idx[u][:], 0)
                                             ).then_inc(gathered[u], 16)

        @block.tensor
        def _(pe):
            pe.sem_inc(x_turned, 2)
            pe.sem_inc(gu_done, 2)
            pe.sem_inc(down_done, 2)
            nb = number_of_blocks(pe)

            def turn(n, i, u):
                pe.wait_ge(gathered[u], i * 16 + 16)
                x8 = xg[u][:].rearrange("s (p c) -> s c p", c=DC)
                for c in range(DC):
                    mm = nc.tensor.transpose(pT[:, c // 4, (c % 4) * P:(c % 4 + 1) * P], x8[:, c], k.ident[:])
                mm.then_inc(x_turned, 1)

            def gate_up(n, i, u):
                pe.wait_ge(xT_act, n + 1)
                pe.wait_ge(xT_dve, n + 1)
                pe.wait_ge(gu_loaded[u], i * 32 + 32)
                for w, at in ((wg, 0), (wu, 2 * P)):
                    for f in range(2):
                        for c in range(DC):
                            mm = nc.tensor.matmul(pG[u][:, at + f * P:at + (f + 1) * P], w[u][:, c, f:FE:2], xT[u][:, c],
                                                  start=(c == 0), stop=(c == DC - 1))
                mm.then_inc(gu_done, 1)

            def down(n, i, u):
                pe.wait_ge(h_ready, n + 1)
                pe.wait_ge(down_loaded[u], i * 16 + 16)
                for h in range(2):
                    for f in range(2):
                        mm = nc.tensor.matmul(pY[u][:, h], hT[u][:, f * P:(f + 1) * P], wd[u][:, f, h * 512:(h + 1) * 512],
                                              start=(f == 0), stop=(f == 1))
                mm.then_inc(down_done, 1)

            turn(0, 0, 0)
            gate_up(0, 0, 0)
            with pe.Fori(0, NBLK // 2) as i:
                for u in range(2):
                    n = i * 2 + u
                    nxt = i + u
                    with pe.If(nb > n):
                        with pe.If(nb > n + 1):
                            turn(n + 1, nxt, 1 - u)
                        down(n, i, u)
                        with pe.If(nb > n + 1):
                            gate_up(n + 1, nxt, 1 - u)

        def x_half(eng, copy, done, h, n, u):
            eng.wait_ge(x_turned, n + 3)
            copy(xT[u][:, h * 4:h * 4 + 4], pT[:, h].rearrange("p (c r) -> p c r", r=P)).then_inc(done, 1)

        def y_half(eng, copy, done, h, n, i, u):
            eng.wait_ge(down_done, n + 3)
            eng.wait_ge(y_stored[u], i * 16 + 16)
            copy(ysb[u][:, h], pY[u][:, h]).then_inc(done, 1)

        @block.scalar
        def _(act):
            nb = number_of_blocks(act)

            def silu(n, u):
                act.wait_ge(gu_done, n + 3)
                nc.scalar.activation(sg[u][:], pG[u][:, 0:2 * P], ACT.Silu).then_inc(silu_ready, 1)

            x_half(act, nc.scalar.copy, xT_act, 0, 0, 0)
            silu(0, 0)
            with act.Fori(0, NBLK // 2) as i:
                for u in range(2):
                    n = i * 2 + u
                    with act.If(nb > n):
                        with act.If(nb > n + 1):
                            x_half(act, nc.scalar.copy, xT_act, 0, n + 1, 1 - u)
                        y_half(act, nc.scalar.copy, y_act, 0, n, i, u)
                        with act.If(nb > n + 1):
                            silu(n + 1, 1 - u)

        @block.vector
        def _(v):
            v.sem_inc(y_stored[0], 16)
            v.sem_inc(y_stored[1], 16)
            nb = number_of_blocks(v)

            def hidden(n, u):
                v.wait_ge(silu_ready, n + 1)
                nc.vector.tensor_tensor(hT[u][:], sg[u][:], pG[u][:, 2 * P:4 * P], ALU.mult).then_inc(h_ready, 1)

            x_half(v, nc.vector.tensor_copy, xT_dve, 1, 0, 0)
            hidden(0, 0)
            with v.Fori(0, NBLK // 2) as i:
                for u in range(2):
                    n = i * 2 + u
                    with v.If(nb > n):
                        with v.If(nb > n + 1):
                            x_half(v, nc.vector.tensor_copy, xT_dve, 1, n + 1, 1 - u)
                        y_half(v, nc.vector.tensor_copy, y_dve, 1, n, i, u)
                        with v.If(nb > n + 1):
                            hidden(n + 1, 1 - u)


def combine(nc, k, d):
    with ExitStack() as ctx:
        def sb(name, shape, dt=F32):
            return ctx.enter_context(nc.sbuf_tensor(name, shape, dt))

        def sem(name):
            k.sems.append(ctx.enter_context(nc.semaphore(name)))
            return k.sems[-1]

        gain, bias = sb("ln2_g_sb", [P, D]), sb("ln2_b_sb", [P, D])
        idx = [sb(f"c_idx{c}", [P, 1], I32) for c in range(TOPK)]
        yk = [sb(f"c_y{c}", [P, D]) for c in range(TOPK)]
        acc, out = sb("c_acc", [P, D]), sb("c_out", [P, D])
        stats, mv, rstd = sb("stats2", [P, 2, 6]), sb("mv2", [P, 2]), sb("rstd2", [P, 2])
        mhalf, eps = sb("mhalf2", [P, 1]), sb("eps2", [P, 1])
        consts, acc_loaded, acc_used, yk_used, stats_ready, rstd_ready, out_ready, out_stored = (
            sem(n) for n in ("c_consts", "c_acc_loaded", "c_acc_used", "yk_used", "c_stats", "c_rstd", "c_out_ready", "c_out_stored"))
        yk_loaded = [sem(f"yk_loaded{c}") for c in range(TOPK)]
        block = ctx.enter_context(nc.Block())

        @block.sync
        def _(sp):
            sp.dma_start(gain[:], bcast(d["ln2_g"], [P, D])).then_inc(consts, 16)
            sp.dma_start(bias[:], bcast(d["ln2_b"], [P, D])).then_inc(consts, 16)
            sp.dma_start(acc[:], d["acc"][0:P]).then_inc(acc_loaded, 16)
            with sp.Fori(0, NT - 1) as t:
                sp.wait_ge(acc_used, t + 1)
                sp.dma_start(acc[:], d["acc"][bass.ds(t * P + P, P)]).then_inc(acc_loaded, 16)
                sp.wait_ge(out_ready, t + 1)
                sp.dma_start(d["y_prompt"][bass.ds(t * P, P)], out[:]).then_inc(out_stored, 16)
            sp.wait_ge(acc_used, NT)
            sp.dma_start(acc[0:NS], d["acc"][SEQ:NTOK]).then_inc(acc_loaded, 16)
            sp.wait_ge(out_ready, NT)
            sp.dma_start(d["y_prompt"][SEQ - P:SEQ], out[:]).then_inc(out_stored, 16)
            sp.wait_ge(out_ready, NT + 1)
            sp.dma_start(d["y_sample"], out[0:NS]).then_inc(out_stored, 16)
            sp.wait_ge(out_stored, 16 * (NT + 2))

        @block.gpsimd
        def _(g):
            g.memset(eps[:], EPS)
            g.memset(mhalf[:], -0.5)
            g.drain()

            def inv_std(t, R):
                g.wait_ge(stats_ready, t + 1)
                nc.gpsimd.tensor_tensor(rstd[0:R, 0:1], mv[0:R, 1:2], eps[0:R, :], ALU.add)
                g.drain()
                nc.gpsimd.tensor_tensor(rstd[0:R, 1:2], rstd[0:R, 0:1], mhalf[0:R, :], ALU.pow).then_inc(rstd_ready, 1)

            def gather(t, R):
                for c in range(TOPK):
                    g.wait_ge(yk_used, t * TOPK + c + 1)
                    g.nop()
                    nc.gpsimd.tensor_copy(idx[c][0:R], k.dest[0:R, bass.ds(t, 1), c])
                    g.drain()
                    g.indirect_dma_start(yk[c][0:R], None, d["y_slots"], bass.IndirectOffsetOnAxis(idx[c][0:R], 0)
                                         ).then_inc(yk_loaded[c], 16)

            gather(0, P)
            with g.Fori(0, NT - 1) as t:
                gather(t + 1, P)
                inv_std(t, P)
            gather(NT, NS)
            inv_std(NT - 1, P)
            inv_std(NT, NS)

        @block.vector
        def _(v):
            v.sem_inc(yk_used, TOPK)
            v.sem_inc(out_stored, 16)
            v.wait_ge(consts, 32)

            def tile(t, R):
                v.wait_ge(acc_loaded, t * 16 + 16)
                for c in range(TOPK):
                    v.wait_ge(yk_loaded[c], t * 16 + 16)
                    nc.vector.scalar_tensor_tensor(out=acc[0:R], in0=yk[c][0:R], scalar=k.wsel[0:R, bass.ds(t, 1), c], in1=acc[0:R],
                                                   op0=ALU.mult, op1=ALU.add)
                    v.drain().then_inc(yk_used, 1)
                for i in range(2):
                    nc.vector.bn_stats(stats[0:R, i, :], acc[0:R, i * 512:(i + 1) * 512])
                v.drain()
                nc.vector.bn_aggr(mv[0:R, :], stats[0:R])
                v.drain().then_inc(stats_ready, 1)
                v.wait_ge(rstd_ready, t + 1)
                v.wait_ge(out_stored, t * 16 + 16)
                nc.vector.tensor_scalar(out[0:R, :], acc[0:R, :], mv[0:R, 0:1], rstd[0:R, 1:2], ALU.subtract, ALU.mult)
                v.drain().then_inc(acc_used, 1)
                nc.vector.tensor_tensor(out[0:R, :], out[0:R, :], gain[0:R, :], ALU.mult)
                v.drain()
                nc.vector.tensor_tensor(out[0:R, :], out[0:R, :], bias[0:R, :], ALU.add)
                v.drain().then_inc(out_ready, 1)

            with v.Fori(0, NT) as t:
                tile(t, P)
            tile(NT, NS)


def more_constants():
    i=np.arange(P)
    j = np.arange(2 * NT)
    vis = (j[None, :] + 1) * 64 - 1 <= np.arange(SEQ)[:, None]
    vis = vis.reshape(NT, P, 2 * NT).transpose(1, 0, 2)
    return {
        "mask_diag": np.where(i[None, :] <= i[:, None], 0.0, NEG), "cmp_vis": vis, "cmp_mask": np.where(vis, 0.0, NEG),
        "spread16": np.arange(16)[:, None] == i[None, :] % 16, "slot_mask": i[:, None] // 16 == np.arange(8)[None, :],
        "grp4": np.arange(64)[:, None] // 4 == np.arange(16)[None, :],
        "pick_bg": (np.arange(16)[:, None, None] // 2 == i[None, None, :] // NJ) & (np.arange(16)[:, None, None] % 2 == np.arange(2)[None, :, None]),
        "e8": np.arange(8)[:, None] == i[None, :] // NJ, "e8t": i[:, None] // NJ == np.arange(8)[None, :],
        "jmask": i[:, None] % NJ == np.arange(NJ)[None, :], "iota": np.broadcast_to(i, (P, P)),
        "parity": np.broadcast_to(i % 2, (P, P)), "wmask": np.where(i % NJ == NJ - 1, 0.0, NEG)[:, None],
        "mask_lt": i[:, None] < i[None, :], "iota_p": i[:, None],
        "block_starts": np.broadcast_to(np.arange(16) * P, (P, 16)),
        "token_ids": np.arange(NT + 1)[None, :] * P + i[:, None],
        "mask_neg": np.where(i[:, None] <= i[None, :], 0.0, NEG),
        "expand_h": np.arange(NH)[:, None] == np.arange(512)[None, :] // HD,
    }
def more_inputs(a, r):
    return {
        "conv_w": a["conv_w"][0].reshape(4, DC, P).transpose(2, 1, 0), "conv_b": a["conv_b"][0].reshape(DC, P).T,
        "dt_bias": a["dt_bias"], "a_log": a["a_log"], "d_skip": a["d_skip"], "ssd_norm_w": a["ssd_norm_w"],
        "state_conv": a["state_conv"][0].reshape(NS, 3, DC, P).transpose(3, 2, 1, 0),
        "state_conv_rows": a["state_conv"][0], "state_ssm": a["state_ssm"][0].reshape(NS, NH * HD, P),
        "cache_kv_win": a["cache_kv_win"][0].reshape(NS, 512, KV),
        "cache_kv_sel": a["cache_kv_sel"][0].reshape(-1, QR * KV),
        "w_out": np.concatenate([a["w_out"][0][0:512], a["w_out"][0][r]]), "ln1_g": a["ln1_g"], "ln1_b": a["ln1_b"],
        "router_w": np.concatenate([a["router_w"][0], np.zeros((D, P - NE), np.float32)], 1), "router_bias": a["router_bias"],
        "sh_gate": a["sh_w_gate"][0], "sh_up": a["sh_w_up"][0], "sh_down": a["sh_w_down"][0],
        "exp_gate": a["exp_w_gate"][0].reshape(NE * P, DC * FE), "exp_up": a["exp_w_up"][0].reshape(NE * P, DC * FE),
        "exp_down": a["exp_w_down"][0].reshape(NE * P, 2 * D), "ln2_g": a["ln2_g"], "ln2_b": a["ln2_b"],
        "page_table": a["page_table"].reshape(1, NS * NPAGE), "cache_kv_cmp": (a["cache_kv_cmp"][0].reshape(-1, 2, 64, 2, 2, 2, HD // 2)
                         .transpose(0, 5, 2, 6, 3, 1, 4).reshape(-1, KV)),
        "pe_page": (np.broadcast_to(a["cmp_pe"][0].reshape(1, 1, 2, 64, 2, HD // 2), (2, 2, 2, 64, 2, HD // 2))
                    .transpose(4, 3, 0, 2, 1, 5).reshape(P, KV)),
        "cmp_w1": a["cmp_w1"][0].reshape(2, 64, 2, HD // 2, P).transpose(2, 1, 0, 3, 4).reshape(P, 2, HD // 2, P),
        "cmp_w2": a["cmp_w2"][0], "cmp_b1": a["cmp_b1"][0].T,
        "cmp_b2k": np.tile(a["cmp_b2"][0, 0], 2)[:, None], "cmp_b2v": a["cmp_b2"][0, 1:2],
    }
STEPS = [project, ssd, compress, attend, sample, route, experts, combine]


OUTS = [
    ("y_prompt", (1, SEQ, D)), ("y_sample", (NS, 1, D)),
    ("kv_cmp_prompt", (1, 1, SEQ, 2, 2, HD)), ("kv_sel_prompt", (1, 1, SEQ, 2, 2, HD)),
    ("kv_win_prompt", (1, 1, 512, 2, 2, HD)), ("ssm_prompt", (1, 1, NH, HD, P)),
    ("conv_prompt", (1, 1, 3, D)),
    ("kv_cmp_sample", (1, NS, 1, 2, 2, HD)), ("kv_sel_sample", (1, NS, 1, 2, 2, HD)),
    ("kv_win_sample", (1, NS, 512, 2, 2, HD)), ("ssm_sample", (1, NS, NH, HD, P)),
    ("conv_sample", (1, NS, 3, D)),
]
FORMS = {
    "y_prompt": (SEQ, D), "y_sample": (NS, D), "kv_cmp_prompt": (SEQ, KV), "kv_sel_prompt": (SEQ, KV),
    "kv_win_prompt": (512, KV), "ssm_prompt": (NH * HD, P), "conv_prompt": (3, D), "kv_cmp_sample": (NS, KV),
    "kv_sel_sample": (NS, KV), "kv_win_sample": (NS, 512, KV), "ssm_sample": (NS, NH * HD, P),
    "conv_sample": (NS, 3, D),
}
SCRATCH = {
    "xres": (NTOK, D), "z_silu": (NTOK, 512), "kv_win_all": (NTOK, KV), "mix": (NTOK, D), "x1": (NTOK, D),
    "y_slots": (NBLK * P, D), "acc": (NTOK, D),
}


def constants():
    i = np.arange(P)
    inv = (500000.0 ** (-np.arange(RH, dtype=np.float32) / RH)).astype(np.float32)
    pos = np.concatenate([np.arange(SEQ), np.full(P, PAST)]).astype(np.float32)
    ang = pos[:, None] * inv[None]
    cos, sin = np.cos(ang), np.sin(ang)

    def by_tile(a):
        return np.ascontiguousarray(a.reshape(NT + 1, P, -1).transpose(1, 0, 2)).astype(np.float32)

    out = {
        "ident": np.eye(P), "mask_le": i[:, None] <= i[None, :], "ones": np.ones((P, P)),
        "rope_c": by_tile(np.concatenate([cos, cos], 1)), "rope_s": by_tile(np.concatenate([-sin, sin], 1)),
    }
    out.update(more_constants())
    return {n: np.ascontiguousarray(a).astype(np.float32) for n, a in out.items()}


def laid_out(a):
    cols = np.cumsum([0, 512, 1024, 8, 512, 128, 128, 128, 128, 128, 128, 24])
    z, xbc, dt, q, kc, vc, ks, vs, kw, vw, g = (np.arange(cols[n], cols[n + 1]) for n in range(11))
    pair = np.array([g_ * GQA + c for c in range(GQA) for g_ in range(2)])
    q = q.reshape(NH, HD)[pair].ravel()
    g = g.reshape(NH, 3)[pair].T.ravel()
    order = np.concatenate([q, kc, vc, ks, vs, kw, vw, g, dt, z, xbc])
    nsa_rows = 512 + (pair[:, None] * HD + np.arange(HD)).ravel()
    c = np.ascontiguousarray
    out = {
        "x": np.concatenate([a["x_prompt"].reshape(SEQ, D), a["x_sample"].reshape(NS, D)]),
        "w_in": c(a["w_in"][0][:, order]),
        "emb_ln_g": a["emb_ln_g"][None], "emb_ln_b": a["emb_ln_b"][None],
    }
    out.update(more_inputs(a, nsa_rows))
    return {n: c(v) for n, v in out.items()}


def build(nc, d, phases=99):
    with ExitStack() as ctx:
        k = persistent(nc, ctx)
        steps = STEPS[:phases]
        with ExitStack() as kept:
            alloc_kept(nc, kept, k)
            with ExitStack() as early:
                alloc_xbc(nc, early, k)
                for step in steps[:2]:
                    step(nc, k, d)
            for step in steps[2:5]:
                step(nc, k, d)
        alloc_routing(nc, ctx, k)
        for step in steps[5:]:
            if step is experts:
                for s in k.sems[:len(k.sems) // 2]:
                    nc.sync.sem_clear(s)
                nc.all_engine_barrier()
            step(nc, k, d)


def kernel(**inputs):
    import concourse.bacc as bacc
    from concourse.bass_utils import run_bass_kernel_spmd

    a = {n: np.asarray(v) for n, v in inputs.items()}
    arrays = laid_out(a)
    arrays.update(constants())
    nc = bacc.Bacc("TRN2", target_bir_lowering=False, num_devices=1)
    d = {n: nc.dram_tensor("i_" + n, v.shape, mybir.dt.from_np(v.dtype), kind="ExternalInput").ap()
         for n, v in arrays.items()}
    for name, shape in FORMS.items():
        d[name] = nc.dram_tensor("o_" + name, shape, F32, kind="ExternalOutput").ap()
    for name, shape in SCRATCH.items():
        d[name] = nc.dram_tensor("s_" + name, shape, F32, kind="Internal").ap()
    d["slot_tok"] = nc.dram_tensor("s_slot_tok", (NBLK * P, 1), I32, kind="Internal").ap()
    build(nc, d)
    got = run_bass_kernel_spmd(nc, [{"i_" + n: v for n, v in arrays.items()}], core_ids=[0]).results[0]
    return tuple(got["o_" + name].reshape(shape) for name, shape in OUTS)
```

```python
from contextlib import ExitStack

import numpy as np
import concourse.bass as bass
from concourse import mybir

F32 = mybir.dt.float32
I32 = mybir.dt.int32
U32 = mybir.dt.uint32
ALU = mybir.AluOpType
ACT = mybir.ActivationFunctionType
AX = mybir.AxisListType

P = 128
D = 1024
DC = D // P
SEQ = 1024
NT = SEQ // P
NS = 8
NTOK = SEQ + NS
PAST = 8192
PAGE = 128
NPAGE = PAST // PAGE
HD = 64
NH = 8
GQA = 4
RH = 8
KV = 256
NEG = -1e30
ALPHA = 2.0 ** 0.25
EPS = 1e-5
SCALE = HD ** -0.5
C_Q, C_KV, C_WG, C_Z, C_X = 0, 512, 1024, 1312, 1824
D_IN = 2848
WG = 288


class Names:
    pass


def bcast(ap, shape):
    return ap.to_broadcast(shape)


def persistent(nc, ctx):
    k = Names()
    k.sems = []

    def sb(name, shape, dt=F32):
        t = ctx.enter_context(nc.sbuf_tensor(name, shape, dt))
        return t

    k.ident = sb("ident", [P, P])
    k.mask_le = sb("mask_le", [P, P])
    k.ones = sb("ones", [P, P])
    k.gd = sb("gd", [P, NT + 1, 32])
    return k


def project(nc, k, d):
    with ExitStack() as ctx:
        def sb(name, shape, dt=F32):
            return ctx.enter_context(nc.sbuf_tensor(name, shape, dt))

        def ps(name, shape):
            return ctx.enter_context(nc.psum_tensor(name, shape, F32))

        def sem(name):
            k.sems.append(ctx.enter_context(nc.semaphore(name)))
            return k.sems[-1]

        w = sb("w_in_sb", [P, DC, D_IN])
        room = k.w1[:].rearrange("p k c f -> p (k c f)")
        gain, bias, xin, xn = (room[:, i * D:(i + 1) * D] for i in range(4))
        hT = room[:, 4 * D:5 * D].rearrange("p (c r) -> p c r", r=P)
        rope_c, rope_s = sb("rope_c", [P, NT + 1, 2 * RH]), sb("rope_s", [P, NT + 1, 2 * RH])
        st = room[:, 5 * D:5 * D + 1792]
        zst = room[:, 5 * D + 1792:5 * D + 1792 + 512]
        stats, mv, rstd = sb("stats", [P, 2, 6]), sb("mv", [P, 2]), sb("rstd", [P, 2])
        mhalf, eps = sb("mhalf", [P, 1]), sb("eps", [P, 1])
        rt = sb("rt", [P, 8, 2 * RH])
        rt2 = sb("rt2", [P, 8, 2 * RH])
        pT = ps("pT", [P, 2, 512])
        pQ, pKV, pW, pZ = (ps(n, [P, 512]) for n in ("pQ", "pKV", "pW", "pZ"))
        pX = ps("pX", [P, 2, 512])

        w_in_loaded = [sem(f"w_in_loaded{i}") for i in range(2)]
        consts, x_loaded, x_taken = sem("consts"), sem("x_loaded"), sem("x_taken")
        stats_ready, rstd_ready, xn_ready, xn_stored = sem("stats_ready"), sem("rstd_ready"), sem("xn_ready"), sem("xn_stored")
        hT_in_psum, hT_ready = sem("hT_in_psum"), sem("hT_ready")
        kv_done, q_done, wg_done, xbc_done, z_done = sem("kv_done"), sem("q_done"), sem("wg_done"), sem("xbc_done"), sem("z_done")
        kv_out, wg_out, qr_out, q_out, xbc_out, z_out = (sem(n) for n in ("kv_out", "wg_out", "qr_out", "q_out", "xbc_out", "z_out"))
        roped, rows_stored, z_stored, heads_in_psum, heads_out = (sem(n) for n in ("roped", "rows_stored", "z_stored", "heads_in_psum", "heads_out"))

        block = ctx.enter_context(nc.Block())

        @block.sync
        def _(sp):
            sp.dma_start(k.ident[:], d["ident"]).then_inc(consts, 16)
            sp.dma_start(gain[:], bcast(d["emb_ln_g"], [P, D])).then_inc(consts, 16)
            sp.dma_start(bias[:], bcast(d["emb_ln_b"], [P, D])).then_inc(consts, 16)
            sp.dma_start(xin[:], d["x"][0:P]).then_inc(x_loaded, 16)
            w_dram = d["w_in"].rearrange("(c p) n -> p c n", p=P)
            sp.dma_start(w[:, :, 0:C_WG], w_dram[:, :, 0:C_WG]).then_inc(w_in_loaded[0], 16)
            sp.dma_start(w[:, :, C_WG:D_IN], w_dram[:, :, C_WG:D_IN]).then_inc(w_in_loaded[1], 16)
            sp.dma_start(rope_c[:], d["rope_c"]).then_inc(consts, 16)
            sp.dma_start(rope_s[:], d["rope_s"]).then_inc(consts, 16)
            sp.dma_start(k.mask_le[:], d["mask_le"]).then_inc(consts, 16)
            sp.dma_start(k.ones[:], d["ones"]).then_inc(consts, 16)

            def store_x(t, R):
                sp.wait_ge(xn_ready, t + 1)
                sp.dma_start(d["xres"][bass.ds(t * P, R)], xn[0:R, :]).then_inc(xn_stored, 16)

            def store_rows(t, R, cmp_rows, sel_rows):
                sp.wait_ge(roped, t + 1)
                sp.dma_start(cmp_rows, st[0:R, 1024:1280]).then_inc(rows_stored, 16)
                sp.dma_start(sel_rows, st[0:R, 1280:1536]).then_inc(rows_stored, 16)
                sp.dma_start(d["kv_win_all"][bass.ds(t * P, R)], st[0:R, 1536:1792]).then_inc(rows_stored, 16)
                sp.wait_ge(z_out, t + 2)
                sp.dma_start(d["z_silu"][bass.ds(t * P, R)], zst[0:R, :]).then_inc(z_stored, 16)

            with sp.Fori(0, NT - 1) as t:
                sp.wait_ge(x_taken, t + 1)
                sp.dma_start(xin[:], d["x"][bass.ds(t * P + P, P)]).then_inc(x_loaded, 16)
                store_x(t, P)
                store_rows(t, P, d["kv_cmp_prompt"][bass.ds(t * P, P)], d["kv_sel_prompt"][bass.ds(t * P, P)])
            sp.wait_ge(x_taken, NT)
            sp.dma_start(xin[0:NS, :], d["x"][SEQ:NTOK]).then_inc(x_loaded, 16)
            store_x(NT - 1, P)
            store_x(NT, NS)
            store_rows(NT - 1, P, d["kv_cmp_prompt"][SEQ - P:SEQ], d["kv_sel_prompt"][SEQ - P:SEQ])
            store_rows(NT, NS, d["kv_cmp_sample"], d["kv_sel_sample"])
            sp.wait_ge(rows_stored, 48 * (NT + 2))
            sp.wait_ge(z_stored, 16 * (NT + 2))
            sp.wait_ge(xn_stored, 16 * (NT + 1) + 16)

        @block.vector
        def _(v):
            v.memset(k.gd[:], 0.0)
            v.memset(k.xbcT[:, :, 0:3], 0.0)
            v.sem_inc(xn_stored, 16)
            v.sem_inc(rows_stored, 48)
            v.wait_ge(consts, 16 * 7)

            def layer_norm(t, R):
                v.wait_ge(x_loaded, t * 16 + 16)
                for i in range(2):
                    nc.vector.bn_stats(stats[0:R, i, :], xin[0:R, i * 512:(i + 1) * 512])
                v.drain()
                nc.vector.bn_aggr(mv[0:R, :], stats[0:R]).then_inc(stats_ready, 1)
                v.wait_ge(rstd_ready, t + 1)
                v.wait_ge(xn_stored, t * 16 + 16)
                v.wait_ge(hT_in_psum, t + 1)
                nc.vector.tensor_scalar(xn[0:R, :], xin[0:R, :], mv[0:R, 0:1], rstd[0:R, 1:2],
                                        ALU.subtract, ALU.mult).then_inc(x_taken, 1)
                v.drain()
                nc.vector.tensor_tensor(xn[0:R, :], xn[0:R, :], gain[0:R, :], ALU.mult)
                v.drain()
                nc.vector.tensor_tensor(xn[0:R, :], xn[0:R, :], bias[0:R, :], ALU.add).then_inc(xn_ready, 1)

            def rotate(dst, src, t, R, n):
                c = rope_c[0:R, bass.ds(t, 1), :].to_broadcast([R, n, 2 * RH])
                s = rope_s[0:R, bass.ds(t, 1), :].to_broadcast([R, n, 2 * RH])
                nc.vector.tensor_tensor(rt[0:R, 0:n, :], src[:, :, 0:2 * RH], c, ALU.mult)
                nc.vector.tensor_tensor(rt2[0:R, 0:n, 0:RH], src[:, :, RH:2 * RH], s[:, :, 0:RH], ALU.mult)
                nc.vector.tensor_tensor(rt2[0:R, 0:n, RH:2 * RH], src[:, :, 0:RH], s[:, :, RH:2 * RH], ALU.mult)
                v.drain()
                nc.vector.tensor_tensor(dst[:, :, 0:2 * RH], rt[0:R, 0:n, :], rt2[0:R, 0:n, :], ALU.add)

            def evacuate(t, R):
                v.wait_ge(kv_done, t + 1)
                v.wait_ge(rows_stored, t * 48 + 48)
                v.wait_ge(heads_in_psum, t + 1)
                nc.vector.tensor_copy(st[0:R, 1024:1536], pKV[0:R, :]).then_inc(kv_out, 1)
                v.wait_ge(q_done, t + 1)
                nc.vector.tensor_copy(st[0:R, 512:1024], pQ[0:R, :]).then_inc(qr_out, 1)
                v.wait_ge(wg_done, t + 1)
                nc.vector.tensor_copy(st[0:R, 1536:1792], pW[0:R, 0:256])
                nc.vector.tensor_copy(k.gd[0:R, bass.ds(t, 1), :].rearrange("p a b -> p (a b)"),
                                      pW[0:R, 256:288]).then_inc(wg_out, 1)
                v.drain()
                q8 = st[0:R, 512:1024].rearrange("p (h e) -> p h e", e=HD)
                rotate(q8, q8, t, R, NH)
                for base in (1280, 1536):
                    v.drain()
                    k2 = st[0:R, base:base + 128].rearrange("p (h e) -> p h e", e=HD)
                    rotate(k2, k2, t, R, 2)
                v.drain().then_inc(roped, 1)

            layer_norm(0, P)
            with v.Fori(0, NT - 1) as t:
                layer_norm(t + 1, P)
                evacuate(t, P)
            layer_norm(NT, NS)
            evacuate(NT - 1, P)
            evacuate(NT, NS)

        @block.gpsimd
        def _(g):
            g.memset(eps[:], EPS)
            g.memset(mhalf[:], -0.5)
            g.drain()

            def inv_std(t, R):
                g.wait_ge(stats_ready, t + 1)
                nc.gpsimd.tensor_tensor(rstd[0:R, 0:1], mv[0:R, 1:2], eps[0:R, :], ALU.add)
                g.drain()
                nc.gpsimd.tensor_tensor(rstd[0:R, 1:2], rstd[0:R, 0:1], mhalf[0:R, :], ALU.pow).then_inc(rstd_ready, 1)

            inv_std(0, P)
            with g.Fori(0, NT - 1) as t:
                inv_std(t + 1, P)
            inv_std(NT, NS)

        @block.tensor
        def _(pe):
            pe.sem_inc(hT_in_psum, 1)
            pe.sem_inc(heads_in_psum, 1)
            pe.wait_ge(consts, 16 * 7)

            def tile(t, R):
                pe.wait_ge(xn_ready, t + 1)
                pe.wait_ge(heads_out, t + 1)
                for c in range(DC):
                    last = nc.tensor.transpose(pT[:, c // 4, (c % 4) * P:(c % 4) * P + R],
                                               xn[0:R, c * P:(c + 1) * P], k.ident[0:R, 0:R])
                last.then_inc(hT_in_psum, 1)
                pe.wait_ge(hT_ready, t + 1)

                def rows(out, c0, n):
                    for c in range(DC):
                        mm = nc.tensor.matmul(out[0:R, 0:n], hT[:, c, 0:R], w[:, c, c0:c0 + n],
                                              start=(c == 0), stop=(c == DC - 1))
                    return mm

                pe.wait_ge(w_in_loaded[0], 16)
                rows(pKV, C_KV, 512).then_inc(kv_done, 1)
                pe.wait_ge(qr_out, t + 1)
                pe.wait_ge(q_out, t + 1)
                rows(pQ, C_Q, 512).then_inc(q_done, 1)
                pe.wait_ge(w_in_loaded[1], 16)
                pe.wait_ge(wg_out, t + 1)
                rows(pW, C_WG, WG).then_inc(wg_done, 1)
                pe.wait_ge(xbc_out, t + 1)
                for ch in range(DC):
                    for c in range(DC):
                        mm = nc.tensor.matmul(pX[:, ch // 4, (ch % 4) * P:(ch % 4) * P + R],
                                              w[:, c, C_X + ch * P:C_X + (ch + 1) * P], hT[:, c, 0:R],
                                              start=(c == 0), stop=(c == DC - 1))
                mm.then_inc(xbc_done, 1)
                pe.wait_ge(z_out, t + 1)
                rows(pZ, C_Z, 512).then_inc(z_done, 1)
                pe.wait_ge(q_out, t + 2)
                pe.wait_ge(roped, t + 1)
                pe.wait_ge(kv_out, t + 1)
                for c in range(4):
                    nc.tensor.transpose(pT[:, 0, c * P:c * P + R], st[0:R, c * P:(c + 1) * P], k.ident[0:R, 0:R])
                for c in range(4):
                    nc.tensor.transpose(pT[:, 1, c * P:c * P + R], st[0:R, 512 + c * P:512 + (c + 1) * P],
                                        k.ident[0:R, 0:R])
                nc.tensor.transpose(pKV[:, 0:R], st[0:R, 1280:1408], k.ident[0:R, 0:R])
                nc.tensor.transpose(pKV[:, P:P + R], st[0:R, 1536:1664],
                                    k.ident[0:R, 0:R]).then_inc(heads_in_psum, 1)

            with pe.Fori(0, NT) as t:
                tile(t, P)
            tile(NT, NS)

        @block.scalar
        def _(act):
            for free in (heads_out, qr_out, q_out, wg_out, xbc_out, z_out):
                act.sem_inc(free, 1)
            act.sem_inc(z_stored, 16)

            def tile(t, R, xbc_dst):
                act.wait_ge(hT_in_psum, t + 2)
                for i in range(2):
                    last = nc.scalar.copy(hT[:, i * 4:i * 4 + 4, 0:R],
                                          pT[:, i, :].rearrange("p (c r) -> p c r", r=P)[:, :, 0:R])
                last.then_inc(hT_ready, 1)
                act.wait_ge(qr_out, t + 2)
                nc.scalar.copy(st[0:R, 0:512], pQ[0:R, :]).then_inc(q_out, 1)
                act.wait_ge(xbc_done, t + 1)
                nc.scalar.copy(xbc_dst, pX[:, :, :].rearrange("p b (c r) -> p (b c) r", r=P)[:, :, 0:R]
                               ).then_inc(xbc_out, 1)
                act.wait_ge(z_done, t + 1)
                act.wait_ge(z_stored, t * 16 + 16)
                nc.scalar.activation(zst[0:R, :], pZ[0:R, :], ACT.Silu).then_inc(z_out, 1)
                act.wait_ge(heads_in_psum, t + 2)
                at = bass.ds(t * P, R)
                nc.scalar.copy(k.qT[:, :, at], pT[:, 0, :].rearrange("p (c r) -> p c r", r=P)[:, :, 0:R])
                nc.scalar.copy(k.qrT[:, :, at], pT[:, 1, :].rearrange("p (c r) -> p c r", r=P)[:, :, 0:R])
                nc.scalar.copy(k.kselT[:, at], pKV[:, 0:R])
                nc.scalar.copy(k.kwinT[:, at], pKV[:, P:P + R]).then_inc(heads_out, 1)

            with act.Fori(0, NT) as t:
                tile(t, P, k.xbcT[:, :, bass.ds(t * P + 3, P)])
            tile(NT, NS, k.xbcS[:, :, :])


def alloc_kept(nc, ctx, k):
    def sb(name, shape, dt=F32):
        return ctx.enter_context(nc.sbuf_tensor(name, shape, dt))
    k.qT, k.qrT = sb("qT", [P, 4, NTOK]), sb("qrT", [P, 4, NTOK])
    k.kselT, k.kwinT = sb("kselT", [P, NTOK]), sb("kwinT", [P, NTOK])
    k.kcT_p, k.vc_p = sb("kcT_p", [P, 2 * NT]), sb("vc_p", [2 * NT, 2, HD])
    k.kcT_s, k.vc_s = sb("kcT_s", [P, NS, P]), sb("vc_s", [P, NS, 2, HD])


def alloc_xbc(nc, ctx, k):
    def sb(name, shape, dt=F32):
        return ctx.enter_context(nc.sbuf_tensor(name, shape, dt))
    k.xbcT, k.xbcS = sb("xbcT", [P, DC, 3 + SEQ]), sb("xbcS", [P, DC, NS])


def alloc_w1(nc, ctx, k):
    k.w1 = ctx.enter_context(nc.sbuf_tensor("cmp_w1_sb", [P, 2, HD // 2, P], F32))
    k.w1_loaded = ctx.enter_context(nc.semaphore("w1_loaded"))


def ssd(nc, k, d):
    with ExitStack() as ctx:
        def sb(name, shape, dt=F32):
            return ctx.enter_context(nc.sbuf_tensor(name, shape, dt))

        def ps(name, shape):
            return ctx.enter_context(nc.psum_tensor(name, shape, F32))

        def sem(name):
            k.sems.append(ctx.enter_context(nc.semaphore(name)))
            return k.sems[-1]

        NG = 512
        G = 24
        cw, cb = sb("conv_w_sb", [P, DC, 4]), sb("conv_b_sb", [P, DC])
        dtb, alog = sb("dt_bias_sb", [P, 8]), sb("a_log_sb", [P, 8])
        dskip, normw = sb("d_skip_sb", [P, 8]), sb("norm_w_sb", [P, NG])
        mneg, expand = sb("mneg", [P, P]), sb("expand_h", [8, NG])
        sconv = sb("state_conv_sb", [P, DC, 3, NS])
        h0 = sb("state_ssm_sb", [P, NS, 4, P])
        cv = sb("cv", [P, DC, SEQ])
        cvs, cvt = sb("cvs", [P, DC, NS]), sb("cvt", [P, DC, NS])
        sp1, sp2, sp3, sp4 = (sb(f"softplus{i}", [P, NT + 1, 8]) for i in range(4))
        dt = sb("dt", [P, NT + 1, 8])
        dtA = sb("dtA", [P, NT + 1, 8])
        pr = sb("pr", [P, NT, 6, 8])
        prs, cs = sb("prs", [P, 6, 8]), sb("cs", [P, DC, P])
        Dm, xdt, xdd, Dx = sb("Dm", [P, 8, P]), sb("xdt", [P, NG]), sb("xdd", [P, NG]), sb("Dx", [P, NG])
        Bt, H = sb("Bt", [P, 256]), sb("H", [P, NG])
        y, y2, zt, sq = sb("y", [P, NG]), sb("y2", [P, NG]), sb("zt", [P, NG]), sb("sq", [P, NG])
        ms, mhalf = sb("ms", [P, 4]), sb("mhalf_ssd", [P, 2])
        dT, dE = sb("dT", [8, 17]), sb("dE", [P, 4, 17])
        bc, bcm = sb("bc", [8, NG]), sb("bcm", [8, NG])
        hx, ys = sb("hx", [P, 4, P]), sb("ys", [P, 4, NS])
        xdtS = sb("xdtS", [P, 4, NS])
        Hout = sb("Hout", [P, 4, P])
        cvo, cvp = (t[0:8].rearrange("p c n -> p (c n)") for t in (Dm, cs))

        pX, pB, pS, pY1, pY2 = (ps(n, [P, 512]) for n in ("ssd_pX", "ssd_pB", "ssd_pS", "ssd_pY1", "ssd_pY2"))
        pR = ps("ssd_pR", [P, 2, 512])

        consts, z_loaded, silu_done = sem("ssd_consts"), sem("z_loaded"), sem("silu_done")
        conv_done, sp_v, sp_a, pr_ready, sums_done = sem("conv_done"), sem("sp_v"), sem("sp_a"), sem("pr_ready"), sem("sums_done")
        staged, in_psum, d_ready, exp_ready, m_ready = sem("staged"), sem("chunk_in_psum"), sem("d_ready"), sem("exp_ready"), sem("m_ready")
        yoff_done, ydiag_done, state_done, h_ready, xd_ready = (sem(n) for n in ("yoff_done", "ydiag_done", "state_done", "h_ready", "xd_ready"))
        ms_ready, rms_ready, y_ready, y_stored, chunk_done = (sem(n) for n in ("ms_ready", "rms_ready", "y_ready", "y_stored", "chunk_done"))
        side_ps, side_sb, side_st, bc_ready, bc_ps, hn_ready = (sem(n) for n in ("side_ps", "side_sb", "side_st", "bc_ready", "bc_ps", "hn_ready"))
        prep, y_used = sem("ssd_prep"), sem("y_used")
        block = ctx.enter_context(nc.Block())
        NCONST = 10

        @block.sync
        def _(sp):
            for dst, src in ((cw, d["conv_w"]), (cb, d["conv_b"]), (mneg, d["mask_neg"]), (expand, d["expand_h"]),
                             (sconv, d["state_conv"])):
                sp.dma_start(dst[:], src).then_inc(consts, 16)
            for dst, src in ((dtb, d["dt_bias"]), (alog, d["a_log"]), (dskip, d["d_skip"])):
                sp.dma_start(dst[:], bcast(src, [P, 8])).then_inc(consts, 16)
            sp.dma_start(normw[:], bcast(d["ssd_norm_w"], [P, NG])).then_inc(consts, 16)
            sp.dma_start(dT[:, 16:17], d["d_skip"].rearrange("a h -> h a")).then_inc(consts, 16)
            sp.dma_start(d["kv_win_prompt"], d["kv_win_all"][SEQ - 512:SEQ]).then_inc(side_st, 16)
            sp.dma_start(d["conv_sample"][:, 0:2, :], d["state_conv_rows"][:, 1:3, :]).then_inc(side_st, 16)
            sp.dma_start(zt[:], d["z_silu"][0:P]).then_inc(z_loaded, 16)
            sp.dma_start(k.w1[:], d["cmp_w1"]).then_inc(k.w1_loaded, 16)
            for b in range(NS):
                sp.dma_start(h0[:, b], d["state_ssm"][b].rearrange("(c q) n -> q c n", q=P)).then_inc(prep, 16)
            with sp.Fori(0, NT - 1) as c:
                sp.wait_ge(y_ready, c + 1)
                sp.dma_start(zt[:], d["z_silu"][bass.ds(c * P + P, P)]).then_inc(z_loaded, 16)
                sp.dma_start(d["mix"][bass.ds(c * P, P), 0:NG], y2[:]).then_inc(y_stored, 16)
            sp.wait_ge(y_ready, NT)
            sp.dma_start(zt[0:NS], d["z_silu"][SEQ:NTOK]).then_inc(z_loaded, 16)
            sp.dma_start(d["mix"][SEQ - P:SEQ, 0:NG], y2[:]).then_inc(y_stored, 16)
            sp.wait_ge(side_sb, 1)
            sp.dma_start(d["conv_sample"][:, 2, :], cvo[:]).then_inc(side_st, 16)
            sp.dma_start(d["conv_prompt"], cvp[0:3]).then_inc(side_st, 16)
            sp.wait_ge(side_sb, 2)
            sp.dma_start(d["ssm_prompt"].rearrange("(c q) n -> q c n", q=P), Hout[:]).then_inc(side_st, 16)
            with sp.Fori(0, NS) as b:
                sp.wait_ge(hn_ready, b + 1)
                sp.dma_start(d["ssm_sample"][bass.ds(b, 1)].rearrange("b (c q) n -> q (b c) n", q=P),
                             h0[:, bass.ds(b, 1)].rearrange("q b c n -> q (b c) n")).then_inc(side_st, 16)
            sp.wait_ge(y_ready, NT + 1)
            sp.dma_start(d["mix"][SEQ:NTOK, 0:NG], y2[0:NS]).then_inc(y_stored, 16)
            sp.wait_ge(y_stored, 16 * (NT + 2))
            sp.wait_ge(side_st, 16 * (5 + NS))

        @block.gpsimd
        def _(g):
            g.memset(mhalf[:], -0.5)
            g.drain()

            def inv_rms(n, R):
                g.wait_ge(ms_ready, n + 1)
                nc.gpsimd.tensor_tensor(ms[0:R, 2:4], ms[0:R, 0:2], mhalf[0:R, :], ALU.pow).then_inc(rms_ready, 1)

            g.wait_ge(silu_done, DC)
            g.wait_ge(pr_ready, 1)
            with g.Fori(0, NT) as c:
                g.wait_ge(chunk_done, c + 1)
                g.nop()
                nc.gpsimd.tensor_copy(prs[:], pr[:, bass.ds(c, 1)].rearrange("p a k h -> p (a k) h"))
                nc.gpsimd.tensor_copy(cs[:], cv[:, :, bass.ds(c * P, P)])
                g.drain().then_inc(staged, 1)
                inv_rms(c, P)
            inv_rms(NT, NS)

        @block.vector
        def _(v):
            v.memset(H[:], 0.0)
            v.sem_inc(chunk_done, 1)
            v.sem_inc(h_ready, 1)
            v.sem_inc(y_stored, 16)
            v.wait_ge(consts, 16 * NCONST)
            for ch in range(DC):
                nc.vector.tensor_scalar(cv[:, ch], k.xbcT[:, ch, 0:SEQ], cw[:, ch, 0:1], None, ALU.mult)
                for tap in range(1, 4):
                    v.drain()
                    nc.vector.scalar_tensor_tensor(out=cv[:, ch], in0=k.xbcT[:, ch, tap:tap + SEQ],
                                                   scalar=cw[:, ch, tap:tap + 1], in1=cv[:, ch],
                                                   op0=ALU.mult, op1=ALU.add)
                v.drain().then_inc(conv_done, 1)

            def tap_w(tap):
                return bcast(cw[:, :, tap:tap + 1], [P, DC, NS])
            nc.vector.tensor_tensor(cvs[:], k.xbcS[:], tap_w(3), ALU.mult)
            for tap in range(3):
                nc.vector.tensor_tensor(cvt[:], sconv[:, :, tap, :], tap_w(tap), ALU.mult)
                v.drain()
                nc.vector.tensor_tensor(cvs[:], cvs[:], cvt[:], ALU.add)
                v.drain()
            nc.vector.tensor_tensor(cvs[:], cvs[:], bcast(cb[:].rearrange("p (c a) -> p c a", a=1), [P, DC, NS]), ALU.add)
            v.drain().then_inc(conv_done, 1)

            raw = k.gd[:, :, G:G + 8]
            b9 = bcast(dtb[:].rearrange("p (a h) -> p a h", a=1), [P, NT + 1, 8])
            nc.vector.tensor_tensor(sp1[:], raw, b9, ALU.add)
            v.drain()
            nc.vector.tensor_scalar(sp2[:], sp1[:], -1.0, None, ALU.mult)
            v.drain()
            nc.vector.tensor_tensor(sp2[:], sp2[:], sp1[:], ALU.min)
            nc.vector.tensor_scalar(dt[:], sp1[:], 0.0, None, ALU.max)
            v.drain().then_inc(sp_v, 1)
            v.wait_ge(sp_a, 1)
            nc.vector.tensor_scalar(sp1[:], sp2[:], 1.0, None, ALU.add)
            v.drain()
            nc.vector.tensor_scalar(sp1[:], sp1[:], 1.0, None, ALU.subtract)
            v.drain()
            nc.vector.tensor_scalar(sp4[:], sp1[:], 0.0, None, ALU.is_equal)
            nc.vector.tensor_scalar(sp1[:], sp1[:], 1e-30, None, ALU.max)
            v.drain()
            nc.vector.reciprocal(sp1[:], sp1[:])
            v.drain()
            nc.vector.tensor_tensor(sp3[:], sp3[:], sp1[:], ALU.mult)
            v.drain()
            nc.vector.tensor_tensor(sp3[:], sp3[:], sp4[:], ALU.add)
            v.drain()
            nc.vector.tensor_tensor(sp3[:], sp3[:], sp2[:], ALU.mult)
            v.drain()
            nc.vector.tensor_tensor(dt[:], dt[:], sp3[:], ALU.add)
            nc.vector.tensor_scalar(alog[:], alog[:], -1.0, None, ALU.mult)
            v.drain()
            nc.vector.tensor_tensor(dtA[:], dt[:], bcast(alog[:].rearrange("p (a h) -> p a h", a=1), [P, NT + 1, 8]), ALU.mult)
            nc.vector.tensor_scalar(k.gd[:, :, 0:G], k.gd[:, :, 0:G], 1.0, None, ALU.add)
            v.drain().then_inc(sp_v, 1)
            nc.vector.reciprocal(k.gd[:, :, 0:G], k.gd[:, :, 0:G])
            v.wait_ge(sums_done, 1)
            acum = pB[:, 0:64].rearrange("p (c h) -> p c h", h=8)
            nc.vector.tensor_copy(pr[:, :, 0], dt[:, 0:NT])
            nc.vector.tensor_copy(pr[:, :, 1], dtA[:, 0:NT])
            nc.vector.tensor_copy(pr[:, :, 2], acum)
            v.drain()
            nc.vector.tensor_tensor(pr[:, :, 4], pB[:, 64:128].rearrange("p (c h) -> p c h", h=8), pr[:, :, 2], ALU.subtract)
            nc.vector.tensor_copy(pr[:, :, 5], pB[:, 64:128].rearrange("p (c h) -> p c h", h=8))
            v.drain().then_inc(sp_v, 1)
            v.wait_ge(sp_a, 2)
            nc.vector.tensor_tensor(pr[:, :, 4], pr[:, :, 4], pr[:, :, 0], ALU.mult)
            v.drain().then_inc(pr_ready, 1)

            def gate_norm(yin, R, n):
                v.wait_ge(z_loaded, n * 16 + 16)
                v.wait_ge(y_stored, n * 16 + 16)
                nc.vector.tensor_tensor(y2[0:R], yin, zt[0:R], ALU.mult)
                v.drain()
                for gr in range(2):
                    nc.vector.tensor_tensor_reduce(sq[0:R, gr * 256:gr * 256 + 256], y2[0:R, gr * 256:gr * 256 + 256],
                                                   y2[0:R, gr * 256:gr * 256 + 256], 1.0 / 256, EPS, ALU.mult, ALU.add,
                                                   ms[0:R, gr:gr + 1])
                v.drain().then_inc(ms_ready, 1)
                v.wait_ge(rms_ready, n + 1)
                for gr in range(2):
                    cols = slice(gr * 256, gr * 256 + 256)
                    nc.vector.scalar_tensor_tensor(out=y2[0:R, cols], in0=y2[0:R, cols], scalar=ms[0:R, 2 + gr:3 + gr],
                                                   in1=normw[0:R, cols], op0=ALU.mult, op1=ALU.mult)
                v.drain().then_inc(y_ready, 1)

            def heads(ap):
                return ap.rearrange("p (h e) -> p h e", e=HD)

            def per_head(kind):
                return bcast(prs[:, kind, :].rearrange("p (h a) -> p h a", a=1), [P, 8, HD])

            dsk = bcast(dskip[:].rearrange("p (h a) -> p h a", a=1), [P, 8, HD])
            with v.Fori(0, NT) as c:
                v.wait_ge(in_psum, c + 1)
                for h in range(8):
                    nc.vector.scalar_tensor_tensor(out=Dm[:, h], in0=pR[:, h // 4, (h % 4) * P:(h % 4 + 1) * P],
                                                   scalar=prs[:, 2, h:h + 1], in1=mneg[:], op0=ALU.subtract, op1=ALU.add)
                v.drain().then_inc(d_ready, 1)
                nc.vector.tensor_tensor(heads(xdt[:]), heads(pX[:]), per_head(0), ALU.mult)
                nc.vector.tensor_tensor(heads(xdd[:]), heads(pX[:]), per_head(4), ALU.mult)
                nc.vector.tensor_tensor(heads(Dx[:]), heads(pX[:]), dsk, ALU.mult)
                nc.vector.tensor_copy(Bt[:], pB[:, 0:256])
                v.drain().then_inc(xd_ready, 1)
                v.wait_ge(exp_ready, c + 1)
                for gr in range(2):
                    cbt = bcast(pB[:, 256 + gr * P:384 + gr * P].rearrange("p (a l) -> p a l", a=1), [P, 4, P])
                    nc.vector.tensor_tensor(Dm[:, gr * 4:gr * 4 + 4], Dm[:, gr * 4:gr * 4 + 4], cbt, ALU.mult)
                v.drain().then_inc(m_ready, 1)
                v.wait_ge(yoff_done, c + 1)
                nc.vector.tensor_tensor(heads(H[:]), heads(H[:]), per_head(5), ALU.mult)
                nc.vector.tensor_tensor(heads(y[:]), heads(pY2[:]), per_head(3), ALU.mult)
                v.drain()
                nc.vector.tensor_tensor(y[:], y[:], Dx[:], ALU.add)
                v.wait_ge(state_done, c + 1)
                nc.vector.tensor_tensor(H[:], H[:], pS[:], ALU.add)
                v.drain().then_inc(h_ready, 1)
                nc.vector.tensor_tensor(y[:], y[:], pY1[:], ALU.add)
                v.drain().then_inc(chunk_done, 1)
                gate_norm(y[:], P, c)

            v.wait_ge(side_ps, 1)
            nc.vector.tensor_copy(cvo[:, 0:512], pX[0:8, :])
            nc.vector.tensor_copy(cvo[:, 512:D], pY1[0:8, :])
            nc.vector.tensor_copy(cvp[0:3, 0:512], pY2[0:3, :])
            nc.vector.tensor_copy(cvp[0:3, 512:D], pS[0:3, :])
            v.drain().then_inc(side_sb, 1)
            v.wait_ge(side_ps, 2)
            nc.vector.tensor_copy(Hout[:], pX[:].rearrange("p (c n) -> p c n", n=P))
            v.drain().then_inc(side_sb, 1)
            v.wait_ge(side_ps, 3)
            nc.vector.tensor_copy(dT[:, 0:16], pY1[0:8, 0:16])
            nc.vector.tensor_copy(bc[:], pY2[0:8, :])
            v.drain().then_inc(side_sb, 1)
            v.wait_ge(side_ps, 4)
            nc.vector.tensor_copy(dE[:], pS[:, 0:68].rearrange("p (c n) -> p c n", n=17))
            v.drain()
            nc.vector.tensor_tensor(xdtS[:], cvs[:, 0:4], dE[:, :, 0:8], ALU.mult)
            v.wait_ge(prep, 16 * NS)
            v.drain()
            with v.Fori(0, NS) as b:
                v.wait_ge(bc_ps, b + 1)
                nc.vector.tensor_scalar(bcm[:], bc[:], k.ident[0:8, bass.ds(b, 1)], None, ALU.mult)
                v.drain().then_inc(bc_ready, 1)
                hb = h0[:, bass.ds(b, 1)].rearrange("q b c n -> q (b c) n")
                nc.vector.tensor_tensor(hb, hb, bcast(dE[:, :, bass.ds(b + 8, 1)], [P, 4, P]), ALU.mult)
                v.wait_ge(bc_ps, b + 2)
                for gr in range(2):
                    bb = bcast(pX[:, gr * P:gr * P + P].rearrange("p (a l) -> p a l", a=1), [P, 2, P])
                    nc.vector.tensor_tensor(hx[:, 2 * gr:2 * gr + 2], bb,
                                            bcast(xdtS[:, 2 * gr:2 * gr + 2, bass.ds(b, 1)], [P, 2, P]), ALU.mult)
                v.drain()
                nc.vector.tensor_tensor(hb, hb, hx[:], ALU.add)
                v.drain().then_inc(hn_ready, 1)
                for gr in range(2):
                    cc = bcast(pX[:, 256 + gr * P:384 + gr * P].rearrange("p (a l) -> p a l", a=1), [P, 2, P])
                    hg = h0[:, bass.ds(b, 1), 2 * gr:2 * gr + 2].rearrange("q b c n -> q (b c) n")
                    nc.vector.tensor_tensor(hx[:, 2 * gr:2 * gr + 2], hg, cc, ALU.mult)
                v.drain()
                nc.vector.tensor_reduce(ys[:, :, bass.ds(b, 1)], hx[:], AX.X, ALU.add)
                v.drain()
            nc.vector.tensor_tensor(xdtS[:], cvs[:, 0:4], bcast(dE[:, :, 16:17], [P, 4, NS]), ALU.mult)
            v.drain()
            nc.vector.tensor_tensor(ys[:], ys[:], xdtS[:], ALU.add)
            v.drain().then_inc(bc_ready, 1)
            v.wait_ge(side_ps, 5)
            gate_norm(pY1[0:NS, :], NS, NT)

        @block.scalar
        def _(act):
            for ch in range(DC):
                act.wait_ge(conv_done, ch + 1)
                nc.scalar.activation(cv[:, ch], cv[:, ch], ACT.Silu, bias=cb[:, ch:ch + 1]).then_inc(silu_done, 1)
            act.wait_ge(conv_done, DC + 1)
            nc.scalar.activation(cvs[:], cvs[:], ACT.Silu).then_inc(silu_done, 1)
            nc.scalar.activation(k.gd[:, :, 0:G], k.gd[:, :, 0:G], ACT.Exp, scale=-1.0)
            nc.scalar.activation(alog[:], alog[:], ACT.Exp)
            act.wait_ge(sp_v, 1)
            nc.scalar.activation(sp2[:], sp2[:], ACT.Exp)
            act.drain()
            nc.scalar.activation(sp3[:], sp2[:], ACT.Ln, bias=1.0)
            act.drain().then_inc(sp_a, 1)
            act.wait_ge(sp_v, 3)
            nc.scalar.activation(pr[:, :, 3], pr[:, :, 2], ACT.Exp)
            nc.scalar.activation(pr[:, :, 4:6], pr[:, :, 4:6], ACT.Exp)
            nc.scalar.activation(sp1[0:8, NT], dtA[0:8, NT], ACT.Exp)
            act.drain().then_inc(sp_a, 1)
            with act.Fori(0, NT) as c:
                act.wait_ge(d_ready, c + 1)
                nc.scalar.activation(Dm[:], Dm[:], ACT.Exp).then_inc(exp_ready, 1)

        @block.tensor
        def _(pe):
            pe.sem_inc(bc_ps, 1)
            pe.wait_ge(sp_v, 2)
            nc.tensor.matmul(pB[:, 0:64], k.mask_le[:], dtA[:, 0:NT].rearrange("p c h -> p (c h)"), start=True, stop=True)
            nc.tensor.matmul(pB[:, 64:128], k.ones[:], dtA[:, 0:NT].rearrange("p c h -> p (c h)"), start=True,
                             stop=True).then_inc(sums_done, 1)
            with pe.Fori(0, NT) as c:
                pe.wait_ge(staged, c + 1)
                for i in range(4):
                    nc.tensor.transpose(pX[:, i * P:(i + 1) * P], cs[:, i], k.ident[:])
                for i in range(2):
                    nc.tensor.transpose(pB[:, i * P:(i + 1) * P], cs[:, 4 + i], k.ident[:])
                for gr in range(2):
                    nc.tensor.matmul(pB[:, 256 + gr * P:384 + gr * P], cs[:, 4 + gr], cs[:, 6 + gr], start=True, stop=True)
                for h in range(8):
                    mm = nc.tensor.matmul(pR[:, h // 4, (h % 4) * P:(h % 4 + 1) * P],
                                          bcast(prs[:, 1, h:h + 1], [P, P]), k.mask_le[:], start=True, stop=True)
                mm.then_inc(in_psum, 1)
                pe.wait_ge(h_ready, c + 1)
                for gr in range(2):
                    mm = nc.tensor.matmul(pY2[:, gr * 256:gr * 256 + 256], cs[:, 6 + gr], H[:, gr * 256:gr * 256 + 256],
                                          start=True, stop=True)
                mm.then_inc(yoff_done, 1)
                pe.wait_ge(m_ready, c + 1)
                for h in range(8):
                    mm = nc.tensor.matmul(pY1[:, h * HD:(h + 1) * HD], Dm[:, h], xdt[:, h * HD:(h + 1) * HD],
                                          start=True, stop=True)
                mm.then_inc(ydiag_done, 1)
                pe.wait_ge(xd_ready, c + 1)
                for gr in range(2):
                    mm = nc.tensor.matmul(pS[:, gr * 256:gr * 256 + 256], Bt[:, gr * P:(gr + 1) * P],
                                          xdd[:, gr * 256:gr * 256 + 256], start=True, stop=True)
                mm.then_inc(state_done, 1)
            pe.wait_ge(chunk_done, NT + 1)
            for i in range(DC):
                nc.tensor.transpose((pX if i < 4 else pY1)[0:8, (i % 4) * P:(i % 4 + 1) * P], k.xbcS[:, i], k.ident[:])
            for i in range(DC):
                mm = nc.tensor.transpose((pY2 if i < 4 else pS)[0:3, (i % 4) * P:(i % 4 + 1) * P],
                                         k.xbcT[:, i, SEQ:SEQ + 3], k.ident[:])
            mm.then_inc(side_ps, 1)
            pe.wait_ge(side_sb, 1)
            for i in range(4):
                mm = nc.tensor.transpose(pX[:, i * P:(i + 1) * P], H[:, i * P:(i + 1) * P], k.ident[:])
            mm.then_inc(side_ps, 1)
            pe.wait_ge(side_sb, 2)
            pe.wait_ge(silu_done, DC + 1)
            pe.wait_ge(sp_a, 2)
            nc.tensor.transpose(pY1[0:8, 0:8], dt[0:8, NT], k.ident[0:8, 0:8])
            nc.tensor.transpose(pY1[0:8, 8:16], sp1[0:8, NT], k.ident[0:8, 0:8])
            for i in range(4):
                mm = nc.tensor.transpose(pY2[0:8, i * P:(i + 1) * P], cvs[:, 4 + i], k.ident[:])
            mm.then_inc(side_ps, 1)
            pe.wait_ge(side_sb, 3)
            for i in range(4):
                mm = nc.tensor.matmul(pS[:, i * 17:(i + 1) * 17], expand[:, i * P:(i + 1) * P], dT[:], start=True, stop=True)
            mm.then_inc(side_ps, 1)
            with pe.Fori(0, NS) as b:
                pe.wait_ge(bc_ready, b + 1)
                nc.tensor.matmul(pX[:], k.ones[0:8, :], bcm[:], start=True, stop=True).then_inc(bc_ps, 1)
            pe.wait_ge(bc_ready, NS + 1)
            for i in range(4):
                mm = nc.tensor.transpose(pY1[0:8, i * P:(i + 1) * P], ys[:, i], k.ident[:])
            mm.then_inc(side_ps, 1)


GP = 32
EC = HD // 2
PB = 4
SP_PAGES, ACT_PAGES, POOL_PAGES = (0, 12), (12, 24), (24, GP)
PROMPT_DMAS = 16 * (2 * 2 * NT + 1)


def compress(nc, k, d):
    with ExitStack() as ctx:
        def sb(name, shape, dt=F32):
            return ctx.enter_context(nc.sbuf_tensor(name, shape, dt))

        def ps(name, shape):
            return ctx.enter_context(nc.psum_tensor(name, shape, F32))

        def sem(name):
            k.sems.append(ctx.enter_context(nc.semaphore(name)))
            return k.sems[-1]

        w1 = k.w1
        w2 = sb("cmp_w2_sb", [P, 2, HD])
        b1, b1p = sb("cmp_b1_sb", [P, 2]), sb("cmp_b1_pe", [P, 2])
        b2k, b2v = sb("cmp_b2k", [P, 1]), sb("cmp_b2v", [P, HD])
        pt = sb("page_row", [1, NS * NPAGE], I32)
        X = [sb(f"pages{u}", [P, GP * KV]) for u in range(2)]
        hid = [sb(f"hid{u}", [P, 2, 2, 2 * GP]) for u in range(2)]
        ph = [ps(f"ph{u}", [P, 512]) for u in range(2)]
        pk, pv = ps("cmp_pk", [P, 512]), ps("cmp_pv", [P, 512])

        consts = sem("cmp_consts")
        pages_loaded = [sem(f"pages_loaded{u}") for u in range(2)]
        pool_pages_loaded = [sem(f"pool_pages_loaded{u}") for u in range(2)]
        pages_used = [sem(f"pages_used{u}") for u in range(2)]
        hid_ready = [sem(f"hid_ready{u}") for u in range(2)]
        pe_folded, kv_in_psum, kv_copied = sem("pe_folded"), sem("cmp_kv_in_psum"), sem("cmp_kv_copied")
        pt_loaded = sem("pt_loaded")
        block = ctx.enter_context(nc.Block())
        NPP = SEQ // PAGE
        cached = [X[u][:].rearrange("p (g c k b) -> p c k g b", c=EC, k=2, b=4) for u in range(2)]
        prompt = X[0][:].rearrange("p (g b k h c) -> p g b k h c", b=2, k=2, h=2, c=EC)

        def load_pages(eng, b, u, share, loaded):
            for i in range(*share, PB):
                _, pages = nc.values_load_multi_w_load_instructions(
                    pt[0:1, bass.ds(b * NPAGE + (GP if u == 0 else 0) + i, PB)], engines=[eng.engine],
                    min_val=0, max_val=d["cache_kv_cmp"].shape[0] // PAGE - 1,
                    skip_runtime_bounds_check_because="a page table names pages of the pool")
                for n, page in enumerate(pages):
                    at = (i + n) * KV
                    eng.dma_start(X[u][:, at:at + KV],
                                  d["cache_kv_cmp"][bass.ds(page * PAGE, PAGE)]).then_inc(loaded[u], 16)

        @block.sync
        def _(sp):
            sp.dma_start(pt[:], d["page_table"]).then_inc(pt_loaded, 16)
            rows = d["kv_cmp_prompt"].rearrange("(g b l) (k h s c) -> s l g b k h c", b=2, l=64, k=2, h=2, s=2)
            for s in range(2):
                for g in range(NPP):
                    for b in range(2):
                        sp.dma_start(prompt[s * 64:s * 64 + 64, g, b], rows[s, :, g, b]).then_inc(pages_loaded[0], 16)
            sp.dma_start(X[0][:, NPP * KV:(NPP + 1) * KV], d["pe_page"]).then_inc(pages_loaded[0], 16)
            sp.dma_start(w2[:], d["cmp_w2"].rearrange("k f e -> f k e")).then_inc(consts, 16)
            sp.dma_start(b1[:], d["cmp_b1"]).then_inc(consts, 16)
            sp.dma_start(b2k[:], d["cmp_b2k"]).then_inc(consts, 16)
            sp.dma_start(b2v[:], bcast(d["cmp_b2v"], [P, HD])).then_inc(consts, 16)
            sp.wait_ge(pt_loaded, 16)
            with sp.Fori(0, NS) as b:
                for u in (1, 0):
                    sp.wait_ge(pages_used[u], b + 1)
                    load_pages(sp, b, u, SP_PAGES, pages_loaded)

        @block.gpsimd
        def _(g):
            g.wait_ge(pt_loaded, 16)
            with g.Fori(0, NS) as b:
                for u in (1, 0):
                    g.wait_ge(pages_used[u], b + 1)
                    load_pages(g, b, u, POOL_PAGES, pool_pages_loaded)

        def layer1(u, moving, n):
            for kv in range(2):
                for c in range(EC):
                    mm = nc.tensor.matmul(ph[u][:, kv * P:kv * P + n], w1[:, kv, c], moving(c, kv),
                                          start=(c == 0), stop=(c == EC - 1))
            mm.then_inc(pages_used[u], 1)

        @block.tensor
        def _(pe):
            pe.wait_ge(k.w1_loaded, 16)
            pe.wait_ge(pages_loaded[0], PROMPT_DMAS)
            layer1(0, lambda c, kv: prompt[:, 0:NPP + 1, :, kv, :, c], 4 * (NPP + 1))
            pe.wait_ge(consts, 64)
            pe.wait_ge(hid_ready[0], 1)
            for g in range(2):
                nc.tensor.matmul(pk[g * 64:g * 64 + 64, 0:2 * NPP], w2[:, 0], hid[0][:, 0, g, 0:2 * NPP],
                                 start=True, stop=True)
                mm = nc.tensor.matmul(pv[0:2 * NPP, g * 64:g * 64 + 64], hid[0][:, 1, g, 0:2 * NPP], w2[:, 1],
                                      start=True, stop=True)
            mm.then_inc(kv_in_psum, 1)
            with pe.Fori(0, NS) as b:
                for u in (1, 0):
                    direct, pool = 16 * ACT_PAGES[1], 16 * (GP - POOL_PAGES[0])
                    pe.wait_ge(pages_loaded[u], b * direct + direct + (PROMPT_DMAS if u == 0 else 0))
                    pe.wait_ge(pool_pages_loaded[u], b * pool + pool)
                    pe.wait_ge(hid_ready[u], b + 1)
                    layer1(u, lambda c, kv: cached[u][:, c, kv], 4 * GP)
                pe.wait_ge(kv_copied, b + 1)
                for u in (1, 0):
                    pe.wait_ge(hid_ready[u], b + 2)
                    at = GP * 2 if u == 0 else 0
                    for g in range(2):
                        nc.tensor.matmul(pk[g * 64:g * 64 + 64, at:at + 2 * GP], w2[:, 0], hid[u][:, 0, g],
                                         start=True, stop=True)
                        mm = nc.tensor.matmul(pv[at:at + 2 * GP, g * 64:g * 64 + 64], hid[u][:, 1, g], w2[:, 1],
                                              start=True, stop=True)
                mm.then_inc(kv_in_psum, 1)

        @block.scalar
        def _(act):
            act.sem_inc(hid_ready[1], 1)
            act.sem_inc(pages_used[1], 1)

            def silu(u, npages):
                for kv in range(2):
                    src = ph[u][:, kv * P:kv * P + 4 * npages].rearrange("f (gb h) -> f h gb", h=2)
                    nc.scalar.activation(hid[u][:, kv, :, 0:2 * npages], src, ACT.Silu, bias=b1p[:, kv:kv + 1])
                act.drain().then_inc(hid_ready[u], 1)

            act.wait_ge(pt_loaded, 16)
            load_pages(act, 0, 1, ACT_PAGES, pages_loaded)
            act.wait_ge(pages_used[0], 1)
            act.wait_ge(pe_folded, 1)
            silu(0, NPP)
            load_pages(act, 0, 0, ACT_PAGES, pages_loaded)

            def sample(b, last):
                for u in (1, 0):
                    act.wait_ge(pages_used[u], b + 2)
                    act.wait_ge(kv_in_psum, b + 1)
                    silu(u, GP)
                    if not last:
                        load_pages(act, b + 1, u, ACT_PAGES, pages_loaded)

            with act.Fori(0, NS - 1) as b:
                sample(b, False)
            sample(NS - 1, True)

        @block.vector
        def _(v):
            v.wait_ge(consts, 64)
            v.wait_ge(pages_used[0], 1)
            nc.vector.tensor_tensor(b1p[:], b1[:], ph[0][:, 4 * NPP:4 * NPP + P + 1:P], ALU.add)
            v.drain().then_inc(pe_folded, 1)
            v.wait_ge(kv_in_psum, 1)
            n = 2 * NPP
            nc.vector.tensor_scalar(k.kcT_p[:], pk[:, 0:n], b2k[:, 0:1], None, ALU.add)
            nc.vector.tensor_tensor(k.vc_p[:], pv[0:n, 0:P].rearrange("p (h e) -> p h e", h=2),
                                    bcast(b2v[0:n].rearrange("p (a e) -> p a e", a=1), [n, 2, HD]), ALU.add)
            v.drain().then_inc(kv_copied, 1)
            with v.Fori(0, NS) as b:
                v.wait_ge(kv_in_psum, b + 2)
                nc.vector.tensor_scalar(k.kcT_s[:, bass.ds(b, 1)].rearrange("p a n -> p (a n)"), pk[:, 0:P],
                                        b2k[:, 0:1], None, ALU.add)
                nc.vector.tensor_tensor(k.vc_s[:, bass.ds(b, 1)].rearrange("p a h e -> p (a h) e"),
                                        pv[:, 0:P].rearrange("p (h e) -> p h e", h=2),
                                        bcast(b2v[:].rearrange("p (a e) -> p a e", a=1), [P, 2, HD]), ALU.add)
                v.drain().then_inc(kv_copied, 1)


WIN_T = 512 // P


def attend(nc, k, d):
    with ExitStack() as ctx:
        def sb(name, shape, dt=F32):
            return ctx.enter_context(nc.sbuf_tensor(name, shape, dt))

        def ps(name, shape):
            return ctx.enter_context(nc.psum_tensor(name, shape, F32))

        def sem(name):
            k.sems.append(ctx.enter_context(nc.semaphore(name)))
            return k.sems[-1]

        V = [sb(f"v_rows{br}", [P, NT, P]) for br in range(2)]
        K = [k.kselT, k.kwinT]
        diag, oldest = sb("mask_diag", [P, P]), sb("mask_oldest", [P, P])
        visn, vis = sb("cmp_mask", [P, NT, 16]), sb("cmp_vis", [P, NT, 16])
        spread, slot = sb("spread16", [16, P]), sb("slot_mask", [P, 8])
        kbd, vbd = sb("kc_blockdiag", [P, 32]), sb("vc_blockdiag", [P, 512])
        qst = [sb(f"q_staged{g}", [P, P]) for g in range(2)]
        Pr = [sb(f"probs{u}", [P, SEQ]) for u in range(2)]
        PT = [sb(f"probsT{u}", [P, NT, P]) for u in range(2)]
        y = sb("nsa_y", [P, NT, 512])
        nm, L, r = sb("neg_max", [P, 4]), sb("row_sum", [P, 4]), sb("gate_over_sum", [P, 4])
        Pc, PcT = sb("cmp_probs", [P, NT, P]), sb("cmp_probsT", [P, NT, P])
        mc, lc = sb("cmp_max", [P, NT, 8]), sb("cmp_sum", [P, NT, 8])
        pS = [ps(f"att_pS{u}", [P, 2, 512]) for u in range(2)]
        pT = ps("att_pT", [P, 2, 512])
        pO = [ps(f"att_pO{u}", [P, 512]) for u in range(2)]

        consts = sem("att_consts")
        c_scores, c_shift, c_exp, c_probs, c_turned, c_turned_sb, c_out, y_start = (
            sem(n) for n in ("c_scores", "c_shift", "c_exp", "c_probs", "c_turned", "c_turned_sb", "c_out", "y_start"))
        staged, s_done, max_ready, exp_done, t_done, pt_copied, pv_done, o_used = (
            sem(n) for n in ("q_is_staged", "s_done", "max_ready", "exp_done", "t_done", "pt_copied", "pv_done", "o_used"))
        y_stored, y_free = sem("nsa_y_stored"), sem("vbd_ready")
        exp_free = sem("exp_free")
        zeros_ready, filled = sem("zeros_ready"), sem("slots_filled")
        zeros = sb("zero_rows", [P, D])
        block = ctx.enter_context(nc.Block())
        NC_ = 8

        def branch(j):
            return j // 2, j % 2

        def first_key(t, br):
            return 0 if br == 0 else max(0, t - WIN_T) * P

        def keys(t, br):
            return (t + 1) * P - first_key(t, br)

        def pipeline(eng, t, stages):
            depth = len(stages) - 1

            def step(c, j, first):
                for i, stage in enumerate(stages):
                    if stage is None or (first and j - i < 0):
                        continue
                    stage(t, c if j - i >= 0 else c - 1, (j - i) % 4)

            for j in range(4):
                step(0, j, True)
            with eng.Fori(1, 4) as c:
                for j in range(4):
                    step(c, j, False)
            for j in range(depth):
                for i in range(j + 1, depth + 1):
                    if stages[i] is not None:
                        stages[i](t, 3, 4 + j - i)

        @block.sync
        def _(sp):
            for dst, src in ((diag, "mask_diag"), (oldest, "mask_neg"), (visn, "cmp_mask"), (vis, "cmp_vis"),
                             (spread, "spread16"), (slot, "slot_mask")):
                sp.dma_start(dst[:], d[src]).then_inc(consts, 16)
            for v_sb, rows in zip(V, (d["kv_sel_prompt"], d["kv_win_all"][0:SEQ])):
                sp.dma_start(v_sb[:], rows.rearrange("(t p) c -> p t c", p=P)[:, :, P:KV]).then_inc(consts, 16)
            sp.wait_ge(zeros_ready, 1)
            sp.dma_start(d["x1"][NTOK:NTOK + P], zeros[:]).then_inc(filled, 16)
            sp.dma_start(d["acc"][NTOK:NTOK + P], zeros[:]).then_inc(filled, 16)
            for t in range(NT):
                sp.wait_ge(o_used, 16 * (t + 1) + 2)
                sp.dma_start(d["mix"][t * P:(t + 1) * P, 512:D], y[:, t]).then_inc(y_stored, 16)
            sp.wait_ge(y_stored, 16 * NT)
            sp.wait_ge(filled, 32)

        @block.gpsimd
        def _(g):
            g.memset(qst[0][:], 0.0)
            g.memset(qst[1][:], 0.0)
            g.memset(zeros[:], 0.0)
            g.drain().then_inc(zeros_ready, 1)
            for t in range(NT):
                with g.Fori(0, 4) as c:
                    g.wait_ge(s_done, c * 4 + (t * 16 + 4))
                    g.nop()
                    for gr in range(2):
                        rows = slice(gr * 64, gr * 64 + 64)
                        nc.gpsimd.tensor_copy(qst[gr][rows, :],
                                              k.qrT[rows, bass.ds(c, 1), t * P:(t + 1) * P].rearrange("p a n -> p (a n)"))
                    g.drain().then_inc(staged, 1)

        @block.tensor
        def _(pe):
            pe.sem_inc(s_done, 4)
            pe.sem_inc(pv_done, 2)
            pe.wait_ge(consts, 16 * NC_)
            nc.tensor.matmul(pT[:, 0, 0:P], spread[:], k.vc_p[:].rearrange("p h e -> p (h e)"), start=True,
                             stop=True).then_inc(c_turned, 1)

            def scores(t, c, j):
                br, gr = branch(j)
                k0, n = first_key(t, br), keys(t, br)
                for i in range(0, n, 512):
                    w = min(512, n - i)
                    mm = nc.tensor.matmul(pS[j % 2][:, i // 512, 0:w], qst[gr][:], K[br][:, k0 + i:k0 + i + w],
                                          start=True, stop=True)
                mm.then_inc(s_done, 1)

            def scores_staged(t, c, j):
                if j == 0:
                    pe.wait_ge(staged, c + (t * 4 + 1))
                pe.wait_ge(exp_free, c * 4 + (t * 16 + j + 1))
                scores(t, c, j)

            def turn(t, c, j):
                br, gr = branch(j)
                pe.wait_ge(exp_done, c * 4 + (t * 16 + j + 1))
                pe.wait_ge(pt_copied, c * 4 + (t * 16 + j + 1))
                for i in range(keys(t, br) // P):
                    mm = nc.tensor.transpose(pT[:, i // 4, (i % 4) * P:(i % 4 + 1) * P], Pr[j % 2][:, i * P:(i + 1) * P],
                                             k.ident[:])
                mm.then_inc(t_done, 1)

            def values(t, c, j):
                br, gr = branch(j)
                k0, n = first_key(t, br) // P, keys(t, br) // P
                unit = c * 4 + (t * 16 + j)
                pe.wait_ge(pt_copied, unit + 2)
                pe.wait_ge(o_used, unit + 1)
                for i in range(n):
                    mm = nc.tensor.matmul(pO[j % 2][:, 0:P], PT[j % 2][:, i], V[br][:, k0 + i], start=(i == 0), stop=(i == n - 1))
                mm.then_inc(pv_done, 1)

            pe.wait_ge(y_free, 1)
            for t in range(NT):
                for c in range(4):
                    mm = nc.tensor.matmul(pS[0][:, t // 4, (t % 4) * P + c * 32:(t % 4) * P + c * 32 + 32],
                                          k.qT[:, c, t * P:(t + 1) * P], kbd[:], start=True, stop=True)
            mm.then_inc(c_scores, 1)
            pe.wait_ge(c_probs, 1)
            for t in range(NT):
                mm = nc.tensor.transpose(pT[:, t // 4, (t % 4) * P:(t % 4 + 1) * P], Pc[:, t], k.ident[:])
            mm.then_inc(c_turned, 1)
            pe.wait_ge(c_turned_sb, 1)
            for t in range(NT):
                if t >= 2:
                    pe.wait_ge(y_start, t - 1)
                nc.tensor.matmul(pO[t % 2][:], PcT[:, t], vbd[:], start=True, stop=True).then_inc(c_out, 1)
            pe.wait_ge(y_start, NT)
            for t in range(NT):
                pipeline(pe, t, (scores_staged, turn, values))

        @block.vector
        def _(v):
            v.sem_inc(o_used, 2)
            v.memset(kbd[:], 0.0)
            v.drain()
            nc.vector.tensor_copy(kbd[0:64, 0:16], k.kcT_p[0:64])
            nc.vector.tensor_copy(kbd[64:P, 16:32], k.kcT_p[64:P])
            v.wait_ge(c_turned, 1)
            for c in range(4):
                nc.vector.tensor_tensor(vbd[:, c * P:(c + 1) * P].rearrange("p (h e) -> p h e", e=HD),
                                        pT[:, 0, 0:P].rearrange("p (h e) -> p h e", e=HD),
                                        bcast(slot[:, 2 * c:2 * c + 2].rearrange("p (h a) -> p h a", a=1), [P, 2, HD]), ALU.mult)
            v.drain().then_inc(y_free, 1)

            def softmax_max(t, c, j):
                br, gr = branch(j)
                n = keys(t, br)
                S = pS[j % 2][:].rearrange("p a b -> p (a b)")
                v.wait_ge(s_done, c * 4 + (t * 16 + j + 5))
                nc.vector.tensor_tensor(S[:, n - P:n], S[:, n - P:n], diag[:], ALU.add)
                if br == 1 and t >= WIN_T:
                    nc.vector.tensor_tensor(S[:, 0:P], S[:, 0:P], oldest[:], ALU.add)
                v.drain()
                nc.vector.tensor_reduce(nm[:, j:j + 1], S[:, 0:n], AX.X, ALU.max)
                v.drain()
                nc.vector.tensor_scalar(nm[:, j:j + 1], nm[:, j:j + 1], -SCALE, None, ALU.mult).then_inc(max_ready, 1)

            def add_out(t, c, j):
                br, gr = branch(j)
                unit = c * 4 + (t * 16 + j)
                v.wait_ge(pv_done, unit + 3)
                nc.vector.reciprocal(r[:, j:j + 1], L[:, j:j + 1])
                v.drain()
                nc.vector.tensor_tensor(r[:, j:j + 1], r[:, j:j + 1],
                                        k.gd[:, t, bass.ds(c * 2 + ((br + 1) * 8 + gr), 1)], ALU.mult)
                v.drain()
                ys = y[:, t, bass.ds(c * P + gr * HD, HD)]
                nc.vector.scalar_tensor_tensor(out=ys, in0=pO[j % 2][:, gr * HD:gr * HD + HD], scalar=r[:, j:j + 1], in1=ys,
                                               op0=ALU.mult, op1=ALU.add)
                v.drain().then_inc(o_used, 1)

            v.wait_ge(c_scores, 1)
            hs = Pc[:].rearrange("p t (h j) -> p t h j", j=16)
            n8 = [P, NT, 8, 16]
            for t in range(NT):
                nc.vector.tensor_tensor(hs[:, t], pS[0][:, t // 4, (t % 4) * P:(t % 4 + 1) * P].rearrange("p (h j) -> p h j", j=16),
                                        bcast(visn[:, t:t + 1], [P, 8, 16]), ALU.add)
            v.drain()
            nc.vector.tensor_reduce(mc[:], hs, AX.X, ALU.max)
            v.drain()
            nc.vector.tensor_tensor(hs, hs, bcast(mc[:].rearrange("p t (h a) -> p t h a", a=1), n8), ALU.subtract)
            v.drain().then_inc(c_shift, 1)
            v.wait_ge(c_exp, 1)
            nc.vector.tensor_reduce(lc[:], hs, AX.X, ALU.add)
            v.drain()
            nc.vector.tensor_tensor(hs, hs, bcast(vis[:].rearrange("p t (a j) -> p t a j", a=1), n8), ALU.mult)
            nc.vector.reciprocal(lc[:], lc[:])
            v.drain()
            nc.vector.tensor_tensor(lc[:], lc[:], k.gd[:, 0:NT, 0:8], ALU.mult)
            v.drain()
            nc.vector.tensor_tensor(hs, hs, bcast(lc[:].rearrange("p t (h a) -> p t h a", a=1), n8), ALU.mult)
            v.drain().then_inc(c_probs, 1)
            v.wait_ge(c_turned, 2)
            nc.vector.tensor_copy(PcT[:], pT[:].rearrange("p a (b q) -> p (a b) q", q=P))
            v.drain().then_inc(c_turned_sb, 1)
            for t in range(NT):
                v.wait_ge(c_out, t + 1)
                nc.vector.tensor_copy(y[:, t], pO[t % 2][:])
                v.drain().then_inc(y_start, 1)
            for t in range(NT):
                pipeline(v, t, (softmax_max, None, None, add_out))

        @block.scalar
        def _(act):
            act.sem_inc(pt_copied, 1)
            act.sem_inc(exp_free, 2)
            def exp(t, c, j):
                br, gr = branch(j)
                n = keys(t, br)
                act.wait_ge(max_ready, c * 4 + (t * 16 + j + 1))
                nc.scalar.activation(Pr[j % 2][:, 0:n], pS[j % 2][:].rearrange("p a b -> p (a b)")[:, 0:n], ACT.Exp,
                                     bias=nm[:, j:j + 1], scale=SCALE, accum_out=L[:, j:j + 1])
                act.drain().then_inc(exp_done, 1)
                act.sem_inc(exp_free, 1)

            def turned(t, c, j):
                br, gr = branch(j)
                unit = c * 4 + (t * 16 + j)
                n = keys(t, br) // P
                act.wait_ge(t_done, unit + 1)
                act.wait_ge(pv_done, unit + 1)
                nc.scalar.copy(PT[j % 2][:].rearrange("p a b -> p (a b)")[:, 0:n * P],
                               pT[:].rearrange("p a b -> p (a b)")[:, 0:n * P]).then_inc(pt_copied, 1)

            act.wait_ge(c_shift, 1)
            nc.scalar.activation(Pc[:], Pc[:], ACT.Exp, scale=SCALE).then_inc(c_exp, 1)
            for t in range(NT):
                pipeline(act, t, (exp, turned))


NJ = 16
QR = 32
UNITS = [(0, 0, 0), (0, 0, 1), (0, 1, 0), (0, 1, 1), (1, 0, 0), (1, 1, 0)]


def sample(nc, k, d):
    with ExitStack() as ctx:
        def sb(name, shape, dt=F32):
            return ctx.enter_context(nc.sbuf_tensor(name, shape, dt))

        def ps(name, shape):
            return ctx.enter_context(nc.psum_tensor(name, shape, F32))

        def sem(name):
            k.sems.append(ctx.enter_context(nc.semaphore(name)))
            return k.sems[-1]

        grp4, pick, e8, e8t = sb("grp4", [64, 16]), sb("pick_bg", [16, 2, P]), sb("e8", [8, P]), sb("e8t", [P, 8])
        jmask, iota, parity, wmask = sb("jmask", [P, NJ]), sb("iota128", [P, P]), sb("parity", [P, P]), sb("wmask", [P, 1])
        pti, ptf = sb("pt_int", [8, NPAGE], I32), sb("pt_f", [8, NPAGE])
        sA, sP, sPT = sb("cmpS", [P, 64]), sb("cmpP", [64, P]), sb("cmpPT", [P, 64])
        st1 = sb("cmp_stat", [64, 4])
        score, score2 = sb("score", [16, P]), sb("score2", [16, P])
        top, topi = sb("top", [16, 2, 8]), sb("topi", [16, 2, 8], U32)
        topf = sb("topf", [16, 16])
        pj, blk, T2, oh = sb("pj", [P, 2, NJ]), sb("blk", [P, 2]), sb("T2", [P, P]), sb("oh", [P, P])
        half, idxf, idx = sb("half", [P, 2]), sb("idxf", [P, 2, 2]), sb("idx", [P, 4], U32)
        oc, qtok, qb = sb("oc", [64, 8, 8]), sb("qtok", [8, 512]), sb("qb", [P, 512])
        W = QR + 1
        tile = [sb(f"kv_piece{u}", [P, W, 2, 2, HD]) for u in range(2)]
        prod = sb("prod", [P, 4 * W * HD])
        S = sb("piece_S", [P, 4, W])
        m, l = sb("piece_m", [P, 6, 4]), sb("piece_l", [P, 6, 4])
        O = sb("piece_O", [P, 6, 4, HD])
        mm_, mt, mtx = sb("both_m", [P, 2, 2, 4]), sb("m_by_sample", [16, 8]), sb("m_spread", [16, 8, NJ])
        Ms, w = sb("M", [P, 2, 2, 4]), sb("w", [P, 6, 4])
        lw, Ow = sb("lw", [P, 2, 2, 4]), sb("Ow", [P, 2, 2, 4, HD])
        g3, y, t8 = sb("g3", [8, 2, 2, 4]), sb("y8", [8, 4, 2, HD]), sb("t8", [8, 4, 2, HD])
        pA, pB, pC, pD = (ps(f"smp_p{c}", [P, 512]) for c in "ABCD")

        consts, dve, pe_, act_ = sem("smp_consts"), sem("smp_dve"), sem("smp_pe"), sem("smp_act")
        piece_loaded = [sem(f"piece_loaded{u}") for u in range(2)]
        gathered = [sem(f"gathered{u}") for u in range(2)]
        piece_used, idx_ready, shifted, expd, new_rows, stored, y_ready = (
            sem(n) for n in ("piece_used", "idx_ready", "shifted", "expd", "new_rows", "smp_stored", "y8_ready"))
        block = ctx.enter_context(nc.Block())
        NC_ = 10

        @block.sync
        def _(sp):
            for dst, name in ((grp4, "grp4"), (pick, "pick_bg"), (e8, "e8"), (e8t, "e8t"), (jmask, "jmask"), (iota, "iota"),
                              (parity, "parity"), (wmask, "wmask")):
                sp.dma_start(dst[:], d[name]).then_inc(consts, 16)
            sp.dma_start(pti[:], d["page_table"].rearrange("a (b p) -> (a b) p", p=NPAGE)).then_inc(consts, 16)
            sp.dma_start(d["kv_win_sample"][:, 0:511, :], d["cache_kv_win"][:, 1:512, :]).then_inc(stored, 16)
            sp.dma_start(d["kv_win_sample"][:, 511, :], d["kv_win_all"][SEQ:NTOK]).then_inc(stored, 16)
            sp.dma_start(tile[0][:, 0:QR].rearrange("p r a h e -> p (r a h e)"),
                         d["cache_kv_win"].rearrange("b (j r) c -> (b j) (r c)", r=QR)).then_inc(piece_loaded[0], 16)
            for b in range(NS):
                sp.dma_start(tile[0][b * NJ:(b + 1) * NJ, QR].rearrange("p a h e -> p (a h e)"),
                             bcast(d["kv_win_all"][SEQ + b:SEQ + b + 1], [NJ, KV])).then_inc(piece_loaded[0], 16)
            for n in range(4):
                u = (n + 1) % 2
                sp.wait_ge(gathered[u], 16 * (n // 2 + 1))
                for b in range(NS):
                    sp.dma_start(tile[u][b * NJ + NJ - 1:b * NJ + NJ, 0:QR].rearrange("p r a h e -> p r (a h e)"),
                                 bcast(d["kv_sel_sample"][b:b + 1].rearrange("a (c e) -> a c e", c=1), [1, QR, KV])
                                 ).then_inc(piece_loaded[u], 16)
            sp.wait_ge(y_ready, 1)
            sp.dma_start(d["mix"][SEQ:NTOK, 512:D], y[:].rearrange("p a b c -> p (a b c)")).then_inc(stored, 16)
            sp.wait_ge(stored, 48)

        @block.gpsimd
        def _(g):
            g.wait_ge(idx_ready, 1)
            for n in range(4):
                u = (n + 1) % 2
                if n:
                    g.wait_ge(piece_used, n)
                g.indirect_dma_start(tile[u][:, 0:QR].rearrange("p r a h e -> p (r a h e)"), None, d["cache_kv_sel"],
                                     bass.IndirectOffsetOnAxis(idx[:, n:n + 1], 0)).then_inc(gathered[u], 16)

        @block.tensor
        def _(pe):
            pe.wait_ge(consts, 16 * (NC_ - 1))
            for b in range(NS):
                for gr in range(2):
                    rows = slice(gr * 64, gr * 64 + 64)
                    nc.tensor.matmul((pA, pC)[gr][:, b * 4:b * 4 + 4], k.kcT_s[rows, b], k.qT[rows, :, SEQ + b],
                                     start=True, stop=True)
            for c in range(4):
                mm = nc.tensor.transpose(pB[0:8, c * P:(c + 1) * P], k.qrT[:, c, SEQ:NTOK], k.ident[:])
            mm.then_inc(pe_, 1)
            pe.wait_ge(dve, 1)
            nc.tensor.transpose(pC[0:64, 0:P], sA[:], k.ident[:]).then_inc(pe_, 1)
            nc.tensor.matmul(pD[:], e8[:], qtok[:], start=True, stop=True).then_inc(pe_, 1)
            nc.tensor.matmul(pA[:, 0:NPAGE], e8[:], ptf[:], start=True, stop=True).then_inc(pe_, 1)
            pe.wait_ge(dve, 2)
            nc.tensor.matmul(pC[0:16, P:2 * P], grp4[:], sP[:], start=True, stop=True)
            nc.tensor.transpose(pC[:, 2 * P:2 * P + 64], sP[:], k.ident[0:64, 0:64]).then_inc(pe_, 1)
            pe.wait_ge(dve, 3)
            for gr in range(2):
                mm = nc.tensor.matmul(pB[:, gr * NJ:(gr + 1) * NJ], pick[:, gr], topf[:], start=True, stop=True)
            mm.then_inc(pe_, 1)
            pe.wait_ge(dve, 4)
            for b in range(NS):
                for gr in range(2):
                    at = b * 8 + gr * 4
                    mm = nc.tensor.matmul(pA[0:64, at:at + 4], k.vc_s[:, b, gr], sPT[:, at:at + 4], start=True, stop=True)
            mm.then_inc(pe_, 1)
            pe.wait_ge(dve, 5)
            for h in range(8):
                mm = nc.tensor.transpose(pD[0:8, h * HD:(h + 1) * HD], oc[:, h], k.ident[0:64, 0:64])
            mm.then_inc(pe_, 1)
            pe.wait_ge(dve, 6)
            nc.tensor.transpose(pC[0:16, 0:P], mm_[:].rearrange("p a b c -> p (a b c)"), k.ident[:]).then_inc(pe_, 1)
            pe.wait_ge(dve, 7)
            nc.tensor.transpose(pC[:, P:P + 16], mtx[:].rearrange("p a b -> p (a b)"), k.ident[0:16, 0:16]).then_inc(pe_, 1)
            pe.wait_ge(dve, 8)
            nc.tensor.matmul(pC[0:8, 0:16], e8t[:], lw[:].rearrange("p a b c -> p (a b c)"), start=True, stop=True)
            for br, out in enumerate((pA, pB)):
                mm = nc.tensor.matmul(out[0:8, :], e8t[:], Ow[:, br].rearrange("p b c e -> p (b c e)"), start=True, stop=True)
            mm.then_inc(pe_, 1)

        @block.scalar
        def _(act):
            act.wait_ge(shifted, 1)
            nc.scalar.activation(sP[:], sP[:], ACT.Exp, scale=SCALE, accum_out=st1[:, 1:2])
            act.drain().then_inc(expd, 1)
            for n in range(6):
                act.wait_ge(shifted, n + 2)
                rows = QR + (1 if n < 2 else 0)
                nc.scalar.activation(S[:, :, 0:rows], S[:, :, 0:rows], ACT.Exp, scale=SCALE).then_inc(expd, 1)
            act.wait_ge(shifted, 8)
            nc.scalar.activation(w[:], w[:], ACT.Exp, scale=SCALE).then_inc(expd, 1)

        @block.vector
        def _(v):
            v.wait_ge(consts, 16 * (NC_ - 1))
            v.wait_ge(pe_, 1)
            for gr in range(2):
                nc.vector.tensor_copy(sA[:].rearrange("p (b g c) -> p b g c", b=8, g=2)[:, :, gr],
                                      (pA, pC)[gr][:, 0:32].rearrange("p (b c) -> p b c", c=4))
            nc.vector.tensor_copy(qtok[:], pB[0:8, :])
            nc.vector.tensor_copy(ptf[:], pti[:])
            v.drain().then_inc(dve, 1)
            v.wait_ge(pe_, 2)
            nc.vector.tensor_reduce(st1[:, 0:1], pC[0:64, 0:P], AX.X, ALU.max)
            v.drain()
            nc.vector.tensor_scalar(sP[:], pC[0:64, 0:P], st1[:, 0:1], None, ALU.subtract)
            v.drain().then_inc(shifted, 1)
            v.wait_ge(pe_, 3)
            nc.vector.tensor_copy(qb[:], pD[:])
            v.wait_ge(pe_, 4)
            T3 = T2[:].rearrange("p (a two) -> p a two", two=2)
            nc.vector.scalar_tensor_tensor(out=T3, in0=bcast(pA[:, 0:NPAGE].rearrange("p (a b) -> p a b", b=1), [P, NPAGE, 2]),
                                           scalar=2.0, in1=parity[:].rearrange("p (a two) -> p a two", two=2), op0=ALU.mult,
                                           op1=ALU.add)
            v.wait_ge(expd, 1)
            nc.vector.reciprocal(st1[:, 2:3], st1[:, 1:2])
            v.drain()
            nc.vector.tensor_scalar(sP[:], sP[:], st1[:, 2:3], None, ALU.mult)
            v.drain().then_inc(dve, 1)
            v.wait_ge(pe_, 5)
            nc.vector.tensor_copy(score[:], pC[0:16, P:2 * P])
            nc.vector.tensor_copy(sPT[:], pC[:, 2 * P:2 * P + 64])
            v.drain()
            v.memset(score[:, 0:P:P - 1], 1e4)
            v.drain()
            nc.vector.max(top[:, 0], score[:])
            v.drain()
            nc.vector.max_index(topi[:, 0], top[:, 0], score[:])
            nc.vector.match_replace(score2[:], top[:, 0], score[:], -1.0)
            v.drain()
            nc.vector.max(top[:, 1], score2[:])
            v.drain()
            nc.vector.max_index(topi[:, 1], top[:, 1], score2[:])
            v.drain()
            nc.vector.tensor_copy(topf[:], topi[:].rearrange("p a b -> p (a b)"))
            v.drain().then_inc(dve, 1)
            v.wait_ge(pe_, 6)
            nc.vector.tensor_tensor(pj[:], pB[:, 0:2 * NJ].rearrange("p (g j) -> p g j", g=2),
                                    bcast(jmask[:].rearrange("p (a j) -> p a j", a=1), [P, 2, NJ]), ALU.mult)
            v.drain()
            nc.vector.tensor_reduce(blk[:], pj[:], AX.X, ALU.add)
            for gr in range(2):
                v.drain()
                nc.vector.tensor_scalar(oh[:], iota[:], blk[:, gr:gr + 1], None, ALU.is_equal)
                v.drain()
                nc.vector.tensor_tensor(oh[:], oh[:], T2[:], ALU.mult)
                v.drain()
                nc.vector.tensor_reduce(half[:, gr:gr + 1], oh[:], AX.X, ALU.add)
            v.drain()
            for q in range(2):
                nc.vector.tensor_scalar(idxf[:, :, q], half[:], 2.0, float(q), ALU.mult, ALU.add)
            v.drain()
            nc.vector.tensor_copy(idx[:], idxf[:].rearrange("p g q -> p (g q)"))
            v.drain().then_inc(idx_ready, 1)
            v.drain().then_inc(dve, 1)
            v.wait_ge(pe_, 7)
            nc.vector.tensor_copy(oc[:].rearrange("p (c g) b -> p b g c", g=2),
                                  pA[0:64, 0:64].rearrange("p (b g c) -> p b g c", b=8, g=2))
            v.drain().then_inc(dve, 1)

            def piece(n, u, unit, rows):
                br, gr, _ = UNITS[unit]
                Kr = tile[u][:, 0:rows, 0, gr]
                Vr = tile[u][:, 0:rows, 1, gr]
                pk = prod[:, 0:4 * rows * HD].rearrange("p (c r e) -> p c r e", c=4, e=HD)
                for c in range(4):
                    nc.vector.tensor_tensor(pk[:, c], Kr, bcast(qb[:, (c * 2 + gr) * HD:(c * 2 + gr + 1) * HD].rearrange(
                        "p (a e) -> p a e", a=1), [P, rows, HD]), ALU.mult)
                v.drain()
                nc.vector.tensor_reduce(S[:, :, 0:rows], pk, AX.X, ALU.add)
                v.drain()
                if rows > QR:
                    nc.vector.tensor_scalar(S[:, :, QR], S[:, :, QR], wmask[:, 0:1], None, ALU.add)
                    v.drain()
                nc.vector.tensor_reduce(m[:, unit], S[:, :, 0:rows], AX.X, ALU.max)
                v.drain()
                nc.vector.tensor_tensor(S[:, :, 0:rows], S[:, :, 0:rows],
                                        bcast(m[:, unit].rearrange("p (c a) -> p c a", a=1), [P, 4, rows]), ALU.subtract)
                v.drain().then_inc(shifted, 1)
                v.wait_ge(expd, n + 2)
                nc.vector.tensor_reduce(l[:, unit], S[:, :, 0:rows], AX.X, ALU.add)
                pv = prod[:, 0:4 * rows * HD].rearrange("p (c e r) -> p c e r", c=4, e=HD)
                for c in range(4):
                    nc.vector.tensor_tensor(pv[:, c], Vr.rearrange("p r e -> p e r"),
                                            bcast(S[:, c:c + 1, 0:rows], [P, HD, rows]), ALU.mult)
                v.drain()
                nc.vector.tensor_reduce(O[:, unit], pv, AX.X, ALU.add)
                v.drain()

            v.wait_ge(piece_loaded[0], 16 * (1 + NS))
            piece(0, 0, 4, QR + 1)
            piece(1, 0, 5, QR + 1)
            v.drain().then_inc(piece_used, 1)
            for n in range(4):
                u = (n + 1) % 2
                v.wait_ge(piece_loaded[u], (16 * (1 + NS) if u == 0 else 0) + 16 * NS * (n // 2 + 1))
                v.wait_ge(gathered[u], 16 * (n // 2 + 1))
                piece(n + 2, u, n, QR)
                v.drain().then_inc(piece_used, 1)

            ms = m[:, 0:4].rearrange("p (g q) c -> p g q c", g=2)
            nc.vector.tensor_tensor(mm_[:, 0], ms[:, :, 0], ms[:, :, 1], ALU.max)
            nc.vector.tensor_copy(mm_[:, 1], m[:, 4:6])
            v.drain().then_inc(dve, 1)
            v.wait_ge(pe_, 9)
            nc.vector.tensor_reduce(mt[:], pC[0:16, 0:P].rearrange("p (b j) -> p b j", j=NJ), AX.X, ALU.max)
            v.drain()
            nc.vector.tensor_copy(mtx[:], bcast(mt[:].rearrange("p (b a) -> p b a", a=1), [16, 8, NJ]))
            v.drain().then_inc(dve, 1)
            v.wait_ge(pe_, 10)
            nc.vector.tensor_copy(Ms[:].rearrange("p a b c -> p (a b c)"), pC[:, P:P + 16])
            v.drain()
            for q in range(2):
                nc.vector.tensor_tensor(w[:, 0:4].rearrange("p (g q) c -> p g q c", g=2)[:, :, q], ms[:, :, q], Ms[:, 0], ALU.subtract)
            nc.vector.tensor_tensor(w[:, 4:6], m[:, 4:6], Ms[:, 1], ALU.subtract)
            v.drain().then_inc(shifted, 1)
            v.wait_ge(expd, 8)
            nc.vector.tensor_tensor(l[:], l[:], w[:], ALU.mult)
            nc.vector.tensor_tensor(O[:].rearrange("p u c e -> p (u c) e"), O[:].rearrange("p u c e -> p (u c) e"),
                                    bcast(w[:].rearrange("p u (c a) -> p (u c) a", a=1), [P, 24, HD]), ALU.mult)
            v.drain()
            l4 = l[:, 0:4].rearrange("p (g q) c -> p g q c", g=2)
            O4 = O[:, 0:4].rearrange("p (g q) c e -> p g q (c e)", g=2)
            nc.vector.tensor_tensor(lw[:, 0], l4[:, :, 0], l4[:, :, 1], ALU.add)
            nc.vector.tensor_copy(lw[:, 1], l[:, 4:6])
            nc.vector.tensor_tensor(Ow[:, 0].rearrange("p g c e -> p g (c e)"), O4[:, :, 0], O4[:, :, 1], ALU.add)
            nc.vector.tensor_copy(Ow[:, 1], O[:, 4:6])
            v.drain().then_inc(dve, 1)
            v.wait_ge(pe_, 11)
            nc.vector.reciprocal(g3[:].rearrange("p a b c -> p (a b c)"), pC[0:8, 0:16])
            v.drain()
            for br in range(2):
                nc.vector.tensor_tensor(g3[:, br], g3[:, br], k.gd[0:8, NT, 8 * (br + 1):8 * (br + 2)].rearrange(
                    "p (c g) -> p g c", g=2), ALU.mult)
            nc.vector.tensor_tensor(y[:], pD[0:8, :].rearrange("p (c g e) -> p c g e", g=2, e=HD),
                                    bcast(k.gd[0:8, NT, 0:8].rearrange("p (c g a) -> p c g a", g=2, a=1), [8, 4, 2, HD]), ALU.mult)
            for br, src in enumerate((pA, pB)):
                v.drain()
                for gr in range(2):
                    nc.vector.tensor_tensor(t8[:, :, gr], src[0:8, gr * 256:gr * 256 + 256].rearrange("p (c e) -> p c e", e=HD),
                                            bcast(g3[:, br, gr].rearrange("p (c a) -> p c a", a=1), [8, 4, HD]), ALU.mult)
                v.drain()
                nc.vector.tensor_tensor(y[:], y[:], t8[:], ALU.add)
            v.drain().then_inc(y_ready, 1)


NE, TOPK, NGRP, KGRP = 64, 6, 8, 4
NBLK = (NTOK * TOPK + NE * (P - 1)) // P + 1
MIN_BLK = NTOK * TOPK // P
FE = 256


def alloc_routing(nc, ctx, k):
    def sb(name, shape, dt=F32):
        return ctx.enter_context(nc.sbuf_tensor(name, shape, dt))
    k.toks = sb("slot_token", [P, P], I32)
    k.slot_w = sb("slot_weight", [P, NBLK])
    k.plan = sb("block_plan", [1, P], I32)


def route(nc, k, d):
    with ExitStack() as ctx:
        def sb(name, shape, dt=F32):
            return ctx.enter_context(nc.sbuf_tensor(name, shape, dt))

        def ps(name, shape):
            return ctx.enter_context(nc.psum_tensor(name, shape, F32))

        def sem(name):
            k.sems.append(ctx.enter_context(nc.semaphore(name)))
            return k.sems[-1]

        wo, wr = sb("w_out_sb", [P, DC, D]), sb("router_sb", [P, DC, P])
        sgu, sd = sb("shared_gu", [P, DC, 2 * FE]), sb("shared_down", [P, 2, D])
        gain, bias, rbias = sb("ln1_g_sb", [P, D]), sb("ln1_b_sb", [P, D]), sb("router_bias_sb", [P, NE])
        mx, xr, xs = sb("mix_tile", [P, D]), sb("res_tile", [P, D]), sb("x1_tile", [P, D])
        acc = sb("acc_tile", [P, D])
        mT, xT = sb("mixT", [P, DC, P]), sb("x1T", [P, DC, P])
        hs, eg, hT = sb("sh_h", [P, FE]), sb("sh_e", [P, FE]), sb("sh_hT", [P, 2, P])
        stats, mv, rstd = sb("stats1", [P, 2, 6]), sb("mv1", [P, 2]), sb("rstd1", [P, 2])
        mhalf, eps = sb("mhalf1", [P, 1]), sb("eps1", [P, 1])
        sc_, bi = sb("scores", [P, NE]), sb("biased", [P, NE])
        g8, gs, gt, gi, gif = sb("grp_top", [P, 8, 8]), sb("grp_score", [P, 8]), sb("grp_sorted", [P, 8]), sb("grp_idx", [P, 8], U32), sb("grp_idx_f", [P, 8])
        gk, keep = sb("grp_oh", [P, 8, KGRP]), sb("grp_keep", [P, 8])
        et, ei, ef = sb("exp_top", [P, 8]), sb("exp_idx", [P, 8], U32), sb("exp_choice", [P, NT + 1, TOPK])
        io64, lt, thr = sb("iota64", [P, NE]), sb("mask_lt", [P, P]), sb("block_starts", [P, 16])
        oh, ohw = sb("choice_oh", [P, TOPK, NE]), sb("choice_prod", [P, TOPK, NE])
        ws = sb("w_sum", [P, 2])
        mask, pre, dst = sb("chosen", [P, NT + 1, NE]), sb("tokens_before", [P, NT + 1, NE]), sb("dest_all", [P, NT + 1, NE])
        cmp_, nbl, incl = sb("cnt_cmp", [P, NE, 16]), sb("n_blocks_e", [P, NE]), sb("blocks_incl", [P, NE])
        dstf = sb("dest_f", [P, NT + 1, TOPK])
        dest = sb("dest_slot", [P, NT + 1, TOPK], I32)
        choice = sb("token_and_weight", [P, NT + 1, TOPK, 2])
        tokf = sb("tok_f", [P, NT + 1])
        ip, ble, be = sb("iota_p", [P, 1]), sb("blk_cmp", [P, NE]), sb("blk_expert", [P, 1])
        half_counts = sb("half_counts", [1, NE])
        io128 = sb("slot_in_block", [P, P])
        empty, slots = sb("empty_slots", [NBLK, P, 2]), sb("slot_rows", [NBLK, P, 2])
        pT = ps("r_pT", [P, 2, 512])
        pO = ps("r_pO", [P, 2, 512])
        pR, pG, pH = ps("r_pR", [P, 512]), ps("r_pG", [P, 512]), ps("r_pH", [P, 512])

        consts, w_loaded, in_loaded, mix_in_psum, mixT_ready, proj_done, in_used = (
            sem(n) for n in ("r_consts", "w_out_loaded", "in_loaded", "mix_in_psum", "mixT_ready", "proj_done", "in_used"))
        stats_ready, rstd_ready, x1_ready, x1_stored, x1_in_psum, x1T_ready, router_done, gu_done = (
            sem(n) for n in ("r_stats", "r_rstd", "x1_ready", "x1_stored", "x1_in_psum", "x1T_ready", "router_done", "gu_done"))
        exp_ready, h_ready, h_in_psum, hT_ready, down_done, acc_ready, acc_stored, r_free = (
            sem(n) for n in ("r_exp", "sh_h_ready", "sh_h_in_psum", "sh_hT_ready", "sh_down_done", "acc_ready", "acc_stored", "router_read"))
        dv, pp, zero_stored, dest_ready, scattered, slots_loaded, po_free = (
            sem(n) for n in ("d_steps", "p_steps", "zero_stored", "dest_ready", "scattered", "slots_loaded", "po_free"))
        block = ctx.enter_context(nc.Block())

        @block.sync
        def _(sp):
            sp.dma_start(wo[:], d["w_out"].rearrange("(c p) n -> p c n", p=P)).then_inc(w_loaded, 16)

            def load(t, R):
                sp.wait_ge(in_used, t + 1)
                sp.dma_start(mx[0:R], d["mix"][bass.ds(t * P, R)]).then_inc(in_loaded, 16)
                sp.dma_start(xr[0:R], d["xres"][bass.ds(t * P, R)]).then_inc(in_loaded, 16)

            def store(t, R):
                sp.wait_ge(x1_ready, t + 1)
                sp.dma_start(d["x1"][bass.ds(t * P, R)], xs[0:R]).then_inc(x1_stored, 16)
                sp.wait_ge(acc_ready, t + 1)
                sp.dma_start(d["acc"][bass.ds(t * P, R)], acc[0:R]).then_inc(acc_stored, 16)

            load(0, P)
            for dst_, src in ((gain, bcast(d["ln1_g"], [P, D])), (bias, bcast(d["ln1_b"], [P, D])),
                              (rbias, bcast(d["router_bias"], [P, NE])), (wr, d["router_w"].rearrange("(c p) n -> p c n", p=P)),
                              (sgu[:, :, 0:FE], d["sh_gate"].rearrange("(c p) n -> p c n", p=P)),
                              (sgu[:, :, FE:2 * FE], d["sh_up"].rearrange("(c p) n -> p c n", p=P)),
                              (sd, d["sh_down"].rearrange("(c p) n -> p c n", p=P)), (io64, d["iota"][:, 0:NE]), (io128, d["iota"]),
                              (lt, d["mask_lt"]), (thr, d["block_starts"]), (tokf, d["token_ids"]), (ip, d["iota_p"])):
                sp.dma_start(dst_[:] if not isinstance(dst_, bass.AP) else dst_, src).then_inc(consts, 16)
            with sp.Fori(0, NT - 1) as t:
                load(t + 1, P)
                store(t, P)
            load(NT, NS)
            store(NT - 1, P)
            store(NT, NS)
            sp.wait_ge(dv, 1)
            sp.dma_start(d["slot_rows"].rearrange("(n s) a -> n (s a)", s=P), empty[:].rearrange("n s a -> n (s a)")
                         ).then_inc(zero_stored, 16)
            sp.wait_ge(scattered, 16 * TOPK * (NT + 1))
            sp.wait_ge(zero_stored, 16)
            sp.dma_start(slots[:].rearrange("n s a -> n (s a)"), d["slot_rows"].rearrange("(n s) a -> n (s a)", s=P)
                         ).then_inc(slots_loaded, 16)
            sp.wait_ge(x1_stored, 16 * (NT + 2))
            sp.wait_ge(acc_stored, 16 * (NT + 2))

        @block.gpsimd
        def _(g):
            g.memset(eps[:], EPS)
            g.memset(mhalf[:], -0.5)
            g.drain()

            def inv_std(t, R):
                g.wait_ge(stats_ready, t + 1)
                nc.gpsimd.tensor_tensor(rstd[0:R, 0:1], mv[0:R, 1:2], eps[0:R, :], ALU.add)
                g.drain()
                nc.gpsimd.tensor_tensor(rstd[0:R, 1:2], rstd[0:R, 0:1], mhalf[0:R, :], ALU.pow).then_inc(rstd_ready, 1)

            with g.Fori(0, NT) as t:
                inv_std(t, P)
            inv_std(NT, NS)
            g.wait_ge(dest_ready, 1)
            g.wait_ge(zero_stored, 16)
            for t in range(NT + 1):
                R = P if t < NT else NS
                for c in range(TOPK):
                    g.indirect_dma_start(d["slot_rows"], bass.IndirectOffsetOnAxis(dest[0:R, t, c:c + 1], 0),
                                         choice[0:R, t, c], None).then_inc(scattered, 16)

        @block.tensor
        def _(pe):
            pe.wait_ge(consts, 16 * 13)

            def tile(t, R):
                pe.wait_ge(in_loaded, t * 32 + 32)
                for c in range(DC):
                    mm = nc.tensor.transpose(pT[:, c // 4, (c % 4) * P:(c % 4) * P + R], mx[0:R, c * P:(c + 1) * P],
                                             k.ident[0:R, 0:R])
                mm.then_inc(mix_in_psum, 1)
                pe.wait_ge(mixT_ready, t + 1)
                pe.wait_ge(w_loaded, 16)
                pe.wait_ge(po_free, t + 1)
                for i in range(2):
                    for c in range(DC):
                        mm = nc.tensor.matmul(pO[0:R, i], mT[:, c, 0:R], wo[:, c, i * 512:(i + 1) * 512],
                                              start=(c == 0), stop=(c == DC - 1))
                mm.then_inc(proj_done, 1)
                pe.wait_ge(x1_ready, t + 1)
                for c in range(DC):
                    mm = nc.tensor.transpose(pT[:, c // 4, (c % 4) * P:(c % 4) * P + R], xs[0:R, c * P:(c + 1) * P],
                                             k.ident[0:R, 0:R])
                mm.then_inc(x1_in_psum, 1)
                pe.wait_ge(x1T_ready, t + 1)
                for c in range(DC):
                    mm = nc.tensor.matmul(pR[0:R, 0:P], xT[:, c, 0:R], wr[:, c], start=(c == 0), stop=(c == DC - 1))
                mm.then_inc(router_done, 1)
                for c in range(DC):
                    mm = nc.tensor.matmul(pG[0:R], xT[:, c, 0:R], sgu[:, c], start=(c == 0), stop=(c == DC - 1))
                mm.then_inc(gu_done, 1)
                pe.wait_ge(h_ready, t + 1)
                for i in range(2):
                    mm = nc.tensor.transpose(pH[:, i * P:i * P + R], hs[0:R, i * P:(i + 1) * P], k.ident[0:R, 0:R])
                mm.then_inc(h_in_psum, 1)
                pe.wait_ge(hT_ready, t + 1)
                for i in range(2):
                    for c in range(2):
                        mm = nc.tensor.matmul(pO[0:R, i], hT[:, c, 0:R], sd[:, c, i * 512:(i + 1) * 512],
                                              start=(c == 0), stop=(c == 1))
                mm.then_inc(down_done, 1)

            with pe.Fori(0, NT) as t:
                tile(t, P)
            tile(NT, NS)
            pe.wait_ge(dv, 1)
            m2 = mask[:].rearrange("p t e -> p (t e)")
            for i, (a, b) in enumerate(((0, 512), (512, (NT + 1) * NE))):
                nc.tensor.matmul(pT[:, i, 0:b - a], lt[:], m2[:, a:b], start=True, stop=True)
                mm = nc.tensor.matmul(pO[:, i, 0:b - a], k.ones[:], m2[:, a:b], start=True, stop=True)
            mm.then_inc(pp, 1)
            pe.wait_ge(dv, 2)
            nc.tensor.transpose(pR[0:1, 0:P], be[:], k.ident[:]).then_inc(pp, 1)
            pe.wait_ge(slots_loaded, 16)
            for a in range(2):
                mm = nc.tensor.transpose(pG[:, a * P:a * P + NBLK], slots[:, :, a], k.ident[0:NBLK, 0:NBLK])
            mm.then_inc(pp, 1)

        @block.scalar
        def _(act):
            def tile(t, R):
                act.wait_ge(mix_in_psum, t + 1)
                for i in range(2):
                    nc.scalar.copy(mT[:, i * 4:i * 4 + 4, 0:R], pT[:, i, :].rearrange("p (c r) -> p c r", r=P)[:, :, 0:R])
                act.drain().then_inc(mixT_ready, 1)
                act.wait_ge(x1_in_psum, t + 1)
                for i in range(2):
                    nc.scalar.copy(xT[:, i * 4:i * 4 + 4, 0:R], pT[:, i, :].rearrange("p (c r) -> p c r", r=P)[:, :, 0:R])
                act.drain().then_inc(x1T_ready, 1)
                act.wait_ge(router_done, t + 1)
                act.wait_ge(r_free, t + 1)
                nc.scalar.activation(sc_[0:R], pR[0:R, 0:NE], ACT.Exp, scale=-1.0)
                act.wait_ge(gu_done, t + 1)
                nc.scalar.activation(eg[0:R], pG[0:R, 0:FE], ACT.Exp, scale=-1.0)
                act.drain().then_inc(exp_ready, 1)
                act.wait_ge(h_in_psum, t + 1)
                nc.scalar.copy(hT[:, :, 0:R], pH[:, 0:2 * P].rearrange("p (c r) -> p c r", r=P)[:, :, 0:R]).then_inc(hT_ready, 1)

            with act.Fori(0, NT) as t:
                tile(t, P)
            tile(NT, NS)

        @block.vector
        def _(v):
            v.sem_inc(in_used, 1)
            v.sem_inc(po_free, 1)
            v.sem_inc(r_free, 1)
            v.sem_inc(x1_stored, 16)
            v.sem_inc(acc_stored, 16)
            v.memset(mask[:], 0.0)
            v.memset(ef[:], 0.0)
            v.memset(choice[:], 0.0)
            v.memset(empty[:], 0.0)
            v.wait_ge(consts, 16 * 13)
            v.drain()
            nc.vector.tensor_scalar(empty[:, :, 0], io128[0:NBLK], float(NTOK), None, ALU.add)
            for c in range(TOPK):
                nc.vector.tensor_copy(choice[:, :, c, 0], tokf[:])
            v.drain()

            def e3(ap, shape):
                return bcast(ap, shape)

            def tile(t, R):
                v.wait_ge(proj_done, t + 1)
                v.wait_ge(in_loaded, t * 32 + 32)
                v.wait_ge(x1_stored, t * 16 + 16)
                nc.vector.scalar_tensor_tensor(out=xs[0:R], in0=xr[0:R], scalar=ALPHA, in1=pO[0:R].rearrange("p a b -> p (a b)"),
                                               op0=ALU.mult, op1=ALU.add)
                v.drain().then_inc(in_used, 1)
                for i in range(2):
                    nc.vector.bn_stats(stats[0:R, i, :], xs[0:R, i * 512:(i + 1) * 512])
                v.drain()
                nc.vector.bn_aggr(mv[0:R, :], stats[0:R])
                v.drain().then_inc(stats_ready, 1)
                v.wait_ge(rstd_ready, t + 1)
                nc.vector.tensor_scalar(xs[0:R, :], xs[0:R, :], mv[0:R, 0:1], rstd[0:R, 1:2], ALU.subtract, ALU.mult)
                v.drain()
                nc.vector.tensor_tensor(xs[0:R, :], xs[0:R, :], gain[0:R, :], ALU.mult)
                v.drain()
                nc.vector.tensor_tensor(xs[0:R, :], xs[0:R, :], bias[0:R, :], ALU.add)
                v.drain().then_inc(x1_ready, 1)
                v.wait_ge(exp_ready, t + 1)
                nc.vector.tensor_scalar(eg[0:R], eg[0:R], 1.0, None, ALU.add)
                nc.vector.tensor_scalar(sc_[0:R], sc_[0:R], 1.0, None, ALU.add)
                v.drain()
                nc.vector.reciprocal(eg[0:R], eg[0:R])
                nc.vector.reciprocal(sc_[0:R], sc_[0:R])
                v.drain()
                nc.vector.tensor_tensor(hs[0:R], eg[0:R], pG[0:R, 0:FE], ALU.mult)
                v.drain()
                nc.vector.tensor_tensor(hs[0:R], hs[0:R], pG[0:R, FE:2 * FE], ALU.mult)
                v.drain().then_inc(h_ready, 1)
                nc.vector.tensor_tensor(bi[0:R], sc_[0:R], rbias[0:R], ALU.add)
                v.drain()
                for gr in range(NGRP):
                    nc.vector.max(g8[0:R, gr], bi[0:R, gr * 8:gr * 8 + 8])
                v.drain()
                nc.vector.tensor_tensor(gs[0:R], g8[0:R, :, 0], g8[0:R, :, 1], ALU.add)
                v.drain()
                nc.vector.max(gt[0:R], gs[0:R])
                v.drain()
                nc.vector.max_index(gi[0:R], gt[0:R], gs[0:R])
                v.drain()
                nc.vector.tensor_copy(gif[0:R], gi[0:R])
                v.drain()
                nc.vector.tensor_tensor(gk[0:R], e3(io64[0:R, 0:8].rearrange("p (g a) -> p g a", a=1), [R, 8, KGRP]),
                                        e3(gif[0:R, 0:KGRP].rearrange("p (a j) -> p a j", a=1), [R, 8, KGRP]), ALU.is_equal)
                v.drain()
                nc.vector.tensor_reduce(keep[0:R], gk[0:R], AX.X, ALU.add)
                v.drain()
                b3 = bi[0:R].rearrange("p (g e) -> p g e", e=8)
                k3 = e3(keep[0:R].rearrange("p (g a) -> p g a", a=1), [R, 8, 8])
                nc.vector.tensor_tensor(b3, b3, k3, ALU.mult)
                nc.vector.tensor_scalar(gs[0:R], keep[0:R], 1.0, 1e30, ALU.subtract, ALU.mult)
                v.drain()
                nc.vector.tensor_tensor(b3, b3, e3(gs[0:R].rearrange("p (g a) -> p g a", a=1), [R, 8, 8]), ALU.add)
                v.drain()
                nc.vector.max(et[0:R], bi[0:R])
                v.drain()
                nc.vector.max_index(ei[0:R], et[0:R], bi[0:R])
                v.drain()
                efs = ef[0:R, bass.ds(t, 1)].rearrange("p a c -> p (a c)")
                nc.vector.tensor_copy(efs, ei[0:R, 0:TOPK])
                v.drain()
                i3 = e3(io64[0:R].rearrange("p (a e) -> p a e", a=1), [R, TOPK, NE])
                nc.vector.tensor_tensor(oh[0:R], i3, e3(ef[0:R, bass.ds(t, 1)].rearrange("p a c -> p c a"), [R, TOPK, NE]),
                                        ALU.is_equal)
                v.drain()
                nc.vector.tensor_reduce(mask[0:R, bass.ds(t, 1)].rearrange("p a e -> p (a e)"),
                                        oh[0:R].rearrange("p c e -> p e c"), AX.X, ALU.add)
                nc.vector.tensor_tensor(ohw[0:R], oh[0:R], e3(sc_[0:R].rearrange("p (a e) -> p a e", a=1), [R, TOPK, NE]), ALU.mult)
                v.drain().then_inc(r_free, 1)
                wt = choice[0:R, bass.ds(t, 1), :, 1].rearrange("p a c -> p (a c)")
                nc.vector.tensor_reduce(wt, ohw[0:R], AX.X, ALU.add)
                v.drain()
                nc.vector.tensor_reduce(ws[0:R, 0:1], wt, AX.X, ALU.add)
                v.drain()
                nc.vector.reciprocal(ws[0:R, 1:2], ws[0:R, 0:1])
                v.drain()
                nc.vector.tensor_scalar(wt, wt, ws[0:R, 1:2], 2.5, ALU.mult, ALU.mult)
                v.wait_ge(down_done, t + 1)
                v.wait_ge(acc_stored, t * 16 + 16)
                nc.vector.scalar_tensor_tensor(out=acc[0:R], in0=xs[0:R], scalar=ALPHA, in1=pO[0:R].rearrange("p a b -> p (a b)"),
                                               op0=ALU.mult, op1=ALU.add)
                v.drain().then_inc(acc_ready, 1)
                v.sem_inc(po_free, 1)

            with v.Fori(0, NT) as t:
                tile(t, P)
            tile(NT, NS)
            v.drain().then_inc(dv, 1)
            v.wait_ge(pp, 1)
            TE = (NT + 1) * NE
            d2 = dst[:].rearrange("p t e -> p (t e)")
            p2 = pre[:].rearrange("p t e -> p (t e)")
            nc.vector.tensor_copy(d2[:, 0:512], pT[:, 0])
            nc.vector.tensor_copy(d2[:, 512:TE], pT[:, 1, 0:TE - 512])
            v.memset(pre[:, 0], 0.0)
            v.drain()
            for t in range(NT):
                src = pO[:, 0, t * NE:(t + 1) * NE] if t < 8 else pO[:, 1, 0:NE]
                nc.vector.tensor_tensor(pre[:, t + 1], pre[:, t], src, ALU.add)
                v.drain()
            nc.vector.tensor_tensor(d2, d2, p2, ALU.add)
            nc.vector.tensor_tensor(ble[:], pre[:, NT], pO[:, 1, 0:NE], ALU.add)
            v.drain()
            nc.vector.tensor_tensor(cmp_[:], e3(ble[:].rearrange("p (e a) -> p e a", a=1), [P, NE, 16]),
                                    e3(thr[:].rearrange("p (a j) -> p a j", a=1), [P, NE, 16]), ALU.is_gt)
            v.drain()
            nc.vector.tensor_reduce(nbl[:], cmp_[:], AX.X, ALU.add)
            v.drain()
            nc.vector.tensor_tensor_scan(incl[:], k.ones[:, 0:NE], nbl[:], 0.0, ALU.mult, ALU.add)
            v.drain()
            nc.vector.tensor_tensor(nbl[:], incl[:], nbl[:], ALU.subtract)
            nc.vector.tensor_scalar(ble[:], incl[:], ip[:, 0:1], None, ALU.is_le)
            v.drain()
            nc.vector.tensor_reduce(be[:], ble[:], AX.X, ALU.add)
            nc.vector.tensor_scalar(nbl[:], nbl[:], float(P), None, ALU.mult)
            v.drain()
            nc.vector.tensor_scalar(be[:], be[:], float(NE - 1), None, ALU.min)
            v.drain().then_inc(dv, 1)
            nc.vector.tensor_tensor(dst[:], dst[:], e3(nbl[:].rearrange("p (a e) -> p a e", a=1), [P, NT + 1, NE]), ALU.add)
            v.drain()
            for t in range(NT + 1):
                nc.vector.tensor_tensor(oh[:], e3(io64[:].rearrange("p (a e) -> p a e", a=1), [P, TOPK, NE]),
                                        e3(ef[:, t].rearrange("p (c a) -> p c a", a=1), [P, TOPK, NE]), ALU.is_equal)
                v.drain()
                nc.vector.tensor_tensor(oh[:], oh[:], e3(dst[:, t].rearrange("p (a e) -> p a e", a=1), [P, TOPK, NE]), ALU.mult)
                v.drain()
                nc.vector.tensor_reduce(dstf[:, t], oh[:], AX.X, ALU.add)
                v.drain()
            nc.vector.tensor_copy(dest[:], dstf[:])
            v.drain().then_inc(dest_ready, 1)
            v.wait_ge(pp, 2)
            nc.vector.tensor_copy(k.plan[:, 0:NBLK], pR[0:1, 0:NBLK])
            nc.vector.tensor_copy(k.plan[:, P - 1:P], incl[0:1, NE - 1:NE])
            nc.vector.tensor_scalar(half_counts[:, 0:NBLK // 2], io64[0:1, 0:NBLK // 2], 2.0, incl[0:1, NE - 1:NE], ALU.mult, ALU.is_lt)
            v.drain()
            nc.vector.tensor_reduce(ws[0:1, 0:1], half_counts[:, 0:NBLK // 2], AX.X, ALU.add)
            v.drain()
            nc.vector.tensor_tensor(ws[0:1, 1:2], incl[0:1, NE - 1:NE], ws[0:1, 0:1], ALU.subtract)
            v.drain()
            nc.vector.tensor_copy(k.plan[:, P - 3:P - 1], ws[0:1, 0:2])
            v.wait_ge(pp, 3)
            nc.vector.tensor_copy(k.toks[:, 0:NBLK], pG[:, 0:NBLK])
            nc.vector.tensor_copy(k.slot_w[:], pG[:, P:P + NBLK])


def experts(nc, k, d):
    with ExitStack() as ctx:
        def sb(name, shape, dt=F32):
            return ctx.enter_context(nc.sbuf_tensor(name, shape, dt))

        def ps(name, shape):
            return ctx.enter_context(nc.psum_tensor(name, shape, F32))

        def sem(name):
            k.sems.append(ctx.enter_context(nc.semaphore(name)))
            return k.sems[-1]

        def two(make, name, *a):
            return [make(f"{name}{u}", *a) for u in range(2)]

        wg, wu, wd = two(sb, "e_gate", [P, DC, FE]), two(sb, "e_up", [P, DC, FE]), two(sb, "e_down", [P, 2, D])
        xg, xT = two(sb, "e_x", [P, D]), two(sb, "e_xT", [P, DC, P])
        gather_rows, add_rows = two(sb, "gather_rows", [P, 1], I32), two(sb, "add_rows", [P, 1], I32)
        sg, hT, ysb = two(sb, "e_silu", [P, 2 * P]), two(sb, "e_hT", [P, 2 * P]), two(sb, "e_y", [P, 2, 512])
        pT = ps("e_pT", [P, 2, 512])
        pG, pY = two(ps, "e_pG", [P, 512]), two(ps, "e_pY", [P, 2, 512])

        gu_loaded, down_loaded, gathered = two(sem, "gu_loaded"), two(sem, "down_loaded"), two(sem, "x_gathered")
        y_added, ysb_free = sem("y_added"), sem("ysb_free")
        x_turned, xT_act, xT_dve, gu_done, silu_ready, h_ready, down_done, y_act, y_dve = (
            sem(n) for n in ("x_turned", "xT_act", "xT_dve", "e_gu_done", "e_silu_ready", "e_h_ready", "e_down_done", "y_act", "y_dve"))
        block = ctx.enter_context(nc.Block())

        def number_of_blocks(eng):
            return plan_entry(eng, P - 1, 1, NBLK)

        def plan_entry(eng, at, low, high):
            return eng.value_load(k.plan[0:1, at:at + 1], min_val=low, max_val=high)

        @block.sync
        def _(sp):
            nb = number_of_blocks(sp)

            def load(n, i, u):
                e = sp.value_load(k.plan[0:1, bass.ds(n, 1)], min_val=0, max_val=NE - 1)
                rows = bass.ds(e * P, P)
                sp.wait_ge(gu_done, n + 1)
                sp.dma_start(wg[u][:].rearrange("p c f -> p (c f)"), d["exp_gate"][rows]).then_inc(gu_loaded[u], 16)
                sp.dma_start(wu[u][:].rearrange("p c f -> p (c f)"), d["exp_up"][rows]).then_inc(gu_loaded[u], 16)
                sp.wait_ge(down_done, n + 1)
                sp.dma_start(wd[u][:].rearrange("p c f -> p (c f)"), d["exp_down"][rows]).then_inc(down_loaded[u], 16)

            load(0, 0, 0)
            load(1, 0, 1)
            with sp.Fori(0, NBLK // 2) as i:
                for u in range(2):
                    n = i * 2 + u
                    with sp.If(nb > n + 2):
                        load(n + 2, i + 1, u)

        @block.gpsimd
        def _(g):
            nb = number_of_blocks(g)

            def gather(n, u):
                nc.gpsimd.tensor_copy(gather_rows[u][:], k.toks[:, bass.ds(n, 1)])
                g.drain()
                g.indirect_dma_start(xg[u][:], None, d["x1"], bass.IndirectOffsetOnAxis(gather_rows[u][:], 0)
                                     ).then_inc(gathered[u], 16)

            def add(n, u, first=False):
                if not first:
                    g.wait_ge(y_added, n * 16)
                    g.sem_inc(ysb_free, 1)
                g.wait_ge(y_act, n + 1)
                g.nop()
                g.wait_ge(y_dve, n + 1)
                g.nop()
                nc.gpsimd.tensor_copy(add_rows[u][:], k.toks[:, bass.ds(n, 1)])
                g.drain()
                g.indirect_dma_start(d["acc"], bass.IndirectOffsetOnAxis(add_rows[u][:], 0), ysb[u][:].rearrange("p a b -> p (a b)"),
                                     None, compute_op=ALU.add).then_inc(y_added, 16)

            def block_pair(i, first=False):
                for u in range(2):
                    n = i * 2 + u
                    with g.If(nb > n + 3):
                        g.wait_ge(x_turned, n + 4)
                        g.nop()
                        gather(n + 3, 1 - u)
                    with g.If(nb > n):
                        add(n, u, first and u == 0)

            gather(0, 0)
            gather(1, 1)
            g.wait_ge(x_turned, 3)
            gather(2, 0)
            block_pair(0, first=True)
            with g.Fori(1, NBLK // 2) as i:
                block_pair(i)
            g.wait_ge(y_added, nb * 16)
            g.nop()

        @block.tensor
        def _(pe):
            pe.sem_inc(x_turned, 2)
            pe.sem_inc(gu_done, 2)
            pe.sem_inc(down_done, 2)
            nb = number_of_blocks(pe)

            def turn(n, i, u):
                pe.wait_ge(gathered[u], i * 16 + 16)
                x8 = xg[u][:].rearrange("s (p c) -> s c p", c=DC)
                for c in range(DC):
                    mm = nc.tensor.transpose(pT[:, c // 4, (c % 4) * P:(c % 4 + 1) * P], x8[:, c], k.ident[:])
                mm.then_inc(x_turned, 1)

            def gate_up(n, i, u):
                pe.wait_ge(xT_act, n + 1)
                pe.wait_ge(xT_dve, n + 1)
                pe.wait_ge(gu_loaded[u], i * 32 + 32)
                for w, at in ((wg, 0), (wu, 2 * P)):
                    for f in range(2):
                        for c in range(DC):
                            mm = nc.tensor.matmul(pG[u][:, at + f * P:at + (f + 1) * P], w[u][:, c, f:FE:2], xT[u][:, c],
                                                  start=(c == 0), stop=(c == DC - 1))
                mm.then_inc(gu_done, 1)

            def down(n, i, u):
                pe.wait_ge(h_ready, n + 1)
                pe.wait_ge(down_loaded[u], i * 16 + 16)
                for h in range(2):
                    for f in range(2):
                        mm = nc.tensor.matmul(pY[u][:, h], hT[u][:, f * P:(f + 1) * P], wd[u][:, f, h * 512:(h + 1) * 512],
                                              start=(f == 0), stop=(f == 1))
                mm.then_inc(down_done, 1)

            turn(0, 0, 0)
            gate_up(0, 0, 0)
            with pe.Fori(0, NBLK // 2) as i:
                for u in range(2):
                    n = i * 2 + u
                    nxt = i + u
                    with pe.If(nb > n):
                        with pe.If(nb > n + 1):
                            turn(n + 1, nxt, 1 - u)
                        down(n, i, u)
                        with pe.If(nb > n + 1):
                            gate_up(n + 1, nxt, 1 - u)

        def x_half(eng, copy, done, h, n, u):
            eng.wait_ge(x_turned, n + 3)
            copy(xT[u][:, h * 4:h * 4 + 4], pT[:, h].rearrange("p (c r) -> p c r", r=P)).then_inc(done, 1)

        def y_ready(eng, n):
            eng.wait_ge(down_done, n + 3)
            eng.wait_ge(ysb_free, n + 1)

        @block.scalar
        def _(act):
            nb = number_of_blocks(act)

            def silu(n, u):
                act.wait_ge(gu_done, n + 3)
                nc.scalar.activation(sg[u][:], pG[u][:, 0:2 * P], ACT.Silu).then_inc(silu_ready, 1)

            x_half(act, nc.scalar.copy, xT_act, 0, 0, 0)
            silu(0, 0)
            with act.Fori(0, NBLK // 2) as i:
                for u in range(2):
                    n = i * 2 + u
                    with act.If(nb > n):
                        with act.If(nb > n + 1):
                            x_half(act, nc.scalar.copy, xT_act, 0, n + 1, 1 - u)
                        y_ready(act, n)
                        nc.scalar.activation(ysb[u][:, 0], pY[u][:, 0], ACT.Copy, scale=k.slot_w[:, bass.ds(n, 1)]).then_inc(y_act, 1)
                        with act.If(nb > n + 1):
                            silu(n + 1, 1 - u)

        @block.vector
        def _(v):
            v.sem_inc(ysb_free, 2)
            nb = number_of_blocks(v)

            def hidden(n, u):
                v.wait_ge(silu_ready, n + 1)
                nc.vector.tensor_tensor(hT[u][:], sg[u][:], pG[u][:, 2 * P:4 * P], ALU.mult).then_inc(h_ready, 1)

            x_half(v, nc.vector.tensor_copy, xT_dve, 1, 0, 0)
            hidden(0, 0)
            with v.Fori(0, NBLK // 2) as i:
                for u in range(2):
                    n = i * 2 + u
                    with v.If(nb > n):
                        with v.If(nb > n + 1):
                            x_half(v, nc.vector.tensor_copy, xT_dve, 1, n + 1, 1 - u)
                        y_ready(v, n)
                        nc.vector.tensor_scalar(ysb[u][:, 1], pY[u][:, 1], k.slot_w[:, bass.ds(n, 1)], None, ALU.mult).then_inc(y_dve, 1)
                        with v.If(nb > n + 1):
                            hidden(n + 1, 1 - u)


def finish(nc, k, d):
    with ExitStack() as ctx:
        def sb(name, shape, dt=F32):
            return ctx.enter_context(nc.sbuf_tensor(name, shape, dt))

        def sem(name):
            k.sems.append(ctx.enter_context(nc.semaphore(name)))
            return k.sems[-1]

        gain, bias = sb("ln2_g_sb", [P, D]), sb("ln2_b_sb", [P, D])
        acc, out = sb("f_acc", [P, NT + 1, D]), sb("f_out", [P, NT + 1, D])
        stats, mv, rstd = sb("stats2", [P, 2, 2, 6]), sb("mv2", [P, NT + 1, 2]), sb("rstd2", [P, NT + 1])
        shift, eps, mhalf = sb("shift2", [P, NT + 1]), sb("eps2", [P, 1]), sb("mhalf2", [P, 1])
        consts, mv_ready, rstd_ready, shift_ready, normed, scaled, out_ready, out_stored = (
            sem(n) for n in ("f_consts", "f_mv_ready", "f_rstd_ready", "f_shift_ready", "f_normed", "f_scaled", "f_out_ready", "f_out_stored"))
        acc_loaded = [sem(f"f_acc_loaded{t}") for t in range(NT + 1)]
        block = ctx.enter_context(nc.Block())
        rows = [P] * NT + [NS]

        @block.sync
        def _(sp):
            for t, R in enumerate(rows):
                sp.dma_start(acc[0:R, t], d["acc"][t * P:t * P + R]).then_inc(acc_loaded[t], 16)
                if t == 0:
                    sp.dma_start(gain[:], bcast(d["ln2_g"], [P, D])).then_inc(consts, 16)
                    sp.dma_start(bias[:], bcast(d["ln2_b"], [P, D])).then_inc(consts, 16)
            for t, R in enumerate(rows):
                sp.wait_ge(out_ready, t + 1)
                dst = d["y_prompt"][t * P:t * P + P] if t < NT else d["y_sample"]
                sp.dma_start(dst, out[0:R, t]).then_inc(out_stored, 16)
            sp.wait_ge(out_stored, 16 * (NT + 1))

        @block.gpsimd
        def _(g):
            g.memset(eps[:], EPS)
            g.memset(mhalf[:], -0.5)
            g.drain()
            g.wait_ge(consts, 32)

            def inv_std(t, R):
                g.wait_ge(mv_ready, t + 1)
                nc.gpsimd.tensor_tensor(rstd[0:R, t:t + 1], mv[0:R, t, 1:2], eps[0:R, :], ALU.add)
                g.drain()
                nc.gpsimd.tensor_tensor(rstd[0:R, t:t + 1], rstd[0:R, t:t + 1], mhalf[0:R, :], ALU.pow).then_inc(rstd_ready, 1)

            def add_bias(t, R):
                g.wait_ge(scaled, t + 1)
                nc.gpsimd.tensor_tensor(out[0:R, t], out[0:R, t], bias[0:R], ALU.add).then_inc(out_ready, 1)

            inv_std(0, P)
            for t, R in enumerate(rows):
                if t < NT:
                    inv_std(t + 1, rows[t + 1])
                add_bias(t, R)

        @block.scalar
        def _(act):
            for t, R in enumerate(rows):
                act.wait_ge(shift_ready, t + 1)
                nc.scalar.activation(out[0:R, t], acc[0:R, t], ACT.Identity, bias=shift[0:R, t:t + 1], scale=rstd[0:R, t:t + 1]
                                     ).then_inc(normed, 1)

        @block.vector
        def _(v):
            v.wait_ge(consts, 32)

            def stats_of(t, R):
                v.wait_ge(acc_loaded[t], 16)
                for i in range(2):
                    nc.vector.bn_stats(stats[0:R, t % 2, i, :], acc[0:R, t, i * 512:(i + 1) * 512])
                v.drain()
                nc.vector.bn_aggr(mv[0:R, t], stats[0:R, t % 2])
                v.drain().then_inc(mv_ready, 1)

            def shift_of(t, R):
                v.wait_ge(rstd_ready, t + 1)
                nc.vector.scalar_tensor_tensor(out=shift[0:R, t:t + 1], in0=mv[0:R, t, 0:1], scalar=-1.0, in1=rstd[0:R, t:t + 1],
                                               op0=ALU.mult, op1=ALU.mult).then_inc(shift_ready, 1)

            def gain_of(t, R):
                v.wait_ge(normed, t + 1)
                nc.vector.tensor_tensor(out[0:R, t], out[0:R, t], gain[0:R], ALU.mult).then_inc(scaled, 1)

            for t in range(NT + 3):
                if t <= NT:
                    stats_of(t, rows[t])
                if 1 <= t <= NT + 1:
                    shift_of(t - 1, rows[t - 1])
                if t >= 2:
                    gain_of(t - 2, rows[t - 2])



def more_constants():
    i=np.arange(P)
    j = np.arange(2 * NT)
    vis = (j[None, :] + 1) * 64 - 1 <= np.arange(SEQ)[:, None]
    vis = vis.reshape(NT, P, 2 * NT).transpose(1, 0, 2)
    return {
        "mask_diag": np.where(i[None, :] <= i[:, None], 0.0, NEG), "cmp_vis": vis, "cmp_mask": np.where(vis, 0.0, NEG),
        "spread16": np.arange(16)[:, None] == i[None, :] % 16, "slot_mask": i[:, None] // 16 == np.arange(8)[None, :],
        "grp4": np.arange(64)[:, None] // 4 == np.arange(16)[None, :],
        "pick_bg": (np.arange(16)[:, None, None] // 2 == i[None, None, :] // NJ) & (np.arange(16)[:, None, None] % 2 == np.arange(2)[None, :, None]),
        "e8": np.arange(8)[:, None] == i[None, :] // NJ, "e8t": i[:, None] // NJ == np.arange(8)[None, :],
        "jmask": i[:, None] % NJ == np.arange(NJ)[None, :], "iota": np.broadcast_to(i, (P, P)),
        "parity": np.broadcast_to(i % 2, (P, P)), "wmask": np.where(i % NJ == NJ - 1, 0.0, NEG)[:, None],
        "mask_lt": i[:, None] < i[None, :], "iota_p": i[:, None],
        "block_starts": np.broadcast_to(np.arange(16) * P, (P, 16)),
        "token_ids": np.arange(NT + 1)[None, :] * P + i[:, None],
        "mask_neg": np.where(i[:, None] <= i[None, :], 0.0, NEG),
        "expand_h": np.arange(NH)[:, None] == np.arange(512)[None, :] // HD,
    }
def more_inputs(a, r):
    return {
        "conv_w": a["conv_w"][0].reshape(4, DC, P).transpose(2, 1, 0), "conv_b": a["conv_b"][0].reshape(DC, P).T,
        "dt_bias": a["dt_bias"], "a_log": a["a_log"], "d_skip": a["d_skip"], "ssd_norm_w": a["ssd_norm_w"],
        "state_conv": a["state_conv"][0].reshape(NS, 3, DC, P).transpose(3, 2, 1, 0),
        "state_conv_rows": a["state_conv"][0], "state_ssm": a["state_ssm"][0].reshape(NS, NH * HD, P),
        "cache_kv_win": a["cache_kv_win"][0].reshape(NS, 512, KV),
        "cache_kv_sel": a["cache_kv_sel"][0].reshape(-1, QR * KV),
        "w_out": np.concatenate([a["w_out"][0][0:512], a["w_out"][0][r]]), "ln1_g": a["ln1_g"], "ln1_b": a["ln1_b"],
        "router_w": np.concatenate([a["router_w"][0], np.zeros((D, P - NE), np.float32)], 1), "router_bias": a["router_bias"],
        "sh_gate": a["sh_w_gate"][0], "sh_up": a["sh_w_up"][0], "sh_down": a["sh_w_down"][0],
        "exp_gate": a["exp_w_gate"][0].reshape(NE * P, DC * FE), "exp_up": a["exp_w_up"][0].reshape(NE * P, DC * FE),
        "exp_down": a["exp_w_down"][0].reshape(NE * P, 2 * D), "ln2_g": a["ln2_g"], "ln2_b": a["ln2_b"],
        "page_table": a["page_table"].reshape(1, NS * NPAGE), "cache_kv_cmp": (a["cache_kv_cmp"][0].reshape(-1, 2, 64, 2, 2, 2, HD // 2)
                         .transpose(0, 5, 2, 6, 3, 1, 4).reshape(-1, KV)),
        "pe_page": (np.broadcast_to(a["cmp_pe"][0].reshape(1, 1, 2, 64, 2, HD // 2), (2, 2, 2, 64, 2, HD // 2))
                    .transpose(4, 3, 0, 2, 1, 5).reshape(P, KV)),
        "cmp_w1": a["cmp_w1"][0].reshape(2, 64, 2, HD // 2, P).transpose(2, 1, 0, 3, 4).reshape(P, 2, HD // 2, P),
        "cmp_w2": a["cmp_w2"][0], "cmp_b1": a["cmp_b1"][0].T,
        "cmp_b2k": np.tile(a["cmp_b2"][0, 0], 2)[:, None], "cmp_b2v": a["cmp_b2"][0, 1:2],
    }
STEPS = [project, ssd, compress, attend, sample, route, experts, finish]


OUTS = [
    ("y_prompt", (1, SEQ, D)), ("y_sample", (NS, 1, D)),
    ("kv_cmp_prompt", (1, 1, SEQ, 2, 2, HD)), ("kv_sel_prompt", (1, 1, SEQ, 2, 2, HD)),
    ("kv_win_prompt", (1, 1, 512, 2, 2, HD)), ("ssm_prompt", (1, 1, NH, HD, P)),
    ("conv_prompt", (1, 1, 3, D)),
    ("kv_cmp_sample", (1, NS, 1, 2, 2, HD)), ("kv_sel_sample", (1, NS, 1, 2, 2, HD)),
    ("kv_win_sample", (1, NS, 512, 2, 2, HD)), ("ssm_sample", (1, NS, NH, HD, P)),
    ("conv_sample", (1, NS, 3, D)),
]
FORMS = {
    "y_prompt": (SEQ, D), "y_sample": (NS, D), "kv_cmp_prompt": (SEQ, KV), "kv_sel_prompt": (SEQ, KV),
    "kv_win_prompt": (512, KV), "ssm_prompt": (NH * HD, P), "conv_prompt": (3, D), "kv_cmp_sample": (NS, KV),
    "kv_sel_sample": (NS, KV), "kv_win_sample": (NS, 512, KV), "ssm_sample": (NS, NH * HD, P),
    "conv_sample": (NS, 3, D),
}
SCRATCH = {
    "xres": (NTOK, D), "z_silu": (NTOK, 512), "kv_win_all": (NTOK, KV), "mix": (NTOK, D), "x1": (NTOK + P, D),
    "acc": (NTOK + P, D), "slot_rows": (NBLK * P, 2),
}


def constants():
    i = np.arange(P)
    inv = (500000.0 ** (-np.arange(RH, dtype=np.float32) / RH)).astype(np.float32)
    pos = np.concatenate([np.arange(SEQ), np.full(P, PAST)]).astype(np.float32)
    ang = pos[:, None] * inv[None]
    cos, sin = np.cos(ang), np.sin(ang)

    def by_tile(a):
        return np.ascontiguousarray(a.reshape(NT + 1, P, -1).transpose(1, 0, 2)).astype(np.float32)

    out = {
        "ident": np.eye(P), "mask_le": i[:, None] <= i[None, :], "ones": np.ones((P, P)),
        "rope_c": by_tile(np.concatenate([cos, cos], 1)), "rope_s": by_tile(np.concatenate([-sin, sin], 1)),
    }
    out.update(more_constants())
    return {n: np.ascontiguousarray(a).astype(np.float32) for n, a in out.items()}


def laid_out(a):
    cols = np.cumsum([0, 512, 1024, 8, 512, 128, 128, 128, 128, 128, 128, 24])
    z, xbc, dt, q, kc, vc, ks, vs, kw, vw, g = (np.arange(cols[n], cols[n + 1]) for n in range(11))
    pair = np.array([g_ * GQA + c for c in range(GQA) for g_ in range(2)])
    q = q.reshape(NH, HD)[pair].ravel()
    g = g.reshape(NH, 3)[pair].T.ravel()
    order = np.concatenate([q, kc, vc, ks, vs, kw, vw, g, dt, z, xbc])
    nsa_rows = 512 + (pair[:, None] * HD + np.arange(HD)).ravel()
    c = np.ascontiguousarray
    out = {
        "x": np.concatenate([a["x_prompt"].reshape(SEQ, D), a["x_sample"].reshape(NS, D)]),
        "w_in": c(a["w_in"][0][:, order]),
        "emb_ln_g": a["emb_ln_g"][None], "emb_ln_b": a["emb_ln_b"][None],
    }
    out.update(more_inputs(a, nsa_rows))
    return {n: c(v) for n, v in out.items()}


def build(nc, d, phases=99):
    with ExitStack() as ctx:
        k = persistent(nc, ctx)
        steps = STEPS[:phases]
        with ExitStack() as kept:
            alloc_kept(nc, kept, k)
            with ExitStack() as until_compressed:
                alloc_w1(nc, until_compressed, k)
                with ExitStack() as early:
                    alloc_xbc(nc, early, k)
                    for step in steps[:2]:
                        step(nc, k, d)
                for step in steps[2:3]:
                    step(nc, k, d)
            for step in steps[3:5]:
                step(nc, k, d)
        alloc_routing(nc, ctx, k)
        for step in steps[5:]:
            if step is experts:
                for s in k.sems[:len(k.sems) // 2]:
                    nc.sync.sem_clear(s)
                nc.all_engine_barrier()
            step(nc, k, d)


def kernel(**inputs):
    import concourse.bacc as bacc
    from concourse.bass_utils import run_bass_kernel_spmd

    a = {n: np.asarray(v) for n, v in inputs.items()}
    arrays = laid_out(a)
    arrays.update(constants())
    nc = bacc.Bacc("TRN2", target_bir_lowering=False, num_devices=1)
    d = {n: nc.dram_tensor("i_" + n, v.shape, mybir.dt.from_np(v.dtype), kind="ExternalInput").ap()
         for n, v in arrays.items()}
    for name, shape in FORMS.items():
        d[name] = nc.dram_tensor("o_" + name, shape, F32, kind="ExternalOutput").ap()
    for name, shape in SCRATCH.items():
        d[name] = nc.dram_tensor("s_" + name, shape, F32, kind="Internal").ap()
    build(nc, d)
    got = run_bass_kernel_spmd(nc, [{"i_" + n: v for n, v in arrays.items()}], core_ids=[0]).results[0]
    return tuple(got["o_" + name].reshape(shape) for name, shape in OUTS)
```

```python
from contextlib import ExitStack

import numpy as np
import concourse.bass as bass
from concourse import mybir

F32 = mybir.dt.float32
I32 = mybir.dt.int32
U32 = mybir.dt.uint32
ALU = mybir.AluOpType
ACT = mybir.ActivationFunctionType
AX = mybir.AxisListType

P = 128
D = 1024
DC = D // P
SEQ = 1024
NT = SEQ // P
NS = 8
NTOK = SEQ + NS
PAST = 8192
PAGE = 128
NPAGE = PAST // PAGE
HD = 64
NH = 8
GQA = 4
RH = 8
KV = 256
NEG = -1e30
ALPHA = 2.0 ** 0.25
EPS = 1e-5
SCALE = HD ** -0.5
C_Q, C_KV, C_WG, C_Z, C_X = 0, 512, 1024, 1312, 1824
D_IN = 2848
WG = 288


class Names:
    pass


def bcast(ap, shape):
    return ap.to_broadcast(shape)


def persistent(nc, ctx):
    k = Names()
    k.sems = []

    def sb(name, shape, dt=F32):
        t = ctx.enter_context(nc.sbuf_tensor(name, shape, dt))
        return t

    k.ident = sb("ident", [P, P])
    k.mask_le = sb("mask_le", [P, P])
    k.ones = sb("ones", [P, P])
    k.gd = sb("gd", [P, NT + 1, 32])
    return k


def project(nc, k, d):
    with ExitStack() as ctx:
        def sb(name, shape, dt=F32):
            return ctx.enter_context(nc.sbuf_tensor(name, shape, dt))

        def ps(name, shape):
            return ctx.enter_context(nc.psum_tensor(name, shape, F32))

        def sem(name):
            k.sems.append(ctx.enter_context(nc.semaphore(name)))
            return k.sems[-1]

        w = sb("w_in_sb", [P, DC, D_IN])
        room = k.room
        gain, bias, xin, xn = (room[:, i * D:(i + 1) * D] for i in range(4))
        hT = room[:, 4 * D:5 * D].rearrange("p (c r) -> p c r", r=P)
        rope_c, rope_s = (room[:, 7 * D + 512 + i * 256:7 * D + 512 + i * 256 + (NT + 1) * 2 * RH]
                          .rearrange("p (t r) -> p t r", r=2 * RH) for i in range(2))
        st = room[:, 5 * D:5 * D + 1792]
        zst = room[:, 5 * D + 1792:5 * D + 1792 + 512]
        stats, mv, rstd = sb("stats", [P, 2, 6]), sb("mv", [P, 2]), sb("rstd", [P, 2])
        mhalf, eps = sb("mhalf", [P, 1]), sb("eps", [P, 1])
        rt = sb("rt", [P, 8, 2 * RH])
        rt2 = sb("rt2", [P, 8, 2 * RH])
        pT = ps("pT", [P, 2, 512])
        pQ, pKV, pW, pZ = (ps(n, [P, 512]) for n in ("pQ", "pKV", "pW", "pZ"))
        pX = ps("pX", [P, 2, 512])

        w_in_loaded = [sem(f"w_in_loaded{i}") for i in range(5)]
        consts, x_loaded, x_taken = sem("consts"), sem("x_loaded"), sem("x_taken")
        stats_ready, rstd_ready, xn_ready, xn_stored = sem("stats_ready"), sem("rstd_ready"), sem("xn_ready"), sem("xn_stored")
        hT_in_psum, hT_ready = sem("hT_in_psum"), sem("hT_ready")
        kv_done, q_done, wg_done, xbc_done, z_done = sem("kv_done"), sem("q_done"), sem("wg_done"), sem("xbc_done"), sem("z_done")
        kv_out, wg_out, qr_out, q_out, xbc_out, z_out = (sem(n) for n in ("kv_out", "wg_out", "qr_out", "q_out", "xbc_out", "z_out"))
        roped, rows_stored, z_stored, heads_in_psum, heads_out = (sem(n) for n in ("roped", "rows_stored", "z_stored", "heads_in_psum", "heads_out"))

        conv_ready, conv_taken = sem("conv_ready"), sem("conv_taken")
        conv = k.kcT_s
        block = ctx.enter_context(nc.Block())

        @block.sync
        def _(sp):
            sp.dma_start(xin[:], d["x"][0:P]).then_inc(x_loaded, 16)
            sp.dma_start(gain[:], bcast(d["emb_ln_g"], [P, D])).then_inc(consts, 16)
            sp.dma_start(bias[:], bcast(d["emb_ln_b"], [P, D])).then_inc(consts, 16)
            sp.dma_start(k.ident[:], d["ident"]).then_inc(consts, 16)
            w_dram = d["w_in"].rearrange("(c p) n -> p c n", p=P)

            sp.dma_start(rope_c[:], d["rope_c"]).then_inc(consts, 16)
            sp.dma_start(rope_s[:], d["rope_s"]).then_inc(consts, 16)
            sp.dma_start(k.mask_le[:], d["mask_le"]).then_inc(consts, 16)
            sp.dma_start(k.ones[:], d["ones"]).then_inc(consts, 16)
            sp.dma_start(k.cw[:], d["conv_w"]).then_inc(consts, 16)
            sp.dma_start(k.cb[:], d["conv_b"]).then_inc(consts, 16)
            for n, (a, b) in enumerate(((C_KV, C_WG), (C_Q, C_KV), (C_WG, C_Z), (C_X, D_IN), (C_Z, C_X))):
                sp.dma_start(w[:, :, a:b], w_dram[:, :, a:b]).then_inc(w_in_loaded[n], 16)

            def store_x(t, R):
                sp.wait_ge(xn_ready, t + 1)
                sp.dma_start(d["xres"][bass.ds(t * P, R)], xn[0:R, :]).then_inc(xn_stored, 16)

            def store_rows(t, R, cmp_rows, sel_rows):
                sp.wait_ge(roped, t + 1)
                sp.dma_start(cmp_rows, st[0:R, 1024:1280]).then_inc(rows_stored, 16)
                sp.dma_start(sel_rows, st[0:R, 1280:1536]).then_inc(rows_stored, 16)
                sp.dma_start(d["kv_win_all"][bass.ds(t * P, R)], st[0:R, 1536:1792]).then_inc(rows_stored, 16)
                sp.wait_ge(z_out, t + 2)
                sp.dma_start(d["z_silu"][bass.ds(t * P, R)], zst[0:R, :]).then_inc(z_stored, 16)

            with sp.Fori(0, NT - 1) as t:
                sp.wait_ge(x_taken, t + 1)
                sp.dma_start(xin[:], d["x"][bass.ds(t * P + P, P)]).then_inc(x_loaded, 16)
                store_x(t, P)
                store_rows(t, P, d["kv_cmp_prompt"][bass.ds(t * P, P)], d["kv_sel_prompt"][bass.ds(t * P, P)])
            sp.wait_ge(x_taken, NT)
            sp.dma_start(xin[0:NS, :], d["x"][SEQ:NTOK]).then_inc(x_loaded, 16)
            store_x(NT - 1, P)
            store_x(NT, NS)
            store_rows(NT - 1, P, d["kv_cmp_prompt"][SEQ - P:SEQ], d["kv_sel_prompt"][SEQ - P:SEQ])
            store_rows(NT, NS, d["kv_cmp_sample"], d["kv_sel_sample"])
            sp.wait_ge(rows_stored, 48 * (NT + 2))
            sp.wait_ge(z_stored, 16 * (NT + 2))
            sp.wait_ge(xn_stored, 16 * (NT + 1) + 16)

        @block.vector
        def _(v):
            v.memset(k.gd[:], 0.0)
            v.memset(k.xbcT[:, :, 0:3], 0.0)
            v.sem_inc(xn_stored, 16)
            v.sem_inc(rows_stored, 48)
            v.wait_ge(consts, 16 * 9)

            def layer_norm(t, R):
                v.wait_ge(x_loaded, t * 16 + 16)
                for i in range(2):
                    nc.vector.bn_stats(stats[0:R, i, :], xin[0:R, i * 512:(i + 1) * 512])
                v.drain()
                nc.vector.bn_aggr(mv[0:R, :], stats[0:R]).then_inc(stats_ready, 1)
                v.wait_ge(rstd_ready, t + 1)
                v.wait_ge(xn_stored, t * 16 + 16)
                v.wait_ge(hT_in_psum, t + 1)
                nc.vector.tensor_scalar(xn[0:R, :], xin[0:R, :], mv[0:R, 0:1], rstd[0:R, 1:2],
                                        ALU.subtract, ALU.mult).then_inc(x_taken, 1)
                v.drain()
                nc.vector.tensor_tensor(xn[0:R, :], xn[0:R, :], gain[0:R, :], ALU.mult)
                v.drain()
                nc.vector.tensor_tensor(xn[0:R, :], xn[0:R, :], bias[0:R, :], ALU.add).then_inc(xn_ready, 1)

            def rotate(dst, src, t, R, n):
                c = rope_c[0:R, bass.ds(t, 1), :].to_broadcast([R, n, 2 * RH])
                s = rope_s[0:R, bass.ds(t, 1), :].to_broadcast([R, n, 2 * RH])
                nc.vector.tensor_tensor(rt[0:R, 0:n, :], src[:, :, 0:2 * RH], c, ALU.mult)
                nc.vector.tensor_tensor(rt2[0:R, 0:n, 0:RH], src[:, :, RH:2 * RH], s[:, :, 0:RH], ALU.mult)
                nc.vector.tensor_tensor(rt2[0:R, 0:n, RH:2 * RH], src[:, :, 0:RH], s[:, :, RH:2 * RH], ALU.mult)
                v.drain()
                nc.vector.tensor_tensor(dst[:, :, 0:2 * RH], rt[0:R, 0:n, :], rt2[0:R, 0:n, :], ALU.add)

            def evacuate(t, R):
                v.wait_ge(kv_done, t + 1)
                v.wait_ge(rows_stored, t * 48 + 48)
                v.wait_ge(heads_in_psum, t + 1)
                nc.vector.tensor_copy(st[0:R, 1024:1536], pKV[0:R, :]).then_inc(kv_out, 1)
                v.wait_ge(q_done, t + 1)
                nc.vector.tensor_copy(st[0:R, 512:1024], pQ[0:R, :]).then_inc(qr_out, 1)
                v.wait_ge(wg_done, t + 1)
                nc.vector.tensor_copy(st[0:R, 1536:1792], pW[0:R, 0:256])
                nc.vector.tensor_copy(k.gd[0:R, bass.ds(t, 1), :].rearrange("p a b -> p (a b)"),
                                      pW[0:R, 256:288]).then_inc(wg_out, 1)
                v.drain()
                q8 = st[0:R, 512:1024].rearrange("p (h e) -> p h e", e=HD)
                rotate(q8, q8, t, R, NH)
                for base in (1280, 1536):
                    v.drain()
                    k2 = st[0:R, base:base + 128].rearrange("p (h e) -> p h e", e=HD)
                    rotate(k2, k2, t, R, 2)
                v.drain().then_inc(roped, 1)

            def convolve(t):
                v.wait_ge(xbc_out, t + 2)
                v.wait_ge(conv_taken, t + 1)
                for tap in range(4):
                    for ch in range(DC):
                        src = k.xbcT[:, ch, bass.ds(t * P + tap, P)]
                        if tap == 0:
                            nc.vector.tensor_scalar(conv[:, ch], src, k.cw[:, ch, 0:1], k.cb[:, ch:ch + 1], ALU.mult, ALU.add)
                        else:
                            nc.vector.scalar_tensor_tensor(out=conv[:, ch], in0=src, scalar=k.cw[:, ch, tap:tap + 1],
                                                           in1=conv[:, ch], op0=ALU.mult, op1=ALU.add)
                    v.drain()
                v.drain().then_inc(conv_ready, 1)

            layer_norm(0, P)
            with v.Fori(0, NT - 1) as t:
                layer_norm(t + 1, P)
                evacuate(t, P)
                convolve(t)
            layer_norm(NT, NS)
            evacuate(NT - 1, P)
            convolve(NT - 1)
            evacuate(NT, NS)

        @block.gpsimd
        def _(g):
            g.memset(eps[:], EPS)
            g.memset(mhalf[:], -0.5)
            g.drain()

            def inv_std(t, R):
                g.wait_ge(stats_ready, t + 1)
                nc.gpsimd.tensor_tensor(rstd[0:R, 0:1], mv[0:R, 1:2], eps[0:R, :], ALU.add)
                g.drain()
                nc.gpsimd.tensor_tensor(rstd[0:R, 1:2], rstd[0:R, 0:1], mhalf[0:R, :], ALU.pow).then_inc(rstd_ready, 1)

            inv_std(0, P)
            with g.Fori(0, NT - 1) as t:
                inv_std(t + 1, P)
            inv_std(NT, NS)

        @block.tensor
        def _(pe):
            pe.sem_inc(hT_in_psum, 1)
            pe.sem_inc(heads_in_psum, 1)
            pe.wait_ge(consts, 16 * 9)

            def tile(t, R):
                pe.wait_ge(xn_ready, t + 1)
                pe.wait_ge(heads_out, t + 1)
                for c in range(DC):
                    last = nc.tensor.transpose(pT[:, c // 4, (c % 4) * P:(c % 4) * P + R],
                                               xn[0:R, c * P:(c + 1) * P], k.ident[0:R, 0:R])
                last.then_inc(hT_in_psum, 1)
                pe.wait_ge(hT_ready, t + 1)

                def rows(out, c0, n):
                    for c in range(DC):
                        mm = nc.tensor.matmul(out[0:R, 0:n], hT[:, c, 0:R], w[:, c, c0:c0 + n],
                                              start=(c == 0), stop=(c == DC - 1))
                    return mm

                pe.wait_ge(w_in_loaded[0], 16)
                rows(pKV, C_KV, 512).then_inc(kv_done, 1)
                pe.wait_ge(w_in_loaded[1], 16)
                pe.wait_ge(qr_out, t + 1)
                pe.wait_ge(q_out, t + 1)
                rows(pQ, C_Q, 512).then_inc(q_done, 1)
                pe.wait_ge(w_in_loaded[2], 16)
                pe.wait_ge(wg_out, t + 1)
                rows(pW, C_WG, WG).then_inc(wg_done, 1)
                pe.wait_ge(w_in_loaded[3], 16)
                pe.wait_ge(xbc_out, t + 1)
                for ch in range(DC):
                    for c in range(DC):
                        mm = nc.tensor.matmul(pX[:, ch // 4, (ch % 4) * P:(ch % 4) * P + R],
                                              w[:, c, C_X + ch * P:C_X + (ch + 1) * P], hT[:, c, 0:R],
                                              start=(c == 0), stop=(c == DC - 1))
                mm.then_inc(xbc_done, 1)
                pe.wait_ge(q_out, t + 2)
                pe.wait_ge(roped, t + 1)
                pe.wait_ge(kv_out, t + 1)
                for c in range(4):
                    nc.tensor.transpose(pT[:, 0, c * P:c * P + R], st[0:R, c * P:(c + 1) * P], k.ident[0:R, 0:R])
                for c in range(4):
                    nc.tensor.transpose(pT[:, 1, c * P:c * P + R], st[0:R, 512 + c * P:512 + (c + 1) * P],
                                        k.ident[0:R, 0:R])
                nc.tensor.transpose(pKV[:, 0:R], st[0:R, 1280:1408], k.ident[0:R, 0:R])
                nc.tensor.transpose(pKV[:, P:P + R], st[0:R, 1536:1664],
                                    k.ident[0:R, 0:R]).then_inc(heads_in_psum, 1)
                pe.wait_ge(w_in_loaded[4], 16)
                pe.wait_ge(z_out, t + 1)
                rows(pZ, C_Z, 512).then_inc(z_done, 1)

            with pe.Fori(0, NT) as t:
                tile(t, P)
            tile(NT, NS)

        @block.scalar
        def _(act):
            for free in (heads_out, qr_out, q_out, wg_out, xbc_out, z_out, conv_taken):
                act.sem_inc(free, 1)
            act.sem_inc(z_stored, 16)

            def convolved(t):
                act.wait_ge(conv_ready, t + 1)
                nc.scalar.activation(k.xbcT[:, :, bass.ds(t * P, P)], conv[:], ACT.Silu).then_inc(conv_taken, 1)

            def tile(t, R, xbc_dst, first=False):
                act.wait_ge(hT_in_psum, t + 2)
                for i in range(2):
                    last = nc.scalar.copy(hT[:, i * 4:i * 4 + 4, 0:R],
                                          pT[:, i, :].rearrange("p (c r) -> p c r", r=P)[:, :, 0:R])
                last.then_inc(hT_ready, 1)
                act.wait_ge(qr_out, t + 2)
                nc.scalar.copy(st[0:R, 0:512], pQ[0:R, :]).then_inc(q_out, 1)
                if not first:
                    convolved(t - 1)
                act.wait_ge(xbc_done, t + 1)
                nc.scalar.copy(xbc_dst, pX[:, :, :].rearrange("p b (c r) -> p (b c) r", r=P)[:, :, 0:R]
                               ).then_inc(xbc_out, 1)
                act.wait_ge(heads_in_psum, t + 2)
                at = bass.ds(t * P, R)
                nc.scalar.copy(k.qT[:, :, at], pT[:, 0, :].rearrange("p (c r) -> p c r", r=P)[:, :, 0:R])
                nc.scalar.copy(k.qrT[:, :, at], pT[:, 1, :].rearrange("p (c r) -> p c r", r=P)[:, :, 0:R])
                nc.scalar.copy(k.kselT[:, at], pKV[:, 0:R])
                nc.scalar.copy(k.kwinT[:, at], pKV[:, P:P + R]).then_inc(heads_out, 1)
                act.wait_ge(z_done, t + 1)
                act.wait_ge(z_stored, t * 16 + 16)
                nc.scalar.activation(zst[0:R, :], pZ[0:R, :], ACT.Silu).then_inc(z_out, 1)

            tile(0, P, k.xbcT[:, :, 3:3 + P], first=True)
            with act.Fori(1, NT) as t:
                tile(t, P, k.xbcT[:, :, bass.ds(t * P + 3, P)])
            tile(NT, NS, k.xbcS[:, :, :])


def alloc_kept(nc, ctx, k):
    def sb(name, shape, dt=F32):
        return ctx.enter_context(nc.sbuf_tensor(name, shape, dt))
    k.qT, k.qrT = sb("qT", [P, 4, NTOK]), sb("qrT", [P, 4, NTOK])
    k.kselT, k.kwinT = sb("kselT", [P, NTOK]), sb("kwinT", [P, NTOK])
    k.kcT_p, k.vc_p = sb("kcT_p", [P, 2 * NT]), sb("vc_p", [2 * NT, 2, HD])
    k.kcT_s, k.vc_s = sb("kcT_s", [P, NS, P]), sb("vc_s", [P, NS, 2, HD])


def alloc_xbc(nc, ctx, k):
    def sb(name, shape, dt=F32):
        return ctx.enter_context(nc.sbuf_tensor(name, shape, dt))
    k.xbcT, k.xbcS = sb("xbcT", [P, DC, 3 + SEQ]), sb("xbcS", [P, DC, NS])
    k.cw, k.cb = sb("conv_w_sb", [P, DC, 4]), sb("conv_b_sb", [P, DC])


def alloc_room(nc, ctx, k):
    room = ctx.enter_context(nc.sbuf_tensor("weight_room", [P, DC * D], F32))[:]
    k.room = room
    k.w1 = room.rearrange("p (k c f) -> p k c f", k=2, f=P)
    k.w_out = room.rearrange("p (c n) -> p c n", c=DC)
    k.w1_loaded, k.w_out_loaded = (ctx.enter_context(nc.semaphore(n)) for n in ("w1_loaded", "w_out_loaded"))


def ssd(nc, k, d):
    with ExitStack() as ctx:
        def sb(name, shape, dt=F32):
            return ctx.enter_context(nc.sbuf_tensor(name, shape, dt))

        def ps(name, shape):
            return ctx.enter_context(nc.psum_tensor(name, shape, F32))

        def sem(name):
            k.sems.append(ctx.enter_context(nc.semaphore(name)))
            return k.sems[-1]

        NG = 512
        G = 24
        cw, cb, cv = k.cw, k.cb, k.xbcT
        dtb, alog = sb("dt_bias_sb", [P, 8]), sb("a_log_sb", [P, 8])
        dskip, normw = sb("d_skip_sb", [P, 8]), sb("norm_w_sb", [P, NG])
        mneg, expand = sb("mneg", [P, P]), sb("expand_h", [8, NG])
        sconv = sb("state_conv_sb", [P, DC, 3, NS])
        h0 = sb("state_ssm_sb", [P, NS, 4, P])
        cvs, cvt = sb("cvs", [P, DC, NS]), sb("cvt", [P, DC, NS])
        sp1, sp2, sp3, sp4 = (sb(f"softplus{i}", [P, NT + 1, 8]) for i in range(4))
        dt = sb("dt", [P, NT + 1, 8])
        dtA = sb("dtA", [P, NT + 1, 8])
        pr = sb("pr", [P, NT, 6, 8])
        prs_, cs_ = [sb(f"prs{u}", [P, 6, 8]) for u in range(2)], [sb(f"cs{u}", [P, DC, P]) for u in range(2)]
        Dm, xdt, xdd, Dx = sb("Dm", [P, 8, P]), sb("xdt", [P, NG]), sb("xdd", [P, NG]), sb("Dx", [P, NG])
        Bt, H = sb("Bt", [P, 256]), sb("H", [P, NG])
        y, y2, zt, sq = sb("y", [P, NG]), sb("y2", [P, NG]), sb("zt", [P, NG]), sb("sq", [P, NG])
        ms, mhalf = sb("ms", [P, 4]), sb("mhalf_ssd", [P, 2])
        dT, dE = sb("dT", [8, 17]), sb("dE", [P, 4, 17])
        bc, bcm = sb("bc", [8, NG]), sb("bcm", [8, NG])
        hx, ys = sb("hx", [P, 4, P]), sb("ys", [P, 4, NS])
        xdtS = sb("xdtS", [P, 4, NS])
        Hout = xdt[:].rearrange("p (c n) -> p c n", n=P)
        cvo, cvp = (t[0:8].rearrange("p c n -> p (c n)") for t in (Dm, cs_[0]))

        pX, pB, pS, pY1, pY2 = (ps(n, [P, 512]) for n in ("ssd_pX", "ssd_pB", "ssd_pS", "ssd_pY1", "ssd_pY2"))
        pR = ps("ssd_pR", [P, 2, 512])

        consts, z_loaded, silu_done = sem("ssd_consts"), sem("z_loaded"), sem("silu_done")
        conv_done, sp_v, sp_a, pr_ready, sums_done = sem("conv_done"), sem("sp_v"), sem("sp_a"), sem("pr_ready"), sem("sums_done")
        staged, in_psum, d_ready, exp_ready, m_ready = sem("staged"), sem("chunk_in_psum"), sem("d_ready"), sem("exp_ready"), sem("m_ready")
        yoff_done, ydiag_done, state_done, h_ready, xd_ready = (sem(n) for n in ("yoff_done", "ydiag_done", "state_done", "h_ready", "xd_ready"))
        ms_ready, rms_ready, y_ready, y_stored, chunk_done = (sem(n) for n in ("ms_ready", "rms_ready", "y_ready", "y_stored", "chunk_done"))
        side_ps, side_sb, side_st, bc_ready, bc_ps, hn_ready = (sem(n) for n in ("side_ps", "side_sb", "side_st", "bc_ready", "bc_ps", "hn_ready"))
        prep, y_used = sem("ssd_prep"), sem("y_used")
        block = ctx.enter_context(nc.Block())
        NCONST = 8

        @block.sync
        def _(sp):
            for dst, src in ((mneg, d["mask_neg"]), (expand, d["expand_h"]),
                             (sconv, d["state_conv"])):
                sp.dma_start(dst[:], src).then_inc(consts, 16)
            for dst, src in ((dtb, d["dt_bias"]), (alog, d["a_log"]), (dskip, d["d_skip"])):
                sp.dma_start(dst[:], bcast(src, [P, 8])).then_inc(consts, 16)
            sp.dma_start(normw[:], bcast(d["ssd_norm_w"], [P, NG])).then_inc(consts, 16)
            sp.dma_start(dT[:, 16:17], d["d_skip"].rearrange("a h -> h a")).then_inc(consts, 16)
            sp.dma_start(d["kv_win_prompt"], d["kv_win_all"][SEQ - 512:SEQ]).then_inc(side_st, 16)
            sp.dma_start(d["conv_sample"][:, 0:2, :], d["state_conv_rows"][:, 1:3, :]).then_inc(side_st, 16)
            sp.dma_start(zt[:], d["z_silu"][0:P]).then_inc(z_loaded, 16)
            sp.dma_start(k.w1, d["cmp_w1"]).then_inc(k.w1_loaded, 16)
            for b in range(NS):
                sp.dma_start(h0[:, b], d["state_ssm"][b].rearrange("(c q) n -> q c n", q=P)).then_inc(prep, 16)
            with sp.Fori(0, NT - 1) as c:
                sp.wait_ge(y_ready, c + 1)
                sp.dma_start(zt[:], d["z_silu"][bass.ds(c * P + P, P)]).then_inc(z_loaded, 16)
                sp.dma_start(d["mix"][bass.ds(c * P, P), 0:NG], y2[:]).then_inc(y_stored, 16)
            sp.wait_ge(y_ready, NT)
            sp.dma_start(zt[0:NS], d["z_silu"][SEQ:NTOK]).then_inc(z_loaded, 16)
            sp.dma_start(d["mix"][SEQ - P:SEQ, 0:NG], y2[:]).then_inc(y_stored, 16)
            sp.wait_ge(side_sb, 1)
            sp.dma_start(d["conv_sample"][:, 2, :], cvo[:]).then_inc(side_st, 16)
            sp.dma_start(d["conv_prompt"], cvp[0:3]).then_inc(side_st, 16)
            sp.wait_ge(side_sb, 2)
            sp.dma_start(d["ssm_prompt"].rearrange("(c q) n -> q c n", q=P), Hout[:]).then_inc(side_st, 16)
            with sp.Fori(0, NS) as b:
                sp.wait_ge(hn_ready, b + 1)
                sp.dma_start(d["ssm_sample"][bass.ds(b, 1)].rearrange("b (c q) n -> q (b c) n", q=P),
                             h0[:, bass.ds(b, 1)].rearrange("q b c n -> q (b c) n")).then_inc(side_st, 16)
            sp.wait_ge(y_ready, NT + 1)
            sp.dma_start(d["mix"][SEQ:NTOK, 0:NG], y2[0:NS]).then_inc(y_stored, 16)
            sp.wait_ge(y_stored, 16 * (NT + 2))
            sp.wait_ge(side_st, 16 * (5 + NS))

        @block.gpsimd
        def _(g):
            g.memset(mhalf[:], -0.5)
            g.drain()

            def inv_rms(n, R):
                g.wait_ge(ms_ready, n + 1)
                nc.gpsimd.tensor_tensor(ms[0:R, 2:4], ms[0:R, 0:2], mhalf[0:R, :], ALU.pow).then_inc(rms_ready, 1)

            g.wait_ge(pr_ready, 1)

            def stage(c, u):
                nc.gpsimd.tensor_copy(prs_[u][:], pr[:, bass.ds(c, 1)].rearrange("p a k h -> p (a k) h"))
                nc.gpsimd.tensor_copy(cs_[u][:], cv[:, :, bass.ds(c * P, P)])
                g.drain().then_inc(staged, 1)

            stage(0, 0)
            stage(1, 1)
            with g.Fori(0, NT // 2 - 1) as i:
                for u in range(2):
                    c = i * 2 + u
                    g.wait_ge(chunk_done, c + 1)
                    g.nop()
                    stage(c + 2, u)
                    inv_rms(c, P)
            inv_rms(NT - 2, P)
            inv_rms(NT - 1, P)
            inv_rms(NT, NS)

        @block.vector
        def _(v):
            v.memset(H[:], 0.0)
            v.sem_inc(h_ready, 1)
            v.sem_inc(y_stored, 16)
            v.wait_ge(consts, 16 * NCONST)
            def tap_w(tap):
                return bcast(cw[:, :, tap:tap + 1], [P, DC, NS])
            nc.vector.tensor_tensor(cvs[:], k.xbcS[:], tap_w(3), ALU.mult)
            for tap in range(3):
                nc.vector.tensor_tensor(cvt[:], sconv[:, :, tap, :], tap_w(tap), ALU.mult)
                v.drain()
                nc.vector.tensor_tensor(cvs[:], cvs[:], cvt[:], ALU.add)
                v.drain()
            nc.vector.tensor_tensor(cvs[:], cvs[:], bcast(cb[:].rearrange("p (c a) -> p c a", a=1), [P, DC, NS]), ALU.add)
            v.drain().then_inc(conv_done, 1)

            raw = k.gd[:, :, G:G + 8]
            b9 = bcast(dtb[:].rearrange("p (a h) -> p a h", a=1), [P, NT + 1, 8])
            nc.vector.tensor_tensor(sp1[:], raw, b9, ALU.add)
            v.drain()
            nc.vector.tensor_scalar(sp2[:], sp1[:], -1.0, None, ALU.mult)
            v.drain()
            nc.vector.tensor_tensor(sp2[:], sp2[:], sp1[:], ALU.min)
            nc.vector.tensor_scalar(dt[:], sp1[:], 0.0, None, ALU.max)
            v.drain().then_inc(sp_v, 1)
            v.wait_ge(sp_a, 1)
            nc.vector.tensor_scalar(sp1[:], sp2[:], 1.0, None, ALU.add)
            v.drain()
            nc.vector.tensor_scalar(sp1[:], sp1[:], 1.0, None, ALU.subtract)
            v.drain()
            nc.vector.tensor_scalar(sp4[:], sp1[:], 0.0, None, ALU.is_equal)
            nc.vector.tensor_scalar(sp1[:], sp1[:], 1e-30, None, ALU.max)
            v.drain()
            nc.vector.reciprocal(sp1[:], sp1[:])
            v.drain()
            nc.vector.tensor_tensor(sp3[:], sp3[:], sp1[:], ALU.mult)
            v.drain()
            nc.vector.tensor_tensor(sp3[:], sp3[:], sp4[:], ALU.add)
            v.drain()
            nc.vector.tensor_tensor(sp3[:], sp3[:], sp2[:], ALU.mult)
            v.drain()
            nc.vector.tensor_tensor(dt[:], dt[:], sp3[:], ALU.add)
            nc.vector.tensor_scalar(alog[:], alog[:], -1.0, None, ALU.mult)
            v.drain()
            nc.vector.tensor_tensor(dtA[:], dt[:], bcast(alog[:].rearrange("p (a h) -> p a h", a=1), [P, NT + 1, 8]), ALU.mult)
            nc.vector.tensor_scalar(k.gd[:, :, 0:G], k.gd[:, :, 0:G], 1.0, None, ALU.add)
            v.drain().then_inc(sp_v, 1)
            nc.vector.reciprocal(k.gd[:, :, 0:G], k.gd[:, :, 0:G])
            v.wait_ge(sums_done, 1)
            acum = pB[:, 0:64].rearrange("p (c h) -> p c h", h=8)
            nc.vector.tensor_copy(pr[:, :, 0], dt[:, 0:NT])
            nc.vector.tensor_copy(pr[:, :, 1], dtA[:, 0:NT])
            nc.vector.tensor_copy(pr[:, :, 2], acum)
            v.drain()
            nc.vector.tensor_tensor(pr[:, :, 4], pB[:, 64:128].rearrange("p (c h) -> p c h", h=8), pr[:, :, 2], ALU.subtract)
            nc.vector.tensor_copy(pr[:, :, 5], pB[:, 64:128].rearrange("p (c h) -> p c h", h=8))
            v.drain().then_inc(sp_v, 1)
            v.wait_ge(sp_a, 2)
            nc.vector.tensor_tensor(pr[:, :, 4], pr[:, :, 4], pr[:, :, 0], ALU.mult)
            v.drain().then_inc(pr_ready, 1)

            def gate(yin, R, n):
                v.wait_ge(z_loaded, n * 16 + 16)
                v.wait_ge(y_stored, n * 16 + 16)
                nc.vector.tensor_tensor(y2[0:R], yin, zt[0:R], ALU.mult)
                v.drain()
                for gr in range(2):
                    nc.vector.tensor_tensor_reduce(sq[0:R, gr * 256:gr * 256 + 256], y2[0:R, gr * 256:gr * 256 + 256],
                                                   y2[0:R, gr * 256:gr * 256 + 256], 1.0 / 256, EPS, ALU.mult, ALU.add,
                                                   ms[0:R, gr:gr + 1])
                v.drain().then_inc(ms_ready, 1)

            def norm(R, n):
                v.wait_ge(rms_ready, n + 1)
                for gr in range(2):
                    cols = slice(gr * 256, gr * 256 + 256)
                    nc.vector.scalar_tensor_tensor(out=y2[0:R, cols], in0=y2[0:R, cols], scalar=ms[0:R, 2 + gr:3 + gr],
                                                   in1=normw[0:R, cols], op0=ALU.mult, op1=ALU.mult)
                v.drain().then_inc(y_ready, 1)

            def heads(ap):
                return ap.rearrange("p (h e) -> p h e", e=HD)

            def per_head(prs, kind):
                return bcast(prs[:, kind, :].rearrange("p (h a) -> p h a", a=1), [P, 8, HD])

            dsk = bcast(dskip[:].rearrange("p (h a) -> p h a", a=1), [P, 8, HD])

            def chunk(c, prs, first=False):
                v.wait_ge(in_psum, c + 1)
                for h in range(8):
                    nc.vector.scalar_tensor_tensor(out=Dm[:, h], in0=pR[:, h // 4, (h % 4) * P:(h % 4 + 1) * P],
                                                   scalar=prs[:, 2, h:h + 1], in1=mneg[:], op0=ALU.subtract, op1=ALU.add)
                v.drain().then_inc(d_ready, 1)
                nc.vector.tensor_tensor(heads(xdt[:]), heads(pX[:]), per_head(prs, 0), ALU.mult)
                nc.vector.tensor_tensor(heads(xdd[:]), heads(pX[:]), per_head(prs, 4), ALU.mult)
                nc.vector.tensor_tensor(heads(Dx[:]), heads(pX[:]), dsk, ALU.mult)
                nc.vector.tensor_copy(Bt[:], pB[:, 0:256])
                v.drain().then_inc(xd_ready, 1)
                if not first:
                    gate(y[:], P, c - 1)
                v.wait_ge(exp_ready, c + 1)
                for gr in range(2):
                    cbt = bcast(pB[:, 256 + gr * P:384 + gr * P].rearrange("p (a l) -> p a l", a=1), [P, 4, P])
                    nc.vector.tensor_tensor(Dm[:, gr * 4:gr * 4 + 4], Dm[:, gr * 4:gr * 4 + 4], cbt, ALU.mult)
                v.drain().then_inc(m_ready, 1)
                if not first:
                    norm(P, c - 1)
                v.wait_ge(yoff_done, c + 1)
                nc.vector.tensor_tensor(heads(H[:]), heads(H[:]), per_head(prs, 5), ALU.mult)
                nc.vector.tensor_tensor(heads(y[:]), heads(pY2[:]), per_head(prs, 3), ALU.mult)
                v.drain()
                nc.vector.tensor_tensor(y[:], y[:], Dx[:], ALU.add)
                v.wait_ge(state_done, c + 1)
                nc.vector.tensor_tensor(H[:], H[:], pS[:], ALU.add)
                v.drain().then_inc(h_ready, 1)
                nc.vector.tensor_tensor(y[:], y[:], pY1[:], ALU.add)
                v.drain().then_inc(chunk_done, 1)

            chunk(0, prs_[0], first=True)
            chunk(1, prs_[1])
            with v.Fori(1, NT // 2) as i:
                for u in range(2):
                    chunk(i * 2 + u, prs_[u])
            gate(y[:], P, NT - 1)
            norm(P, NT - 1)

            v.wait_ge(side_ps, 1)
            nc.vector.tensor_copy(cvo[:, 0:512], pX[0:8, :])
            nc.vector.tensor_copy(cvo[:, 512:D], pY1[0:8, :])
            nc.vector.tensor_copy(cvp[0:3, 0:512], pY2[0:3, :])
            nc.vector.tensor_copy(cvp[0:3, 512:D], pS[0:3, :])
            v.drain().then_inc(side_sb, 1)
            v.wait_ge(side_ps, 2)
            nc.vector.tensor_copy(Hout[:], pX[:].rearrange("p (c n) -> p c n", n=P))
            v.drain().then_inc(side_sb, 1)
            v.wait_ge(side_ps, 3)
            nc.vector.tensor_copy(dT[:, 0:16], pY1[0:8, 0:16])
            nc.vector.tensor_copy(bc[:], pY2[0:8, :])
            v.drain().then_inc(side_sb, 1)
            v.wait_ge(side_ps, 4)
            nc.vector.tensor_copy(dE[:], pS[:, 0:68].rearrange("p (c n) -> p c n", n=17))
            v.drain()
            nc.vector.tensor_tensor(xdtS[:], cvs[:, 0:4], dE[:, :, 0:8], ALU.mult)
            v.wait_ge(prep, 16 * NS)
            v.drain()
            with v.Fori(0, NS) as b:
                v.wait_ge(bc_ps, b + 1)
                nc.vector.tensor_scalar(bcm[:], bc[:], k.ident[0:8, bass.ds(b, 1)], None, ALU.mult)
                v.drain().then_inc(bc_ready, 1)
                hb = h0[:, bass.ds(b, 1)].rearrange("q b c n -> q (b c) n")
                nc.vector.tensor_tensor(hb, hb, bcast(dE[:, :, bass.ds(b + 8, 1)], [P, 4, P]), ALU.mult)
                v.wait_ge(bc_ps, b + 2)
                for gr in range(2):
                    bb = bcast(pX[:, gr * P:gr * P + P].rearrange("p (a l) -> p a l", a=1), [P, 2, P])
                    nc.vector.tensor_tensor(hx[:, 2 * gr:2 * gr + 2], bb,
                                            bcast(xdtS[:, 2 * gr:2 * gr + 2, bass.ds(b, 1)], [P, 2, P]), ALU.mult)
                v.drain()
                nc.vector.tensor_tensor(hb, hb, hx[:], ALU.add)
                v.drain().then_inc(hn_ready, 1)
                for gr in range(2):
                    cc = bcast(pX[:, 256 + gr * P:384 + gr * P].rearrange("p (a l) -> p a l", a=1), [P, 2, P])
                    hg = h0[:, bass.ds(b, 1), 2 * gr:2 * gr + 2].rearrange("q b c n -> q (b c) n")
                    nc.vector.tensor_tensor(hx[:, 2 * gr:2 * gr + 2], hg, cc, ALU.mult)
                v.drain()
                nc.vector.tensor_reduce(ys[:, :, bass.ds(b, 1)], hx[:], AX.X, ALU.add)
                v.drain()
            nc.vector.tensor_tensor(xdtS[:], cvs[:, 0:4], bcast(dE[:, :, 16:17], [P, 4, NS]), ALU.mult)
            v.drain()
            nc.vector.tensor_tensor(ys[:], ys[:], xdtS[:], ALU.add)
            v.drain().then_inc(bc_ready, 1)
            v.wait_ge(side_ps, 5)
            gate(pY1[0:NS, :], NS, NT)
            norm(NS, NT)

        @block.scalar
        def _(act):
            act.wait_ge(consts, 16 * NCONST)
            act.wait_ge(conv_done, 1)
            nc.scalar.activation(cvs[:], cvs[:], ACT.Silu).then_inc(silu_done, 1)
            nc.scalar.activation(k.gd[:, :, 0:G], k.gd[:, :, 0:G], ACT.Exp, scale=-1.0)
            nc.scalar.activation(alog[:], alog[:], ACT.Exp)
            act.wait_ge(sp_v, 1)
            nc.scalar.activation(sp2[:], sp2[:], ACT.Exp)
            act.drain()
            nc.scalar.activation(sp3[:], sp2[:], ACT.Ln, bias=1.0)
            act.drain().then_inc(sp_a, 1)
            act.wait_ge(sp_v, 3)
            nc.scalar.activation(pr[:, :, 3], pr[:, :, 2], ACT.Exp)
            nc.scalar.activation(pr[:, :, 4:6], pr[:, :, 4:6], ACT.Exp)
            nc.scalar.activation(sp1[0:8, NT], dtA[0:8, NT], ACT.Exp)
            act.drain().then_inc(sp_a, 1)
            with act.Fori(0, NT) as c:
                act.wait_ge(d_ready, c + 1)
                nc.scalar.activation(Dm[:], Dm[:], ACT.Exp).then_inc(exp_ready, 1)

        @block.tensor
        def _(pe):
            pe.sem_inc(bc_ps, 1)
            pe.wait_ge(sp_v, 2)
            nc.tensor.matmul(pB[:, 0:64], k.mask_le[:], dtA[:, 0:NT].rearrange("p c h -> p (c h)"), start=True, stop=True)
            nc.tensor.matmul(pB[:, 64:128], k.ones[:], dtA[:, 0:NT].rearrange("p c h -> p (c h)"), start=True,
                             stop=True).then_inc(sums_done, 1)
            def chunk(c, prs, cs):
                pe.wait_ge(staged, c + 1)
                for i in range(4):
                    nc.tensor.transpose(pX[:, i * P:(i + 1) * P], cs[:, i], k.ident[:])
                for i in range(2):
                    nc.tensor.transpose(pB[:, i * P:(i + 1) * P], cs[:, 4 + i], k.ident[:])
                for gr in range(2):
                    nc.tensor.matmul(pB[:, 256 + gr * P:384 + gr * P], cs[:, 4 + gr], cs[:, 6 + gr], start=True, stop=True)
                for h in range(8):
                    mm = nc.tensor.matmul(pR[:, h // 4, (h % 4) * P:(h % 4 + 1) * P],
                                          bcast(prs[:, 1, h:h + 1], [P, P]), k.mask_le[:], start=True, stop=True)
                mm.then_inc(in_psum, 1)
                pe.wait_ge(h_ready, c + 1)
                for gr in range(2):
                    mm = nc.tensor.matmul(pY2[:, gr * 256:gr * 256 + 256], cs[:, 6 + gr], H[:, gr * 256:gr * 256 + 256],
                                          start=True, stop=True)
                mm.then_inc(yoff_done, 1)
                pe.wait_ge(m_ready, c + 1)
                for h in range(8):
                    mm = nc.tensor.matmul(pY1[:, h * HD:(h + 1) * HD], Dm[:, h], xdt[:, h * HD:(h + 1) * HD],
                                          start=True, stop=True)
                mm.then_inc(ydiag_done, 1)
                pe.wait_ge(xd_ready, c + 1)
                for gr in range(2):
                    mm = nc.tensor.matmul(pS[:, gr * 256:gr * 256 + 256], Bt[:, gr * P:(gr + 1) * P],
                                          xdd[:, gr * 256:gr * 256 + 256], start=True, stop=True)
                mm.then_inc(state_done, 1)

            with pe.Fori(0, NT // 2) as i:
                for u in range(2):
                    chunk(i * 2 + u, prs_[u], cs_[u])
            pe.wait_ge(chunk_done, NT)
            for i in range(DC):
                nc.tensor.transpose((pX if i < 4 else pY1)[0:8, (i % 4) * P:(i % 4 + 1) * P], k.xbcS[:, i], k.ident[:])
            for i in range(DC):
                mm = nc.tensor.transpose((pY2 if i < 4 else pS)[0:3, (i % 4) * P:(i % 4 + 1) * P],
                                         k.xbcT[:, i, SEQ:SEQ + 3], k.ident[:])
            mm.then_inc(side_ps, 1)
            pe.wait_ge(side_sb, 1)
            for i in range(4):
                mm = nc.tensor.transpose(pX[:, i * P:(i + 1) * P], H[:, i * P:(i + 1) * P], k.ident[:])
            mm.then_inc(side_ps, 1)
            pe.wait_ge(side_sb, 2)
            pe.wait_ge(silu_done, 1)
            pe.wait_ge(sp_a, 2)
            nc.tensor.transpose(pY1[0:8, 0:8], dt[0:8, NT], k.ident[0:8, 0:8])
            nc.tensor.transpose(pY1[0:8, 8:16], sp1[0:8, NT], k.ident[0:8, 0:8])
            for i in range(4):
                mm = nc.tensor.transpose(pY2[0:8, i * P:(i + 1) * P], cvs[:, 4 + i], k.ident[:])
            mm.then_inc(side_ps, 1)
            pe.wait_ge(side_sb, 3)
            for i in range(4):
                mm = nc.tensor.matmul(pS[:, i * 17:(i + 1) * 17], expand[:, i * P:(i + 1) * P], dT[:], start=True, stop=True)
            mm.then_inc(side_ps, 1)
            with pe.Fori(0, NS) as b:
                pe.wait_ge(bc_ready, b + 1)
                nc.tensor.matmul(pX[:], k.ones[0:8, :], bcm[:], start=True, stop=True).then_inc(bc_ps, 1)
            pe.wait_ge(bc_ready, NS + 1)
            for i in range(4):
                mm = nc.tensor.transpose(pY1[0:8, i * P:(i + 1) * P], ys[:, i], k.ident[:])
            mm.then_inc(side_ps, 1)


GP = 32
NB = 3
EC = HD // 2
PB = 4
SP_PAGES, ACT_PAGES, POOL_PAGES = (0, 12), (12, 24), (24, GP)
PROMPT_DMAS = 16 * (2 * 2 * NT + 1)


def compress(nc, k, d):
    with ExitStack() as ctx:
        def sb(name, shape, dt=F32):
            return ctx.enter_context(nc.sbuf_tensor(name, shape, dt))

        def ps(name, shape):
            return ctx.enter_context(nc.psum_tensor(name, shape, F32))

        def sem(name):
            k.sems.append(ctx.enter_context(nc.semaphore(name)))
            return k.sems[-1]

        w1 = k.w1
        w2 = sb("cmp_w2_sb", [P, 2, HD])
        b1, b1p = sb("cmp_b1_sb", [P, 2]), sb("cmp_b1_pe", [P, 2])
        b2k, b2v = sb("cmp_b2k", [P, 1]), sb("cmp_b2v", [P, HD])
        pt = sb("page_row", [1, (NS + 2) * NPAGE], I32)
        X = [sb(f"pages{x}", [P, GP * KV]) for x in range(NB)]
        hid = [sb(f"hid{u}", [P, 2, 2, 2 * GP]) for u in range(2)]
        ph = [ps(f"ph{u}", [P, 512]) for u in range(2)]
        pk, pv = ps("cmp_pk", [P, 512]), ps("cmp_pv", [P, 512])

        consts = sem("cmp_consts")
        pages_loaded = [sem(f"pages_loaded{x}") for x in range(NB)]
        pool_pages_loaded = [sem(f"pool_pages_loaded{x}") for x in range(NB)]
        pages_used = [sem(f"pages_used{x}") for x in range(NB)]
        hid_ready = [sem(f"hid_ready{u}") for u in range(2)]
        pe_folded, kv_in_psum, kv_copied = sem("pe_folded"), sem("cmp_kv_in_psum"), sem("cmp_kv_copied")
        pt_loaded = sem("pt_loaded")
        block = ctx.enter_context(nc.Block())
        PX = NB - 1
        NPP = SEQ // PAGE
        cached = [X[u][:].rearrange("p (g c k b) -> p c k g b", c=EC, k=2, b=4) for u in range(NB)]
        prompt = X[PX][:].rearrange("p (g b k h c) -> p g b k h c", b=2, k=2, h=2, c=EC)

        def groups(eng, step):
            head = 2 * NS % (2 * NB)
            for gr in range(head):
                step(gr // 2, gr % 2, gr % NB, gr // NB, None)
            turns = 2 * NS // (2 * NB)
            with eng.Fori(0, turns) as i:
                for w in range(2 * NB):
                    gr = head + w
                    step(i * NB + gr // 2, gr % 2, gr % NB, i * 2 + gr // NB, (turns - 1 > i) if w >= NB else None)

        def load_pages(eng, b, h, x, share, loaded):
            for i in range(*share, PB):
                _, pages = nc.values_load_multi_w_load_instructions(
                    pt[0:1, bass.ds(b * NPAGE + (h * GP + i), PB)], engines=[eng.engine],
                    min_val=0, max_val=d["cache_kv_cmp"].shape[0] // PAGE - 1,
                    skip_runtime_bounds_check_because="a page table names pages of the pool")
                for n, page in enumerate(pages):
                    at = (i + n) * KV
                    eng.dma_start(X[x][:, at:at + KV],
                                  d["cache_kv_cmp"][bass.ds(page * PAGE, PAGE)]).then_inc(loaded[x], 16)

        def load_prompt(eng, s):
            rows = d["kv_cmp_prompt"].rearrange("(g b l) (k h s c) -> s l g b k h c", b=2, l=64, k=2, h=2, s=2)
            for g in range(NPP):
                for b in range(2):
                    eng.dma_start(prompt[s * 64:s * 64 + 64, g, b], rows[s, :, g, b]).then_inc(pages_loaded[PX], 16)

        @block.sync
        def _(sp):
            sp.dma_start(pt[:, 0:NS * NPAGE], d["page_table"]).then_inc(pt_loaded, 16)
            sp.dma_start(X[PX][:, NPP * KV:(NPP + 1) * KV], d["pe_page"]).then_inc(pages_loaded[PX], 16)
            load_prompt(sp, 0)
            sp.dma_start(w2[:], d["cmp_w2"].rearrange("k f e -> f k e")).then_inc(consts, 16)
            sp.dma_start(b1[:], d["cmp_b1"]).then_inc(consts, 16)
            sp.dma_start(b2k[:], d["cmp_b2k"]).then_inc(consts, 16)
            sp.dma_start(b2v[:], bcast(d["cmp_b2v"], [P, HD])).then_inc(consts, 16)
            sp.wait_ge(pt_loaded, 16)

            def step(b, h, x, n, last):
                sp.wait_ge(pages_used[x], n + 1)
                load_pages(sp, b, h, x, SP_PAGES, pages_loaded)

            groups(sp, step)

        @block.gpsimd
        def _(g):
            g.wait_ge(pt_loaded, 16)

            def step(b, h, x, n, last):
                g.wait_ge(pages_used[x], n + 1)
                load_pages(g, b, h, x, POOL_PAGES, pool_pages_loaded)

            groups(g, step)

        def layer1(x, h, moving, n):
            for kv in range(2):
                for c in range(EC):
                    mm = nc.tensor.matmul(ph[h][:, kv * P:kv * P + n], w1[:, kv, c], moving(c, kv),
                                          start=(c == 0), stop=(c == EC - 1))
            mm.then_inc(pages_used[x], 1)

        @block.tensor
        def _(pe):
            pe.wait_ge(k.w1_loaded, 16)
            pe.wait_ge(pages_loaded[PX], PROMPT_DMAS)
            layer1(PX, 1, lambda c, kv: prompt[:, 0:NPP + 1, :, kv, :, c], 4 * (NPP + 1))
            pe.wait_ge(consts, 64)
            pe.wait_ge(hid_ready[1], 1)
            for g in range(2):
                nc.tensor.matmul(pk[g * 64:g * 64 + 64, 0:2 * NPP], w2[:, 0], hid[1][:, 0, g, 0:2 * NPP],
                                 start=True, stop=True)
                mm = nc.tensor.matmul(pv[0:2 * NPP, g * 64:g * 64 + 64], hid[1][:, 1, g, 0:2 * NPP], w2[:, 1],
                                      start=True, stop=True)
            mm.then_inc(kv_in_psum, 1)

            def layer2(b):
                pe.wait_ge(kv_copied, b + 1)
                for h in range(2):
                    pe.wait_ge(hid_ready[h], b + 2)
                    at = h * GP * 2
                    for g in range(2):
                        nc.tensor.matmul(pk[g * 64:g * 64 + 64, at:at + 2 * GP], w2[:, 0], hid[h][:, 0, g],
                                         start=True, stop=True)
                        mm = nc.tensor.matmul(pv[at:at + 2 * GP, g * 64:g * 64 + 64], hid[h][:, 1, g], w2[:, 1],
                                              start=True, stop=True)
                mm.then_inc(kv_in_psum, 1)

            direct, pool = 16 * ACT_PAGES[1], 16 * (GP - POOL_PAGES[0])

            def step(b, h, x, n, last):
                pe.wait_ge(pages_loaded[x], n * direct + direct + (PROMPT_DMAS if x == PX else 0))
                pe.wait_ge(pool_pages_loaded[x], n * pool + pool)
                pe.wait_ge(hid_ready[h], b + 1)
                layer1(x, h, lambda c, kv: cached[x][:, c, kv], 4 * GP)
                if h == 0 and not (isinstance(b, int) and b == 0):
                    layer2(b - 1)

            groups(pe, step)
            layer2(NS - 1)

        @block.scalar
        def _(act):
            act.sem_inc(hid_ready[0], 1)
            for x in range(NB - 1):
                act.sem_inc(pages_used[x], 1)

            def silu(h, npages):
                for kv in range(2):
                    src = ph[h][:, kv * P:kv * P + 4 * npages].rearrange("f (gb h) -> f h gb", h=2)
                    nc.scalar.activation(hid[h][:, kv, :, 0:2 * npages], src, ACT.Silu, bias=b1p[:, kv:kv + 1])
                act.drain().then_inc(hid_ready[h], 1)

            load_prompt(act, 1)
            act.wait_ge(pt_loaded, 16)
            load_pages(act, 0, 0, 0, ACT_PAGES, pages_loaded)
            load_pages(act, 0, 1, 1, ACT_PAGES, pages_loaded)
            act.wait_ge(pages_used[PX], 1)
            act.wait_ge(pe_folded, 1)
            silu(1, NPP)
            load_pages(act, 1, 0, 2, ACT_PAGES, pages_loaded)

            def step(b, h, x, n, last):
                act.wait_ge(pages_used[x], n + 2)
                act.wait_ge(kv_in_psum, b + 1)
                silu(h, GP)
                with (act.If(last) if last is not None else ExitStack()):
                    load_pages(act, b + 1 + h, 1 - h, x, ACT_PAGES, pages_loaded)

            groups(act, step)

        @block.vector
        def _(v):
            v.wait_ge(consts, 64)
            v.wait_ge(pages_used[PX], 1)
            nc.vector.tensor_tensor(b1p[:], b1[:], ph[1][:, 4 * NPP:4 * NPP + P + 1:P], ALU.add)
            v.drain().then_inc(pe_folded, 1)
            v.wait_ge(kv_in_psum, 1)
            n = 2 * NPP
            nc.vector.tensor_scalar(k.kcT_p[:], pk[:, 0:n], b2k[:, 0:1], None, ALU.add)
            nc.vector.tensor_tensor(k.vc_p[:], pv[0:n, 0:P].rearrange("p (h e) -> p h e", h=2),
                                    bcast(b2v[0:n].rearrange("p (a e) -> p a e", a=1), [n, 2, HD]), ALU.add)
            v.drain().then_inc(kv_copied, 1)
            with v.Fori(0, NS) as b:
                v.wait_ge(kv_in_psum, b + 2)
                nc.vector.tensor_scalar(k.kcT_s[:, bass.ds(b, 1)].rearrange("p a n -> p (a n)"), pk[:, 0:P],
                                        b2k[:, 0:1], None, ALU.add)
                nc.vector.tensor_tensor(k.vc_s[:, bass.ds(b, 1)].rearrange("p a h e -> p (a h) e"),
                                        pv[:, 0:P].rearrange("p (h e) -> p h e", h=2),
                                        bcast(b2v[:].rearrange("p (a e) -> p a e", a=1), [P, 2, HD]), ALU.add)
                v.drain().then_inc(kv_copied, 1)


WIN_T = 512 // P


def attend(nc, k, d):
    with ExitStack() as ctx:
        def sb(name, shape, dt=F32):
            return ctx.enter_context(nc.sbuf_tensor(name, shape, dt))

        def ps(name, shape):
            return ctx.enter_context(nc.psum_tensor(name, shape, F32))

        def sem(name):
            k.sems.append(ctx.enter_context(nc.semaphore(name)))
            return k.sems[-1]

        V = [sb(f"v_rows{br}", [P, NT, P]) for br in range(2)]
        K = [k.kselT, k.kwinT]
        diag, oldest = sb("mask_diag", [P, P]), sb("mask_oldest", [P, P])
        visn, vis = sb("cmp_mask", [P, NT, 16]), sb("cmp_vis", [P, NT, 16])
        spread, slot = sb("spread16", [16, P]), sb("slot_mask", [P, 8])
        kbd, vbd = sb("kc_blockdiag", [P, 32]), sb("vc_blockdiag", [P, 512])
        qst = [sb(f"q_staged{g}", [P, P]) for g in range(2)]
        Pr = [sb(f"probs{u}", [P, SEQ]) for u in range(2)]
        PT = [sb(f"probsT{u}", [P, NT, P]) for u in range(2)]
        y = sb("nsa_y", [P, NT, 512])
        nm, L, r = sb("neg_max", [P, 4]), sb("row_sum", [P, 4]), sb("gate_over_sum", [P, 4])
        Pc, PcT = sb("cmp_probs", [P, NT, P]), sb("cmp_probsT", [P, NT, P])
        mc, lc = sb("cmp_max", [P, NT, 8]), sb("cmp_sum", [P, NT, 8])
        pS = [ps(f"att_pS{u}", [P, 2, 512]) for u in range(2)]
        pT = ps("att_pT", [P, 2, 512])
        pO = [ps(f"att_pO{u}", [P, 512]) for u in range(2)]

        consts = sem("att_consts")
        c_scores, c_shift, c_exp, c_probs, c_turned, c_turned_sb, c_out, y_start = (
            sem(n) for n in ("c_scores", "c_shift", "c_exp", "c_probs", "c_turned", "c_turned_sb", "c_out", "y_start"))
        staged, s_done, max_ready, exp_done, t_done, pt_copied, pv_done, o_used = (
            sem(n) for n in ("q_is_staged", "s_done", "max_ready", "exp_done", "t_done", "pt_copied", "pv_done", "o_used"))
        y_stored, y_free = sem("nsa_y_stored"), sem("vbd_ready")
        exp_free, ratio_ready = sem("exp_free"), sem("ratio_ready")
        scale, minus_one, inv = sb("q_scale", [P, P]), sb("minus_one", [P, 1]), sb("inv_sum", [P, 4])
        zeros_ready, filled = sem("zeros_ready"), sem("slots_filled")
        zeros = sb("zero_rows", [P, D])
        block = ctx.enter_context(nc.Block())
        NC_ = 8

        def branch(j):
            return j // 2, j % 2

        def first_key(t, br):
            return 0 if br == 0 else max(0, t - WIN_T) * P

        def keys(t, br):
            return (t + 1) * P - first_key(t, br)

        def pipeline(eng, t, stages):
            depth = len(stages) - 1

            def step(c, j, first):
                for i, stage in enumerate(stages):
                    if stage is None or (first and j - i < 0):
                        continue
                    stage(t, c if j - i >= 0 else c - 1, (j - i) % 4)

            for j in range(4):
                step(0, j, True)
            with eng.Fori(1, 4) as c:
                for j in range(4):
                    step(c, j, False)
            for j in range(depth):
                for i in range(j + 1, depth + 1):
                    if stages[i] is not None:
                        stages[i](t, 3, 4 + j - i)

        @block.sync
        def _(sp):
            for dst, src in ((diag, "mask_diag"), (oldest, "mask_neg"), (visn, "cmp_mask"), (vis, "cmp_vis"),
                             (spread, "spread16"), (slot, "slot_mask")):
                sp.dma_start(dst[:], d[src]).then_inc(consts, 16)
            for v_sb, rows in zip(V, (d["kv_sel_prompt"], d["kv_win_all"][0:SEQ])):
                sp.dma_start(v_sb[:], rows.rearrange("(t p) c -> p t c", p=P)[:, :, P:KV]).then_inc(consts, 16)
            sp.dma_start(k.w_out, d["w_out"].rearrange("(c p) n -> p c n", p=P)).then_inc(k.w_out_loaded, 16)
            sp.wait_ge(zeros_ready, 1)
            sp.dma_start(d["x1"][NTOK:NTOK + P], zeros[:]).then_inc(filled, 16)
            sp.dma_start(d["acc"][NTOK:NTOK + P], zeros[:]).then_inc(filled, 16)
            for t in range(NT):
                sp.wait_ge(o_used, 16 * (t + 1) + 2)
                sp.dma_start(d["mix"][t * P:(t + 1) * P, 512:D], y[:, t]).then_inc(y_stored, 16)
            sp.wait_ge(y_stored, 16 * NT)
            sp.wait_ge(filled, 32)

        @block.gpsimd
        def _(g):
            g.memset(qst[0][:], 0.0)
            g.memset(qst[1][:], 0.0)
            g.memset(zeros[:], 0.0)
            g.memset(scale[:], SCALE)
            g.memset(minus_one[:], -1.0)
            g.drain().then_inc(zeros_ready, 1)

            def stage(t, c):
                g.wait_ge(s_done, c * 4 + (t * 16 + 4))
                g.nop()
                for gr in range(2):
                    rows = slice(gr * 64, gr * 64 + 64)
                    nc.gpsimd.tensor_tensor(qst[gr][rows, :],
                                            k.qrT[rows, bass.ds(c, 1), t * P:(t + 1) * P].rearrange("p a n -> p (a n)"),
                                            scale[rows, :], ALU.mult)
                g.drain().then_inc(staged, 1)

            def ratio(t, c, j):
                br, gr = branch(j)
                g.wait_ge(exp_done, c * 4 + (t * 16 + j + 1))
                g.nop()
                nc.gpsimd.tensor_tensor(inv[:, j:j + 1], L[:, j:j + 1], minus_one[:], ALU.pow)
                g.drain()
                nc.gpsimd.tensor_tensor(r[:, j:j + 1], k.gd[:, t, bass.ds(c * 2 + ((br + 1) * 8 + gr), 1)], inv[:, j:j + 1],
                                        ALU.mult)
                g.drain().then_inc(ratio_ready, 1)

            def pair(t, c, before):
                stage(t, c)
                if before is not None:
                    ratio(*before, 3)
                for j in range(3):
                    ratio(t, c, j)

            for t in range(NT):
                pair(t, 0, (t - 1, 3) if t else None)
                with g.Fori(1, 4) as c:
                    pair(t, c, (t, c - 1))
            ratio(NT - 1, 3, 3)

        @block.tensor
        def _(pe):
            pe.sem_inc(s_done, 4)
            pe.sem_inc(pv_done, 2)
            pe.wait_ge(consts, 16 * NC_)
            nc.tensor.matmul(pT[:, 0, 0:P], spread[:], k.vc_p[:].rearrange("p h e -> p (h e)"), start=True,
                             stop=True).then_inc(c_turned, 1)

            def scores(t, c, j):
                br, gr = branch(j)
                k0, n = first_key(t, br), keys(t, br)
                for i in range(0, n, 512):
                    w = min(512, n - i)
                    mm = nc.tensor.matmul(pS[j % 2][:, i // 512, 0:w], qst[gr][:], K[br][:, k0 + i:k0 + i + w],
                                          start=True, stop=True)
                mm.then_inc(s_done, 1)

            def scores_staged(t, c, j):
                if j == 0:
                    pe.wait_ge(staged, c + (t * 4 + 1))
                pe.wait_ge(exp_free, c * 4 + (t * 16 + j + 1))
                scores(t, c, j)

            def turn(t, c, j):
                br, gr = branch(j)
                pe.wait_ge(exp_done, c * 4 + (t * 16 + j + 1))
                pe.wait_ge(pt_copied, c * 4 + (t * 16 + j + 1))
                for i in range(keys(t, br) // P):
                    mm = nc.tensor.transpose(pT[:, i // 4, (i % 4) * P:(i % 4 + 1) * P], Pr[j % 2][:, i * P:(i + 1) * P],
                                             k.ident[:])
                mm.then_inc(t_done, 1)

            def values(t, c, j):
                br, gr = branch(j)
                k0, n = first_key(t, br) // P, keys(t, br) // P
                unit = c * 4 + (t * 16 + j)
                pe.wait_ge(pt_copied, unit + 2)
                pe.wait_ge(o_used, unit + 1)
                for i in range(n):
                    mm = nc.tensor.matmul(pO[j % 2][:, 0:P], PT[j % 2][:, i], V[br][:, k0 + i], start=(i == 0), stop=(i == n - 1))
                mm.then_inc(pv_done, 1)

            pe.wait_ge(y_free, 1)
            for t in range(NT):
                for c in range(4):
                    mm = nc.tensor.matmul(pS[0][:, t // 4, (t % 4) * P + c * 32:(t % 4) * P + c * 32 + 32],
                                          k.qT[:, c, t * P:(t + 1) * P], kbd[:], start=True, stop=True)
            mm.then_inc(c_scores, 1)
            pe.wait_ge(c_probs, 1)
            for t in range(NT):
                mm = nc.tensor.transpose(pT[:, t // 4, (t % 4) * P:(t % 4 + 1) * P], Pc[:, t], k.ident[:])
            mm.then_inc(c_turned, 1)
            pe.wait_ge(c_turned_sb, 1)
            for t in range(NT):
                if t >= 2:
                    pe.wait_ge(y_start, t - 1)
                nc.tensor.matmul(pO[t % 2][:], PcT[:, t], vbd[:], start=True, stop=True).then_inc(c_out, 1)
            pe.wait_ge(y_start, NT)
            for t in range(NT):
                pipeline(pe, t, (scores_staged, turn, values))

        @block.vector
        def _(v):
            v.sem_inc(o_used, 2)
            v.memset(kbd[:], 0.0)
            v.drain()
            nc.vector.tensor_copy(kbd[0:64, 0:16], k.kcT_p[0:64])
            nc.vector.tensor_copy(kbd[64:P, 16:32], k.kcT_p[64:P])
            v.wait_ge(c_turned, 1)
            for c in range(4):
                nc.vector.tensor_tensor(vbd[:, c * P:(c + 1) * P].rearrange("p (h e) -> p h e", e=HD),
                                        pT[:, 0, 0:P].rearrange("p (h e) -> p h e", e=HD),
                                        bcast(slot[:, 2 * c:2 * c + 2].rearrange("p (h a) -> p h a", a=1), [P, 2, HD]), ALU.mult)
            v.drain().then_inc(y_free, 1)

            def softmax_max(t, c, j):
                br, gr = branch(j)
                n = keys(t, br)
                S = pS[j % 2][:].rearrange("p a b -> p (a b)")
                v.wait_ge(s_done, c * 4 + (t * 16 + j + 5))
                nc.vector.tensor_tensor(S[:, n - P:n], S[:, n - P:n], diag[:], ALU.add)
                if br == 1 and t >= WIN_T:
                    nc.vector.tensor_tensor(S[:, 0:P], S[:, 0:P], oldest[:], ALU.add)
                v.drain()
                nc.vector.tensor_reduce(nm[:, j:j + 1], S[:, 0:n], AX.X, ALU.max, negate=True).then_inc(max_ready, 1)

            def add_out(t, c, j):
                br, gr = branch(j)
                unit = c * 4 + (t * 16 + j)
                v.wait_ge(pv_done, unit + 3)
                v.wait_ge(ratio_ready, unit + 1)
                ys = y[:, t, bass.ds(c * P + gr * HD, HD)]
                nc.vector.scalar_tensor_tensor(out=ys, in0=pO[j % 2][:, gr * HD:gr * HD + HD], scalar=r[:, j:j + 1], in1=ys,
                                               op0=ALU.mult, op1=ALU.add)
                v.drain().then_inc(o_used, 1)

            v.wait_ge(c_scores, 1)
            hs = Pc[:].rearrange("p t (h j) -> p t h j", j=16)
            n8 = [P, NT, 8, 16]
            for t in range(NT):
                nc.vector.tensor_tensor(hs[:, t], pS[0][:, t // 4, (t % 4) * P:(t % 4 + 1) * P].rearrange("p (h j) -> p h j", j=16),
                                        bcast(visn[:, t:t + 1], [P, 8, 16]), ALU.add)
            v.drain()
            nc.vector.tensor_reduce(mc[:], hs, AX.X, ALU.max)
            v.drain()
            nc.vector.tensor_tensor(hs, hs, bcast(mc[:].rearrange("p t (h a) -> p t h a", a=1), n8), ALU.subtract)
            v.drain().then_inc(c_shift, 1)
            v.wait_ge(c_exp, 1)
            nc.vector.tensor_reduce(lc[:], hs, AX.X, ALU.add)
            v.drain()
            nc.vector.tensor_tensor(hs, hs, bcast(vis[:].rearrange("p t (a j) -> p t a j", a=1), n8), ALU.mult)
            nc.vector.reciprocal(lc[:], lc[:])
            v.drain()
            nc.vector.tensor_tensor(lc[:], lc[:], k.gd[:, 0:NT, 0:8], ALU.mult)
            v.drain()
            nc.vector.tensor_tensor(hs, hs, bcast(lc[:].rearrange("p t (h a) -> p t h a", a=1), n8), ALU.mult)
            v.drain().then_inc(c_probs, 1)
            v.wait_ge(c_turned, 2)
            nc.vector.tensor_copy(PcT[:], pT[:].rearrange("p a (b q) -> p (a b) q", q=P))
            v.drain().then_inc(c_turned_sb, 1)
            for t in range(NT):
                v.wait_ge(c_out, t + 1)
                nc.vector.tensor_copy(y[:, t], pO[t % 2][:])
                v.drain().then_inc(y_start, 1)
            for t in range(NT):
                pipeline(v, t, (softmax_max, None, None, add_out))

        @block.scalar
        def _(act):
            act.sem_inc(pt_copied, 1)
            act.sem_inc(exp_free, 2)
            def exp(t, c, j):
                br, gr = branch(j)
                n = keys(t, br)
                act.wait_ge(max_ready, c * 4 + (t * 16 + j + 1))
                nc.scalar.activation(Pr[j % 2][:, 0:n], pS[j % 2][:].rearrange("p a b -> p (a b)")[:, 0:n], ACT.Exp,
                                     bias=nm[:, j:j + 1], accum_out=L[:, j:j + 1])
                act.drain().then_inc(exp_done, 1)
                act.sem_inc(exp_free, 1)

            def turned(t, c, j):
                br, gr = branch(j)
                unit = c * 4 + (t * 16 + j)
                n = keys(t, br) // P
                act.wait_ge(t_done, unit + 1)
                act.wait_ge(pv_done, unit + 1)
                nc.scalar.copy(PT[j % 2][:].rearrange("p a b -> p (a b)")[:, 0:n * P],
                               pT[:].rearrange("p a b -> p (a b)")[:, 0:n * P]).then_inc(pt_copied, 1)

            act.wait_ge(c_shift, 1)
            nc.scalar.activation(Pc[:], Pc[:], ACT.Exp, scale=SCALE).then_inc(c_exp, 1)
            for t in range(NT):
                pipeline(act, t, (exp, turned))


NJ = 16
QR = 32
PIECES = [None, (0, 0), (0, 1), (1, 0), (1, 1)]


def sample(nc, k, d):
    with ExitStack() as ctx:
        def sb(name, shape, dt=F32):
            return ctx.enter_context(nc.sbuf_tensor(name, shape, dt))

        def ps(name, shape):
            return ctx.enter_context(nc.psum_tensor(name, shape, F32))

        def sem(name):
            k.sems.append(ctx.enter_context(nc.semaphore(name)))
            return k.sems[-1]

        grp4, pick, e8, e8t = sb("grp4", [64, 16]), sb("pick_bg", [16, 2, P]), sb("e8", [8, P]), sb("e8t", [P, 8])
        jmask, iota, parity, wmask = sb("jmask", [P, NJ]), sb("iota128", [P, P]), sb("parity", [P, P]), sb("wmask", [P, 1])
        pti, ptf = sb("pt_int", [8, NPAGE], I32), sb("pt_f", [8, NPAGE])
        sA, sP, sPT = sb("cmpS", [P, 64]), sb("cmpP", [64, P]), sb("cmpPT", [P, 64])
        st1 = sb("cmp_stat", [64, 4])
        score, score2 = sb("score", [16, P]), sb("score2", [16, P])
        top, topi = sb("top", [16, 2, 8]), sb("topi", [16, 2, 8], U32)
        topf = sb("topf", [16, 16])
        pj, blk, T2, oh = sb("pj", [P, 2, NJ]), sb("blk", [P, 2]), sb("T2", [P, P]), sb("oh", [P, P])
        half, idxf, idx = sb("half", [P, 2]), sb("idxf", [P, 2, 2]), sb("idx", [P, 4], U32)
        oc, qtok, qb = sb("oc", [64, 8, 8]), sb("qtok", [8, 512]), sb("qb", [P, 512])
        W = QR + 1
        tile = [sb(f"kv_piece{u}", [P, W, 2, 2, HD]) for u in range(2)]
        prod = sb("prod", [P, 4 * W * HD])
        S, m, M = sb("piece_S", [P, 2, 4, W]), sb("piece_m", [P, 2, 4]), sb("piece_M", [P, 2, 4])
        mt, mtx = sb("m_by_sample", [8, 8]), sb("m_spread", [8, 8, NJ])
        Pd = sb("p_by_sample", [P, W, 2, NS, 4])
        ld, Md = sb("l_by_sample", [P, 2 * NS * 4]), sb("M_by_sample", [P, NS * 4])
        lj, Mj, wj = sb("l_joined", [32, 2, 2]), sb("M_joined", [32, 2, 2]), sb("w_joined", [32, 2, 2])
        Mx, lx, lwin = sb("M_max", [32, 2]), sb("l_sum", [32, 2]), sb("l_win", [64, 1])
        Osel, Owin = sb("O_sel", [32, 2, HD]), sb("O_win", [64, 2, HD])
        y, t8 = (prod[0:8, i * 512:(i + 1) * 512].rearrange("p (c g e) -> p c g e", g=2, e=HD) for i in range(2))
        pA, pB, pC, pD = (ps(f"smp_p{c}", [P, 512]) for c in "ABCD")
        pWin, pSel, pL, pM = (ps(n, [P, 512]) for n in ("pv_window", "pv_selected", "sums", "maxima"))

        consts, dve, pe_, act_ = sem("smp_consts"), sem("smp_dve"), sem("smp_pe"), sem("smp_act")
        piece_loaded = [sem(f"piece_loaded{u}") for u in range(2)]
        gathered = [sem(f"gathered{u}") for u in range(2)]
        local_max, max_turned, max_joined, max_spread, p_ready, pv_done = (
            sem(n) for n in ("local_max", "max_turned", "max_joined", "max_spread", "p_ready", "pv_done"))
        last_head, prod_used = sem("last_head_multiplied"), sem("prod_used")
        idx_ready, shifted, expd, new_rows, stored, y_ready = (
            sem(n) for n in ("idx_ready", "shifted", "expd", "new_rows", "smp_stored", "y8_ready"))
        block = ctx.enter_context(nc.Block())
        NC_ = 10

        @block.sync
        def _(sp):
            for dst, name in ((grp4, "grp4"), (pick, "pick_bg"), (e8, "e8"), (e8t, "e8t"), (jmask, "jmask"), (iota, "iota"),
                              (parity, "parity"), (wmask, "wmask")):
                sp.dma_start(dst[:], d[name]).then_inc(consts, 16)
            sp.dma_start(pti[:], d["page_table"].rearrange("a (b p) -> (a b) p", p=NPAGE)).then_inc(consts, 16)
            sp.dma_start(d["kv_win_sample"][:, 0:511, :], d["cache_kv_win"][:, 1:512, :]).then_inc(stored, 16)
            sp.dma_start(d["kv_win_sample"][:, 511, :], d["kv_win_all"][SEQ:NTOK]).then_inc(stored, 16)
            sp.dma_start(tile[0][:, 0:QR].rearrange("p r a h e -> p (r a h e)"),
                         d["cache_kv_win"].rearrange("b (j r) c -> (b j) (r c)", r=QR)).then_inc(piece_loaded[0], 16)
            for b in range(NS):
                sp.dma_start(tile[0][b * NJ:(b + 1) * NJ, QR].rearrange("p a h e -> p (a h e)"),
                             bcast(d["kv_win_all"][SEQ + b:SEQ + b + 1], [NJ, KV])).then_inc(piece_loaded[0], 16)
            for n in range(4):
                u = (n + 1) % 2
                sp.wait_ge(gathered[u], 16 * (n // 2 + 1))
                for b in range(NS):
                    sp.dma_start(tile[u][b * NJ + NJ - 1:b * NJ + NJ, 0:QR].rearrange("p r a h e -> p r (a h e)"),
                                 bcast(d["kv_sel_sample"][b:b + 1].rearrange("a (c e) -> a c e", c=1), [1, QR, KV])
                                 ).then_inc(piece_loaded[u], 16)
            sp.wait_ge(y_ready, 1)
            sp.dma_start(d["mix"][SEQ:NTOK, 512:D], y.rearrange("p a b c -> p (a b c)")).then_inc(stored, 16)
            sp.wait_ge(stored, 48)

        @block.gpsimd
        def _(g):
            def gather(n):
                u = (n + 1) % 2
                if n:
                    g.wait_ge(pv_done, n)
                g.indirect_dma_start(tile[u][:, 0:QR].rearrange("p r a h e -> p (r a h e)"), None, d["cache_kv_sel"],
                                     bass.IndirectOffsetOnAxis(idx[:, n:n + 1], 0)).then_inc(gathered[u], 16)

            def multiply(use, u, gr, rows):
                if use:
                    g.wait_ge(prod_used, use)
                pk = prod[:, 3 * rows * HD:4 * rows * HD].rearrange("p (r e) -> p r e", e=HD)
                nc.gpsimd.tensor_tensor(pk, tile[u][:, 0:rows, 0, gr], bcast(qb[:, (6 + gr) * HD:(7 + gr) * HD].rearrange(
                    "p (a e) -> p a e", a=1), [P, rows, HD]), ALU.mult).then_inc(last_head, 1)

            g.wait_ge(idx_ready, 1)
            gather(0)
            g.wait_ge(piece_loaded[0], 16 * (1 + NS))
            multiply(0, 0, 0, QR + 1)
            multiply(1, 0, 1, QR + 1)
            for n in range(4):
                u = (n + 1) % 2
                g.wait_ge(piece_loaded[u], (16 * (1 + NS) if u == 0 else 0) + 16 * NS * (n // 2 + 1))
                g.wait_ge(gathered[u], 16 * (n // 2 + 1))
                multiply(n + 2, u, PIECES[n + 1][0], QR)
                if n < 3:
                    gather(n + 1)

        @block.tensor
        def _(pe):
            pe.wait_ge(consts, 16 * (NC_ - 1))
            for b in range(NS):
                for gr in range(2):
                    rows = slice(gr * 64, gr * 64 + 64)
                    nc.tensor.matmul((pA, pC)[gr][:, b * 4:b * 4 + 4], k.kcT_s[rows, b], k.qT[rows, :, SEQ + b],
                                     start=True, stop=True)
            for c in range(4):
                mm = nc.tensor.transpose(pB[0:8, c * P:(c + 1) * P], k.qrT[:, c, SEQ:NTOK], k.ident[:])
            mm.then_inc(pe_, 1)
            pe.wait_ge(dve, 1)
            nc.tensor.transpose(pC[0:64, 0:P], sA[:], k.ident[:]).then_inc(pe_, 1)
            nc.tensor.matmul(pD[:], e8[:], qtok[:], start=True, stop=True).then_inc(pe_, 1)
            nc.tensor.matmul(pA[:, 0:NPAGE], e8[:], ptf[:], start=True, stop=True).then_inc(pe_, 1)
            pe.wait_ge(dve, 2)
            nc.tensor.matmul(pC[0:16, P:2 * P], grp4[:], sP[:], start=True, stop=True)
            nc.tensor.transpose(pC[:, 2 * P:2 * P + 64], sP[:], k.ident[0:64, 0:64]).then_inc(pe_, 1)
            pe.wait_ge(dve, 3)
            for gr in range(2):
                mm = nc.tensor.matmul(pB[:, gr * NJ:(gr + 1) * NJ], pick[:, gr], topf[:], start=True, stop=True)
            mm.then_inc(pe_, 1)
            pe.wait_ge(dve, 4)
            for b in range(NS):
                for gr in range(2):
                    at = b * 8 + gr * 4
                    mm = nc.tensor.matmul(pA[0:64, at:at + 4], k.vc_s[:, b, gr], sPT[:, at:at + 4], start=True, stop=True)
            mm.then_inc(pe_, 1)
            pe.wait_ge(dve, 5)
            for h in range(8):
                mm = nc.tensor.transpose(pD[0:8, h * HD:(h + 1) * HD], oc[:, h], k.ident[0:64, 0:64])
            mm.then_inc(pe_, 1)
            for n, sel in enumerate(PIECES):
                hs, u, rows = (2, 0, QR + 1) if sel is None else (1, n % 2, QR)
                pe.wait_ge(local_max, n + 1)
                nc.tensor.transpose(pM[0:4 * hs, 0:P], m[:, 0:hs].rearrange("p h c -> p (h c)"), k.ident[:]).then_inc(max_turned, 1)
                pe.wait_ge(max_joined, n + 1)
                nc.tensor.transpose(pM[:, P:P + 4 * hs], mtx[0:4 * hs].rearrange("p a b -> p (a b)"),
                                    k.ident[0:4 * hs, 0:4 * hs]).then_inc(max_spread, 1)
                pe.wait_ge(p_ready, n + 1)
                cols = NS * 4 * hs
                out = pWin[0:cols, 0:P] if sel is None else pSel[0:cols, (n - 1) * P:n * P]
                for r in range(rows):
                    nc.tensor.matmul(out, Pd[:, r].rearrange("p h b c -> p (h b c)")[:, 0:cols],
                                     tile[u][:, r, 1].rearrange("p h e -> p (h e)"), start=(r == 0), stop=(r == rows - 1))
                mm = nc.tensor.matmul(pL[0:cols, n * 32:n * 32 + 16], ld[:, 0:cols], k.ones[:, 0:16], start=True, stop=True)
                if sel is not None:
                    mm = nc.tensor.matmul(pL[0:cols, n * 32 + 16:n * 32 + 32], Md[:], k.ones[:, 0:16], start=True, stop=True)
                mm.then_inc(pv_done, 1)
            pe.wait_ge(dve, 6)
            for c in range(4):
                for gr in range(2):
                    at = (c * 2 + gr) * HD
                    nc.tensor.matmul(pA[0:8, at:at + HD], k.ident[0:64, gr * 32 + c:gr * 32 + 32:4], Owin[:, gr], start=True, stop=True)
                    mm = nc.tensor.matmul(pB[0:8, at:at + HD], k.ident[0:32, c:32:4], Osel[:, gr], start=True, stop=True)
            mm.then_inc(pe_, 1)

        @block.scalar
        def _(act):
            act.wait_ge(shifted, 1)
            nc.scalar.activation(sP[:], sP[:], ACT.Exp, scale=SCALE, accum_out=st1[:, 1:2])
            act.drain().then_inc(expd, 1)
            for n, sel in enumerate(PIECES):
                act.wait_ge(shifted, n + 2)
                hs, rows = (2, QR + 1) if sel is None else (1, QR)
                nc.scalar.activation(S[:, 0:hs, :, 0:rows], S[:, 0:hs, :, 0:rows], ACT.Exp, scale=SCALE).then_inc(expd, 1)
            act.wait_ge(shifted, len(PIECES) + 2)
            nc.scalar.activation(wj[:], wj[:], ACT.Exp, scale=SCALE).then_inc(expd, 1)

        @block.vector
        def _(v):
            v.wait_ge(consts, 16 * (NC_ - 1))
            v.wait_ge(pe_, 1)
            for gr in range(2):
                nc.vector.tensor_copy(sA[:].rearrange("p (b g c) -> p b g c", b=8, g=2)[:, :, gr],
                                      (pA, pC)[gr][:, 0:32].rearrange("p (b c) -> p b c", c=4))
            nc.vector.tensor_copy(qtok[:], pB[0:8, :])
            nc.vector.tensor_copy(ptf[:], pti[:])
            v.drain().then_inc(dve, 1)
            v.wait_ge(pe_, 2)
            nc.vector.tensor_reduce(st1[:, 0:1], pC[0:64, 0:P], AX.X, ALU.max)
            v.drain()
            nc.vector.tensor_scalar(sP[:], pC[0:64, 0:P], st1[:, 0:1], None, ALU.subtract)
            v.drain().then_inc(shifted, 1)
            v.wait_ge(pe_, 3)
            nc.vector.tensor_copy(qb[:], pD[:])
            v.wait_ge(pe_, 4)
            T3 = T2[:].rearrange("p (a two) -> p a two", two=2)
            nc.vector.scalar_tensor_tensor(out=T3, in0=bcast(pA[:, 0:NPAGE].rearrange("p (a b) -> p a b", b=1), [P, NPAGE, 2]),
                                           scalar=2.0, in1=parity[:].rearrange("p (a two) -> p a two", two=2), op0=ALU.mult,
                                           op1=ALU.add)
            v.wait_ge(expd, 1)
            nc.vector.reciprocal(st1[:, 2:3], st1[:, 1:2])
            v.drain()
            nc.vector.tensor_scalar(sP[:], sP[:], st1[:, 2:3], None, ALU.mult)
            v.drain().then_inc(dve, 1)
            v.wait_ge(pe_, 5)
            nc.vector.tensor_copy(score[:], pC[0:16, P:2 * P])
            nc.vector.tensor_copy(sPT[:], pC[:, 2 * P:2 * P + 64])
            v.drain()
            v.memset(score[:, 0:P:P - 1], 1e4)
            v.drain()
            nc.vector.max(top[:, 0], score[:])
            v.drain()
            nc.vector.max_index(topi[:, 0], top[:, 0], score[:])
            nc.vector.match_replace(score2[:], top[:, 0], score[:], -1.0)
            v.drain()
            nc.vector.max(top[:, 1], score2[:])
            v.drain()
            nc.vector.max_index(topi[:, 1], top[:, 1], score2[:])
            v.drain()
            nc.vector.tensor_copy(topf[:], topi[:].rearrange("p a b -> p (a b)"))
            v.drain().then_inc(dve, 1)
            v.wait_ge(pe_, 6)
            nc.vector.tensor_tensor(pj[:], pB[:, 0:2 * NJ].rearrange("p (g j) -> p g j", g=2),
                                    bcast(jmask[:].rearrange("p (a j) -> p a j", a=1), [P, 2, NJ]), ALU.mult)
            v.drain()
            nc.vector.tensor_reduce(blk[:], pj[:], AX.X, ALU.add)
            for gr in range(2):
                v.drain()
                nc.vector.tensor_scalar(oh[:], iota[:], blk[:, gr:gr + 1], None, ALU.is_equal)
                v.drain()
                nc.vector.tensor_tensor(oh[:], oh[:], T2[:], ALU.mult)
                v.drain()
                nc.vector.tensor_reduce(half[:, gr:gr + 1], oh[:], AX.X, ALU.add)
            v.drain()
            for q in range(2):
                nc.vector.tensor_scalar(idxf[:, :, q], half[:], 2.0, float(q), ALU.mult, ALU.add)
            v.drain()
            nc.vector.tensor_copy(idx[:], idxf[:].rearrange("p g q -> p (g q)"))
            v.drain().then_inc(idx_ready, 1)
            v.drain().then_inc(dve, 1)
            v.wait_ge(pe_, 7)
            nc.vector.tensor_copy(oc[:].rearrange("p (c g) b -> p b g c", g=2),
                                  pA[0:64, 0:64].rearrange("p (b g c) -> p b g c", b=8, g=2))
            v.drain().then_inc(dve, 1)

            def piece(n, u, heads, rows):
                hs = len(heads)
                Sr = S[:, 0:hs, :, 0:rows]
                for i, gr in enumerate(heads):
                    Kr = tile[u][:, 0:rows, 0, gr]
                    pk = prod[:, 0:4 * rows * HD].rearrange("p (c r e) -> p c r e", c=4, e=HD)
                    for c in range(3):
                        nc.vector.tensor_tensor(pk[:, c], Kr, bcast(qb[:, (c * 2 + gr) * HD:(c * 2 + gr + 1) * HD].rearrange(
                            "p (a e) -> p a e", a=1), [P, rows, HD]), ALU.mult)
                    v.drain()
                    use = n + 1 + i if n == 0 else n + 2
                    v.wait_ge(last_head, use)
                    nc.vector.tensor_reduce(S[:, i, :, 0:rows], pk, AX.X, ALU.add)
                    v.drain().then_inc(prod_used, 1)
                if rows > QR:
                    nc.vector.tensor_scalar(S[:, :, :, QR], S[:, :, :, QR], wmask[:, 0:1], None, ALU.add)
                    v.drain()
                nc.vector.tensor_reduce(m[:, 0:hs], Sr, AX.X, ALU.max)
                v.drain().then_inc(local_max, 1)
                v.wait_ge(max_turned, n + 1)
                nc.vector.tensor_reduce(mt[0:4 * hs], pM[0:4 * hs, 0:P].rearrange("p (b j) -> p b j", j=NJ), AX.X, ALU.max)
                v.drain()
                nc.vector.tensor_copy(mtx[0:4 * hs], bcast(mt[0:4 * hs].rearrange("p (b a) -> p b a", a=1), [4 * hs, 8, NJ]))
                v.drain().then_inc(max_joined, 1)
                v.wait_ge(max_spread, n + 1)
                nc.vector.tensor_copy(M[:, 0:hs].rearrange("p h c -> p (h c)"), pM[:, P:P + 4 * hs])
                v.drain()
                for i in range(hs):
                    nc.vector.tensor_tensor(S[:, i, :, 0:rows], S[:, i, :, 0:rows],
                                            bcast(M[:, i].rearrange("p (c a) -> p c a", a=1), [P, 4, rows]), ALU.subtract)
                v.drain().then_inc(shifted, 1)
                if n:
                    v.wait_ge(pv_done, n)
                    nc.vector.tensor_tensor(Md[:].rearrange("p (b c) -> p b c", c=4), bcast(k.ident[:, 0:P:NJ].rearrange(
                        "p (b a) -> p b a", a=1), [P, NS, 4]), bcast(M[:, 0:1], [P, NS, 4]), ALU.mult)
                v.wait_ge(expd, n + 2)
                for i in range(hs):
                    nc.vector.tensor_tensor(Pd[:, 0:rows, i], bcast(S[:, i, :, 0:rows].rearrange("p c (r a) -> p r a c", a=1),
                                                                    [P, rows, NS, 4]),
                                            bcast(e8t[:].rearrange("p (a b c) -> p a b c", a=1, c=1), [P, rows, NS, 4]), ALU.mult)
                v.drain()
                nc.vector.tensor_reduce(ld[:, 0:32 * hs], Pd[:, 0:rows].rearrange("p r h b c -> p (h b c) r")[:, 0:32 * hs],
                                        AX.X, ALU.add)
                v.drain().then_inc(p_ready, 1)

            v.wait_ge(piece_loaded[0], 16 * (1 + NS))
            piece(0, 0, (0, 1), QR + 1)
            for n in range(4):
                u = (n + 1) % 2
                v.wait_ge(piece_loaded[u], (16 * (1 + NS) if u == 0 else 0) + 16 * NS * (n // 2 + 1))
                v.wait_ge(gathered[u], 16 * (n // 2 + 1))
                piece(n + 1, u, (PIECES[n + 1][0],), QR)

            v.wait_ge(pv_done, len(PIECES))
            by_half = pL[0:32, 32:32 * len(PIECES)].rearrange("p (g q two x) -> p g q two x", g=2, q=2, two=2)
            nc.vector.tensor_copy(lj[:], by_half[:, :, :, 0, 0])
            nc.vector.tensor_copy(Mj[:], by_half[:, :, :, 1, 0])
            nc.vector.reciprocal(lwin[:], pL[0:64, 0:1])
            v.drain()
            nc.vector.tensor_reduce(Mx[:], Mj[:], AX.X, ALU.max)
            nc.vector.tensor_scalar(Owin[:].rearrange("p h e -> p (h e)"), pWin[0:64, 0:P], lwin[:, 0:1], None, ALU.mult)
            v.drain()
            nc.vector.tensor_tensor(wj[:], Mj[:], bcast(Mx[:].rearrange("p (g a) -> p g a", a=1), [32, 2, 2]), ALU.subtract)
            v.drain().then_inc(shifted, 1)
            v.wait_ge(expd, len(PIECES) + 2)
            nc.vector.tensor_tensor(lj[:], lj[:], wj[:], ALU.mult)
            v.drain()
            nc.vector.tensor_reduce(lx[:], lj[:], AX.X, ALU.add)
            v.drain()
            nc.vector.reciprocal(lx[:], lx[:])
            v.drain()
            nc.vector.tensor_tensor(wj[:], wj[:], bcast(lx[:].rearrange("p (g a) -> p g a", a=1), [32, 2, 2]), ALU.mult)
            v.drain()
            for q in range(2):
                for gr in range(2):
                    src = pSel[0:32, (gr * 2 + q) * P + gr * HD:(gr * 2 + q) * P + gr * HD + HD]
                    if q == 0:
                        nc.vector.tensor_scalar(Osel[:, gr], src, wj[:, gr, 0:1], None, ALU.mult)
                    else:
                        nc.vector.scalar_tensor_tensor(out=Osel[:, gr], in0=src, scalar=wj[:, gr, 1:2], in1=Osel[:, gr],
                                                       op0=ALU.mult, op1=ALU.add)
                v.drain()
            v.drain().then_inc(dve, 1)
            v.wait_ge(pe_, 9)
            for br, src in enumerate((pD, pB, pA)):
                gate = bcast(k.gd[0:8, NT, 8 * br:8 * br + 8].rearrange("p (c g a) -> p c g a", g=2, a=1), [8, 4, 2, HD])
                nc.vector.tensor_tensor((t8 if br else y), src[0:8, :].rearrange("p (c g e) -> p c g e", g=2, e=HD), gate, ALU.mult)
                v.drain()
                if br:
                    nc.vector.tensor_tensor(y, y, t8, ALU.add)
                    v.drain()
            v.drain().then_inc(y_ready, 1)


NE, TOPK, NGRP, KGRP = 64, 6, 8, 4
NBLK = (NTOK * TOPK + NE * (P - 1)) // P + 1
MIN_BLK = NTOK * TOPK // P
FE = 256


def alloc_routing(nc, ctx, k):
    def sb(name, shape, dt=F32):
        return ctx.enter_context(nc.sbuf_tensor(name, shape, dt))
    k.toks = sb("slot_token", [P, P], I32)
    k.slot_w = sb("slot_weight", [P, NBLK])
    k.plan = sb("block_plan", [1, P], I32)


def route(nc, k, d):
    with ExitStack() as ctx:
        def sb(name, shape, dt=F32):
            return ctx.enter_context(nc.sbuf_tensor(name, shape, dt))

        def ps(name, shape):
            return ctx.enter_context(nc.psum_tensor(name, shape, F32))

        def sem(name):
            k.sems.append(ctx.enter_context(nc.semaphore(name)))
            return k.sems[-1]

        wr = sb("router_sb", [P, DC, P])
        sgu, sd = sb("shared_gu", [P, DC, 2 * FE]), sb("shared_down", [P, 2, D])
        gain, bias, rbias = sb("ln1_g_sb", [P, D]), sb("ln1_b_sb", [P, D]), sb("router_bias_sb", [P, NE])
        mx, xr = sb("mix_tile", [P, D]), sb("res_tile", [P, D])
        xs = [sb(f"x1_tile{u}", [P, D]) for u in range(2)]
        acc = sb("acc_tile", [P, D])
        mT, xT = sb("mixT", [P, DC, P]), sb("x1T", [P, DC, P])
        hs, eg, hT = sb("sh_h", [P, FE]), sb("sh_e", [P, FE]), sb("sh_hT", [P, 2, P])
        stats, mv, rstd = sb("stats1", [P, 2, 6]), sb("mv1", [P, 2]), sb("rstd1", [P, 2])
        mhalf, eps = sb("mhalf1", [P, 1]), sb("eps1", [P, 1])
        sc_, bi = sb("scores", [P, NE]), sb("biased", [P, NE])
        g8, gs, gt, gi, gif = sb("grp_top", [P, 8, 8]), sb("grp_score", [P, 8]), sb("grp_sorted", [P, 8]), sb("grp_idx", [P, 8], U32), sb("grp_idx_f", [P, 8])
        gk, keep = sb("grp_oh", [P, 8, KGRP]), sb("grp_keep", [P, 8])
        et, ei, ef = sb("exp_top", [P, 8]), sb("exp_idx", [P, 8], U32), sb("exp_choice", [P, NT + 1, TOPK])
        io64, lt, thr = sb("iota64", [P, NE]), sb("mask_lt", [P, P]), sb("block_starts", [P, 16])
        oh, ohw = sb("choice_oh", [P, TOPK, NE]), sb("choice_prod", [P, TOPK, NE])
        ws = sb("w_sum", [P, 2])
        mask, pre, dst = sb("chosen", [P, NT + 1, NE]), sb("tokens_before", [P, NT + 1, NE]), sb("dest_all", [P, NT + 1, NE])
        cmp_, nbl, incl = sb("cnt_cmp", [P, NE, 16]), sb("n_blocks_e", [P, NE]), sb("blocks_incl", [P, NE])
        dstf = sb("dest_f", [P, NT + 1, TOPK])
        dest = sb("dest_slot", [P, NT + 1, TOPK], I32)
        choice = sb("token_and_weight", [P, NT + 1, TOPK, 2])
        tokf = sb("tok_f", [P, NT + 1])
        ip, ble, be = sb("iota_p", [P, 1]), sb("blk_cmp", [P, NE]), sb("blk_expert", [P, 1])
        half_counts = sb("half_counts", [1, NE])
        io128 = sb("slot_in_block", [P, P])
        empty, slots = sb("empty_slots", [NBLK, P, 2]), sb("slot_rows", [NBLK, P, 2])
        pT = ps("r_pT", [P, 2, 512])
        pO, pD = ps("r_pO", [P, 2, 512]), ps("r_pD", [P, 2, 512])
        pRH, pG = ps("r_pRH", [P, 512]), ps("r_pG", [P, 512])
        pR, pH = pRH[:, 0:P], pRH[:, P:3 * P]

        consts, mix_loaded, xr_loaded, mix_in_psum, mixT_ready, proj_done, in_used = (
            sem(n) for n in ("r_consts", "mix_loaded", "xr_loaded", "mix_in_psum", "mixT_ready", "proj_done", "in_used"))
        stats_ready, rstd_ready, x1_ready, x1_in_psum, x1T_ready, router_done, gu_done = (
            sem(n) for n in ("r_stats", "r_rstd", "x1_ready", "x1_in_psum", "x1T_ready", "router_done", "gu_done"))
        exp_ready, h_ready, h_in_psum, hT_ready, down_done, acc_ready, acc_stored, r_free = (
            sem(n) for n in ("r_exp", "sh_h_ready", "sh_h_in_psum", "sh_hT_ready", "sh_down_done", "acc_ready", "acc_stored", "router_read"))
        dv, pp, zero_stored, dest_ready, scattered, slots_loaded = (
            sem(n) for n in ("d_steps", "p_steps", "zero_stored", "dest_ready", "scattered", "slots_loaded"))
        scores_ready = sem("scores_ready")
        x1_stored = [sem(f"x1_stored{u}") for u in range(2)]
        block = ctx.enter_context(nc.Block())

        def pipeline(eng, step, begun=False):
            if not begun:
                step(-2, -1, 0, P, None, None)
            step(-1, -1, 1, P, P, None)
            with eng.Fori(0, NT // 2 - 1) as i:
                for u in range(2):
                    step(i * 2 + u, i, u, P, P, P)
            step(NT - 2, NT // 2 - 1, 0, NS, P, P)
            step(NT - 1, NT // 2 - 1, 1, None, NS, P)
            step(NT, NT // 2, 0, None, None, NS)

        @block.sync
        def _(sp):
            def step(t, i, u, Rm, Rx, Rh):
                if Rm:
                    sp.wait_ge(mix_in_psum, t + 3)
                    sp.dma_start(mx[0:Rm], d["mix"][bass.ds(t * P + 2 * P, Rm)]).then_inc(mix_loaded, 16)
                    sp.wait_ge(in_used, t + 3)
                    sp.dma_start(xr[0:Rm], d["xres"][bass.ds(t * P + 2 * P, Rm)]).then_inc(xr_loaded, 16)
                if Rx:
                    sp.wait_ge(x1_ready, t + 2)
                    sp.dma_start(d["x1"][bass.ds(t * P + P, Rx)], xs[1 - u][0:Rx]).then_inc(x1_stored[1 - u], 16)
                if Rh:
                    sp.wait_ge(acc_ready, t + 2)
                    sp.dma_start(d["acc"][bass.ds(t * P, Rh)], acc[0:Rh]).then_inc(acc_stored, 16)

            step(-2, -1, 0, P, None, None)
            for dst_, src in ((gain, bcast(d["ln1_g"], [P, D])), (bias, bcast(d["ln1_b"], [P, D])),
                              (rbias, bcast(d["router_bias"], [P, NE])), (wr, d["router_w"].rearrange("(c p) n -> p c n", p=P)),
                              (sgu[:, :, 0:FE], d["sh_gate"].rearrange("(c p) n -> p c n", p=P)),
                              (sgu[:, :, FE:2 * FE], d["sh_up"].rearrange("(c p) n -> p c n", p=P)),
                              (sd, d["sh_down"].rearrange("(c p) n -> p c n", p=P)), (io64, d["iota"][:, 0:NE]), (io128, d["iota"]),
                              (lt, d["mask_lt"]), (thr, d["block_starts"]), (tokf, d["token_ids"]), (ip, d["iota_p"])):
                sp.dma_start(dst_[:] if not isinstance(dst_, bass.AP) else dst_, src).then_inc(consts, 16)
            pipeline(sp, step, begun=True)
            sp.wait_ge(dv, 1)
            sp.dma_start(d["slot_rows"].rearrange("(n s) a -> n (s a)", s=P), empty[:].rearrange("n s a -> n (s a)")
                         ).then_inc(zero_stored, 16)
            sp.wait_ge(scattered, 16 * TOPK * (NT + 1))
            sp.wait_ge(zero_stored, 16)
            sp.dma_start(slots[:].rearrange("n s a -> n (s a)"), d["slot_rows"].rearrange("(n s) a -> n (s a)", s=P)
                         ).then_inc(slots_loaded, 16)
            sp.wait_ge(x1_stored[0], 16 * (NT // 2 + 2))
            sp.wait_ge(x1_stored[1], 16 * (NT // 2 + 1))
            sp.wait_ge(acc_stored, 16 * (NT + 2))

        @block.gpsimd
        def _(g):
            g.memset(eps[:], EPS)
            g.memset(mhalf[:], -0.5)
            g.drain()

            def inv_std(t, R):
                g.wait_ge(stats_ready, t + 1)
                nc.gpsimd.tensor_tensor(rstd[0:R, 0:1], mv[0:R, 1:2], eps[0:R, :], ALU.add)
                g.drain()
                nc.gpsimd.tensor_tensor(rstd[0:R, 1:2], rstd[0:R, 0:1], mhalf[0:R, :], ALU.pow).then_inc(rstd_ready, 1)

            with g.Fori(0, NT) as t:
                inv_std(t, P)
            inv_std(NT, NS)
            g.wait_ge(zero_stored, 16)
            for t in range(NT + 1):
                g.wait_ge(dest_ready, t + 1)
                R = P if t < NT else NS
                for c in range(TOPK):
                    g.indirect_dma_start(d["slot_rows"], bass.IndirectOffsetOnAxis(dest[0:R, t, c:c + 1], 0),
                                         choice[0:R, t, c], None).then_inc(scattered, 16)

        @block.tensor
        def _(pe):
            pe.sem_inc(mix_in_psum, 1)
            pe.wait_ge(k.w_out_loaded, 16)

            def turn(src, R, done):
                for c in range(DC):
                    mm = nc.tensor.transpose(pT[:, c // 4, (c % 4) * P:(c % 4) * P + R], src[0:R, c * P:(c + 1) * P],
                                             k.ident[0:R, 0:R])
                mm.then_inc(done, 1)

            def step(t, i, u, Rm, Rx, Rh):
                if Rm:
                    pe.wait_ge(mix_loaded, t * 16 + 48)
                    turn(mx, Rm, mix_in_psum)
                if Rh:
                    pe.wait_ge(scores_ready, t + 1)
                    pe.wait_ge(h_ready, t + 1)
                    for c in range(2):
                        mm = nc.tensor.transpose(pH[:, c * P:c * P + Rh], hs[0:Rh, c * P:(c + 1) * P], k.ident[0:Rh, 0:Rh])
                    mm.then_inc(h_in_psum, 1)
                if Rm:
                    pe.wait_ge(mixT_ready, t + 3)
                if Rx:
                    pe.wait_ge(x1_ready, t + 2)
                    turn(xs[1 - u], Rx, x1_in_psum)
                if Rh:
                    pe.wait_ge(hT_ready, t + 1)
                    pe.wait_ge(acc_ready, t + 1)
                    for n in range(2):
                        for c in range(2):
                            mm = nc.tensor.matmul(pD[0:Rh, n], hT[:, c, 0:Rh], sd[:, c, n * 512:(n + 1) * 512],
                                                  start=(c == 0), stop=(c == 1))
                    mm.then_inc(down_done, 1)
                if Rm:
                    pe.wait_ge(in_used, t + 3)
                    for n in range(2):
                        for c in range(DC):
                            mm = nc.tensor.matmul(pO[0:Rm, n], mT[:, c, 0:Rm], k.w_out[:, c, n * 512:(n + 1) * 512],
                                                  start=(c == 0), stop=(c == DC - 1))
                    mm.then_inc(proj_done, 1)
                if Rx:
                    pe.wait_ge(consts, 16 * 13)
                    pe.wait_ge(x1T_ready, t + 2)
                    for c in range(DC):
                        mm = nc.tensor.matmul(pG[0:Rx], xT[:, c, 0:Rx], sgu[:, c], start=(c == 0), stop=(c == DC - 1))
                    mm.then_inc(gu_done, 1)
                    for c in range(DC):
                        mm = nc.tensor.matmul(pR[0:Rx], xT[:, c, 0:Rx], wr[:, c], start=(c == 0), stop=(c == DC - 1))
                    mm.then_inc(router_done, 1)

            pipeline(pe, step)
            pe.wait_ge(dv, 1)
            m2 = mask[:].rearrange("p t e -> p (t e)")
            for i, (a, b) in enumerate(((0, 512), (512, (NT + 1) * NE))):
                nc.tensor.matmul(pT[:, i, 0:b - a], lt[:], m2[:, a:b], start=True, stop=True)
                mm = nc.tensor.matmul(pO[:, i, 0:b - a], k.ones[:], m2[:, a:b], start=True, stop=True)
            mm.then_inc(pp, 1)
            pe.wait_ge(dv, 2)
            nc.tensor.transpose(pR[0:1], be[:], k.ident[:]).then_inc(pp, 1)
            pe.wait_ge(slots_loaded, 16)
            for a in range(2):
                mm = nc.tensor.transpose(pG[:, a * P:a * P + NBLK], slots[:, :, a], k.ident[0:NBLK, 0:NBLK])
            mm.then_inc(pp, 1)

        @block.scalar
        def _(act):
            def turned(dst, R, done):
                for n in range(2):
                    nc.scalar.copy(dst[:, n * 4:n * 4 + 4, 0:R], pT[:, n, :].rearrange("p (c r) -> p c r", r=P)[:, :, 0:R])
                act.drain().then_inc(done, 1)

            def step(t, i, u, Rm, Rx, Rh):
                if Rm:
                    act.wait_ge(mix_in_psum, t + 4)
                    turned(mT, Rm, mixT_ready)
                if Rh:
                    act.wait_ge(h_in_psum, t + 1)
                    nc.scalar.copy(hT[:, :, 0:Rh], pH.rearrange("p (c r) -> p c r", r=P)[:, :, 0:Rh]).then_inc(hT_ready, 1)
                if Rx:
                    act.wait_ge(x1_in_psum, t + 2)
                    turned(xT, Rx, x1T_ready)
                    act.wait_ge(gu_done, t + 2)
                    nc.scalar.activation(eg[0:Rx], pG[0:Rx, 0:FE], ACT.Exp, scale=-1.0).then_inc(exp_ready, 1)
                    act.wait_ge(router_done, t + 2)
                    act.wait_ge(r_free, t + 2)
                    nc.scalar.activation(sc_[0:Rx], pR[0:Rx, 0:NE], ACT.Exp, scale=-1.0).then_inc(scores_ready, 1)

            pipeline(act, step)

        @block.vector
        def _(v):
            v.sem_inc(in_used, 1)
            v.sem_inc(acc_ready, 1)
            v.sem_inc(r_free, 1)
            v.sem_inc(x1_stored[0], 16)
            v.sem_inc(x1_stored[1], 16)
            v.sem_inc(acc_stored, 16)
            v.memset(mask[:], 0.0)
            v.memset(ef[:], 0.0)
            v.memset(choice[:], 0.0)
            v.memset(empty[:], 0.0)
            v.wait_ge(consts, 16 * 13)
            v.drain()
            nc.vector.tensor_scalar(empty[:, :, 0], io128[0:NBLK], float(NTOK), None, ALU.add)
            for c in range(TOPK):
                nc.vector.tensor_copy(choice[:, :, c, 0], tokf[:])
            v.drain()

            def e3(ap, shape):
                return bcast(ap, shape)

            def norm(t, half, xs, stored, R):
                v.wait_ge(proj_done, t + 1)
                v.wait_ge(xr_loaded, t * 16 + 16)
                v.wait_ge(stored, half * 16 + 16)
                nc.vector.scalar_tensor_tensor(out=xs[0:R], in0=xr[0:R], scalar=ALPHA, in1=pO[0:R].rearrange("p a b -> p (a b)"),
                                               op0=ALU.mult, op1=ALU.add)
                v.drain().then_inc(in_used, 1)
                for i in range(2):
                    nc.vector.bn_stats(stats[0:R, i, :], xs[0:R, i * 512:(i + 1) * 512])
                v.drain()
                nc.vector.bn_aggr(mv[0:R, :], stats[0:R])
                v.drain().then_inc(stats_ready, 1)
                v.wait_ge(rstd_ready, t + 1)
                nc.vector.tensor_scalar(xs[0:R, :], xs[0:R, :], mv[0:R, 0:1], rstd[0:R, 1:2], ALU.subtract, ALU.mult)
                v.drain()
                nc.vector.tensor_tensor(xs[0:R, :], xs[0:R, :], gain[0:R, :], ALU.mult)
                v.drain()
                nc.vector.tensor_tensor(xs[0:R, :], xs[0:R, :], bias[0:R, :], ALU.add)
                v.drain().then_inc(x1_ready, 1)

            def hidden(t, R):
                v.wait_ge(exp_ready, t + 1)
                nc.vector.tensor_scalar(eg[0:R], eg[0:R], 1.0, None, ALU.add)
                v.drain()
                nc.vector.reciprocal(eg[0:R], eg[0:R])
                v.drain()
                nc.vector.tensor_tensor(hs[0:R], eg[0:R], pG[0:R, 0:FE], ALU.mult)
                v.drain()
                nc.vector.tensor_tensor(hs[0:R], hs[0:R], pG[0:R, FE:2 * FE], ALU.mult)
                v.drain().then_inc(h_ready, 1)

            def choose(t, R):
                v.wait_ge(scores_ready, t + 1)
                nc.vector.tensor_scalar(sc_[0:R], sc_[0:R], 1.0, None, ALU.add)
                v.drain()
                nc.vector.reciprocal(sc_[0:R], sc_[0:R])
                v.drain()
                nc.vector.tensor_tensor(bi[0:R], sc_[0:R], rbias[0:R], ALU.add)
                v.drain()
                for gr in range(NGRP):
                    nc.vector.max(g8[0:R, gr], bi[0:R, gr * 8:gr * 8 + 8])
                v.drain()
                nc.vector.tensor_tensor(gs[0:R], g8[0:R, :, 0], g8[0:R, :, 1], ALU.add)
                v.drain()
                nc.vector.max(gt[0:R], gs[0:R])
                v.drain()
                nc.vector.max_index(gi[0:R], gt[0:R], gs[0:R])
                v.drain()
                nc.vector.tensor_copy(gif[0:R], gi[0:R])
                v.drain()
                nc.vector.tensor_tensor(gk[0:R], e3(io64[0:R, 0:8].rearrange("p (g a) -> p g a", a=1), [R, 8, KGRP]),
                                        e3(gif[0:R, 0:KGRP].rearrange("p (a j) -> p a j", a=1), [R, 8, KGRP]), ALU.is_equal)
                v.drain()
                nc.vector.tensor_reduce(keep[0:R], gk[0:R], AX.X, ALU.add)
                v.drain()
                b3 = bi[0:R].rearrange("p (g e) -> p g e", e=8)
                k3 = e3(keep[0:R].rearrange("p (g a) -> p g a", a=1), [R, 8, 8])
                nc.vector.tensor_tensor(b3, b3, k3, ALU.mult)
                nc.vector.tensor_scalar(gs[0:R], keep[0:R], 1.0, 1e30, ALU.subtract, ALU.mult)
                v.drain()
                nc.vector.tensor_tensor(b3, b3, e3(gs[0:R].rearrange("p (g a) -> p g a", a=1), [R, 8, 8]), ALU.add)
                v.drain()
                nc.vector.max(et[0:R], bi[0:R])
                v.drain()
                nc.vector.max_index(ei[0:R], et[0:R], bi[0:R])
                v.drain()
                efs = ef[0:R, bass.ds(t, 1)].rearrange("p a c -> p (a c)")
                nc.vector.tensor_copy(efs, ei[0:R, 0:TOPK])
                v.drain()
                i3 = e3(io64[0:R].rearrange("p (a e) -> p a e", a=1), [R, TOPK, NE])
                nc.vector.tensor_tensor(oh[0:R], i3, e3(ef[0:R, bass.ds(t, 1)].rearrange("p a c -> p c a"), [R, TOPK, NE]),
                                        ALU.is_equal)
                v.drain()
                nc.vector.tensor_reduce(mask[0:R, bass.ds(t, 1)].rearrange("p a e -> p (a e)"),
                                        oh[0:R].rearrange("p c e -> p e c"), AX.X, ALU.add)
                nc.vector.tensor_tensor(ohw[0:R], oh[0:R], e3(sc_[0:R].rearrange("p (a e) -> p a e", a=1), [R, TOPK, NE]), ALU.mult)
                v.drain().then_inc(r_free, 1)
                wt = choice[0:R, bass.ds(t, 1), :, 1].rearrange("p a c -> p (a c)")
                nc.vector.tensor_reduce(wt, ohw[0:R], AX.X, ALU.add)
                v.drain()
                nc.vector.tensor_reduce(ws[0:R, 0:1], wt, AX.X, ALU.add)
                v.drain()
                nc.vector.reciprocal(ws[0:R, 1:2], ws[0:R, 0:1])
                v.drain()
                nc.vector.tensor_scalar(wt, wt, ws[0:R, 1:2], 2.5, ALU.mult, ALU.mult)
                v.drain()

            def add_shared(t, xs, R):
                v.wait_ge(down_done, t + 1)
                v.wait_ge(acc_stored, t * 16 + 16)
                nc.vector.scalar_tensor_tensor(out=acc[0:R], in0=xs[0:R], scalar=ALPHA, in1=pD[0:R].rearrange("p a b -> p (a b)"),
                                               op0=ALU.mult, op1=ALU.add)
                v.drain().then_inc(acc_ready, 1)

            def step(t, i, u, Rm, Rx, Rh):
                if Rh:
                    add_shared(t, xs[u], Rh)
                if Rm:
                    norm(t + 2, i + 1, xs[u], x1_stored[u], Rm)
                if Rx:
                    hidden(t + 1, Rx)
                    choose(t + 1, Rx)

            pipeline(v, step)
            v.drain().then_inc(dv, 1)
            v.wait_ge(pp, 1)
            TE = (NT + 1) * NE
            d2 = dst[:].rearrange("p t e -> p (t e)")
            p2 = pre[:].rearrange("p t e -> p (t e)")
            nc.vector.tensor_copy(d2[:, 0:512], pT[:, 0])
            nc.vector.tensor_copy(d2[:, 512:TE], pT[:, 1, 0:TE - 512])
            v.memset(pre[:, 0], 0.0)
            v.drain()
            for t in range(NT):
                src = pO[:, 0, t * NE:(t + 1) * NE] if t < 8 else pO[:, 1, 0:NE]
                nc.vector.tensor_tensor(pre[:, t + 1], pre[:, t], src, ALU.add)
                v.drain()
            nc.vector.tensor_tensor(d2, d2, p2, ALU.add)
            nc.vector.tensor_tensor(ble[:], pre[:, NT], pO[:, 1, 0:NE], ALU.add)
            v.drain()
            nc.vector.tensor_tensor(cmp_[:], e3(ble[:].rearrange("p (e a) -> p e a", a=1), [P, NE, 16]),
                                    e3(thr[:].rearrange("p (a j) -> p a j", a=1), [P, NE, 16]), ALU.is_gt)
            v.drain()
            nc.vector.tensor_reduce(nbl[:], cmp_[:], AX.X, ALU.add)
            v.drain()
            nc.vector.tensor_tensor_scan(incl[:], k.ones[:, 0:NE], nbl[:], 0.0, ALU.mult, ALU.add)
            v.drain()
            nc.vector.tensor_tensor(nbl[:], incl[:], nbl[:], ALU.subtract)
            nc.vector.tensor_scalar(ble[:], incl[:], ip[:, 0:1], None, ALU.is_le)
            v.drain()
            nc.vector.tensor_reduce(be[:], ble[:], AX.X, ALU.add)
            nc.vector.tensor_scalar(nbl[:], nbl[:], float(P), None, ALU.mult)
            v.drain()
            nc.vector.tensor_scalar(be[:], be[:], float(NE - 1), None, ALU.min)
            v.drain().then_inc(dv, 1)
            nc.vector.tensor_tensor(dst[:], dst[:], e3(nbl[:].rearrange("p (a e) -> p a e", a=1), [P, NT + 1, NE]), ALU.add)
            v.drain()
            for t in range(NT + 1):
                nc.vector.tensor_tensor(oh[:], e3(io64[:].rearrange("p (a e) -> p a e", a=1), [P, TOPK, NE]),
                                        e3(ef[:, t].rearrange("p (c a) -> p c a", a=1), [P, TOPK, NE]), ALU.is_equal)
                v.drain()
                nc.vector.tensor_tensor(oh[:], oh[:], e3(dst[:, t].rearrange("p (a e) -> p a e", a=1), [P, TOPK, NE]), ALU.mult)
                v.drain()
                nc.vector.tensor_reduce(dstf[:, t], oh[:], AX.X, ALU.add)
                v.drain()
                nc.vector.tensor_copy(dest[:, t], dstf[:, t]).then_inc(dest_ready, 1)
            v.wait_ge(pp, 2)
            nc.vector.tensor_copy(k.plan[:, 0:NBLK], pR[0:1, 0:NBLK])
            nc.vector.tensor_copy(k.plan[:, P - 1:P], incl[0:1, NE - 1:NE])
            nc.vector.tensor_scalar(half_counts[:, 0:NBLK // 2], io64[0:1, 0:NBLK // 2], 2.0, incl[0:1, NE - 1:NE], ALU.mult, ALU.is_lt)
            v.drain()
            nc.vector.tensor_reduce(ws[0:1, 0:1], half_counts[:, 0:NBLK // 2], AX.X, ALU.add)
            v.drain()
            nc.vector.tensor_tensor(ws[0:1, 1:2], incl[0:1, NE - 1:NE], ws[0:1, 0:1], ALU.subtract)
            v.drain()
            nc.vector.tensor_copy(k.plan[:, P - 3:P - 1], ws[0:1, 0:2])
            v.wait_ge(pp, 3)
            nc.vector.tensor_copy(k.toks[:, 0:NBLK], pG[:, 0:NBLK])
            nc.vector.tensor_copy(k.slot_w[:], pG[:, P:P + NBLK])


def experts(nc, k, d):
    with ExitStack() as ctx:
        def sb(name, shape, dt=F32):
            return ctx.enter_context(nc.sbuf_tensor(name, shape, dt))

        def ps(name, shape):
            return ctx.enter_context(nc.psum_tensor(name, shape, F32))

        def sem(name):
            k.sems.append(ctx.enter_context(nc.semaphore(name)))
            return k.sems[-1]

        def two(make, name, *a):
            return [make(f"{name}{u}", *a) for u in range(2)]

        wg, wu, wd = two(sb, "e_gate", [P, DC, FE]), two(sb, "e_up", [P, DC, FE]), two(sb, "e_down", [P, 2, D])
        xg, xT = two(sb, "e_x", [P, D]), two(sb, "e_xT", [P, DC, P])
        gather_rows, add_rows = two(sb, "gather_rows", [P, 1], I32), two(sb, "add_rows", [P, 1], I32)
        sg, hT, ysb = two(sb, "e_silu", [P, 2 * P]), two(sb, "e_hT", [P, 2 * P]), two(sb, "e_y", [P, 2, 512])
        pT = ps("e_pT", [P, 2, 512])
        pG, pY = two(ps, "e_pG", [P, 512]), two(ps, "e_pY", [P, 2, 512])

        gu_loaded, down_loaded, gathered = two(sem, "gu_loaded"), two(sem, "down_loaded"), two(sem, "x_gathered")
        y_added, ysb_free = sem("y_added"), sem("ysb_free")
        x_turned, xT_act, xT_dve, gu_done, silu_ready, h_ready, down_done, y_act, y_dve = (
            sem(n) for n in ("x_turned", "xT_act", "xT_dve", "e_gu_done", "e_silu_ready", "e_h_ready", "e_down_done", "y_act", "y_dve"))
        block = ctx.enter_context(nc.Block())

        def number_of_blocks(eng):
            return plan_entry(eng, P - 1, 1, NBLK)

        def plan_entry(eng, at, low, high):
            return eng.value_load(k.plan[0:1, at:at + 1], min_val=low, max_val=high)

        @block.sync
        def _(sp):
            nb = number_of_blocks(sp)

            def load(n, i, u):
                e = sp.value_load(k.plan[0:1, bass.ds(n, 1)], min_val=0, max_val=NE - 1)
                rows = bass.ds(e * P, P)
                sp.wait_ge(gu_done, n + 1)
                sp.dma_start(wg[u][:].rearrange("p c f -> p (c f)"), d["exp_gate"][rows]).then_inc(gu_loaded[u], 16)
                sp.dma_start(wu[u][:].rearrange("p c f -> p (c f)"), d["exp_up"][rows]).then_inc(gu_loaded[u], 16)
                sp.wait_ge(down_done, n + 1)
                sp.dma_start(wd[u][:].rearrange("p c f -> p (c f)"), d["exp_down"][rows]).then_inc(down_loaded[u], 16)

            load(0, 0, 0)
            load(1, 0, 1)
            with sp.Fori(0, NBLK // 2) as i:
                for u in range(2):
                    n = i * 2 + u
                    with sp.If(nb > n + 2):
                        load(n + 2, i + 1, u)

        @block.gpsimd
        def _(g):
            nb = number_of_blocks(g)

            def gather(n, u):
                nc.gpsimd.tensor_copy(gather_rows[u][:], k.toks[:, bass.ds(n, 1)])
                g.drain()
                g.indirect_dma_start(xg[u][:], None, d["x1"], bass.IndirectOffsetOnAxis(gather_rows[u][:], 0)
                                     ).then_inc(gathered[u], 16)

            def add(n, u, first=False):
                if not first:
                    g.wait_ge(y_added, n * 16)
                    g.sem_inc(ysb_free, 1)
                g.wait_ge(y_act, n + 1)
                g.nop()
                g.wait_ge(y_dve, n + 1)
                g.nop()
                nc.gpsimd.tensor_copy(add_rows[u][:], k.toks[:, bass.ds(n, 1)])
                g.drain()
                g.indirect_dma_start(d["acc"], bass.IndirectOffsetOnAxis(add_rows[u][:], 0), ysb[u][:].rearrange("p a b -> p (a b)"),
                                     None, compute_op=ALU.add).then_inc(y_added, 16)

            def block_pair(i, first=False):
                for u in range(2):
                    n = i * 2 + u
                    with g.If(nb > n + 3):
                        g.wait_ge(x_turned, n + 4)
                        g.nop()
                        gather(n + 3, 1 - u)
                    with g.If(nb > n):
                        add(n, u, first and u == 0)

            gather(0, 0)
            gather(1, 1)
            g.wait_ge(x_turned, 3)
            gather(2, 0)
            block_pair(0, first=True)
            with g.Fori(1, NBLK // 2) as i:
                block_pair(i)
            g.wait_ge(y_added, nb * 16)
            g.nop()

        @block.tensor
        def _(pe):
            pe.sem_inc(x_turned, 2)
            pe.sem_inc(gu_done, 2)
            pe.sem_inc(down_done, 2)
            nb = number_of_blocks(pe)

            def turn(n, i, u):
                pe.wait_ge(gathered[u], i * 16 + 16)
                x8 = xg[u][:].rearrange("s (p c) -> s c p", c=DC)
                for c in range(DC):
                    mm = nc.tensor.transpose(pT[:, c // 4, (c % 4) * P:(c % 4 + 1) * P], x8[:, c], k.ident[:])
                mm.then_inc(x_turned, 1)

            def gate_up(n, i, u):
                pe.wait_ge(xT_act, n + 1)
                pe.wait_ge(xT_dve, n + 1)
                pe.wait_ge(gu_loaded[u], i * 32 + 32)
                for w, at in ((wg, 0), (wu, 2 * P)):
                    for f in range(2):
                        for c in range(DC):
                            mm = nc.tensor.matmul(pG[u][:, at + f * P:at + (f + 1) * P], w[u][:, c, f:FE:2], xT[u][:, c],
                                                  start=(c == 0), stop=(c == DC - 1))
                mm.then_inc(gu_done, 1)

            def down(n, i, u):
                pe.wait_ge(h_ready, n + 1)
                pe.wait_ge(down_loaded[u], i * 16 + 16)
                for h in range(2):
                    for f in range(2):
                        mm = nc.tensor.matmul(pY[u][:, h], hT[u][:, f * P:(f + 1) * P], wd[u][:, f, h * 512:(h + 1) * 512],
                                              start=(f == 0), stop=(f == 1))
                mm.then_inc(down_done, 1)

            turn(0, 0, 0)
            gate_up(0, 0, 0)
            with pe.Fori(0, NBLK // 2) as i:
                for u in range(2):
                    n = i * 2 + u
                    nxt = i + u
                    with pe.If(nb > n):
                        with pe.If(nb > n + 1):
                            turn(n + 1, nxt, 1 - u)
                        down(n, i, u)
                        with pe.If(nb > n + 1):
                            gate_up(n + 1, nxt, 1 - u)

        def x_half(eng, copy, done, h, n, u):
            eng.wait_ge(x_turned, n + 3)
            copy(xT[u][:, h * 4:h * 4 + 4], pT[:, h].rearrange("p (c r) -> p c r", r=P)).then_inc(done, 1)

        def y_ready(eng, n):
            eng.wait_ge(down_done, n + 3)
            eng.wait_ge(ysb_free, n + 1)

        @block.scalar
        def _(act):
            nb = number_of_blocks(act)

            def silu(n, u):
                act.wait_ge(gu_done, n + 3)
                nc.scalar.activation(sg[u][:], pG[u][:, 0:2 * P], ACT.Silu).then_inc(silu_ready, 1)

            x_half(act, nc.scalar.copy, xT_act, 0, 0, 0)
            silu(0, 0)
            with act.Fori(0, NBLK // 2) as i:
                for u in range(2):
                    n = i * 2 + u
                    with act.If(nb > n):
                        with act.If(nb > n + 1):
                            x_half(act, nc.scalar.copy, xT_act, 0, n + 1, 1 - u)
                        y_ready(act, n)
                        nc.scalar.activation(ysb[u][:, 0], pY[u][:, 0], ACT.Copy, scale=k.slot_w[:, bass.ds(n, 1)]).then_inc(y_act, 1)
                        with act.If(nb > n + 1):
                            silu(n + 1, 1 - u)

        @block.vector
        def _(v):
            v.sem_inc(ysb_free, 2)
            nb = number_of_blocks(v)

            def hidden(n, u):
                v.wait_ge(silu_ready, n + 1)
                nc.vector.tensor_tensor(hT[u][:], sg[u][:], pG[u][:, 2 * P:4 * P], ALU.mult).then_inc(h_ready, 1)

            x_half(v, nc.vector.tensor_copy, xT_dve, 1, 0, 0)
            hidden(0, 0)
            with v.Fori(0, NBLK // 2) as i:
                for u in range(2):
                    n = i * 2 + u
                    with v.If(nb > n):
                        with v.If(nb > n + 1):
                            x_half(v, nc.vector.tensor_copy, xT_dve, 1, n + 1, 1 - u)
                        y_ready(v, n)
                        nc.vector.tensor_scalar(ysb[u][:, 1], pY[u][:, 1], k.slot_w[:, bass.ds(n, 1)], None, ALU.mult).then_inc(y_dve, 1)
                        with v.If(nb > n + 1):
                            hidden(n + 1, 1 - u)


def finish(nc, k, d):
    with ExitStack() as ctx:
        def sb(name, shape, dt=F32):
            return ctx.enter_context(nc.sbuf_tensor(name, shape, dt))

        def sem(name):
            k.sems.append(ctx.enter_context(nc.semaphore(name)))
            return k.sems[-1]

        gain, bias = sb("ln2_g_sb", [P, D]), sb("ln2_b_sb", [P, D])
        acc, out = sb("f_acc", [P, NT + 1, D]), sb("f_out", [P, NT + 1, D])
        stats, mv, rstd = sb("stats2", [P, 2, 2, 6]), sb("mv2", [P, NT + 1, 2]), sb("rstd2", [P, NT + 1])
        shift, eps, mhalf = sb("shift2", [P, NT + 1]), sb("eps2", [P, 1]), sb("mhalf2", [P, 1])
        consts, mv_ready, rstd_ready, shift_ready, normed, scaled, out_ready, out_stored = (
            sem(n) for n in ("f_consts", "f_mv_ready", "f_rstd_ready", "f_shift_ready", "f_normed", "f_scaled", "f_out_ready", "f_out_stored"))
        acc_loaded = [sem(f"f_acc_loaded{t}") for t in range(NT + 1)]
        block = ctx.enter_context(nc.Block())
        rows = [P] * NT + [NS]

        @block.sync
        def _(sp):
            for t, R in enumerate(rows):
                sp.dma_start(acc[0:R, t], d["acc"][t * P:t * P + R]).then_inc(acc_loaded[t], 16)
                if t == 0:
                    sp.dma_start(gain[:], bcast(d["ln2_g"], [P, D])).then_inc(consts, 16)
                    sp.dma_start(bias[:], bcast(d["ln2_b"], [P, D])).then_inc(consts, 16)
            for t, R in enumerate(rows):
                sp.wait_ge(out_ready, t + 1)
                dst = d["y_prompt"][t * P:t * P + P] if t < NT else d["y_sample"]
                sp.dma_start(dst, out[0:R, t]).then_inc(out_stored, 16)
            sp.wait_ge(out_stored, 16 * (NT + 1))

        @block.gpsimd
        def _(g):
            g.memset(eps[:], EPS)
            g.memset(mhalf[:], -0.5)
            g.drain()

            def inv_std(t, R):
                g.wait_ge(mv_ready, t + 1)
                nc.gpsimd.tensor_tensor(rstd[0:R, t:t + 1], mv[0:R, t, 1:2], eps[0:R, :], ALU.add)
                g.drain()
                nc.gpsimd.tensor_tensor(rstd[0:R, t:t + 1], rstd[0:R, t:t + 1], mhalf[0:R, :], ALU.pow).then_inc(rstd_ready, 1)

            def add_bias(t, R):
                g.wait_ge(consts, 32)
                g.wait_ge(scaled, t + 1)
                nc.gpsimd.tensor_tensor(out[0:R, t], out[0:R, t], bias[0:R], ALU.add).then_inc(out_ready, 1)

            inv_std(0, P)
            for t, R in enumerate(rows):
                if t < NT:
                    inv_std(t + 1, rows[t + 1])
                add_bias(t, R)

        @block.scalar
        def _(act):
            for t, R in enumerate(rows):
                act.wait_ge(shift_ready, t + 1)
                nc.scalar.activation(out[0:R, t], acc[0:R, t], ACT.Identity, bias=shift[0:R, t:t + 1], scale=rstd[0:R, t:t + 1]
                                     ).then_inc(normed, 1)

        @block.vector
        def _(v):
            def stats_of(t, R):
                v.wait_ge(acc_loaded[t], 16)
                for i in range(2):
                    nc.vector.bn_stats(stats[0:R, t % 2, i, :], acc[0:R, t, i * 512:(i + 1) * 512])
                v.drain()
                nc.vector.bn_aggr(mv[0:R, t], stats[0:R, t % 2])
                v.drain().then_inc(mv_ready, 1)

            def shift_of(t, R):
                v.wait_ge(rstd_ready, t + 1)
                nc.vector.scalar_tensor_tensor(out=shift[0:R, t:t + 1], in0=mv[0:R, t, 0:1], scalar=-1.0, in1=rstd[0:R, t:t + 1],
                                               op0=ALU.mult, op1=ALU.mult).then_inc(shift_ready, 1)

            def gain_of(t, R):
                v.wait_ge(consts, 32)
                v.wait_ge(normed, t + 1)
                nc.vector.tensor_tensor(out[0:R, t], out[0:R, t], gain[0:R], ALU.mult).then_inc(scaled, 1)

            for t in range(NT + 3):
                if t <= NT:
                    stats_of(t, rows[t])
                if 1 <= t <= NT + 1:
                    shift_of(t - 1, rows[t - 1])
                if t >= 2:
                    gain_of(t - 2, rows[t - 2])



def more_constants():
    i=np.arange(P)
    j = np.arange(2 * NT)
    vis = (j[None, :] + 1) * 64 - 1 <= np.arange(SEQ)[:, None]
    vis = vis.reshape(NT, P, 2 * NT).transpose(1, 0, 2)
    return {
        "mask_diag": np.where(i[None, :] <= i[:, None], 0.0, NEG), "cmp_vis": vis, "cmp_mask": np.where(vis, 0.0, NEG),
        "spread16": np.arange(16)[:, None] == i[None, :] % 16, "slot_mask": i[:, None] // 16 == np.arange(8)[None, :],
        "grp4": np.arange(64)[:, None] // 4 == np.arange(16)[None, :],
        "pick_bg": (np.arange(16)[:, None, None] // 2 == i[None, None, :] // NJ) & (np.arange(16)[:, None, None] % 2 == np.arange(2)[None, :, None]),
        "e8": np.arange(8)[:, None] == i[None, :] // NJ, "e8t": i[:, None] // NJ == np.arange(8)[None, :],
        "jmask": i[:, None] % NJ == np.arange(NJ)[None, :], "iota": np.broadcast_to(i, (P, P)),
        "parity": np.broadcast_to(i % 2, (P, P)), "wmask": np.where(i % NJ == NJ - 1, 0.0, NEG)[:, None],
        "mask_lt": i[:, None] < i[None, :], "iota_p": i[:, None],
        "block_starts": np.broadcast_to(np.arange(16) * P, (P, 16)),
        "token_ids": np.arange(NT + 1)[None, :] * P + i[:, None],
        "mask_neg": np.where(i[:, None] <= i[None, :], 0.0, NEG),
        "expand_h": np.arange(NH)[:, None] == np.arange(512)[None, :] // HD,
    }
def more_inputs(a, r):
    return {
        "conv_w": a["conv_w"][0].reshape(4, DC, P).transpose(2, 1, 0), "conv_b": a["conv_b"][0].reshape(DC, P).T,
        "dt_bias": a["dt_bias"], "a_log": a["a_log"], "d_skip": a["d_skip"], "ssd_norm_w": a["ssd_norm_w"],
        "state_conv": a["state_conv"][0].reshape(NS, 3, DC, P).transpose(3, 2, 1, 0),
        "state_conv_rows": a["state_conv"][0], "state_ssm": a["state_ssm"][0].reshape(NS, NH * HD, P),
        "cache_kv_win": a["cache_kv_win"][0].reshape(NS, 512, KV),
        "cache_kv_sel": a["cache_kv_sel"][0].reshape(-1, QR * KV),
        "w_out": np.concatenate([a["w_out"][0][0:512], a["w_out"][0][r]]), "ln1_g": a["ln1_g"], "ln1_b": a["ln1_b"],
        "router_w": np.concatenate([a["router_w"][0], np.zeros((D, P - NE), np.float32)], 1), "router_bias": a["router_bias"],
        "sh_gate": a["sh_w_gate"][0], "sh_up": a["sh_w_up"][0], "sh_down": a["sh_w_down"][0],
        "exp_gate": a["exp_w_gate"][0].reshape(NE * P, DC * FE), "exp_up": a["exp_w_up"][0].reshape(NE * P, DC * FE),
        "exp_down": a["exp_w_down"][0].reshape(NE * P, 2 * D), "ln2_g": a["ln2_g"], "ln2_b": a["ln2_b"],
        "page_table": a["page_table"].reshape(1, NS * NPAGE), "cache_kv_cmp": (a["cache_kv_cmp"][0].reshape(-1, 2, 64, 2, 2, 2, HD // 2)
                         .transpose(0, 5, 2, 6, 3, 1, 4).reshape(-1, KV)),
        "pe_page": (np.broadcast_to(a["cmp_pe"][0].reshape(1, 1, 2, 64, 2, HD // 2), (2, 2, 2, 64, 2, HD // 2))
                    .transpose(4, 3, 0, 2, 1, 5).reshape(P, KV)),
        "cmp_w1": a["cmp_w1"][0].reshape(2, 64, 2, HD // 2, P).transpose(2, 1, 0, 3, 4).reshape(P, 2, HD // 2, P),
        "cmp_w2": a["cmp_w2"][0], "cmp_b1": a["cmp_b1"][0].T,
        "cmp_b2k": np.tile(a["cmp_b2"][0, 0], 2)[:, None], "cmp_b2v": a["cmp_b2"][0, 1:2],
    }
STEPS = [project, ssd, compress, attend, sample, route, experts, finish]


OUTS = [
    ("y_prompt", (1, SEQ, D)), ("y_sample", (NS, 1, D)),
    ("kv_cmp_prompt", (1, 1, SEQ, 2, 2, HD)), ("kv_sel_prompt", (1, 1, SEQ, 2, 2, HD)),
    ("kv_win_prompt", (1, 1, 512, 2, 2, HD)), ("ssm_prompt", (1, 1, NH, HD, P)),
    ("conv_prompt", (1, 1, 3, D)),
    ("kv_cmp_sample", (1, NS, 1, 2, 2, HD)), ("kv_sel_sample", (1, NS, 1, 2, 2, HD)),
    ("kv_win_sample", (1, NS, 512, 2, 2, HD)), ("ssm_sample", (1, NS, NH, HD, P)),
    ("conv_sample", (1, NS, 3, D)),
]
FORMS = {
    "y_prompt": (SEQ, D), "y_sample": (NS, D), "kv_cmp_prompt": (SEQ, KV), "kv_sel_prompt": (SEQ, KV),
    "kv_win_prompt": (512, KV), "ssm_prompt": (NH * HD, P), "conv_prompt": (3, D), "kv_cmp_sample": (NS, KV),
    "kv_sel_sample": (NS, KV), "kv_win_sample": (NS, 512, KV), "ssm_sample": (NS, NH * HD, P),
    "conv_sample": (NS, 3, D),
}
SCRATCH = {
    "xres": (NTOK, D), "z_silu": (NTOK, 512), "kv_win_all": (NTOK, KV), "mix": (NTOK, D), "x1": (NTOK + P, D),
    "acc": (NTOK + P, D), "slot_rows": (NBLK * P, 2),
}


def constants():
    i = np.arange(P)
    inv = (500000.0 ** (-np.arange(RH, dtype=np.float32) / RH)).astype(np.float32)
    pos = np.concatenate([np.arange(SEQ), np.full(P, PAST)]).astype(np.float32)
    ang = pos[:, None] * inv[None]
    cos, sin = np.cos(ang), np.sin(ang)

    def by_tile(a):
        return np.ascontiguousarray(a.reshape(NT + 1, P, -1).transpose(1, 0, 2)).astype(np.float32)

    out = {
        "ident": np.eye(P), "mask_le": i[:, None] <= i[None, :], "ones": np.ones((P, P)),
        "rope_c": by_tile(np.concatenate([cos, cos], 1)), "rope_s": by_tile(np.concatenate([-sin, sin], 1)),
    }
    out.update(more_constants())
    return {n: np.ascontiguousarray(a).astype(np.float32) for n, a in out.items()}


def laid_out(a):
    cols = np.cumsum([0, 512, 1024, 8, 512, 128, 128, 128, 128, 128, 128, 24])
    z, xbc, dt, q, kc, vc, ks, vs, kw, vw, g = (np.arange(cols[n], cols[n + 1]) for n in range(11))
    pair = np.array([g_ * GQA + c for c in range(GQA) for g_ in range(2)])
    q = q.reshape(NH, HD)[pair].ravel()
    g = g.reshape(NH, 3)[pair].T.ravel()
    order = np.concatenate([q, kc, vc, ks, vs, kw, vw, g, dt, z, xbc])
    nsa_rows = 512 + (pair[:, None] * HD + np.arange(HD)).ravel()
    c = np.ascontiguousarray
    out = {
        "x": np.concatenate([a["x_prompt"].reshape(SEQ, D), a["x_sample"].reshape(NS, D)]),
        "w_in": c(a["w_in"][0][:, order]),
        "emb_ln_g": a["emb_ln_g"][None], "emb_ln_b": a["emb_ln_b"][None],
    }
    out.update(more_inputs(a, nsa_rows))
    return {n: c(v) for n, v in out.items()}


def build(nc, d, phases=99):
    with ExitStack() as ctx:
        k = persistent(nc, ctx)
        steps = STEPS[:phases]
        alloc_routing(nc, ctx, k)
        with ExitStack() as until_routed:
            alloc_room(nc, until_routed, k)
            with ExitStack() as kept:
                alloc_kept(nc, kept, k)
                with ExitStack() as early:
                    alloc_xbc(nc, early, k)
                    for step in steps[:2]:
                        step(nc, k, d)
                for step in steps[2:5]:
                    step(nc, k, d)
            for step in steps[5:6]:
                step(nc, k, d)
        for step in steps[6:]:
            if step is experts:
                for s in k.sems[:len(k.sems) // 2]:
                    nc.sync.sem_clear(s)
                nc.all_engine_barrier()
            step(nc, k, d)


def kernel(**inputs):
    import concourse.bacc as bacc
    from concourse.bass_utils import run_bass_kernel_spmd

    a = {n: np.asarray(v) for n, v in inputs.items()}
    arrays = laid_out(a)
    arrays.update(constants())
    nc = bacc.Bacc("TRN2", target_bir_lowering=False, num_devices=1)
    d = {n: nc.dram_tensor("i_" + n, v.shape, mybir.dt.from_np(v.dtype), kind="ExternalInput").ap()
         for n, v in arrays.items()}
    for name, shape in FORMS.items():
        d[name] = nc.dram_tensor("o_" + name, shape, F32, kind="ExternalOutput").ap()
    for name, shape in SCRATCH.items():
        d[name] = nc.dram_tensor("s_" + name, shape, F32, kind="Internal").ap()
    build(nc, d)
    got = run_bass_kernel_spmd(nc, [{"i_" + n: v for n, v in arrays.items()}], core_ids=[0]).results[0]
    return tuple(got["o_" + name].reshape(shape) for name, shape in OUTS)
```
